# Optimizing a Trainium2 kernel written in Bass

```python
import jax, jax.numpy as jnp
from jax import lax
import numpy as np

D_MODEL = 1024
BATCH = 1
SEQ = 2048
DEPTH = 1
DEC_BATCH = 8
DEC_SEQ = 8
PAST_LEN = 1024
PAGE_SIZE = 128

DILATED_GROUPS = ((128, 1), (512, 4), (2048, 16))
N_GROUPS = 3
HEADS_PER_GROUP = 4
HEAD_DIM_A = 64
N_HEADS_A = N_GROUPS * HEADS_PER_GROUP
WIDTH_A = N_HEADS_A * HEAD_DIM_A
STEPS_BACK = 128
A_BLOCK = 128

N_HEADS_B = 6
HEAD_DIM_B = 128
WIDTH_B = N_HEADS_B * HEAD_DIM_B
CONV_WIDTH = 4
CONV_DIM = 3 * WIDTH_B
GDN_CHUNK = 64

COL_QA = 0
COL_KA = COL_QA + WIDTH_A
COL_VA = COL_KA + WIDTH_A
COL_ZA = COL_VA + WIDTH_A
COL_QKVB = COL_ZA + WIDTH_A
COL_ZB = COL_QKVB + CONV_DIM
COL_AB = COL_ZB + WIDTH_B
COL_BB = COL_AB + N_HEADS_B
COL_GA = COL_BB + N_HEADS_B
COL_GB = COL_GA + D_MODEL
IN_WIDTH = COL_GB + D_MODEL

DEEPNORM_ALPHA = (2 * DEPTH) ** 0.25
DEEPNORM_BETA = (8 * DEPTH) ** -0.25
LN_EPS = 1e-5
RMS_EPS = 1e-6

kernel_name = 'dilated_swa_gated_deltanet_hybrid_step'

def alibi_slopes():
    i = jnp.arange(1, N_HEADS_A + 1, dtype=jnp.float32)
    return jnp.exp2(-8.0 * i / N_HEADS_A).reshape(N_GROUPS, HEADS_PER_GROUP)

def layer_norm(x, g, b):
    xf = x.astype(jnp.float32)
    mu = xf.mean(-1, keepdims=True)
    var = jnp.mean(jnp.square(xf - mu), -1, keepdims=True)
    return ((xf - mu) * lax.rsqrt(var + LN_EPS) * g.astype(jnp.float32) + b.astype(jnp.float32)).astype(x.dtype)

def l2norm(x):
    return x * lax.rsqrt(jnp.sum(jnp.square(x), -1, keepdims=True) + RMS_EPS)

def softmax_with_lse(s):
    m = s.max(-1, keepdims=True)
    p = jnp.exp(s - m)
    den = p.sum(-1, keepdims=True)
    return p / den, (m + jnp.log(den))[..., 0]

def dilated_group_prompt(q, k, v, dilation, slopes):
    B, S, H, dh = q.shape
    L = S // dilation
    nblk = -(-L // A_BLOCK)
    Lp = nblk * A_BLOCK

    def to_sub(t):
        t = t.reshape(B, L, dilation, H, dh).transpose(0, 2, 1, 3, 4)
        t = jnp.pad(t, ((0, 0), (0, 0), (0, Lp - L), (0, 0), (0, 0)))
        return t.reshape(B, dilation, nblk, A_BLOCK, H, dh)

    def with_prev(t):
        prev = jnp.pad(t[:, :, :-1], ((0, 0), (0, 0), (1, 0), (0, 0), (0, 0), (0, 0)))
        return jnp.concatenate([prev, t], axis=3)

    qs = to_sub(q)
    kk = with_prev(to_sub(k))
    vv = with_prev(to_sub(v))
    s = jnp.einsum('brnqhd,brnkhd->brnhqk', qs, kk, preferred_element_type=jnp.float32) * (dh ** -0.5)
    qi = jnp.arange(A_BLOCK)[:, None]
    kj = jnp.arange(2 * A_BLOCK)[None, :]
    steps = A_BLOCK + qi - kj
    blk = jnp.arange(nblk)[:, None, None]
    valid = (steps >= 0) & (steps <= STEPS_BACK) & (blk * A_BLOCK + kj - A_BLOCK >= 0)
    s = s - slopes[:, None, None] * (steps * dilation).astype(jnp.float32)
    s = jnp.where(valid[:, None], s, -jnp.inf)
    p, lse = softmax_with_lse(s)
    o = jnp.einsum('brnhqk,brnkhd->brnqhd', p, vv.astype(jnp.float32))
    o = o.reshape(B, dilation, Lp, H, dh)[:, :, :L].transpose(0, 2, 1, 3, 4).reshape(B, S, H, dh)
    lse = lse.transpose(0, 1, 2, 4, 3).reshape(B, dilation, Lp, H)[:, :, :L]
    lse = lse.transpose(0, 2, 1, 3).reshape(B, S, H)
    return o.astype(q.dtype), lse

def dilated_group_sample(q, k, v, kv_buf, dilation, slopes):
    B, T, H, dh = q.shape
    Lb = kv_buf.shape[1]
    steps = jnp.arange(STEPS_BACK + 1)
    idx = Lb + jnp.arange(T)[:, None] - steps[None, :] * dilation
    valid = idx >= 0
    new_kv = jnp.stack([k, v], axis=2)
    from_buf = jnp.take(kv_buf, jnp.clip(idx, 0, Lb - 1), axis=1).astype(k.dtype)
    from_new = jnp.take(new_kv, jnp.clip(idx - Lb, 0, T - 1), axis=1)
    kvg = jnp.where((idx < Lb)[None, :, :, None, None, None], from_buf, from_new)
    s = jnp.einsum('bthd,btjhd->bhtj', q, kvg[:, :, :, 0], preferred_element_type=jnp.float32) * (dh ** -0.5)
    s = s - slopes[:, None, None] * (steps * dilation).astype(jnp.float32)
    s = jnp.where(valid, s, -jnp.inf)
    p, lse = softmax_with_lse(s)
    o = jnp.einsum('bhtj,btjhd->bthd', p, kvg[:, :, :, 1].astype(jnp.float32))
    return o.astype(q.dtype), lse.transpose(0, 2, 1), new_kv

def combine_groups(outs, lses):
    alpha = jax.nn.softmax(jnp.stack(lses, 0), axis=0)
    o = jnp.stack(outs, 0) * alpha[..., None].astype(outs[0].dtype)
    G, B, T, H, dh = o.shape
    return o.transpose(1, 2, 0, 3, 4).reshape(B, T, G * H * dh)

def short_conv(u, buf, w):
    T = u.shape[1]
    ext = jnp.concatenate([buf.astype(u.dtype), u], axis=1)
    out = ext[:, 0:T] * w[0]
    for i in range(1, CONV_WIDTH):
        out = out + ext[:, i:i + T] * w[i]
    return jax.nn.silu(out), ext[:, T:]

def gated_delta_rule(q, k, v, g, beta, S0):
    B, T, H, dk = q.shape
    dv = v.shape[-1]
    C = GDN_CHUNK
    n = -(-T // C)
    pad = n * C - T

    def chunks(t):
        t = jnp.pad(t, ((0, 0), (0, pad)) + ((0, 0),) * (t.ndim - 2))
        t = t.reshape((B, n, C) + t.shape[2:])
        return jnp.moveaxis(jnp.moveaxis(t, 3, 2), 1, 0)

    qc, kc, vc, gc, bc = chunks(q), chunks(k), chunks(v), chunks(g), chunks(beta)
    G = jnp.cumsum(gc, axis=-1)
    causal = jnp.tril(jnp.ones((C, C), dtype=bool))
    strict = jnp.tril(jnp.ones((C, C), dtype=bool), -1)
    dmask = jnp.exp(jnp.where(causal, G[..., :, None] - G[..., None, :], -jnp.inf))
    kb = kc * bc[..., None]
    lower = jnp.where(strict, jnp.einsum('...ik,...jk->...ij', kb, kc) * dmask, 0.0)
    rhs = jnp.concatenate([vc * bc[..., None], kb * jnp.exp(G)[..., None]], axis=-1)
    sol = lax.linalg.triangular_solve(jnp.eye(C, dtype=jnp.float32) + lower, rhs, left_side=True, lower=True)
    u, w = sol[..., :dv], sol[..., dv:]
    intra = jnp.einsum('...ik,...jk->...ij', qc, kc) * dmask

    def step(S, xs):
        q_i, k_i, u_i, w_i, G_i, a_i = xs
        v_new = u_i - jnp.einsum('bhck,bhkv->bhcv', w_i, S)
        o = jnp.einsum('bhck,bhkv->bhcv', q_i * jnp.exp(G_i)[..., None], S) + jnp.einsum('bhij,bhjv->bhiv', a_i, v_new)
        g_last = G_i[..., -1]
        S = S * jnp.exp(g_last)[..., None, None] + jnp.einsum(
            'bhck,bhcv->bhkv', k_i * jnp.exp(g_last[..., None] - G_i)[..., None], v_new)
        return S, o

    S, o = lax.scan(step, S0, (qc, kc, u, w, G, intra))
    o = jnp.moveaxis(jnp.moveaxis(o, 0, 1), 2, 3).reshape(B, n * C, H, dv)[:, :T]
    return o, S

def trunk_layer(x, c, w_ada, b_ada, w_in, conv_w, a_log, dt_bias, gdn_norm, w_out_a, w_out_b, w_o, ln_g, ln_b,
                conv_buf, gdn_state, win_bufs):
    B, T, _ = x.shape
    f32 = jnp.float32
    shift, scale, gate = jnp.split((jax.nn.silu(c) @ w_ada + b_ada)[:, None, :], 3, axis=-1)
    h = x * (1 + scale) + shift
    proj = h @ w_in

    head_shape = (B, T, N_GROUPS, HEADS_PER_GROUP, HEAD_DIM_A)
    qa = proj[..., COL_QA:COL_KA].reshape(head_shape)
    ka = proj[..., COL_KA:COL_VA].reshape(head_shape)
    va = proj[..., COL_VA:COL_ZA].reshape(head_shape)
    slopes = alibi_slopes()
    outs, lses, new_kv = [], [], []
    for gi, (window, dil) in enumerate(DILATED_GROUPS):
        if win_bufs is None:
            o, lse = dilated_group_prompt(qa[:, :, gi], ka[:, :, gi], va[:, :, gi], dil, slopes[gi])
            keep = min(window, T)
            new_kv.append(jnp.stack([ka[:, T - keep:, gi], va[:, T - keep:, gi]], axis=2))
        else:
            o, lse, kv = dilated_group_sample(qa[:, :, gi], ka[:, :, gi], va[:, :, gi], win_bufs[gi], dil, slopes[gi])
            new_kv.append(kv)
        outs.append(o)
        lses.append(lse)
    att_a = combine_groups(outs, lses)
    branch_a = (att_a * jax.nn.silu(proj[..., COL_ZA:COL_QKVB])) @ w_out_a

    qkv, new_conv = short_conv(proj[..., COL_QKVB:COL_ZB], conv_buf, conv_w)
    qkv = qkv.astype(f32).reshape(B, T, 3, N_HEADS_B, HEAD_DIM_B)
    qb = l2norm(qkv[:, :, 0]) * (HEAD_DIM_B ** -0.5)
    kb = l2norm(qkv[:, :, 1])
    vb = qkv[:, :, 2]
    g = -jnp.exp(a_log.astype(f32)) * jax.nn.softplus(proj[..., COL_AB:COL_BB].astype(f32) + dt_bias.astype(f32))
    beta = jax.nn.sigmoid(proj[..., COL_BB:COL_GA].astype(f32))
    o_b, S_new = gated_delta_rule(qb, kb, vb, g, beta, gdn_state.astype(f32))
    o_b = o_b * lax.rsqrt(jnp.mean(jnp.square(o_b), -1, keepdims=True) + RMS_EPS) * gdn_norm.astype(f32)
    o_b = o_b.reshape(B, T, WIDTH_B).astype(x.dtype)
    branch_b = (o_b * jax.nn.silu(proj[..., COL_ZB:COL_AB])) @ w_out_b

    merged = jax.nn.sigmoid(proj[..., COL_GA:COL_GB]) * branch_a + jax.nn.sigmoid(proj[..., COL_GB:]) * branch_b
    out = merged @ w_o
    x_new = layer_norm(DEEPNORM_ALPHA * x + gate * out, ln_g, ln_b)
    return x_new, new_kv, new_conv, S_new

def setup_inputs(seed: int = 0) -> dict:
    key = jax.random.key(seed)
    ks = jax.random.split(key, 21)
    f32 = jnp.float32
    nrm = lambda k, shape, s: jax.random.normal(k, shape, f32) * s
    win_len = [min(w, PAST_LEN) for (w, _) in DILATED_GROUPS]
    win_shape = lambda L: (DEPTH, DEC_BATCH, L, 2, HEADS_PER_GROUP, HEAD_DIM_A)
    dt = jnp.exp(jax.random.uniform(ks[14], (DEPTH, N_HEADS_B), f32, np.log(1e-3), np.log(1e-1)))
    return {
        'x_prompt': nrm(ks[0], (BATCH, SEQ, D_MODEL), 1.0),
        'x_sample': nrm(ks[1], (DEC_BATCH, DEC_SEQ, D_MODEL), 1.0),
        'c_prompt': nrm(ks[2], (BATCH, D_MODEL), 1.0),
        'c_sample': nrm(ks[3], (DEC_BATCH, D_MODEL), 1.0),
        'cache_win1': nrm(ks[4], win_shape(win_len[0]), 1.0),
        'cache_win2': nrm(ks[5], win_shape(win_len[1]), 1.0),
        'cache_win3': nrm(ks[6], win_shape(win_len[2]), 1.0),
        'state_gdn': nrm(ks[7], (DEPTH, DEC_BATCH, N_HEADS_B, HEAD_DIM_B, HEAD_DIM_B), 0.2),
        'state_conv': nrm(ks[8], (DEPTH, DEC_BATCH, CONV_WIDTH - 1, CONV_DIM), 1.0),
        'w_ada': nrm(ks[9], (DEPTH, D_MODEL, 3 * D_MODEL), 0.5 * D_MODEL ** -0.5),
        'b_ada': nrm(ks[10], (DEPTH, 3 * D_MODEL), 0.01),
        'w_in': nrm(ks[11], (DEPTH, D_MODEL, IN_WIDTH), D_MODEL ** -0.5),
        'conv_w': nrm(ks[12], (DEPTH, CONV_WIDTH, CONV_DIM), CONV_WIDTH ** -0.5),
        'a_log': jnp.log(jax.random.uniform(ks[13], (DEPTH, N_HEADS_B), f32, 1.0, 16.0)),
        'dt_bias': dt + jnp.log(-jnp.expm1(-dt)),
        'gdn_norm': 1.0 + nrm(ks[15], (DEPTH, HEAD_DIM_B), 0.02),
        'w_out_a': nrm(ks[16], (DEPTH, WIDTH_A, D_MODEL), WIDTH_A ** -0.5),
        'w_out_b': nrm(ks[17], (DEPTH, WIDTH_B, D_MODEL), WIDTH_B ** -0.5),
        'w_o': nrm(ks[18], (DEPTH, D_MODEL, D_MODEL), DEEPNORM_BETA * D_MODEL ** -0.5),
        'ln_g': 1.0 + nrm(ks[19], (DEPTH, D_MODEL), 0.02),
        'ln_b': nrm(ks[20], (DEPTH, D_MODEL), 0.02),
    }

def reference(x_prompt, x_sample, c_prompt, c_sample, cache_win1, cache_win2, cache_win3, state_gdn, state_conv,
              w_ada, b_ada, w_in, conv_w, a_log, dt_bias, gdn_norm, w_out_a, w_out_b, w_o, ln_g, ln_b):
    win_caches = (cache_win1, cache_win2, cache_win3)
    xp, xs = x_prompt, x_sample
    n_p = xp.shape[0]
    zero_conv = jnp.zeros((n_p, CONV_WIDTH - 1, CONV_DIM), x_prompt.dtype)
    zero_state = jnp.zeros((n_p, N_HEADS_B, HEAD_DIM_B, HEAD_DIM_B), jnp.float32)
    acc_p = [[] for _ in range(N_GROUPS + 2)]
    acc_s = [[] for _ in range(N_GROUPS + 2)]
    for l in range(DEPTH):
        lw = (w_ada[l], b_ada[l], w_in[l], conv_w[l], a_log[l], dt_bias[l], gdn_norm[l],
              w_out_a[l], w_out_b[l], w_o[l], ln_g[l], ln_b[l])
        xp, kv_p, cv_p, s_p = trunk_layer(xp, c_prompt, *lw, zero_conv, zero_state, None)
        xs, kv_s, cv_s, s_s = trunk_layer(xs, c_sample, *lw, state_conv[l], state_gdn[l],
                                          (cache_win1[l], cache_win2[l], cache_win3[l]))
        for i, a in enumerate(list(kv_p) + [s_p.astype(x_prompt.dtype), cv_p]):
            acc_p[i].append(a)
        for i, a in enumerate(list(kv_s) + [s_s.astype(state_gdn.dtype), cv_s]):
            acc_s[i].append(a)
    win1_prompt, win2_prompt, win3_prompt, gdn_prompt, conv_prompt = [jnp.stack(a) for a in acc_p]
    win1_sample, win2_sample, win3_sample, gdn_sample, conv_sample = [jnp.stack(a) for a in acc_s]
    return (xp, xs, win1_prompt, win2_prompt, win3_prompt, gdn_prompt, conv_prompt,
            win1_sample, win2_sample, win3_sample, gdn_sample, conv_sample)


_drawn_inputs = setup_inputs


def setup_inputs(seed=0):
    import zlib

    import numpy as np

    out = dict(_drawn_inputs(seed))
    spreads = {}
    factors = {'cache_win1': 8.0,
     'cache_win2': 8.0,
     'cache_win3': 8.0,
     'gdn_norm': 8.0,
     'w_out_a': 4.192,
     'ln_g': 2.839,
     'ln_b': 2.949}
    for name, (base, spread) in spreads.items():
        noise = np.random.default_rng([zlib.crc32(name.encode()), seed]).standard_normal(out[name].shape)
        drawn = base * np.exp(spread * noise) if base else spread * noise
        out[name] = __import__('jax').numpy.asarray(drawn.astype(out[name].dtype))
    for name, factor in factors.items():
        out[name] = (out[name] * factor).astype(out[name].dtype)
    return out
```

```python
from contextlib import ExitStack

import numpy as np
import concourse.bass as bass
from concourse import mybir

F32 = mybir.dt.float32
F32R = mybir.dt.float32r
ALU = mybir.AluOpType
ACT = mybir.ActivationFunctionType
AX = mybir.AxisListType

P = 128
D = 1024
KT = D // P
SEQ = 2048
NSEQ, TS = 8, 8
SAMP = NSEQ * TS
NT = SEQ + SAMP
NC = 1 + NSEQ
GROUPS = ((128, 1), (512, 4), (2048, 16))
NG = len(GROUPS)
HPG, DH = 4, 64
GW = HPG * DH
WA = NG * GW
NHB, DB = 6, 128
WB = NHB * DB
CONV = 3 * WB
TAPS = 4
PAST = tuple(min(w, 1024) for w, _ in GROUPS)
ALPHA = 2.0 ** 0.25
LN_EPS = 1e-5
RMS_EPS = 1e-6
NBLK = SEQ // P
CHUNKS = [(c * 512, 512) for c in range(SEQ // 512)] + [(SEQ, SAMP)]

T_CONV, T_Q, T_K, T_ZA, T_ZB, T_G = CONV // P, WA // P, WA // P, WA // P, WB // P, 2 * D // P
FT = T_CONV + T_Q + T_K + T_ZA + T_ZB + T_G
NAB = 2 * NHB
VW = GW + NAB
SIDE = TAPS + NSEQ * (TAPS - 1)
EXT = TAPS - 1 + TS
U_PRE = TAPS - 1
U_SAMP = U_PRE + SEQ
U_W = U_SAMP + NSEQ * EXT
BLOCKS = ((512, 128, 1), (1, 512, 4), (4, 1, 16))


def f32(ap):
    return ap.bitcast(F32)


def bc(ap, n):
    return ap.unsqueeze(len(ap.shape)).broadcast_to(list(ap.shape) + [n])


def mm3(pe, out, lhs, rhs, start, stop):
    (ah, al), (bh, bl) = lhs, rhs
    pe.matmul(out, ah, bl, start=start, stop=False)
    pe.matmul(out, al, bh, start=False, stop=False)
    return pe.matmul(out, ah, bh, start=False, stop=stop)


def modulate(nc, t, h_hi, h_lo):
    with ExitStack() as ctx:
        sb = lambda name, shape, dt=F32: ctx.enter_context(nc.sbuf_tensor(name, shape, dt))
        sem = t["sem"]
        c_sb = sb("ada_c", [P, KT, NC])
        sc = sb("ada_silu_c", [P, KT, NC])
        w = sb("ada_w", [P, 2, KT, 512])
        b_ss = sb("ada_b_ss", [P, 2 * KT])
        b_gate = sb("ada_b_gate", [NC, D])
        mods = sb("ada_mods", [P, 2 * KT, NC])
        gate = sb("ada_gate", [NC, D])
        x_in = sb("x_in", [P, 2, NT])
        ps_mod = ctx.enter_context(nc.psum_tensor("ps_mod", [P, 512], F32))
        ps_gate = ctx.enter_context(nc.psum_tensor("ps_gate", [P, 2, 512], F32))
        small_in, silu_done, mod_done, gate_done = sem("small_in"), sem("silu_done"), sem("mod_done"), sem("gate_done")
        w_in = [sem(f"ada_w_in{j}") for j in range(2)]
        w_used = sem("ada_w_used")
        mod_ready, gate_ready, gate_out = sem("mod_ready"), sem("gate_ready"), sem("gate_out")
        x_loaded = [sem(f"x_loaded{j}") for j in range(2)]
        h_step, hi_done, lo_done = sem("h_step"), sem("hi_done"), sem("lo_done")
        w_src = t["w_ada"].rearrange("(k p) n -> p k n", p=P)
        block = ctx.enter_context(nc.Block(name="modulate"))

        @block.sync
        def _(sp):
            sp.dma_start(c_sb[:, :, :], t["c_T"]).then_inc(small_in, 16)
            sp.dma_start(b_ss[:, :], t["b_ss"]).then_inc(small_in, 16)
            sp.dma_start(b_gate[:, :], t["b_gate"].partition_broadcast(NC)).then_inc(small_in, 16)
            for n in range(6):
                if n >= 2:
                    sp.wait_ge(w_used, n - 1)
                sp.dma_start(w[:, n % 2], w_src[:, :, n * 512:(n + 1) * 512]).then_inc(w_in[n % 2], 16)
            for k in range(2):
                sp.dma_start(x_in[:, k], t["x_T"][:, k]).then_inc(x_loaded[k], 16)
            sp.wait_ge(gate_ready, 1)
            sp.dma_start(t["gate_d"], gate[:, :]).then_inc(gate_out, 16)
            for k in range(2, KT):
                sp.wait_ge(lo_done, k - 1)
                sp.dma_start(x_in[:, k % 2], t["x_T"][:, k]).then_inc(x_loaded[k % 2], 16)
            sp.wait_ge(gate_out, 16)

        @block.tensor
        def _(pe):
            pe.wait_ge(silu_done, 1)
            for n in range(4):
                pe.wait_ge(w_in[n % 2], 16 * (n // 2 + 1))
                for j in range(4):
                    for k in range(KT):
                        last = pe.matmul(ps_mod[:, (4 * n + j) * NC:(4 * n + j + 1) * NC],
                                         w[:, n % 2, k, j * P:(j + 1) * P], sc[:, k, :],
                                         start=k == 0, stop=k == KT - 1)
                last.then_inc(w_used, 1)
            for n in range(4, 6):
                pe.wait_ge(w_in[n % 2], 16 * (n // 2 + 1))
                for k in range(KT):
                    last = pe.matmul(ps_gate[0:NC, n - 4, :], sc[:, k, :], w[:, n % 2, k, :],
                                     start=k == 0, stop=k == KT - 1)
                last.then_inc(w_used, 1)

        @block.scalar
        def _(act):
            act.wait_ge(small_in, 48)
            act.activation(sc[:, :, :], c_sb[:, :, :], ACT.Silu).then_inc(silu_done, 1)
            for k in range(KT):
                act.wait_ge(h_step, 3 * k + 3)
                act.activation(h_hi[:, k, :], x_in[:, k % 2, :], ACT.Copy).then_inc(hi_done, 1)

        @block.vector
        def _(dve):
            dve.wait_ge(small_in, 48)
            dve.wait_ge(w_used, 4)
            dve.tensor_tensor(mods[:, :, :], ps_mod[:, 0:2 * KT * NC].rearrange("p (f c) -> p f c", c=NC),
                              bc(b_ss[:, :], NC), ALU.add).then_inc(mod_ready, 1)
            dve.wait_ge(mod_ready, 1)
            dve.tensor_scalar(mods[:, KT:, :], mods[:, KT:, :], 1.0, None, ALU.add).then_inc(mod_ready, 1)
            dve.wait_ge(mod_ready, 2)
            dve.wait_ge(w_used, 6)
            dve.tensor_tensor(gate[:, :], ps_gate[0:NC, :, :].rearrange("p a n -> p (a n)"), b_gate[:, :],
                              ALU.add).then_inc(gate_ready, 1)
            for k in range(KT):
                x = x_in[:, k % 2, :]
                xs = x[:, SEQ:].rearrange("p (s t) -> p s t", s=NSEQ)
                dve.wait_ge(x_loaded[k % 2], 16 * (k // 2 + 1))
                dve.tensor_scalar(x[:, 0:SEQ], x[:, 0:SEQ], mods[:, KT + k, 0:1], mods[:, k, 0:1],
                                  ALU.mult, ALU.add).then_inc(h_step, 1)
                dve.tensor_tensor(xs, xs, bc(mods[:, KT + k, 1:], TS), ALU.mult).then_inc(h_step, 1)
                dve.wait_ge(h_step, 3 * k + 2)
                dve.tensor_tensor(xs, xs, bc(mods[:, k, 1:], TS), ALU.add).then_inc(h_step, 1)
                dve.wait_ge(hi_done, k + 1)
                dve.tensor_tensor(h_lo[:, k, :], x, f32(h_hi[:, k, :]), ALU.subtract).then_inc(lo_done, 1)


def project_features(nc, t, h_hi, h_lo):
    PAIRS = FT // 2
    seg, at = {}, 0
    for name, n in (("conv", T_CONV), ("q", T_Q), ("k", T_K), ("z", T_ZA + T_ZB), ("g", T_G)):
        seg[name] = (at // 2, (at + n) // 2)
        at += n
    with ExitStack() as ctx:
        sb = lambda name, shape, dt=F32: ctx.enter_context(nc.sbuf_tensor(name, shape, dt))
        sem = t["sem"]
        w_raw = sb("w_raw", [P, 2, KT * P])
        w_hi = sb("w_hi", [P, 2, KT * P], F32R)
        w_lo = sb("w_lo", [P, 2, KT * P], F32R)
        side = sb("side", [P, 2, SIDE])
        stage = sb("stage", [P, 2, U_W + 1])
        conv = sb("conv", [P, 2, NT])
        ps = ctx.enter_context(nc.psum_tensor("ps_proj", [P, len(CHUNKS), 512], F32))
        raw_loaded = [sem(f"raw_loaded{j}") for j in range(2)]
        side_loaded = [sem(f"side_loaded{j}") for j in range(2)]
        hi_done = [sem(f"w_hi_done{j}") for j in range(2)]
        lo_done = [sem(f"w_lo_done{j}") for j in range(2)]
        bank_full = [sem(f"bank_full{c}") for c in range(len(CHUNKS))]
        bank_read = [sem(f"bank_read{c}") for c in range(len(CHUNKS))]
        stored = [sem(f"stored{j}") for j in range(2)]
        conv_stored = [sem(f"conv_stored{j}") for j in range(2)]
        pad_zero, state_put, conv_step, conv_silu = sem("pad_zero"), sem("state_put"), sem("conv_step"), sem("conv_silu")
        STEPS = 2 * TAPS
        block = ctx.enter_context(nc.Block(name="project_features"))
        first = lambda i: isinstance(i, int) and i == 0

        @block.sync
        def _(sp):
            def load(i, j, is_conv):
                if not first(i):
                    sp.wait_ge(lo_done[j], i)
                sp.dma_start(w_raw[:, j, :], t["w_feat"][bass.ds(2 * i + j, 1)].rearrange("a p n -> p (a n)")
                             ).then_inc(raw_loaded[j], 16)
                if is_conv:
                    if not first(i):
                        sp.wait_ge(conv_step, STEPS * (2 * i + j - 1))
                        sp.wait_ge(state_put, 2 * i + j - 1)
                    sp.dma_start(side[:, j, :], t["conv_side"][bass.ds(2 * i + j, 1)].rearrange("a p n -> p (a n)")
                                 ).then_inc(side_loaded[j], 16)
            for j in range(2):
                load(0, j, True)
            with sp.Fori(1, seg["conv"][1]) as i:
                for j in range(2):
                    load(i, j, True)
            with sp.Fori(seg["conv"][1], PAIRS) as i:
                for j in range(2):
                    load(i, j, False)

        @block.tensor
        def _(pe):
            def pair(i):
                for j in range(2):
                    pe.wait_ge(lo_done[j], i + 1)
                    for c, (at, n) in enumerate(CHUNKS):
                        if not (first(i) and j == 0):
                            pe.wait_ge(bank_read[c], 2 * i + j)
                        for k in range(KT):
                            cols = slice(k * P, (k + 1) * P)
                            last = mm3(pe, ps[:, c, 0:n], (w_hi[:, j, cols], w_lo[:, j, cols]),
                                       (h_hi[:, k, at:at + n], h_lo[:, k, at:at + n]), k == 0, k == KT - 1)
                        last.then_inc(bank_full[c], 1)
            with pe.Fori(0, PAIRS) as i:
                pair(i)

        @block.scalar
        def _(act):
            def split(i, j):
                act.wait_ge(raw_loaded[j], 16 * (i + 1))
                if not first(i):
                    act.wait_ge(bank_full[-1], 2 * i + j - 1)
                act.activation(w_hi[:, j, :], w_raw[:, j, :], ACT.Copy).then_inc(hi_done[j], 1)

            def empty(i, j, func, is_conv):
                if is_conv:
                    act.wait_ge(side_loaded[j], 16 * (i + 1))
                    if not first(i):
                        act.wait_ge(conv_step, STEPS * (2 * i + j - 1))
                        act.wait_ge(stored[j], 16 * i)
                    ext = stage[:, j, U_SAMP:U_W].rearrange("p (s e) -> p s e", e=EXT)
                    act.activation(ext[:, :, 0:U_PRE], side[:, j, TAPS:].rearrange("p (s e) -> p s e", e=U_PRE),
                                   ACT.Copy).then_inc(state_put, 1)
                else:
                    act.wait_ge(stored[j], 16 * i)
                for c, (at, n) in enumerate(CHUNKS):
                    act.wait_ge(bank_full[c], 2 * i + j + 1)
                    src = ps[:, c, 0:n]
                    if not is_conv:
                        dst = stage[:, j, at:at + n]
                    elif n == SAMP:
                        dst, src = ext[:, :, U_PRE:], src.rearrange("p (s e) -> p s e", e=TS)
                    else:
                        dst = stage[:, j, U_PRE + at:U_PRE + at + n]
                    act.activation(dst, src, func).then_inc(bank_read[c], 1)

            def silu(i, j):
                act.wait_ge(conv_step, STEPS * (2 * i + j + 1))
                act.activation(conv[:, j, :], conv[:, j, :], ACT.Silu).then_inc(conv_silu, 1)

            act.wait_ge(pad_zero, 1)
            lo, hi = seg["conv"]
            split(0, 0), split(0, 1)
            for j in range(2):
                empty(0, j, ACT.Copy, True), split(1, j), silu(0, j)
            with act.Fori(1, hi) as i:
                for j in range(2):
                    empty(i, j, ACT.Copy, True), split(i + 1, j), silu(i, j)
            for name, func in (("q", ACT.Copy), ("k", ACT.Copy), ("z", ACT.Silu)):
                with act.Fori(*seg[name]) as i:
                    for j in range(2):
                        empty(i, j, func, False), split(i + 1, j)
            with act.Fori(seg["g"][0], PAIRS - 1) as i:
                for j in range(2):
                    empty(i, j, ACT.Sigmoid, False), split(i + 1, j)
            for j in range(2):
                empty(PAIRS - 1, j, ACT.Sigmoid, False)

        @block.vector
        def _(dve):
            def split(i, j):
                dve.wait_ge(hi_done[j], i + 1)
                dve.tensor_tensor(w_lo[:, j, :], w_raw[:, j, :], f32(w_hi[:, j, :]), ALU.subtract).then_inc(lo_done[j], 1)

            def convolve(i, j):
                for c in range(len(CHUNKS)):
                    dve.wait_ge(bank_read[c], 2 * i + j + 1)
                dve.wait_ge(state_put, 2 * i + j + 1)
                if not first(i):
                    dve.wait_ge(conv_stored[j], 16 * i)
                ext = stage[:, j, U_SAMP:U_W].rearrange("p (s e) -> p s e", e=EXT)
                out_s = conv[:, j, SEQ:].rearrange("p (s e) -> p s e", e=TS)
                for n in range(TAPS):
                    w = side[:, j, n:n + 1]
                    if n == 0:
                        dve.tensor_scalar(conv[:, j, 0:SEQ], stage[:, j, 0:SEQ], w, None, ALU.mult).then_inc(conv_step, 1)
                        dve.tensor_scalar(out_s, ext[:, :, 0:TS], w, None, ALU.mult).then_inc(conv_step, 1)
                        continue
                    dve.wait_ge(conv_step, STEPS * (2 * i + j) + 2 * n - 1)
                    dve.scalar_tensor_tensor(out=conv[:, j, 0:SEQ], in0=stage[:, j, n:n + SEQ], scalar=w,
                                             in1=conv[:, j, 0:SEQ], op0=ALU.mult, op1=ALU.add).then_inc(conv_step, 1)
                    dve.wait_ge(conv_step, STEPS * (2 * i + j) + 2 * n)
                    dve.scalar_tensor_tensor(out=out_s, in0=ext[:, :, n:n + TS], scalar=w, in1=out_s,
                                             op0=ALU.mult, op1=ALU.add).then_inc(conv_step, 1)
            for j in range(2):
                split(0, j)
            for j in range(2):
                split(1, j), convolve(0, j)
            with dve.Fori(1, seg["conv"][1]) as i:
                for j in range(2):
                    split(i + 1, j), convolve(i, j)
            with dve.Fori(seg["conv"][1] + 1, PAIRS) as i:
                for j in range(2):
                    split(i, j)

        @block.gpsimd
        def _(pool):
            pool.memset(stage[:, :, 0:U_PRE], 0.0).then_inc(pad_zero, 1)

            def store(dst, i, j, base):
                for c in range(len(CHUNKS)):
                    pool.wait_ge(bank_read[c], 2 * i + j + 1)
                pool.dma_start(dst[bass.ds(2 * i + j - 2 * base, 1)].rearrange("a p n -> p (a n)"),
                               stage[:, j, 0:NT]).then_inc(stored[j], 16)

            def store_conv(i, j):
                for c in range(len(CHUNKS)):
                    pool.wait_ge(bank_read[c], 2 * i + j + 1)
                pool.dma_start(t["conv_tail"][bass.ds(2 * i + j, 1)].rearrange("a p n -> p (a n)"),
                               stage[:, j, U_SAMP - U_PRE:U_W]).then_inc(stored[j], 16)
                pool.wait_ge(conv_silu, 2 * i + j + 1)
                pool.dma_start(t["conv_d"][bass.ds(2 * i + j, 1)].rearrange("a p n -> p (a n)"),
                               conv[:, j, :]).then_inc(conv_stored[j], 16)
            with pool.Fori(*seg["conv"]) as i:
                for j in range(2):
                    store_conv(i, j)
            for name, dst in (("q", "q_d"), ("k", "k_T"), ("z", "z_d"), ("g", "g_d")):
                with pool.Fori(*seg[name]) as i:
                    for j in range(2):
                        store(t[dst], i, j, seg[name][0])
            for j in range(2):
                pool.wait_ge(stored[j], 16 * PAIRS)
                pool.wait_ge(conv_stored[j], 16 * seg["conv"][1])


def project_values(nc, t, h_hi, h_lo, ab):
    NB = NBLK + 1
    with ExitStack() as ctx:
        sb = lambda name, shape, dt=F32: ctx.enter_context(nc.sbuf_tensor(name, shape, dt))
        sem = t["sem"]
        wv_raw = sb("wv_raw", [P, KT, VW])
        wv_hi = sb("wv_hi", [P, KT, VW], F32R)
        wv_lo = sb("wv_lo", [P, KT, VW], F32R)
        x_hi = sb("tok_hi", [P, 2, KT, P], F32R)
        x_lo = sb("tok_lo", [P, 2, KT, P], F32R)
        v_out = sb("v_out", [P, 2, GW])
        ps = ctx.enter_context(nc.psum_tensor("ps_val", [P, 2, 512], F32))
        w_loaded, w_hi_done, w_lo_done = sem("wv_loaded"), sem("wv_hi_done"), sem("wv_lo_done")
        hi_put = [sem(f"tok_hi_put{j}") for j in range(2)]
        lo_put = [sem(f"tok_lo_put{j}") for j in range(2)]
        full = [sem(f"val_full{j}") for j in range(2)]
        read = [sem(f"val_read{j}") for j in range(2)]
        ab_read = [sem(f"ab_read{j}") for j in range(2)]
        stored = [sem(f"val_stored{j}") for j in range(2)]
        block = ctx.enter_context(nc.Block(name="project_values"))
        PASS = NBLK // 4
        base = lambda g, j: g * (NBLK // 2) + (g if j == 0 else 0)
        use = lambda g, i, j: base(g, j % 2) + 2 * i + j // 2

        def view(x, g, i, j):
            a, b, s = BLOCKS[g]
            if s == 1:
                return x[:, :, bass.ds(a * i + b * j, P)]
            if s == 4:
                return x[:, :, 512 * j:512 * (j + 1)].rearrange("p k (m s) -> p k m s", s=4)[:, :, :, bass.ds(i, 1)]
            return x[:, :, 0:SEQ].rearrange("p k (m s) -> p k m s", s=16)[:, :, :, bass.ds(4 * i + j, 1)]

        @block.sync
        def _(sp):
            for g in range(NG):
                if g:
                    sp.wait_ge(w_lo_done, g)
                sp.dma_start(wv_raw[:, :, :], t["w_val"][g]).then_inc(w_loaded, 16)

        @block.tensor
        def _(pe):
            def tile(g, u, s, n):
                pe.wait_ge(hi_put[s], u + 1)
                pe.wait_ge(lo_put[s], u + 1)
                if not (isinstance(u, int) and u == 0):
                    pe.wait_ge(read[s], u)
                for k in range(KT):
                    last = mm3(pe, ps[:, s, 0:n], (x_hi[:, s, k, :], x_lo[:, s, k, :]),
                               (wv_hi[:, k, 0:n], wv_lo[:, k, 0:n]), k == 0, k == KT - 1)
                last.then_inc(full[s], 1)
            for g in range(NG):
                pe.wait_ge(w_lo_done, g + 1)
                n = VW if g == 0 else GW
                with pe.Fori(0, PASS) as i:
                    for j in range(4):
                        tile(g, use(g, i, j), j % 2, n)
                tile(g, use(g, PASS, 0), 0, n)

        def put(eng, copy, dst, src, done):
            for g in range(NG):
                with eng.Fori(0, PASS) as i:
                    for j in range(4):
                        s, u = j % 2, use(g, i, j)
                        eng.wait_ge(full[s], u)
                        v = view(src, g, i, j)
                        o = dst[:, s] if len(v.shape) == 3 else dst[:, s].unsqueeze(3)
                        copy(o, f32(v)).then_inc(done[s], 1)
                eng.wait_ge(full[0], use(g, PASS, 0))
                copy(dst[:, 0, :, 0:SAMP], f32(src[:, :, SEQ:])).then_inc(done[0], 1)
                yield g

        @block.scalar
        def _(act):
            def split(g):
                act.wait_ge(w_loaded, 16 * (g + 1))
                if g:
                    act.wait_ge(full[0], base(g, 0))
                    act.wait_ge(full[1], base(g, 1))
                act.activation(wv_hi[:, :, :], wv_raw[:, :, :], ACT.Copy).then_inc(w_hi_done, 1)
            split(0)
            for g in put(act, lambda o, i: act.activation(o, i, ACT.Copy), x_hi, h_hi, hi_put):
                if g + 1 < NG:
                    split(g + 1)

        @block.vector
        def _(dve):
            def split(g):
                dve.wait_ge(w_hi_done, g + 1)
                dve.tensor_tensor(wv_lo[:, :, :], wv_raw[:, :, :], f32(wv_hi[:, :, :]), ALU.subtract).then_inc(w_lo_done, 1)

            def empty(g, u, s, b, samples=False):
                dve.wait_ge(full[s], u + 1)
                rows = SAMP if samples else P
                if not (isinstance(u, int) and u == 0):
                    dve.wait_ge(stored[s], 16 * u)
                if g == 0:
                    dve.tensor_copy(ab[0:rows, bass.ds(b, 1), :], ps[0:rows, s, GW:VW].unsqueeze(1)).then_inc(ab_read[s], 1)
                dve.tensor_copy(v_out[0:rows, s, :], ps[0:rows, s, 0:GW]).then_inc(read[s], 1)

            def put_one(g, i, j):
                s, u = j % 2, use(g, i, j)
                if not (isinstance(i, int) and g == 0 and i == 0 and j < 2):
                    dve.wait_ge(full[s], u)
                v = view(h_lo, g, i, j)
                o = x_lo[:, s] if len(v.shape) == 3 else x_lo[:, s].unsqueeze(3)
                dve.tensor_copy(o, f32(v)).then_inc(lo_put[s], 1)

            for g in range(NG):
                split(g)
                with dve.Fori(0, PASS) as i:
                    for j in range(4):
                        put_one(g, i, j)
                        if j:
                            empty(g, use(g, i, j - 1), (j - 1) % 2, 4 * i + j - 1)
                    empty(g, use(g, i, 3), 1, 4 * i + 3)
                dve.wait_ge(full[0], use(g, PASS, 0))
                dve.tensor_copy(x_lo[:, 0, :, 0:SAMP], f32(h_lo[:, :, SEQ:])).then_inc(lo_put[0], 1)
                empty(g, use(g, PASS, 0), 0, NBLK, samples=True)

        @block.gpsimd
        def _(pool):
            for g in range(NG):
                with pool.Fori(0, PASS) as i:
                    for j in range(4):
                        pool.wait_ge(read[j % 2], use(g, i, j) + 1)
                        pool.dma_start(t["v_out"][g, bass.ds(4 * i + j, 1)].rearrange("a p n -> p (a n)"),
                                       v_out[:, j % 2, :]).then_inc(stored[j % 2], 16)
                pool.wait_ge(read[0], use(g, PASS, 0) + 1)
                pool.dma_start(t["v_new"][g], v_out[0:SAMP, 0, :]).then_inc(stored[0], 16)
            for j in range(2):
                pool.wait_ge(stored[j], 16 * base(NG, j))


NSTAT = 2 * HPG
PAIR = 2 * DH
NP_ = HPG // 2
NPT = NG * NP_
MASKED = -1.0e30


def attend_prompt(nc, t):
    with ExitStack() as ctx:
        sb = lambda name, shape, dt=F32: ctx.enter_context(nc.sbuf_tensor(name, shape, dt))
        pb = lambda name, shape: ctx.enter_context(nc.psum_tensor(name, shape, F32))
        sem = t["sem"]
        q_sb = sb("q_sb", [P, NG, NP_, SEQ])
        k_sb = sb("k_sb", [P, NG, NP_, SEQ])
        v_sb = sb("v_sb", [P, NG, NBLK, GW])
        bias = sb("bias_p", [P, NG, HPG, 2 * P])
        ident = sb("ident_a", [P, P])
        q_bd = sb("q_bd", [P, NP_, 2, P])
        scores = sb("scores", [P, NP_, 2, 2 * P])
        probs = sb("probs", [P, NP_, 2, 2 * P])
        probs_T = sb("probs_T", [P, NP_, 4, P])
        top = sb("top", [P, HPG])
        neg = sb("neg", [P, HPG])
        turnstile = sb("turnstile", [P, NP_])
        rows = sb("rows", [P, NBLK, GW])
        stats = sb("stats", [P, NG, NBLK, NSTAT])
        ps_s = [pb(f"ps_s{p}", [P, 2, 2 * P]) for p in range(NP_)]
        ps_t = [pb(f"ps_t{p}", [P, 4, P]) for p in range(NP_)]
        ps_o = pb("ps_o", [P, HPG, DH])
        const_in, zeroed = sem("const_in"), sem("q_zeroed")
        qk_in = [sem(f"qk_in{g}") for g in range(NG)]
        v_in = [sem(f"v_in{g}") for g in range(NG)]
        stat_put = sem("stat_put")
        q_put, neg_put, o_full, o_read = sem("q_put"), sem("neg_put"), sem("o_full"), sem("o_read")
        s_full = [sem(f"s_full{p}") for p in range(NP_)]
        s_read = [sem(f"s_read{p}") for p in range(NP_)]
        exp_done = [sem(f"exp_done{p}") for p in range(NP_)]
        t_full = [sem(f"t_full{p}") for p in range(NP_)]
        t_read = [sem(f"t_read{p}") for p in range(NP_)]
        row_stored = [sem(f"row_stored{g}") for g in range(NG)]
        stats_stored = sem("stats_stored")
        block = ctx.enter_context(nc.Block(name="attend_prompt"))

        class Unit:

            def __init__(self, g, i, j=0):
                self.g, self.i, self.j = g, i, j
                self.b = 4 * i + j if g == 1 else i
                self.u = g * NBLK + self.b
                self.first = g == 0 and isinstance(i, int) and i == 0
                self.kb = 1 if g == 2 or (g == 1 and j == 0) or self.first else 2

            def tokens(self, x, back):
                if self.g == 0:
                    return x[..., bass.ds(P * (self.i - back), P * (1 + back))]
                if self.g == 1:
                    part = x[..., 512 * (self.j - back):512 * (self.j + 1)]
                    return part.rearrange(self.pat(x, 4), s=4)[..., bass.ds(self.i, 1)]
                return x.rearrange(self.pat(x, 16), s=16)[..., bass.ds(self.i, 1)]

            def pat(self, x, s):
                lead = " ".join("abcd"[:len(x.shape) - 1])
                return f"{lead} (m s) -> {lead} m s"

        def schedule(eng, ahead, behind, enter=lambda g: None):
            step = lambda nxt, now: (ahead(nxt), behind(now))
            ahead(Unit(0, 0))
            enter(0)
            step(Unit(0, 1), Unit(0, 0))
            with eng.Fori(1, NBLK - 1) as i:
                step(Unit(0, i + 1), Unit(0, i))
            step(Unit(1, 0, 0), Unit(0, NBLK - 1))
            enter(1)
            with eng.Fori(0, 3) as i:
                for j in range(4):
                    step(Unit(1, i, j + 1) if j < 3 else Unit(1, i + 1, 0), Unit(1, i, j))
            for j in range(4):
                step(Unit(1, 3, j + 1) if j < 3 else Unit(2, 0), Unit(1, 3, j))
            enter(2)
            with eng.Fori(0, NBLK - 1) as i:
                step(Unit(2, i + 1), Unit(2, i))
            behind(Unit(2, NBLK - 1))

        nothing = lambda x: None

        @block.sync
        def _(sp):
            for g in range(NG):
                sp.dma_start(q_sb[:, g], t["q_d"][2 * g:2 * g + 2, :, 0:SEQ].rearrange("a p n -> p a n")).then_inc(qk_in[g], 16)
                sp.dma_start(v_sb[:, g], t["v_out"][g, 0:NBLK].rearrange("b p n -> p b n")).then_inc(v_in[g], 16)
                sp.dma_start(k_sb[:, g], t["k_T"][2 * g:2 * g + 2, :, 0:SEQ].rearrange("a p n -> p a n")).then_inc(qk_in[g], 16)
                if g == 0:
                    sp.dma_start(bias[:, :, :, :], t["bias_prompt"]).then_inc(const_in, 16)
                    sp.dma_start(ident[:, :], t["ident"]).then_inc(const_in, 16)

            def store(x):
                sp.wait_ge(o_read, x.u + 1)
                att = t["att_d"][:, x.g, :]
                if x.g == 0:
                    dst = att[bass.ds(P * x.i, P)]
                elif x.g == 1:
                    dst = att[512 * x.j:512 * (x.j + 1)].rearrange("(m s) n -> m s n", s=4)[:, bass.ds(x.i, 1)]
                else:
                    dst = att.rearrange("(m s) n -> m s n", s=16)[:, bass.ds(x.i, 1)]
                src = rows[:, bass.ds(x.b, 1), :]
                sp.dma_start(dst, src if x.g else src.rearrange("p a n -> p (a n)")).then_inc(row_stored[x.g], 16)
            schedule(sp, nothing, store)
            sp.wait_ge(stat_put, NG * NBLK)
            for p in range(NP_):
                sp.wait_ge(exp_done[p], 2 * NG * NBLK)
            for g, (_, s) in enumerate(GROUPS):
                st = t["stats_d"][:, g, :]
                if g == 0:
                    pairs = [(st.rearrange("(b p) n -> p b n", p=P), stats[:, g])]
                elif g == 1:
                    pairs = [(st[512 * j:512 * (j + 1)].rearrange("(m s) n -> m s n", s=s), stats[:, g, j::4]) for j in range(4)]
                else:
                    pairs = [(st.rearrange("(m s) n -> m s n", s=s), stats[:, g])]
                for dst, src in pairs:
                    sp.dma_start(dst, src).then_inc(stats_stored, 16)
            sp.wait_ge(stats_stored, 16 * 6)
            for g in range(NG):
                sp.wait_ge(row_stored[g], 16 * NBLK)

        @block.gpsimd
        def _(pool):
            pool.memset(q_bd[:, :, :, :], 0.0).then_inc(zeroed, 1)
            pool.wait_ge(zeroed, 1)

            def put(x):
                if x.g == 0 and isinstance(x.i, int) or (x.g and isinstance(x.i, int) and x.i == 0 and x.j == 0):
                    pool.wait_ge(qk_in[x.g], 32)
                if not x.first:
                    for p in range(NP_):
                        pool.wait_ge(s_full[p], x.u)
                for h in range(2):
                    half = slice(DH * h, DH * (h + 1))
                    src = x.tokens(q_sb[half, x.g], 0)
                    dst = q_bd[half, :, h, :]
                    pool.tensor_copy(dst if x.g == 0 else dst.unsqueeze(3), src).then_inc(q_put, 1)
            schedule(pool, put, nothing)

        @block.tensor
        def _(pe):
            pe.wait_ge(const_in, 32)

            def score(x):
                pe.wait_ge(q_put, 2 * (x.u + 1))
                for p in range(NP_):
                    if not x.first:
                        pe.wait_ge(s_read[p], 2 * x.u)
                    k = x.tokens(k_sb[:, x.g, p], x.kb - 1)
                    for h in range(2):
                        out = ps_s[p][:, h, 0:P * x.kb]
                        last = pe.matmul(out if x.g == 0 else out.unsqueeze(2), q_bd[:, p, h, :], k, start=True, stop=True)
                    last.then_inc(s_full[p], 1)

            def combine(x):
                for p in range(NP_):
                    pe.wait_ge(exp_done[p], 2 * (x.u + 1))
                    if not x.first:
                        pe.wait_ge(t_read[p], x.u)
                    for h in range(2):
                        for b in range(x.kb):
                            last = pe.transpose(ps_t[p][:, 2 * h + b, :], probs[:, p, h, b * P:(b + 1) * P], ident[:, :])
                    last.then_inc(t_full[p], 1)
                if not x.first:
                    pe.wait_ge(o_read, x.u)
                for p in range(NP_):
                    pe.wait_ge(t_read[p], x.u + 1)
                    for h in range(2):
                        head = 2 * p + h
                        for b in range(x.kb):
                            v = v_sb[:, x.g, bass.ds(x.b - (x.kb - 1) + b, 1), DH * head:DH * (head + 1)]
                            last = pe.matmul(ps_o[:, head, :].unsqueeze(1), probs_T[:, p, 2 * h + b, :], v,
                                             start=b == 0, stop=b == x.kb - 1)
                last.then_inc(o_full, 1)
            schedule(pe, score, combine, lambda g: pe.wait_ge(v_in[g], 16))

        def turn(eng, copy, p, x):
            eng.wait_ge(t_full[p], x.u + 1)
            if not x.first:
                eng.wait_ge(o_full, x.u)
            src, dst = ps_t[p][:, :, :], probs_T[:, p, :, :]
            if x.kb == 1:
                src, dst = ps_t[p][:, 0:4:2, :], probs_T[:, p, 0:4:2, :]
            copy(dst, src).then_inc(t_read[p], 1)

        @block.vector
        def _(dve):
            dve.wait_ge(const_in, 32)

            def maxima(x):
                for p in range(NP_):
                    dve.wait_ge(s_full[p], x.u + 1)
                    if not x.first:
                        dve.wait_ge(exp_done[p], 2 * x.u)
                        dve.wait_ge(stat_put, x.u)
                    dve.memset(turnstile[:, p:p + 1], 0.0)
                    for h in range(2):
                        head = 2 * p + h
                        off = 2 * P - P * x.kb
                        dve.tensor_tensor_reduce(out=scores[:, p, h, 0:P * x.kb], in0=ps_s[p][:, h, 0:P * x.kb],
                                                 in1=bias[:, x.g, head, off:], scale=DH ** -0.5, scalar=-3.0e38, op0=ALU.add,
                                                 op1=ALU.max, accum_out=top[:, head:head + 1]).then_inc(s_read[p], 1)
                for p in range(NP_):
                    dve.wait_ge(s_read[p], 2 * (x.u + 1))
                dve.tensor_scalar(neg[:, :], top[:, :], -1.0, None, ALU.mult).then_inc(neg_put, 1)
                dve.tensor_scalar(stats[:, x.g, bass.ds(x.b, 1), 0:HPG], top[:, :].unsqueeze(1), -1.0, None,
                                  ALU.mult).then_inc(stat_put, 1)

            def results(x):
                turn(dve, lambda o, i: dve.tensor_copy(o, i), 0, x)
                dve.wait_ge(o_full, x.u + 1)
                dve.tensor_copy(rows[:, bass.ds(x.b, 1), 0:GW], ps_o[:, :, :].rearrange("p h d -> p (h d)").unsqueeze(1)
                                ).then_inc(o_read, 1)

            def enter(g):
                if g:
                    dve.wait_ge(row_stored[g - 1], 16 * NBLK)
            schedule(dve, maxima, results, enter)

        @block.scalar
        def _(act):
            def exps(x):
                act.wait_ge(neg_put, x.u + 1)
                for p in range(NP_):
                    if not x.first:
                        act.wait_ge(t_full[p], x.u)
                    for h in range(2):
                        head = 2 * p + h
                        act.activation(probs[:, p, h, 0:P * x.kb], scores[:, p, h, 0:P * x.kb], ACT.Exp,
                                       bias=neg[:, head:head + 1],
                                       accum_out=stats[:, x.g, bass.ds(x.b, 1), HPG + head]).then_inc(exp_done[p], 1)
            schedule(act, exps, lambda x: turn(act, lambda o, i: act.activation(o, i, ACT.Copy), 1, x))


CACHED = sum(PAST)
KT_C = CACHED // P
HALF = NSEQ // 2
QR = HPG * TS
NEWC = NG * SAMP
BANKS = [P + NEWC, PAST[1]] + [512] * (PAST[2] // 512)
KEYS = sum(BANKS)


def attend_samples(nc, t):
    with ExitStack() as ctx:
        sb = lambda name, shape, dt=F32: ctx.enter_context(nc.sbuf_tensor(name, shape, dt))
        pb = lambda name, shape: ctx.enter_context(nc.psum_tensor(name, shape, F32))
        sem = t["sem"]
        RING = 3
        kc = sb("kc", [P, RING, NP_, CACHED])
        vc = sb("vc", [P, RING, KT_C, GW])
        q_in = sb("q_s", [P, NPT, SAMP])
        k_new = sb("k_new", [P, NPT, SAMP])
        v_new = sb("v_new", [SAMP, NG, GW])
        bias = sb("bias_s", [P, 2, KEYS])
        ident = sb("ident_s", [P, P])
        q_bd = sb("q_bd_s", [P, NPT, NSEQ, HPG, TS])
        probs = sb("probs_s", [P, KEYS])
        probs_T = sb("probs_T_s", [P, KT_C, P])
        new_T = sb("new_T_s", [SAMP, NG, P])
        top = sb("top_s", [P, len(BANKS)])
        neg = sb("neg_s", [P, 1])
        den = sb("den_s", [P, 1])
        rden = sb("rden_s", [P, 1])
        att = sb("att_s", [P, NPT, SAMP])
        ps_s = [pb(f"ps_ss{b}", [P, 512]) for b in range(len(BANKS))]
        ps_t = [pb(f"ps_st{b}", [P, 4, P]) for b in range(2)]
        ps_o = [pb(f"ps_so{b}", [P, NPT, HALF, 2 * TS]) for b in range(2)]
        small_in, zeroed, q_put = sem("small_in_s"), sem("zeroed_s"), sem("q_put_s")
        k_in = [sem(f"kc_in{r}") for r in range(RING)]
        v_in = [sem(f"vc_in{r}") for r in range(RING)]
        scored, attended, maxed, softened = sem("scored"), sem("attended"), sem("maxed"), sem("softened")
        chain, neg_done = sem("chain_s"), sem("neg_done_s")
        exped, t_full, t_read, att_put, att_out = sem("exped"), sem("t_full_s"), sem("t_read_s"), sem("att_put"), sem("att_out")
        block = ctx.enter_context(nc.Block(name="attend_samples"))
        ROUNDS = [list(range(r, min(r + 4, KT_C))) for r in range(0, KT_C, 4)] + ["new"]
        col = [0] + [P + NEWC + P * n for n in range(KT_C - 1)]
        tile0 = [0, PAST[0] // P, (PAST[0] + PAST[1]) // P, KT_C]

        @block.sync
        def _(sp):
            sp.dma_start(q_in[:, :, :], t["q_d"][:, :, SEQ:].rearrange("a p n -> p a n")).then_inc(small_in, 16)
            sp.dma_start(k_new[:, :, :], t["k_T"][:, :, SEQ:].rearrange("a p n -> p a n")).then_inc(small_in, 16)
            sp.dma_start(v_new[:, :, :], t["v_new"].rearrange("g p n -> p g n")).then_inc(small_in, 16)
            sp.dma_start(bias[:, :, :], t["bias_samples"]).then_inc(small_in, 16)
            sp.dma_start(ident[:, :], t["ident"]).then_inc(small_in, 16)
            for s in range(NSEQ):
                if s >= RING:
                    sp.wait_ge(scored, s - RING + 1)
                sp.dma_start(kc[:, s % RING], t["k_cache"][s]).then_inc(k_in[s % RING], 16)
                if s >= RING:
                    sp.wait_ge(attended, s - RING + 1)
                sp.dma_start(vc[:, s % RING], t["v_cache"][s]).then_inc(v_in[s % RING], 16)
            sp.wait_ge(att_put, 4)
            sp.dma_start(t["att_s"], att[:, :, :]).then_inc(att_out, 16)
            sp.wait_ge(att_out, 16)

        @block.gpsimd
        def _(pool):
            pool.memset(q_bd[:, :, :, :, :], 0.0).then_inc(zeroed, 1)
            pool.wait_ge(zeroed, 1)
            pool.wait_ge(small_in, 80)
            for p in range(NP_):
                for h in range(2):
                    half = slice(DH * h, DH * (h + 1))
                    for g in range(NG):
                        pool.tensor_scalar(q_bd[half, NP_ * g + p, :, 2 * p + h, :],
                                           q_in[half, NP_ * g + p, :].rearrange("p (s e) -> p s e", e=TS),
                                           DH ** -0.5, None, ALU.mult).then_inc(q_put, 1)

        @block.tensor
        def _(pe):
            pe.wait_ge(q_put, 4 * NG)

            def score(s):
                pe.wait_ge(k_in[s % RING], 16 * (s // RING + 1))
                out = slice(QR * (s % HALF), QR * (s % HALF + 1))

                def add(dst, g, keys):
                    for p in range(NP_):
                        last = pe.matmul(dst, q_bd[:, NP_ * g + p, s].rearrange("p h e -> p (h e)"), keys(p),
                                         start=p == 0, stop=p == NP_ - 1, tile_position=(0, QR * (s % HALF)))
                    return last
                add(ps_s[0][out, 0:P], 0, lambda p: kc[:, s % RING, p, 0:P])
                for g in range(NG):
                    add(ps_s[0][out, P + SAMP * g:P + SAMP * (g + 1)], g, lambda p: k_new[:, NP_ * g + p, :])
                at = P
                for n in range(1, len(BANKS)):
                    last = add(ps_s[n][out, :], min(n, 2), lambda p: kc[:, s % RING, p, at:at + 512])
                    at += 512
                last.then_inc(scored, 1)

            def turn(a):
                pe.wait_ge(softened, a + 1)
                for r, tiles in enumerate(ROUNDS):
                    u = len(ROUNDS) * a + r
                    if u >= 2:
                        pe.wait_ge(t_read, u - 1)
                    if tiles == "new":
                        for g in range(NG):
                            last = pe.transpose(ps_t[u % 2][0:SAMP, g, :], probs[:, P + SAMP * g:P + SAMP * (g + 1)], ident[:, :])
                    else:
                        for n, k in enumerate(tiles):
                            last = pe.transpose(ps_t[u % 2][:, n, :], probs[:, col[k]:col[k] + P], ident[:, :])
                    last.then_inc(t_full, 1)

            def weigh(s):
                pe.wait_ge(v_in[s % RING], 16 * (s // RING + 1))
                pe.wait_ge(t_read, len(ROUNDS) * (s // HALF + 1))
                for g in range(NG):
                    for p in range(NP_):
                        dst = ps_o[s // HALF][:, NP_ * g + p, s % HALF, :]
                        rows = slice(QR * (s % HALF) + 2 * TS * p, QR * (s % HALF) + 2 * TS * (p + 1))
                        feats = slice(PAIR * p, PAIR * (p + 1))
                        for k in range(tile0[g], tile0[g + 1]):
                            pe.matmul(dst, vc[:, s % RING, k, feats], probs_T[:, k, rows], start=k == tile0[g], stop=False)
                        last = pe.matmul(dst, v_new[:, g, feats], new_T[:, g, rows], start=False, stop=True)
                last.then_inc(attended, 1)
            for a in range(2):
                if a:
                    pe.wait_ge(maxed, 1)
                for s in range(HALF):
                    score(HALF * a + s)
                turn(a)
                for s in range(HALF):
                    weigh(HALF * a + s)

        @block.vector
        def _(dve):
            n = [0]

            def link(ins):
                n[0] += 1
                ins.then_inc(chain, 1)
                dve.wait_ge(chain, n[0])
            for a in range(2):
                dve.wait_ge(small_in, 80)
                dve.wait_ge(scored, HALF * (a + 1))
                if a:
                    dve.wait_ge(t_full, len(ROUNDS))
                at = 0
                for b, w in enumerate(BANKS):
                    ins = dve.tensor_tensor_reduce(out=probs[:, at:at + w], in0=ps_s[b][:, 0:w], in1=bias[:, a, at:at + w],
                                                   scale=1.0, scalar=-3.0e38, op0=ALU.add, op1=ALU.max,
                                                   accum_out=top[:, b:b + 1])
                    at += w
                    if b < len(BANKS) - 1:
                        link(ins)
                ins.then_inc(maxed, 1)
                dve.wait_ge(maxed, a + 1)
                dve.tensor_reduce(neg[:, :], top[:, :], AX.X, ALU.max, negate=True).then_inc(neg_done, 1)
                dve.wait_ge(exped, a + 1)
                link(dve.reciprocal(rden[:, :], den[:, :]))
                dve.tensor_scalar(probs[:, :], probs[:, :], rden[:, :], None, ALU.mult).then_inc(softened, 1)
                for r, tiles in enumerate(ROUNDS):
                    dve.wait_ge(t_full, len(ROUNDS) * a + r + 1)
                    if a and r == 0:
                        dve.wait_ge(attended, HALF)
                    src = ps_t[(len(ROUNDS) * a + r) % 2]
                    if tiles == "new":
                        ins = dve.tensor_copy(new_T[:, :, :], src[0:SAMP, 0:NG, :])
                    else:
                        ins = dve.tensor_copy(probs_T[:, tiles[0]:tiles[-1] + 1, :], src[:, 0:len(tiles), :])
                    ins.then_inc(t_read, 1)
                dve.wait_ge(attended, HALF * (a + 1))
                for h in range(2):
                    half = slice(DH * h, DH * (h + 1))
                    dve.tensor_copy(att[half, :, SAMP // 2 * a:SAMP // 2 * (a + 1)].rearrange("p a (s e) -> p a s e", e=TS),
                                    ps_o[a][half, :, :, TS * h:TS * (h + 1)]).then_inc(att_put, 1)

        @block.scalar
        def _(act):
            for a in range(2):
                act.wait_ge(neg_done, a + 1)
                if a:
                    act.wait_ge(softened, 1)
                act.activation(probs[:, :], probs[:, :], ACT.Exp, bias=neg[:, :], accum_out=den[:, :]).then_inc(exped, 1)


COEF = ("beta", "neg_beta_eG", "eG", "decay_k", "decay_S", "G", "g")
NCO = len(COEF)
LEVELS = [2 ** n for n in range(1, 7)]
BIG = 1.0e30


class Steps:

    def __init__(self, sem, names):
        self.sem, self.names, self.n = sem, names, 0

    def done(self, ins, name):
        assert self.names[self.n % len(self.names)] == name, (name, self.names[self.n % len(self.names)])
        self.n += 1
        ins.then_inc(self.sem, 1)

    def wait(self, eng, name, i=0):
        eng.wait_ge(self.sem, len(self.names) * i + self.names.index(name) + 1)

    def wait_last(self, eng, name, i):
        if not (isinstance(i, int) and i == 0):
            eng.wait_ge(self.sem, len(self.names) * i + self.names.index(name) + 1 - len(self.names))


def lower(x, b):
    return halves(x, b)[..., 0, :]


def upper(x, b):
    return halves(x, b)[..., 1, :]


def halves(x, b):
    lead = "p" if len(x.shape) == 2 else "p h"
    return x.rearrange(f"{lead} (n two b) -> {lead} n two b", two=2, b=b)


def heads(x):
    return x.unsqueeze(1).broadcast_to([x.shape[0], NHB] + list(x.shape[1:]))


def decay_coefficients(nc, t, ab, coef):
    NB = NBLK + 1
    with ExitStack() as ctx:
        sb = lambda name, shape, dt=F32: ctx.enter_context(nc.sbuf_tensor(name, shape, dt))
        sem = t["sem"]
        dt_b = sb("dt_b", [P, NHB])
        a_log = sb("a_log", [P, NHB])
        tri = sb("tri_incl", [P, 2, P])
        same = sb("same", [P, 2, P])
        x = sb("gx", [P, NB, NHB])
        y = sb("gy", [P, NB, NHB])
        ps = ctx.enter_context(nc.psum_tensor("ps_G", [P, 2, 512], F32))
        loaded, v, a, summed = sem("g_loaded"), sem("g_dve"), sem("g_act"), sem("g_summed")
        block = ctx.enter_context(nc.Block(name="decay_coefficients"))
        c = {n: coef[:, :, k, :] for k, n in enumerate(COEF)}
        over = lambda s: s.unsqueeze(1).broadcast_to([P, NB, NHB])

        @block.sync
        def _(sp):
            sp.dma_start(dt_b[:, :], t["dt_bias"].partition_broadcast(P)).then_inc(loaded, 16)
            sp.dma_start(a_log[:, :], t["a_log"].partition_broadcast(P)).then_inc(loaded, 16)
            sp.dma_start(tri[:, :, :], t["tri_incl"]).then_inc(loaded, 16)
            sp.dma_start(same[:, :, :], t["same"]).then_inc(loaded, 16)

        @block.vector
        def _(dve):
            n = [0]

            def link(ins):
                n[0] += 1
                ins.then_inc(v, 1)
                dve.wait_ge(v, n[0])
            dve.wait_ge(loaded, 64)
            link(dve.tensor_tensor(x[:, :, :], ab[:, :, 0:NHB], over(dt_b[:, :]), ALU.add))
            link(dve.scalar_tensor_tensor(out=y[:, :, :], in0=x[:, :, :], scalar=-1.0, in1=x[:, :, :],
                                          op0=ALU.mult, op1=ALU.min))
            link(dve.tensor_scalar(x[:, :, :], x[:, :, :], 0.0, None, ALU.max))
            dve.wait_ge(a, 4)
            link(dve.tensor_tensor(x[:, :, :], x[:, :, :], y[:, :, :], ALU.add))
            link(dve.scalar_tensor_tensor(out=c["g"], in0=x[:, :, :], scalar=-1.0, in1=over(a_log[:, :]),
                                          op0=ALU.mult, op1=ALU.mult))
            dve.wait_ge(summed, 1)
            pairs = [(slice(0, P), slice(0, NBLK), 0), (slice(0, SAMP), slice(NBLK, NB), NBLK * NHB)]
            for rows, bl, at in pairs:
                w = (bl.stop - bl.start) * NHB
                G = ps[rows, 0, at:at + w].rearrange("p (b h) -> p b h", h=NHB)
                last = ps[rows, 1, at:at + w].rearrange("p (b h) -> p b h", h=NHB)
                link(dve.tensor_copy(c["G"][rows, bl], G))
                link(dve.tensor_copy(c["decay_S"][rows, bl], last))
                link(dve.tensor_tensor(c["decay_k"][rows, bl], c["decay_S"][rows, bl], c["G"][rows, bl],
                                       ALU.subtract))
            dve.wait_ge(a, 8)
            dve.scalar_tensor_tensor(out=c["neg_beta_eG"], in0=c["eG"], scalar=-1.0, in1=c["beta"],
                                     op0=ALU.mult, op1=ALU.mult).then_inc(v, 1)

        @block.scalar
        def _(act):
            n = [0]

            def link(ins):
                n[0] += 1
                ins.then_inc(a, 1)
                act.wait_ge(a, n[0])
            link(act.activation(c["beta"], ab[:, :, NHB:], ACT.Sigmoid))
            act.wait_ge(v, 2)
            link(act.activation(y[:, :, :], y[:, :, :], ACT.Exp))
            link(act.activation(y[:, :, :], y[:, :, :], ACT.Ln, bias=1.0))
            act.wait_ge(loaded, 64)
            link(act.activation(a_log[:, :], a_log[:, :], ACT.Exp))
            act.wait_ge(v, 11)
            link(act.activation(c["eG"][:, 0:NBLK], c["G"][:, 0:NBLK], ACT.Exp))
            link(act.activation(c["eG"][0:SAMP, NBLK:], c["G"][0:SAMP, NBLK:], ACT.Exp))
            two = coef[:, 0:NBLK, 3:5, :].rearrange("p b c h -> p b (c h)")
            link(act.activation(two, two, ACT.Exp))
            two = coef[0:SAMP, NBLK:, 3:5, :].rearrange("p b c h -> p b (c h)")
            link(act.activation(two, two, ACT.Exp))

        @block.tensor
        def _(pe):
            pe.wait_ge(v, 5)
            pe.wait_ge(loaded, 64)
            for n, m in enumerate((tri, same)):
                pe.matmul(ps[:, n, 0:NBLK * NHB].rearrange("p (b h) -> p b h", h=NHB), m[:, 0, :], c["g"][:, 0:NBLK],
                          start=True, stop=True)
                last = pe.matmul(ps[0:SAMP, n, NBLK * NHB:NB * NHB].unsqueeze(1), m[0:SAMP, 1, 0:SAMP],
                                 c["g"][0:SAMP, NBLK:], start=True, stop=True)
            last.then_inc(summed, 1)


def delta_prompt(nc, t, coef):
    NP2 = NBLK // 2
    with ExitStack() as ctx:
        sb = lambda name, shape, dt=F32: ctx.enter_context(nc.sbuf_tensor(name, shape, dt))
        pb = lambda name, shape: ctx.enter_context(nc.psum_tensor(name, shape, F32))
        sem = t["sem"]
        two = lambda name, shape: [sb(f"{name}{j}", shape) for j in range(2)]
        HW = [P, NHB, P]
        ident, ones, tri = sb("ident_d", [P, P]), sb("ones_d", [P, P]), sb("tri_d", [P, P])
        upper_big = sb("upper_big", [P, P])
        level0, level0_T = sb("level0", [P, P]), sb("level0_T", [P, P])
        levels = sb("levels", [P, len(LEVELS), P // 2])
        x = two("x_d", [P, T_CONV, P])
        sq = two("sq", [P, 2 * NHB, P])
        cf = two("cf", [P, NCO, NHB])
        rn, t1, t2 = two("rn", [P, 2 * NHB]), two("rn_t1", [P, 2 * NHB]), two("rn_t2", [P, 2 * NHB])
        q_eG = two("q_eG", [P, NHB])
        gU, E, EB, EQ = two("gU", HW), two("E", HW), two("EB", HW), two("EQ", HW)
        k_tok, k_T, k_dec, bv = two("k_tok", HW), two("k_hT", HW), two("k_dec", HW), two("bv", HW)
        L, LT, AT = two("L", HW), two("LT", HW), two("AT", HW)
        A = gU
        T, TT = EB, two("TT", HW)
        Y = [two(f"Y{b}_", HW) for b in LEVELS[:-1]]
        Y.append(E)
        S = sb("S", HW)
        rv, vn, qs, o = sb("rv", HW), sb("vn", HW), sb("qs", HW), two("o_d", HW)
        ps = [[pb(f"ps_p{j}{b}", [P, 4, P]) for b in range(2)] for j in range(2)]
        pss = [[pb(f"ps_c{z}{b}", [P, 4, P]) for b in range(2)] for z in range(2)]
        loaded, zeroed = sem("d_const"), sem("d_zeroed")
        x_in = [sem(f"x_in{j}") for j in range(2)]
        o_out = [sem(f"o_out{j}") for j in range(2)]
        s_out = sem("s_out")
        lv = range(len(LEVELS))
        PE1 = ["norms", "G_rows", "k_turned", "v_turned", "kh_turned", "gram_k", "gram_q", "L_turned", "A_turned"]
        for n in lv:
            PE1 += [f"LT{n}", f"TY{n}", f"YT{n}"] if n < lv[-1] else [f"LT{n}", f"YT{n}"]
        DV1 = ["coef", "gU", "rsum", "newton1", "newton2", "r", "r_q", "q_eG", "rel", "k_tok", "bv", "L", "A",
               "T_pairs", "T_init", "TT_pairs", "TT_init"]
        for n in lv:
            DV1 += [f"Y{n}", f"T{n}", f"TT{n}"] if n < lv[-1] else [f"Y{n}", f"TT{n}"]
        AC1 = ["ln", "rough", "E", "kh_T", "LT", "AT"]
        PL1 = ["sq", "EB", "EQ", "k_dec"]
        pe1 = [Steps(sem(f"pe_prep{j}"), PE1) for j in range(2)]
        dv1 = [Steps(sem(f"dve_prep{j}"), DV1) for j in range(2)]
        ac1 = [Steps(sem(f"act_prep{j}"), AC1) for j in range(2)]
        pl1 = [Steps(sem(f"pool_prep{j}"), PL1) for j in range(2)]
        each = lambda names: [f"{n}{j}" for j in range(2) for n in names]
        pe2 = [Steps(sem(f"pe_scan{z}"), each(["kS", "qS", "Tr", "Av", "kv"])) for z in range(2)]
        dv2 = [Steps(sem(f"dve_scan{z}"), each(["rv", "S", "o"])) for z in range(2)]
        ac2 = [Steps(sem(f"act_scan{z}"), each(["qs", "vn"])) for z in range(2)]
        block = ctx.enter_context(nc.Block(name="delta_prompt"))
        H3 = [slice(0, 3), slice(3, 6)]

        def passes(eng, body):
            body(0)
            with eng.Fori(1, NP2) as i:
                body(i)

        @block.sync
        def _(sp):
            for dst, name in ((ident, "ident"), (ones, "ones"), (tri, "tri"), (upper_big, "upper_big"),
                              (level0, "level0"), (level0_T, "level0_T")):
                sp.dma_start(dst[:, :], t[name]).then_inc(loaded, 16)
            sp.dma_start(levels[:, :, :], t["levels"]).then_inc(loaded, 16)

            def body(i):
                for j in range(2):
                    for z in range(2):
                        pe2[z].wait_last(sp, f"qS{j}", i)
                    pe1[j].wait_last(sp, "gram_q", i)
                    sp.dma_start(x[j][:, :, :], t["conv_d"][:, :, 0:SEQ].rearrange("a p (n two m) -> two p a n m", two=2, m=P)
                                 [j, :, :, bass.ds(i, 1)].rearrange("p a n m -> p a (n m)")).then_inc(x_in[j], 16)
            passes(sp, body)
            for z in range(2):
                dv2[z].wait(sp, "S1", NP2 - 1)
            sp.dma_start(t["gdn_p"].rearrange("h k v -> k h v"), S[:, :, :]).then_inc(s_out, 16)
            sp.wait_ge(s_out, 16)

        @block.gpsimd
        def _(pool):
            for y in Y[:-1]:
                for j in range(2):
                    pool.memset(y[j][:, :, :], 0.0).then_inc(zeroed, 1)
            pool.memset(S[:, :, :], 0.0).then_inc(zeroed, 1)

            def body(i):
                for j in range(2):
                    pool.wait_ge(x_in[j], 16 * (i + 1))
                    pe1[j].wait_last(pool, "norms", i)
                    pl1[j].done(pool.tensor_tensor(sq[j][:, :, :], x[j][:, 0:2 * NHB, :], x[j][:, 0:2 * NHB, :], ALU.mult), "sq")
                for j in range(2):
                    ac1[j].wait(pool, "E", i)
                    pl1[j].done(pool.tensor_tensor(EB[j][:, :, :], E[j][:, :, :], bc(cf[j][:, 0, :], P), ALU.mult), "EB")
                    dv1[j].wait(pool, "r_q", i)
                    pl1[j].done(pool.tensor_tensor(EQ[j][:, :, :], E[j][:, :, :], bc(rn[j][:, 0:NHB], P), ALU.mult), "EQ")
                    dv1[j].wait(pool, "k_tok", i)
                    for z in range(2):
                        pe2[z].wait_last(pool, f"kv{j}", i)
                    pl1[j].done(pool.tensor_tensor(k_dec[j][:, :, :], k_tok[j][:, :, :], bc(cf[j][:, 3, :], P), ALU.mult), "k_dec")
                for j in range(2):
                    for z in range(2):
                        dv2[z].wait(pool, f"o{j}", i)
                    pool.dma_start(t["o_d"][bass.ds(2 * P * i + P * j, P), :], o[j][:, :, :].rearrange("p h v -> p (h v)")
                                   ).then_inc(o_out[j], 16)
            passes(pool, body)
            for j in range(2):
                pool.wait_ge(o_out[j], 16 * NP2)

        @block.tensor
        def _(pe):
            pe.wait_ge(loaded, 16 * 7)
            pe.wait_ge(zeroed, 2 * len(Y) - 1)

            def six(j, f):
                for h in range(NHB):
                    last = f(ps[j][h // 3][:, h % 3, :], h)
                return last

            def prep(i):
                for j in range(2):
                    pl1[j].wait(pe, "sq", i)
                    dv1[j].wait_last(pe, f"TT{lv[-1]}", i)
                    for n in range(2 * NHB):
                        last = pe.matmul(ps[j][0][:, 0, n:n + 1], sq[j][:, n, :], ones[:, 0:1], start=True, stop=True)
                    pe1[j].done(last, "norms")
                for j in range(2):
                    dv1[j].wait(pe, "rsum", i)
                    for z in range(2):
                        last = pe.matmul(ps[j][z][:, 0:3, :].rearrange("p h n -> p (h n)"), ones[:, :],
                                         gU[j][:, H3[z], :].rearrange("p h n -> p (h n)"), start=True, stop=True)
                    pe1[j].done(last, "G_rows")
                for j in range(2):
                    dv1[j].wait(pe, "rel", i)
                    pe1[j].done(six(j, lambda out, h: pe.transpose(out, x[j][:, NHB + h, :], ident[:, :])), "k_turned")
                for j in range(2):
                    dv1[j].wait(pe, "k_tok", i)
                    pe1[j].done(six(j, lambda out, h: pe.transpose(out, x[j][:, 2 * NHB + h, :], ident[:, :])), "v_turned")
                for j in range(2):
                    dv1[j].wait(pe, "bv", i)
                    pe1[j].done(six(j, lambda out, h: pe.transpose(out, k_tok[j][:, h, :], ident[:, :])), "kh_turned")
                for j in range(2):
                    ac1[j].wait(pe, "kh_T", i)
                    pe1[j].done(six(j, lambda out, h: pe.matmul(out, k_T[j][:, h, :], k_T[j][:, h, :], start=True, stop=True)), "gram_k")
                for j in range(2):
                    dv1[j].wait(pe, "L", i)
                    pe1[j].done(six(j, lambda out, h: pe.matmul(out, x[j][:, h, :], k_T[j][:, h, :], start=True, stop=True)), "gram_q")
                for j in range(2):
                    dv1[j].wait(pe, "A", i)
                    pe1[j].done(six(j, lambda out, h: pe.transpose(out, L[j][:, h, :], ident[:, :])), "L_turned")
                for j in range(2):
                    ac1[j].wait(pe, "LT", i)
                    pe1[j].done(six(j, lambda out, h: pe.transpose(out, A[j][:, h, :], ident[:, :])), "A_turned")
                for n, b in enumerate(LEVELS):
                    def level(j, bank, lhs, rhs, name, rows=P):
                        for h in range(NHB):
                            out = bank[0:rows].rearrange("p a n -> p (a n)")[:, 64 * h:64 * (h + 1)].rearrange("p (n b) -> p n b", b=b)
                            last = pe.matmul(out, lhs[:, h, 0:rows], rhs(h), start=True, stop=True)
                        pe1[j].done(last, name)
                    for j in range(2):
                        if n == 0:
                            ac1[j].wait(pe, "AT", i)
                        dv1[j].wait(pe, f"TT{n - 1}" if n else "TT_init", i)
                        level(j, ps[j][0], LT[j], lambda h: lower(T[j][:, h, :], b), f"LT{n}")
                    for j in range(2):
                        dv1[j].wait(pe, f"Y{n}", i)
                        if n < lv[-1]:
                            level(j, ps[j][1], TT[j], lambda h: lower(Y[n][j][:, h, :], b), f"TY{n}")
                        level(j, ps[j][0], Y[n][j], lambda h: upper(TT[j][:, h, :], b), f"YT{n}",
                              P if n < lv[-1] else b)

            def scan(i, j):
                def three(z, b, f):
                    for h in range(3 * z, 3 * z + 3):
                        last = f(pss[z][b][:, h % 3, :], h)
                    return last
                for z in range(2):
                    if j == 0:
                        ac1[j].wait(pe, "kh_T", i)
                        dv2[z].wait_last(pe, "o1", i)
                    else:
                        dv2[z].wait(pe, "o0", i)
                    pe2[z].done(three(z, 0, lambda out, h: pe.matmul(out, k_T[j][:, h, :], S[:, h, :], start=True, stop=True)), f"kS{j}")
                    pe2[z].done(three(z, 1, lambda out, h: pe.matmul(out, x[j][:, h, :], S[:, h, :], start=True, stop=True)), f"qS{j}")
                for z in range(2):
                    dv1[j].wait(pe, f"TT{lv[-1]}", i)
                    dv2[z].wait(pe, f"rv{j}", i)
                    pe2[z].done(three(z, 0, lambda out, h: pe.matmul(out, TT[j][:, h, :], rv[:, h, :], start=True, stop=True)), f"Tr{j}")
                for z in range(2):
                    ac2[z].wait(pe, f"qs{j}", i)
                    ac2[z].wait(pe, f"vn{j}", i)
                    pe2[z].done(three(z, 1, lambda out, h: pe.matmul(out, AT[j][:, h, :], vn[:, h, :], start=True, stop=True)), f"Av{j}")
                    pl1[j].wait(pe, "k_dec", i)
                    pe2[z].done(three(z, 0, lambda out, h: pe.matmul(out, k_dec[j][:, h, :], vn[:, h, :], start=True, stop=True)), f"kv{j}")

            def body(i):
                prep(i)
                scan(i, 0)
                scan(i, 1)
            passes(pe, body)

        @block.vector
        def _(dve):
            dve.wait_ge(loaded, 16 * 7)
            dve.wait_ge(zeroed, 2 * len(Y) - 1)

            def both(j, f):
                for z in range(2):
                    last = f(ps[j][z][:, 0:3, :], H3[z])
                return last

            def prep(i):
                for j in range(2):
                    C, R = cf[j], rn[j]
                    for z in range(2):
                        dv2[z].wait_last(dve, f"S{j}", i)
                    dv1[j].wait_last(dve, f"TT{lv[-1]}", i)
                    pl1[j].wait_last(dve, "k_dec", i)
                    dv1[j].done(dve.tensor_copy(C[:, :, :].rearrange("p c h -> p (c h)").unsqueeze(1),
                                                coef[:, bass.ds(2 * i + j, 1), :, :].rearrange("p a c h -> p a (c h)")), "coef")
                    dv1[j].wait(dve, "coef", i)
                    pe1[j].wait_last(dve, "A_turned", i)
                    dv1[j].done(dve.tensor_tensor(gU[j][:, :, :], heads2(tri), bc(C[:, 6, :], P), ALU.mult), "gU")
                    pe1[j].wait(dve, "norms", i)
                    ac1[j].wait_last(dve, "rough", i)
                    dv1[j].done(dve.tensor_scalar(t1[j][:, :], ps[j][0][:, 0, 0:2 * NHB], RMS_EPS, None, ALU.add), "rsum")
                for j in range(2):
                    R = rn[j]
                    ac1[j].wait(dve, "rough", i)
                    dv1[j].done(dve.tensor_tensor(t2[j][:, :], R[:, :], R[:, :], ALU.mult), "newton1")
                    dv1[j].wait(dve, "newton1", i)
                    dv1[j].done(dve.scalar_tensor_tensor(out=t2[j][:, :], in0=t1[j][:, :], scalar=-0.5, in1=t2[j][:, :],
                                                         op0=ALU.mult, op1=ALU.mult), "newton2")
                    dv1[j].wait(dve, "newton2", i)
                    dv1[j].done(dve.scalar_tensor_tensor(out=R[:, :], in0=t2[j][:, :], scalar=1.5, in1=R[:, :],
                                                         op0=ALU.add, op1=ALU.mult), "r")
                    dv1[j].wait(dve, "r", i)
                    dv1[j].done(dve.tensor_scalar(R[:, 0:NHB], R[:, 0:NHB], DB ** -0.5, None, ALU.mult), "r_q")
                    dv1[j].wait(dve, "r_q", i)
                    dv1[j].done(dve.tensor_tensor(q_eG[j][:, :], R[:, 0:NHB], cf[j][:, 2, :], ALU.mult), "q_eG")
                for j in range(2):
                    pe1[j].wait(dve, "G_rows", i)
                    for h in range(NHB):
                        last = dve.scalar_tensor_tensor(out=E[j][:, h, :], in0=ps[j][h // 3][:, h % 3, :],
                                                        scalar=cf[j][:, 5, h:h + 1], in1=upper_big[:, :],
                                                        op0=ALU.subtract, op1=ALU.max)
                    dv1[j].done(last, "rel")
                for j in range(2):
                    pe1[j].wait(dve, "k_turned", i)
                    dv1[j].done(both(j, lambda p, h: dve.tensor_tensor(k_tok[j][:, h, :], p, bc(rn[j][:, NHB:][:, h], P), ALU.mult)), "k_tok")
                for j in range(2):
                    pe1[j].wait(dve, "v_turned", i)
                    dv1[j].done(both(j, lambda p, h: dve.tensor_tensor(bv[j][:, h, :], p, bc(cf[j][:, 0, h], P), ALU.mult)), "bv")
                for j in range(2):
                    pe1[j].wait(dve, "gram_k", i)
                    pl1[j].wait(dve, "EB", i)
                    dv1[j].done(both(j, lambda p, h: dve.tensor_tensor(L[j][:, h, :], p, EB[j][:, h, :], ALU.mult)), "L")
                for j in range(2):
                    pe1[j].wait(dve, "gram_q", i)
                    pl1[j].wait(dve, "EQ", i)
                    dv1[j].done(both(j, lambda p, h: dve.tensor_tensor(A[j][:, h, :], p, EQ[j][:, h, :], ALU.mult)), "A")
                for j in range(2):
                    dv1[j].wait(dve, "L", i)
                    dv1[j].done(dve.tensor_tensor(T[j][:, :, :], L[j][:, :, :], heads2(level0), ALU.mult), "T_pairs")
                    dv1[j].wait(dve, "T_pairs", i)
                    dv1[j].done(dve.tensor_tensor(T[j][:, :, :], T[j][:, :, :], heads2(ident), ALU.add), "T_init")
                    ac1[j].wait(dve, "LT", i)
                    dv1[j].done(dve.tensor_tensor(TT[j][:, :, :], LT[j][:, :, :], heads2(level0_T), ALU.mult), "TT_pairs")
                    dv1[j].wait(dve, "TT_pairs", i)
                    dv1[j].done(dve.tensor_tensor(TT[j][:, :, :], TT[j][:, :, :], heads2(ident), ALU.add), "TT_init")
                for n, b in enumerate(LEVELS):
                    got = lambda bank: bank[:, 0:3, :].rearrange("p a n -> p (a n)").rearrange("p (h n b) -> p h n b", h=NHB, b=b)
                    mask = heads(levels[:, n, :].rearrange("p (n b) -> p n b", b=b))
                    for j in range(2):
                        pe1[j].wait(dve, f"LT{n}", i)
                        y = Y[n][j]
                        dv1[j].done(dve.tensor_tensor(lower(y[:, :, :], b), got(ps[j][0]), mask, ALU.mult), f"Y{n}")
                    for j in range(2):
                        if n < lv[-1]:
                            pe1[j].wait(dve, f"TY{n}", i)
                            v = lower(T[j][:, :, :], b)
                            dv1[j].done(dve.tensor_tensor(v, v, got(ps[j][1]), ALU.subtract), f"T{n}")
                        pe1[j].wait(dve, f"YT{n}", i)
                        r = P if n < lv[-1] else b
                        v = upper(TT[j][0:r, :, :], b)
                        dv1[j].done(dve.tensor_tensor(v, v, got(ps[j][0][0:r]), ALU.subtract), f"TT{n}")

            def scan(i, j):
                for z in range(2):
                    pe2[z].wait(dve, f"kS{j}", i)
                    for h in range(3 * z, 3 * z + 3):
                        last = dve.scalar_tensor_tensor(out=rv[:, h, :], in0=pss[z][0][:, h % 3, :],
                                                        scalar=cf[j][:, 1, h:h + 1], in1=bv[j][:, h, :],
                                                        op0=ALU.mult, op1=ALU.add)
                    dv2[z].done(last, f"rv{j}")
                for z in range(2):
                    pe2[z].wait(dve, f"kv{j}", i)
                    for h in range(3 * z, 3 * z + 3):
                        last = dve.scalar_tensor_tensor(out=S[:, h, :], in0=S[:, h, :], scalar=cf[j][:, 4, h:h + 1],
                                                        in1=pss[z][0][:, h % 3, :], op0=ALU.mult, op1=ALU.add)
                    dv2[z].done(last, f"S{j}")
                    pe2[z].wait(dve, f"Av{j}", i)
                    if not (isinstance(i, int) and i == 0):
                        dve.wait_ge(o_out[j], 16 * i)
                    dv2[z].done(dve.tensor_tensor(o[j][:, H3[z], :], pss[z][1][:, 0:3, :], qs[:, H3[z], :], ALU.add), f"o{j}")

            def body(i):
                prep(i)
                scan(i, 0)
                scan(i, 1)
            passes(dve, body)

        @block.scalar
        def _(act):
            def turn(j, dst, name, src, i):
                pe1[j].wait(act, src, i)
                for z in range(2):
                    last = act.activation(dst[:, H3[z], :], ps[j][z][:, 0:3, :], ACT.Copy)
                ac1[j].done(last, name)

            def prep(i):
                for j in range(2):
                    dv1[j].wait(act, "rsum", i)
                    pl1[j].wait_last(act, "EQ", i)
                    for z in range(2):
                        dv2[z].wait_last(act, f"rv{j}", i)
                    ac1[j].done(act.activation(rn[j][:, :], t1[j][:, :], ACT.Ln), "ln")
                    ac1[j].wait(act, "ln", i)
                    ac1[j].done(act.activation(rn[j][:, :], rn[j][:, :], ACT.Exp, scale=-0.5), "rough")
                for j in range(2):
                    dv1[j].wait(act, "rel", i)
                    ac1[j].done(act.activation(E[j][:, :, :], E[j][:, :, :], ACT.Exp, scale=-1.0), "E")
                for j in range(2):
                    for z in range(2):
                        pe2[z].wait_last(act, f"kS{j}", i)
                    turn(j, k_T[j], "kh_T", "kh_turned", i)
                for j in range(2):
                    turn(j, LT[j], "LT", "L_turned", i)
                for j in range(2):
                    for z in range(2):
                        pe2[z].wait_last(act, f"Av{j}", i)
                    turn(j, AT[j], "AT", "A_turned", i)

            def scan(i, j):
                for z in range(2):
                    pe2[z].wait(act, f"qS{j}", i)
                    if j == 0:
                        dv2[z].wait_last(act, "o1", i)
                    else:
                        dv2[z].wait(act, "o0", i)
                    for h in range(3 * z, 3 * z + 3):
                        last = act.activation(qs[:, h, :], pss[z][1][:, h % 3, :], ACT.Copy, scale=q_eG[j][:, h:h + 1])
                    ac2[z].done(last, f"qs{j}")
                for z in range(2):
                    pe2[z].wait(act, f"Tr{j}", i)
                    ac2[z].done(act.activation(vn[:, H3[z], :], pss[z][0][:, 0:3, :], ACT.Copy), f"vn{j}")

            def body(i):
                prep(i)
                scan(i, 0)
                scan(i, 1)
            passes(act, body)


def heads2(x):
    return x[:, :].unsqueeze(1).broadcast_to([P, NHB, P])


def delta_samples(nc, t, coef):
    with ExitStack() as ctx:
        sb = lambda name, shape, dt=F32: ctx.enter_context(nc.sbuf_tensor(name, shape, dt))
        pb = lambda name, shape: ctx.enter_context(nc.psum_tensor(name, shape, F32))
        sem = t["sem"]
        R = SAMP
        ident, ones = sb("ident_e", [P, P]), sb("ones_e", [P, P])
        tri, limit = sb("tri_e", [P, 2, P]), sb("limit_e", [P, P])
        level0, level0_T, levels = sb("level0_e", [P, P]), sb("level0_T_e", [P, P]), sb("levels_e", [P, len(LEVELS), P // 2])
        of_seq, in_seq = sb("of_seq", [P, NSEQ, R]), sb("in_seq", [P, NSEQ])
        x = sb("x_e", [P, T_CONV, R])
        sq = sb("sq_e", [P, 2 * NHB, R])
        st = sb("state_e", [P, NHB, NSEQ, P])
        rn, t1, t2, q_eG = sb("rn_e", [R, 2 * NHB]), sb("t1_e", [R, 2 * NHB]), sb("t2_e", [R, 2 * NHB]), sb("q_eG_e", [R, NHB])
        gs, decay = sb("gs", [R, NHB, NSEQ]), sb("decay_e", [P, NHB, NSEQ])
        gU, E, L, A = sb("gU_e", [R, NHB, R]), sb("E_e", [R, NHB, R]), sb("L_e", [R, NHB, R]), sb("A_e", [R, NHB, R])
        EB, EQ = sb("EB_e", [R, NHB, R]), sb("EQ_e", [R, NHB, R])
        LT, AT, T, TT = sb("LT_e", [R, NHB, R]), sb("AT_e", [R, NHB, R]), sb("T_e", [R, NHB, R]), sb("TT_e", [R, NHB, R])
        LV = [2, 4]
        Y = [sb(f"Y{b}_e", [R, NHB, R]) for b in LV]
        k_tok, bv, k_dec, k_T = sb("k_tok_e", [R, NHB, P]), sb("bv_e", [R, NHB, P]), sb("k_dec_e", [R, NHB, P]), sb("k_T_e", [P, NHB, R])
        k_seq, q_seq = sb("k_seq", [P, NHB, NSEQ, R]), sb("q_seq", [P, NHB, NSEQ, R])
        rv, vn, qs, o = sb("rv_e", [R, NHB, P]), sb("vn_e", [R, NHB, P]), sb("qs_e", [R, NHB, P]), sb("o_e", [R, NHB, P])
        v_seq = sb("v_seq", [R, 2, NSEQ, P])
        bank = [pb(f"ps_e{b}", [P, 512]) for b in range(8)]
        loaded, out = sem("e_loaded"), sem("e_out")
        D_, A_, T_ = ["zero0", "zero1", "sq", "gs", "gU", "rsum", "n1", "n2", "r", "rq", "q_eG", "decay", "rel", "k_tok", "bv", "EB", "EQ",
                      "k_dec", "L", "A", "T_pairs", "T_init", "TT_pairs", "TT_init", "Y0", "T0", "TT0", "Y1", "T1", "TT1", "k_seq",
                      "q_seq", "rv", "o"] + [f"{n}{h}" for h in range(NHB) for n in ("vs", "st")], \
            ["ln", "rough", "decay", "E", "k_T", "LT", "AT", "qs", "vn"], \
            ["norms", "decay", "G_rows", "k", "v", "k_T", "gk", "gq", "LT", "AT", "LT0", "TY0", "YT0", "LT1", "TY1", "YT1",
             "kS", "qS", "Tr", "Av"] + [f"kv{h}" for h in range(NHB)]
        dv, ac, pe_ = Steps(sem("e_dve"), D_), Steps(sem("e_act"), A_), Steps(sem("e_pe"), T_)
        block = ctx.enter_context(nc.Block(name="delta_samples"))
        c = {n: coef[0:R, NBLK, k, :] for k, n in enumerate(COEF)}
        six = lambda x: x.unsqueeze(1).broadcast_to([x.shape[0], NHB] + list(x.shape[1:]))
        sixty = lambda b, n=R: bank[b][0:n, 0:NHB * R].rearrange("p (h n) -> p h n", n=R)
        wide = lambda z: bank[z][0:R, 0:3 * P].rearrange("p (h n) -> p h n", n=P)
        H3 = [slice(0, 3), slice(3, 6)]

        @block.sync
        def _(sp):
            for dst, src in ((ident, "ident"), (ones, "ones"), (limit, "limit"), (level0, "level0"), (level0_T, "level0_T")):
                sp.dma_start(dst[:, :], t[src]).then_inc(loaded, 16)
            for dst, src in ((tri, "tri_incl"), (levels, "levels"), (of_seq, "of_seq")):
                sp.dma_start(dst[:, :, :], t[src]).then_inc(loaded, 16)
            sp.dma_start(in_seq[:, :], t["in_seq"]).then_inc(loaded, 16)
            sp.dma_start(x[:, :, :], t["conv_d"][:, :, SEQ:].rearrange("a p n -> p a n")).then_inc(loaded, 16)
            for s in range(NSEQ):
                sp.dma_start(st[:, :, s, :], t["state_gdn"][s].rearrange("h k v -> k h v")).then_inc(loaded, 16)
            dv.wait(sp, "o")
            sp.dma_start(t["o_d"][SEQ:], o[:, :, :].rearrange("p h v -> p (h v)")).then_inc(out, 16)
            dv.wait(sp, f"st{NHB - 1}")
            for s in range(NSEQ):
                sp.dma_start(t["gdn_s"][s].rearrange("h k v -> k h v"), st[:, :, s, :]).then_inc(out, 16)
            sp.wait_ge(out, 16 * (NSEQ + 1))

        @block.tensor
        def _(pe):
            pe.wait_ge(loaded, 16 * (10 + NSEQ))

            def per_head(b, rows, f, n=R):
                for h in range(NHB):
                    last = f(bank[b][0:rows, n * h:n * (h + 1)], h)
                return last

            def halves3(z0, f):
                for h in range(NHB):
                    last = f(bank[z0 + h // 3][0:R, P * (h % 3):P * (h % 3 + 1)], h)
                return last
            mm = lambda out, a, b: pe.matmul(out, a, b, start=True, stop=True)
            dv.wait(pe, "sq")
            for n in range(2 * NHB):
                last = mm(bank[0][0:R, n:n + 1], sq[:, n, :], ones[:, 0:1])
            pe_.done(last, "norms")
            dv.wait(pe, "gs")
            pe_.done(mm(bank[1][:, 0:NHB * NSEQ], ones[0:R, :], gs[:, :, :].rearrange("p h s -> p (h s)")), "decay")
            dv.wait(pe, "gU")
            pe_.done(mm(bank[2][0:R, 0:NHB * R], ones[0:R, 0:R], gU[:, :, :].rearrange("p h n -> p (h n)")), "G_rows")
            pe_.done(halves3(4, lambda out, h: pe.transpose(out, x[:, NHB + h, :], ident[:, :])), "k")
            pe_.done(halves3(6, lambda out, h: pe.transpose(out, x[:, 2 * NHB + h, :], ident[:, :])), "v")
            dv.wait(pe, "k_tok")
            pe_.done(per_head(0, P, lambda out, h: pe.transpose(out, k_tok[:, h, :], ident[0:R, 0:R])), "k_T")
            ac.wait(pe, "k_T")
            dv.wait(pe, "rel")
            pe_.done(per_head(1, R, lambda out, h: mm(out, k_T[:, h, :], k_T[:, h, :])), "gk")
            pe_.done(per_head(2, R, lambda out, h: mm(out, x[:, h, :], k_T[:, h, :])), "gq")
            dv.wait(pe, "L")
            pe_.done(per_head(3, R, lambda out, h: pe.transpose(out, L[:, h, :], ident[0:R, 0:R])), "LT")
            dv.wait(pe, "A")
            pe_.done(per_head(0, R, lambda out, h: pe.transpose(out, A[:, h, :], ident[0:R, 0:R])), "AT")
            for n, b in enumerate(LV):
                cols = lambda bk: (lambda h: bank[bk][0:R, 32 * h:32 * (h + 1)].rearrange("p (n b) -> p n b", b=b))

                def level(bk, lhs, rhs, name):
                    for h in range(NHB):
                        last = mm(cols(bk)(h), lhs[:, h, :], rhs(h))
                    pe_.done(last, name)
                dv.wait(pe, f"TT{n - 1}" if n else "TT_init")
                level(1, LT, lambda h: lower(T[:, h, :], b), f"LT{n}")
                dv.wait(pe, f"Y{n}")
                level(2, TT, lambda h: lower(Y[n][:, h, :], b), f"TY{n}")
                level(1, Y[n], lambda h: upper(TT[:, h, :], b), f"YT{n}")
            dv.wait(pe, "q_seq")
            for name, w, z0 in (("kS", k_seq, 4), ("qS", q_seq, 6)):
                for h in range(NHB):
                    for s in range(NSEQ):
                        last = pe.matmul(bank[z0 + h // 3][0:R, P * (h % 3):P * (h % 3 + 1)], w[:, h, s, :], st[:, h, s, :],
                                         start=s == 0, stop=s == NSEQ - 1)
                pe_.done(last, name)
            dv.wait(pe, "rv")
            pe_.done(halves3(4, lambda out, h: mm(out, TT[:, h, :], rv[:, h, :])), "Tr")
            ac.wait(pe, "vn")
            pe_.done(halves3(6, lambda out, h: mm(out, AT[:, h, :], vn[:, h, :])), "Av")
            for h in range(NHB):
                dv.wait(pe, f"vs{h}")
                for z in range(2):
                    last = mm(bank[2 * (h % 2) + z][:, :], k_dec[:, h, :],
                              v_seq[:, h % 2, 4 * z:4 * (z + 1), :].rearrange("p s v -> p (s v)"))
                pe_.done(last, f"kv{h}")

        @block.scalar
        def _(act):
            dv.wait(act, "rsum")
            ac.done(act.activation(rn[:, :], t1[:, :], ACT.Ln), "ln")
            ac.wait(act, "ln")
            ac.done(act.activation(rn[:, :], rn[:, :], ACT.Exp, scale=-0.5), "rough")
            dv.wait(act, "decay")
            ac.done(act.activation(decay[:, :, :], decay[:, :, :], ACT.Exp), "decay")
            dv.wait(act, "rel")
            ac.done(act.activation(E[:, :, :], E[:, :, :], ACT.Exp, scale=-1.0), "E")
            pe_.wait(act, "k_T")
            ac.done(act.activation(k_T[:, :, :], sixty(0, P), ACT.Copy), "k_T")
            pe_.wait(act, "LT")
            ac.done(act.activation(LT[:, :, :], sixty(3), ACT.Copy), "LT")
            pe_.wait(act, "AT")
            ac.done(act.activation(AT[:, :, :], sixty(0), ACT.Copy), "AT")
            pe_.wait(act, "qS")
            for h in range(NHB):
                last = act.activation(qs[:, h, :], wide(6 + h // 3)[:, h % 3, :], ACT.Copy, scale=q_eG[:, h:h + 1])
            ac.done(last, "qs")
            pe_.wait(act, "Tr")
            for z in range(2):
                last = act.activation(vn[:, H3[z], :], wide(4 + z), ACT.Copy)
            ac.done(last, "vn")

        @block.vector
        def _(dve):
            def do(ins, name):
                dv.done(ins, name)
                dv.wait(dve, name)
            tt, sts = dve.tensor_tensor, dve.scalar_tensor_tensor
            do(dve.memset(Y[0][:, :, :], 0.0), "zero0")
            do(dve.memset(Y[1][:, :, :], 0.0), "zero1")
            dve.wait_ge(loaded, 16 * (10 + NSEQ))
            do(tt(sq[:, :, :], x[:, 0:2 * NHB, :], x[:, 0:2 * NHB, :], ALU.mult), "sq")
            do(tt(gs[:, :, :], bc(c["g"], NSEQ), six(in_seq[0:R, :]), ALU.mult), "gs")
            do(tt(gU[:, :, :], six(tri[0:R, 1, 0:R]), bc(c["g"], R), ALU.mult), "gU")
            pe_.wait(dve, "norms")
            do(dve.tensor_scalar(t1[:, :], bank[0][0:R, 0:2 * NHB], RMS_EPS, None, ALU.add), "rsum")
            ac.wait(dve, "rough")
            do(tt(t2[:, :], rn[:, :], rn[:, :], ALU.mult), "n1")
            do(sts(out=t2[:, :], in0=t1[:, :], scalar=-0.5, in1=t2[:, :], op0=ALU.mult, op1=ALU.mult), "n2")
            do(sts(out=rn[:, :], in0=t2[:, :], scalar=1.5, in1=rn[:, :], op0=ALU.add, op1=ALU.mult), "r")
            do(dve.tensor_scalar(rn[:, 0:NHB], rn[:, 0:NHB], DB ** -0.5, None, ALU.mult), "rq")
            do(tt(q_eG[:, :], rn[:, 0:NHB], c["eG"], ALU.mult), "q_eG")
            pe_.wait(dve, "decay")
            do(dve.tensor_copy(decay[:, :, :], bank[1][:, 0:NHB * NSEQ].rearrange("p (h s) -> p h s", s=NSEQ)), "decay")
            pe_.wait(dve, "G_rows")
            for h in range(NHB):
                last = sts(out=E[:, h, :], in0=sixty(2)[:, h, :], scalar=c["G"][:, h:h + 1], in1=limit[0:R, 0:R],
                           op0=ALU.subtract, op1=ALU.max)
            do(last, "rel")
            pe_.wait(dve, "k")
            for z in range(2):
                last = tt(k_tok[:, H3[z], :], wide(4 + z), bc(rn[:, NHB:][:, H3[z]], P), ALU.mult)
            do(last, "k_tok")
            pe_.wait(dve, "v")
            for z in range(2):
                last = tt(bv[:, H3[z], :], wide(6 + z), bc(c["beta"][:, H3[z]], P), ALU.mult)
            do(last, "bv")
            ac.wait(dve, "E")
            do(tt(EB[:, :, :], E[:, :, :], bc(c["beta"], R), ALU.mult), "EB")
            do(tt(EQ[:, :, :], E[:, :, :], bc(rn[:, 0:NHB], R), ALU.mult), "EQ")
            do(tt(k_dec[:, :, :], k_tok[:, :, :], bc(c["decay_k"], P), ALU.mult), "k_dec")
            pe_.wait(dve, "gk")
            do(tt(L[:, :, :], sixty(1), EB[:, :, :], ALU.mult), "L")
            pe_.wait(dve, "gq")
            do(tt(A[:, :, :], sixty(2), EQ[:, :, :], ALU.mult), "A")
            do(tt(T[:, :, :], L[:, :, :], six(level0[0:R, 0:R]), ALU.mult), "T_pairs")
            do(tt(T[:, :, :], T[:, :, :], six(ident[0:R, 0:R]), ALU.add), "T_init")
            ac.wait(dve, "LT")
            do(tt(TT[:, :, :], LT[:, :, :], six(level0_T[0:R, 0:R]), ALU.mult), "TT_pairs")
            do(tt(TT[:, :, :], TT[:, :, :], six(ident[0:R, 0:R]), ALU.add), "TT_init")
            for n, b in enumerate(LV):
                got = lambda bk: bank[bk][0:R, 0:NHB * 32].rearrange("p (h n b) -> p h n b", h=NHB, b=b)
                pe_.wait(dve, f"LT{n}")
                do(tt(lower(Y[n][:, :, :], b), got(1), six(levels[0:R, n, 0:32].rearrange("p (n b) -> p n b", b=b)), ALU.mult), f"Y{n}")
                pe_.wait(dve, f"TY{n}")
                do(tt(lower(T[:, :, :], b), lower(T[:, :, :], b), got(2), ALU.subtract), f"T{n}")
                pe_.wait(dve, f"YT{n}")
                do(tt(upper(TT[:, :, :], b), upper(TT[:, :, :], b), got(1), ALU.subtract), f"TT{n}")
            ac.wait(dve, "k_T")
            over_s = lambda a: a.unsqueeze(1).broadcast_to([P, NSEQ, R])
            for h in range(NHB):
                last = tt(k_seq[:, h], over_s(k_T[:, h, :]), of_seq[:, :, :], ALU.mult)
            do(last, "k_seq")
            for h in range(NHB):
                last = tt(q_seq[:, h], over_s(x[:, h, :]), of_seq[:, :, :], ALU.mult)
            do(last, "q_seq")
            pe_.wait(dve, "kS")
            for h in range(NHB):
                last = sts(out=rv[:, h, :], in0=wide(4 + h // 3)[:, h % 3, :], scalar=c["neg_beta_eG"][:, h:h + 1],
                           in1=bv[:, h, :], op0=ALU.mult, op1=ALU.add)
            do(last, "rv")
            pe_.wait(dve, "Av")
            for z in range(2):
                last = tt(o[:, H3[z], :], wide(6 + z), qs[:, H3[z], :], ALU.add)
            do(last, "o")
            for h in range(NHB):
                if h >= 2:
                    pe_.wait(dve, f"kv{h - 2}")
                do(tt(v_seq[:, h % 2], vn[:, h, :].unsqueeze(1).broadcast_to([R, NSEQ, P]), bc(in_seq[0:R, :], P), ALU.mult), f"vs{h}")
                pe_.wait(dve, f"kv{h}")
                for s in range(NSEQ):
                    last = sts(out=st[:, h, s, :], in0=st[:, h, s, :], scalar=decay[:, h, s:s + 1],
                               in1=bank[2 * (h % 2) + s // 4][:, P * (s % 4):P * (s % 4 + 1)], op0=ALU.mult, op1=ALU.add)
                do(last, f"st{h}")


SUP = 256
NSUP = SEQ // SUP
KA = WA // P
FEW = T_ZA + T_ZB


def merge_branches(nc, t):
    with ExitStack() as ctx:
        sb = lambda name, shape, dt=F32: ctx.enter_context(nc.sbuf_tensor(name, shape, dt))
        pb = lambda name, shape: ctx.enter_context(nc.psum_tensor(name, shape, F32))
        sem = t["sem"]
        w_hi, w_lo = sb("wab_hi", [P, 2 * KA, D], F32R), sb("wab_lo", [P, 2 * KA, D], F32R)
        u_hi, u_lo = sb("u_hi", [P, 2, FEW, SUP], F32R), sb("u_lo", [P, 2, FEW, SUP], F32R)
        w_raw = sb("wab_raw", [P, 2, D])
        ident, norm = sb("ident_f", [P, P]), sb("norm_f", [P, 1])
        rows = sb("rows_f", [P, 2 * KA, P])
        stat = sb("stat_f", [P, NG, NSTAT])
        z = sb("z_f", [P, FEW, P])
        gated = sb("gated", [P, FEW, P])
        least, share, total = sb("least", [P, HPG]), sb("share", [P, NG, HPG]), sb("total", [P, HPG])
        wd = sb("wd", [P, NG, HPG])
        ss, root, rs = sb("ss", [P, NHB]), sb("root", [P, NHB]), sb("rs", [P, NHB])
        sqs = gated[:, T_ZA:, :]
        gates = sb("gates", [P, 2, 2, SUP])
        prod = sb("prod", [P, 2, 2, SUP])
        merged = sb("merged", [P, 2, SUP])
        ps_t = [pb(f"ps_ft{b}", [P, 4, P]) for b in range(3)]
        ps_m = [pb(f"ps_fm{b}", [P, 2, SUP]) for b in range(2)]
        const_in = sem("f_const")
        wr_in = [sem(f"f_wr_in{j}") for j in range(2)]
        w_hi_done, w_lo_done = sem("f_w_hi"), sem("f_w_lo")
        row_in, z_in, gate_in = sem("f_rows"), sem("f_z"), [sem(f"f_gate{j}") for j in range(2)]
        d_steps = Steps(sem("f_dve"), ["least", "diff", "wd", "total", "rtotal", "share", "att", "ss", "eps", "rs", "o"]
                        + [f"g{b}" for b in range(3)] + ["split"])
        a_steps = Steps(sem("f_act"), ["share", "squares", "root", "hi"])
        p_steps = Steps(sem("f_pe"), [f"turn{b}" for b in range(3)])
        mm_done, prod_done, sum_done = sem("f_mm"), sem("f_prod"), sem("f_sum")
        out = [sem(f"f_out{j}") for j in range(2)]
        block = ctx.enter_context(nc.Block(name="merge_branches"))
        NF = D // P

        def blocks(n):
            return [2 * n] if isinstance(n, int) and n == NSUP else [2 * n, 2 * n + 1]

        def flow(eng, prep, mult):
            prep(0, 0)
            for n in range(1, 2):
                prep(n, n % 2), mult(n - 1, (n - 1) % 2)
            with eng.Fori(0, NSUP // 2 - 1) as i:
                prep(2 * i + 2, 0), mult(2 * i + 1, 1)
                prep(2 * i + 3, 1), mult(2 * i + 2, 0)
            prep(NSUP, 0), mult(NSUP - 1, 1)
            mult(NSUP, 0)
        size = lambda n: SAMP if isinstance(n, int) and n == NSUP else SUP
        rows_of = lambda n: SAMP if isinstance(n, int) and n == NSUP else P

        @block.sync
        def _(sp):
            sp.dma_start(ident[:, :], t["ident"]).then_inc(const_in, 16)
            sp.dma_start(norm[:, :], t["gdn_norm"].rearrange("(p a) -> p a", a=1)).then_inc(const_in, 16)

            def prep(n, j):
                for k, b in enumerate(blocks(n)):
                    m = rows_of(n)
                    if not (isinstance(n, int) and n == 0 and k == 0):
                        p_steps.wait(sp, "turn2", b - 1)
                        d_steps.wait(sp, "g2" if m == P else "split", b - 1)
                    if m == P:
                        tok = bass.ds(P * b, P)
                        sp.dma_start(rows[:, 0:KA, :].rearrange("p a n -> p (a n)"),
                                     t["att_d"][tok].rearrange("p g n -> p (g n)")).then_inc(row_in, 16)
                        sp.dma_start(stat[:, :, :], t["stats_d"][tok]).then_inc(row_in, 16)
                    else:
                        tok = slice(SEQ, NT)
                        sp.dma_start(gated[:, 0:T_ZA, 0:SAMP], t["att_s"]).then_inc(row_in, 16)
                        sp.dma_start(stat[0:SAMP, :, :], t["stats_d"][0:SAMP]).then_inc(row_in, 16)
                    sp.dma_start(rows[0:m, KA:, :].rearrange("p a n -> p (a n)"), t["o_d"][tok]).then_inc(row_in, 16)
                    sp.dma_start(z[:, :, 0:m], t["z_d"][:, :, tok].rearrange("a p n -> p a n")).then_inc(z_in, 16)

            def mult(n, j):
                w = size(n)
                tok = bass.ds(SUP * n, SUP) if w == SUP else slice(SEQ, NT)
                for f in range(NF):
                    u = NF * n + f
                    if not (isinstance(n, int) and n == 0 and f < 2):
                        sp.wait_ge(prod_done, u - 1)
                    sp.dma_start(gates[:, f % 2, :, 0:w], t["g_d"][f::NF, :, tok].rearrange("a p n -> p a n")
                                 ).then_inc(gate_in[f % 2], 16)
            flow(sp, prep, mult)

        @block.tensor
        def _(pe):
            pe.wait_ge(const_in, 32)

            def prep(n, j):
                for k, b in enumerate(blocks(n)):
                    m = rows_of(n)
                    for r in range(3):
                        if not (isinstance(n, int) and n == 0 and k == 0):
                            d_steps.wait(pe, f"g{r}", b - 1)
                        if r == 0:
                            d_steps.wait(pe, "o", b)
                        for a in range(4):
                            last = pe.transpose(ps_t[r][:, a, 0:m], rows[0:m, 4 * r + a, :], ident[0:m, 0:m])
                        p_steps.done(last, f"turn{r}")

            def mult(n, j):
                w = size(n)
                if isinstance(n, int) and n == 0:
                    pe.wait_ge(w_lo_done, 2 * KA)
                d_steps.wait(pe, "split", blocks(n)[-1])
                for f in range(NF):
                    u = NF * n + f
                    if not (isinstance(n, int) and n == 0 and f < 2):
                        pe.wait_ge(prod_done, u - 1)
                    for side in range(2):
                        for k in range(KA):
                            kk = KA * side + k
                            cols = slice(P * f, P * (f + 1))
                            last = mm3(pe, ps_m[f % 2][:, side, 0:w], (w_hi[:, kk, cols], w_lo[:, kk, cols]),
                                       (u_hi[:, j, kk, 0:w], u_lo[:, j, kk, 0:w]), k == 0, k == KA - 1)
                    last.then_inc(mm_done, 1)
            flow(pe, prep, mult)

        @block.vector
        def _(dve):
            dve.wait_ge(const_in, 32)
            tt, sts = dve.tensor_tensor, dve.scalar_tensor_tensor
            over_g = lambda x, m: x[0:m, :].unsqueeze(1).broadcast_to([m, NG, HPG])

            def prep(n, j):
                for k, b in enumerate(blocks(n)):
                    m = rows_of(n)

                    def do(ins, name):
                        d_steps.done(ins, name)
                        d_steps.wait(dve, name, b)
                    dve.wait_ge(row_in, 48 * (b + 1))
                    do(dve.tensor_reduce(least[0:m, :], stat[0:m, :, 0:HPG].rearrange("p g h -> p h g"), AX.X, ALU.min), "least")
                    do(tt(share[0:m], over_g(least, m), stat[0:m, :, 0:HPG], ALU.subtract), "diff")
                    a_steps.wait(dve, "share", b)
                    do(tt(wd[0:m], share[0:m], stat[0:m, :, HPG:], ALU.mult), "wd")
                    do(dve.tensor_reduce(total[0:m, :], wd[0:m].rearrange("p g h -> p h g"), AX.X, ALU.add), "total")
                    do(dve.reciprocal(total[0:m, :], total[0:m, :]), "rtotal")
                    do(tt(share[0:m], share[0:m], over_g(total, m), ALU.mult), "share")
                    att = rows[0:m, 0:KA, :].rearrange("p a n -> p (a n)").rearrange("p (g d) -> p g d", d=DH)
                    if m == P:
                        do(tt(att, att, bc(share[0:m].rearrange("p g h -> p (g h)"), DH), ALU.mult), "att")
                    else:
                        do(dve.memset(rows[0:m, 0:KA, :], 0.0), "att")
                    a_steps.wait(dve, "squares", b)
                    do(dve.tensor_reduce(ss[0:m, :], sqs[0:m], AX.X, ALU.add), "ss")
                    do(dve.tensor_scalar(ss[0:m, :], ss[0:m, :], 1.0 / DB, RMS_EPS, ALU.mult, ALU.add), "eps")
                    a_steps.wait(dve, "root", b)
                    do(dve.reciprocal(rs[0:m, :], root[0:m, :]), "rs")
                    do(tt(rows[0:m, KA:, :], rows[0:m, KA:, :], bc(rs[0:m, :], P), ALU.mult), "o")
                    dve.wait_ge(z_in, 16 * (b + 1))
                    for r in range(3):
                        p_steps.wait(dve, f"turn{r}", b)
                        cut = [(4 * r, 4 * r + 4)] if r != 1 else [(4, 6), (6, 8)]
                        for lo, hi in cut:
                            src = ps_t[r][:, lo - 4 * r:hi - 4 * r, 0:m]
                            if hi <= KA and m < P:
                                ins = tt(gated[:, lo:hi, 0:m], gated[:, lo:hi, 0:m], z[:, lo:hi, 0:m], ALU.mult)
                            elif hi <= KA:
                                ins = tt(gated[:, lo:hi, 0:m], src, z[:, lo:hi, 0:m], ALU.mult)
                            else:
                                ins = sts(out=gated[:, lo:hi, 0:m], in0=src, scalar=norm[:, 0:1], in1=z[:, lo:hi, 0:m],
                                          op0=ALU.mult, op1=ALU.mult)
                        do(ins, f"g{r}")
                    a_steps.wait(dve, "hi", b)
                    at = slice(P * k, P * k + m)
                    do(tt(u_lo[:, j, :, at], gated[:, :, 0:m], f32(u_hi[:, j, :, at]), ALU.subtract), "split")

            def mult(n, j):
                w = size(n)
                for f in range(NF):
                    u = NF * n + f
                    dve.wait_ge(mm_done, u + 1)
                    dve.wait_ge(gate_in[f % 2], 16 * (NF // 2 * n + f // 2 + 1))
                    dve.tensor_tensor(prod[:, f % 2, :, 0:w], ps_m[f % 2][:, :, 0:w], gates[:, f % 2, :, 0:w],
                                      ALU.mult).then_inc(prod_done, 1)
                    dve.wait_ge(prod_done, u + 1)
                    if not (isinstance(n, int) and n == 0 and f < 2):
                        dve.wait_ge(out[f % 2], 16 * (NF // 2 * n + f // 2))
                    dve.tensor_tensor(merged[:, f % 2, 0:w], prod[:, f % 2, 0, 0:w], prod[:, f % 2, 1, 0:w],
                                      ALU.add).then_inc(sum_done, 1)
            for k in range(2 * KA):
                dve.wait_ge(w_hi_done, k + 1)
                dve.tensor_tensor(w_lo[:, k, :], w_raw[:, k % 2, :], f32(w_hi[:, k, :]), ALU.subtract).then_inc(w_lo_done, 1)
            flow(dve, prep, mult)

        @block.scalar
        def _(act):
            def prep(n, j):
                for k, b in enumerate(blocks(n)):
                    m = rows_of(n)
                    act.wait_ge(row_in, 48 * (b + 1))
                    d_steps.wait(act, "diff", b)
                    a_steps.done(act.activation(share[0:m], share[0:m], ACT.Exp), "share")
                    a_steps.done(act.activation(sqs[0:m], rows[0:m, KA:, :], ACT.Square), "squares")
                    d_steps.wait(act, "eps", b)
                    a_steps.done(act.activation(root[0:m, :], ss[0:m, :], ACT.Sqrt), "root")
                    d_steps.wait(act, "g2", b)
                    if not (isinstance(n, int) and n < 2):
                        act.wait_ge(mm_done, NF * (n - 1))
                    a_steps.done(act.activation(u_hi[:, j, :, P * k:P * k + m], gated[:, :, 0:m], ACT.Copy), "hi")
            for k in range(2 * KA):
                if k >= 2:
                    act.wait_ge(w_lo_done, k - 1)
                act.dma_start(w_raw[:, k % 2, :], t["w_out"][P * k:P * (k + 1), :]).then_inc(wr_in[k % 2], 16)
                act.wait_ge(wr_in[k % 2], 16 * (k // 2 + 1))
                act.activation(w_hi[:, k, :], w_raw[:, k % 2, :], ACT.Copy).then_inc(w_hi_done, 1)
            flow(act, prep, lambda n, j: None)

        @block.gpsimd
        def _(pool):
            def mult(n, j):
                w = size(n)
                tok = bass.ds(SUP * n, SUP) if w == SUP else slice(SEQ, NT)
                for f in range(NF):
                    pool.wait_ge(sum_done, NF * n + f + 1)
                    pool.dma_start(t["merged_d"][f, :, tok], merged[:, f % 2, 0:w]).then_inc(out[f % 2], 16)
            flow(pool, lambda n, j: None, mult)
            for j in range(2):
                pool.wait_ge(out[j], 16 * (NF // 2) * (NSUP + 1))


def finish(nc, t):
    with ExitStack() as ctx:
        sb = lambda name, shape, dt=F32: ctx.enter_context(nc.sbuf_tensor(name, shape, dt))
        pb = lambda name, shape: ctx.enter_context(nc.psum_tensor(name, shape, F32))
        sem = t["sem"]
        w_hi, w_lo, w_raw = sb("wo_hi", [P, KT, D], F32R), sb("wo_lo", [P, KT, D], F32R), sb("wo_raw", [P, 2, D])
        m_raw = sb("m_raw", [P, 2, KT, P])
        m_hi, m_lo = sb("m_hi", [P, 2, KT, P], F32R), sb("m_lo", [P, 2, KT, P], F32R)
        x = sb("x_res", [P, 2, D])
        gate_p, gate_s = sb("gate_p", [P, D]), sb("gate_s", [SAMP, D])
        ln_g, ln_b = sb("ln_g", [P, D]), sb("ln_b", [P, D])
        y = sb("y_res", [P, 2, D])
        junk = sb("ln_junk", [P, D])
        total, mean, ssq = sb("ln_total", [P, 1]), sb("ln_mean", [P, 1]), sb("ln_ssq", [P, 1])
        var, root, rstd, shift = sb("ln_var", [P, 1]), sb("ln_root", [P, 1]), sb("ln_rstd", [P, 1]), sb("ln_shift", [P, 1])
        ps = [pb(f"ps_out{j}", [P, 2, 512]) for j in range(2)]
        const_in, w_hi_done, w_lo_done = sem("o_const"), sem("o_w_hi"), sem("o_w_lo")
        wr_in = [sem(f"o_wr_in{j}") for j in range(2)]
        m_in = [sem(f"o_m_in{j}") for j in range(2)]
        x_in = [sem(f"o_x_in{j}") for j in range(2)]
        out = [sem(f"o_out_{j}") for j in range(2)]
        mm_done = [sem(f"o_mm{j}") for j in range(2)]
        d_steps = Steps(sem("o_dve"), ["gated", "sum", "mean", "var", "rstd", "shift", "scaled", "y"])
        split_done = [sem(f"o_split{j}") for j in range(2)]
        hi_done = [sem(f"o_hi{j}") for j in range(2)]
        a_steps = Steps(sem("o_act"), ["total", "squares", "root", "norm"])
        block = ctx.enter_context(nc.Block(name="finish"))
        NB = NBLK + 1

        @block.sync
        def _(sp):
            sp.dma_start(gate_p[:, :], t["gate_d"][0].partition_broadcast(P)).then_inc(const_in, 16)
            for s in range(NSEQ):
                sp.dma_start(gate_s[TS * s:TS * (s + 1), :], t["gate_d"][1 + s].partition_broadcast(TS)).then_inc(const_in, 16)
            sp.dma_start(ln_g[:, :], t["ln_g"].partition_broadcast(P)).then_inc(const_in, 16)
            sp.dma_start(ln_b[:, :], t["ln_b"].partition_broadcast(P)).then_inc(const_in, 16)

            def body(i, j):
                if not (isinstance(i, int) and i == 0):
                    sp.wait_ge(split_done[j], i)
                m = SAMP if isinstance(i, int) and i == NBLK // 2 else P
                tok = slice(SEQ, NT) if m < P else bass.ds(2 * P * i + P * j, P)
                sp.dma_start(m_raw[:, j, :, 0:m], t["merged_d"][:, :, tok].rearrange("a p n -> p a n")).then_inc(m_in[j], 16)
                if not (isinstance(i, int) and i == 0):
                    d_steps.wait(sp, "sum", 2 * i + j - 2)
                sp.dma_start(x[0:m, j, :], t["x_rows"][tok]).then_inc(x_in[j], 16)
            body(0, 0)
            body(0, 1)
            with sp.Fori(1, NBLK // 2) as i:
                body(i, 0)
                body(i, 1)
            body(NBLK // 2, 0)

        @block.scalar
        def _(act):
            for k in range(KT):
                if k >= 2:
                    act.wait_ge(w_lo_done, k - 1)
                act.dma_start(w_raw[:, k % 2, :], t["w_o"][P * k:P * (k + 1), :]).then_inc(wr_in[k % 2], 16)
                act.wait_ge(wr_in[k % 2], 16 * (k // 2 + 1))
                act.activation(w_hi[:, k, :], w_raw[:, k % 2, :], ACT.Copy).then_inc(w_hi_done, 1)

            def split(i, j, m=P):
                act.wait_ge(m_in[j], 16 * (i + 1))
                if not (isinstance(i, int) and i == 0):
                    act.wait_ge(mm_done[j], i)
                act.activation(m_hi[:, j, :, 0:m], m_raw[:, j, :, 0:m], ACT.Copy).then_inc(hi_done[j], 1)

            def rest(i, j, m=P):
                b = 2 * i + j
                d_steps.wait(act, "sum", b)
                a_steps.done(act.activation(junk[0:m], y[0:m, j, :], ACT.Copy, accum_out=total[0:m]), "total")
                d_steps.wait(act, "mean", b)
                a_steps.done(act.activation(junk[0:m], y[0:m, j, :], ACT.Square, bias=mean[0:m], accum_out=ssq[0:m]), "squares")
                d_steps.wait(act, "var", b)
                a_steps.done(act.activation(root[0:m], var[0:m], ACT.Sqrt), "root")
                d_steps.wait(act, "shift", b)
                a_steps.done(act.activation(y[0:m, j, :], y[0:m, j, :], ACT.Identity, bias=shift[0:m], scale=rstd[0:m]), "norm")
            split(0, 0)
            with act.Fori(0, NBLK // 2 - 1) as i:
                split(i, 1), rest(i, 0)
                split(i + 1, 0), rest(i, 1)
            i = NBLK // 2 - 1
            split(i, 1), rest(i, 0)
            split(i + 1, 0, SAMP), rest(i, 1)
            rest(i + 1, 0, SAMP)

        @block.vector
        def _(dve):
            for k in range(KT):
                dve.wait_ge(w_hi_done, k + 1)
                dve.tensor_tensor(w_lo[:, k, :], w_raw[:, k % 2, :], f32(w_hi[:, k, :]), ALU.subtract).then_inc(w_lo_done, 1)
            dve.wait_ge(const_in, 16 * (3 + NSEQ))

            def split(i, j, m=P):
                dve.wait_ge(hi_done[j], i + 1)
                dve.tensor_tensor(m_lo[:, j, :, 0:m], m_raw[:, j, :, 0:m], f32(m_hi[:, j, :, 0:m]), ALU.subtract).then_inc(split_done[j], 1)

            def rest(i, j, m=P):
                b = 2 * i + j

                def do(ins, name):
                    d_steps.done(ins, name)
                    d_steps.wait(dve, name, b)
                yj = y[0:m, j, :]
                dve.wait_ge(mm_done[j], i + 1)
                if not (isinstance(i, int) and i == 0):
                    dve.wait_ge(out[j], 16 * i)
                do(dve.tensor_tensor(yj, ps[j][0:m].rearrange("p a n -> p (a n)"), (gate_p if m == P else gate_s)[0:m, :], ALU.mult), "gated")
                dve.wait_ge(x_in[j], 16 * (i + 1))
                do(dve.scalar_tensor_tensor(out=yj, in0=x[0:m, j, :], scalar=ALPHA, in1=yj, op0=ALU.mult, op1=ALU.add), "sum")
                a_steps.wait(dve, "total", b)
                do(dve.tensor_scalar(mean[0:m], total[0:m], -1.0 / D, None, ALU.mult), "mean")
                a_steps.wait(dve, "squares", b)
                do(dve.tensor_scalar(var[0:m], ssq[0:m], 1.0 / D, LN_EPS, ALU.mult, ALU.add), "var")
                a_steps.wait(dve, "root", b)
                do(dve.reciprocal(rstd[0:m], root[0:m]), "rstd")
                do(dve.tensor_tensor(shift[0:m], mean[0:m], rstd[0:m], ALU.mult), "shift")
                a_steps.wait(dve, "norm", b)
                do(dve.tensor_tensor(yj, yj, ln_g[0:m, :], ALU.mult), "scaled")
                d_steps.done(dve.tensor_tensor(yj, yj, ln_b[0:m, :], ALU.add), "y")
            split(0, 0)
            with dve.Fori(0, NBLK // 2 - 1) as i:
                split(i, 1), rest(i, 0)
                split(i + 1, 0), rest(i, 1)
            i = NBLK // 2 - 1
            split(i, 1), rest(i, 0)
            split(i + 1, 0, SAMP), rest(i, 1)
            rest(i + 1, 0, SAMP)

        @block.tensor
        def _(pe):
            pe.wait_ge(w_lo_done, KT)

            def body(i, j, m=P):
                pe.wait_ge(split_done[j], i + 1)
                if not (isinstance(i, int) and i == 0):
                    d_steps.wait(pe, "gated", 2 * i + j - 2)
                for h in range(2):
                    for k in range(KT):
                        cols = slice(512 * h, 512 * (h + 1))
                        last = mm3(pe, ps[j][:, h, :], (m_hi[:, j, k, :], m_lo[:, j, k, :]),
                                   (w_hi[:, k, cols], w_lo[:, k, cols]), k == 0, k == KT - 1)
                last.then_inc(mm_done[j], 1)
            body(0, 0), body(0, 1)
            with pe.Fori(1, NBLK // 2) as i:
                body(i, 0), body(i, 1)
            body(NBLK // 2, 0)

        @block.gpsimd
        def _(pool):
            def body(i, j, m=P):
                d_steps.wait(pool, "y", 2 * i + j)
                tok = slice(SEQ, NT) if m < P else bass.ds(2 * P * i + P * j, P)
                pool.dma_start(t["y_rows"][tok], y[0:m, j, :]).then_inc(out[j], 16)
            with pool.Fori(0, NBLK // 2) as i:
                body(i, 0), body(i, 1)
            body(NBLK // 2, 0, SAMP)
            pool.wait_ge(out[0], 16 * (NBLK // 2 + 1))
            pool.wait_ge(out[1], 16 * (NBLK // 2))


def layouts(x_prompt, x_sample, c_prompt, c_sample, state_conv, w_ada, b_ada, w_in, conv_w, **_):
    A = np.ascontiguousarray
    x = np.concatenate([x_prompt[0], x_sample.reshape(SAMP, D)])
    w = w_in[0]
    q, k, v, z, c, zb, a, b, g = np.split(w, np.cumsum([WA, WA, WA, WA, CONV, WB, NHB, NHB]), axis=1)
    tiles = lambda m: m.reshape(KT, P, -1, P).transpose(2, 1, 0, 3).reshape(-1, P, KT * P)
    val = np.zeros((NG, P, KT, VW), np.float32)
    for n in range(NG):
        val[n, :, :, :GW] = v[:, n * GW:(n + 1) * GW].reshape(KT, P, GW).transpose(1, 0, 2)
    val[0, :, :, GW:] = np.concatenate([a, b], 1).reshape(KT, P, NAB).transpose(1, 0, 2)
    side = np.concatenate([conv_w[0].reshape(TAPS, T_CONV, P).transpose(1, 2, 0),
                           state_conv[0].reshape(NSEQ, TAPS - 1, T_CONV, P).transpose(2, 3, 0, 1)
                           .reshape(T_CONV, P, -1)], 2)
    return dict(
        x_T=A(x.reshape(NT, KT, P).transpose(2, 1, 0)), x_rows=x,
        c_T=A(np.concatenate([c_prompt, c_sample]).reshape(NC, KT, P).transpose(2, 1, 0)),
        b_ss=A(b_ada[0, :2 * D].reshape(2 * KT, P).T), b_gate=A(b_ada[0, 2 * D:]),
        w_ada=w_ada[0], w_feat=A(np.concatenate([tiles(m) for m in (c, q, k, z, zb, g)])),
        w_val=val, conv_side=A(side))


def tables():
    f = np.float32
    heads = NG * HPG
    slopes = np.exp2(f(-8.0) * np.arange(1, heads + 1, dtype=f) / f(heads)).astype(f).reshape(NG, HPG)
    steps = P + np.arange(P)[:, None] - np.arange(2 * P)[None, :]
    bias = np.full((P, NG, HPG, 2 * P), MASKED, f)
    for g, (_, dil) in enumerate(GROUPS):
        for h in range(HPG):
            bias[:, g, h] = np.where((steps >= 0) & (steps <= P), -slopes[g, h] * (steps * dil).astype(f), f(MASKED))
    bs = np.full((2, HALF, HPG, TS, KEYS), MASKED, f)
    tok = np.arange(TS)
    at = [0, P + NEWC, P + NEWC + PAST[1]]
    for g, (_, dil) in enumerate(GROUPS):
        dist = PAST[g] + tok[:, None] - np.arange(PAST[g])[None, :]
        seen = (dist % dil == 0) & (dist <= P * dil)
        new = tok[:, None] - tok[None, :]
        new_seen = (new >= 0) & (new % dil == 0)
        for h in range(HPG):
            bs[:, :, h, :, at[g]:at[g] + PAST[g]] = np.where(seen, -slopes[g, h] * dist.astype(f), f(MASKED))
            for a in range(2):
                for s in range(HALF):
                    c = P + SAMP * g + TS * (HALF * a + s)
                    bs[a, s, h, :, c:c + TS] = np.where(new_seen, -slopes[g, h] * new.astype(f), f(MASKED))
    i, j = np.arange(P)[:, None], np.arange(P)[None, :]
    seq = (i // TS == j // TS)
    one = np.ones((P, P), f)
    pair = lambda b: ((i // (2 * b) == j // (2 * b)) & (i // b % 2 == 1) & (j // b % 2 == 0)).astype(f)
    low = lambda m, b: m.reshape(P, -1, 2, b)[:, :, 0, :].reshape(P, P // 2)
    tri = (i <= j).astype(f)
    more = dict(ones=one, tri=tri, tri_incl=np.stack([tri, tri * seq], 1), same=np.stack([one, one * seq], 1),
                upper_big=np.where(j > i, f(BIG), f(0)), level0=-pair(1), level0_T=np.ascontiguousarray(-pair(1).T),
                limit=np.where((j > i) | ~seq, f(BIG), f(0)),
                of_seq=np.tile((np.arange(NSEQ)[:, None] == np.arange(SAMP) // TS).astype(f), (P, 1, 1)),
                in_seq=(np.arange(P)[:, None] // TS == np.arange(NSEQ)).astype(f),
                levels=np.stack([low(pair(b), b) for b in LEVELS], 1))
    return dict(**more, bias_prompt=bias / f(DH ** -0.5), bias_samples=bs.reshape(2, P, KEYS).transpose(1, 0, 2).copy(), ident=np.eye(P, dtype=f))


def caches(cache_win1, cache_win2, cache_win3, **_):
    c = np.concatenate([cache_win1[0], cache_win2[0], cache_win3[0]], axis=1)
    k = c[:, :, 0].reshape(NSEQ, CACHED, NP_, PAIR).transpose(0, 3, 2, 1)
    v = c[:, :, 1].reshape(NSEQ, KT_C, P, GW).transpose(0, 2, 1, 3)
    return dict(k_cache=np.ascontiguousarray(k), v_cache=np.ascontiguousarray(v))


def program(nc, t):
    with ExitStack() as ctx:
        sb = lambda name, shape, dt=F32: ctx.enter_context(nc.sbuf_tensor(name, shape, dt))
        taken = []

        def sem(name):
            taken.append(nc.alloc_semaphore(name=name))
            return taken[-1]
        t = dict(t, sem=sem)
        coef = sb("coef", [P, NBLK + 1, len(COEF), NHB])
        ab = sb("ab", [P, NBLK + 1, NAB])
        with nc.Block(name="clear") as block:
            @block.vector
            def _(dve):
                dve.memset(coef[:, :, :, :], 0.0)
                dve.memset(ab[:, :, :], 0.0)
        with ExitStack() as inner:
            h_hi = inner.enter_context(nc.sbuf_tensor("h_hi", [P, KT, NT], F32R))
            h_lo = inner.enter_context(nc.sbuf_tensor("h_lo", [P, KT, NT], F32R))
            modulate(nc, t, h_hi, h_lo)
            project_features(nc, t, h_hi, h_lo)
            project_values(nc, t, h_hi, h_lo, ab)
        nc.clear_and_free_semaphores(taken)
        nc.all_engine_barrier()
        attend_prompt(nc, t)
        attend_samples(nc, t)
        decay_coefficients(nc, t, ab, coef)
        delta_prompt(nc, t, coef)
        delta_samples(nc, t, coef)
        merge_branches(nc, t)
        finish(nc, t)


_SCRATCH = dict(gate_d=(NC, D), conv_d=(T_CONV, P, NT), q_d=(T_Q, P, NT), z_d=(T_ZA + T_ZB, P, NT), g_d=(T_G, P, NT),
                att_d=(SEQ, NG, GW), stats_d=(SEQ, NG, NSTAT), att_s=(P, NPT, SAMP), o_d=(NT, WB), merged_d=(KT, P, NT))
_OUTS = dict(y_rows=(NT, D), k_T=(T_K, P, NT), v_out=(NG, NBLK, P, GW), v_new=(NG, SAMP, GW),
             conv_tail=(T_CONV, P, U_W - U_SAMP + U_PRE), gdn_p=(NHB, P, P), gdn_s=(NSEQ, NHB, P, P))


def kernel(**inputs):
    import concourse.bacc as _bacc
    from concourse.bass_utils import run_bass_kernel_spmd as _run

    inputs = {k: np.asarray(v) for k, v in inputs.items()}
    arrays = {**layouts(**inputs), **caches(**inputs), **tables()}
    for name in ("dt_bias", "a_log", "gdn_norm", "w_o", "ln_g", "ln_b", "state_gdn"):
        arrays[name] = inputs[name][0]
    arrays["w_out"] = np.concatenate([inputs["w_out_a"][0], inputs["w_out_b"][0]])
    nc = _bacc.Bacc("TRN2", target_bir_lowering=False, num_devices=1)
    sent, t = {}, {}
    for name, a in arrays.items():
        a = np.ascontiguousarray(a)
        sent[f"in_{name}"] = a
        t[name] = nc.dram_tensor(f"in_{name}", a.shape, F32, kind="ExternalInput").ap()
    for name, shape in _SCRATCH.items():
        t[name] = nc.dram_tensor(f"scratch_{name}", shape, F32).ap()
    for name, shape in _OUTS.items():
        t[name] = nc.dram_tensor(f"out_{name}", shape, F32, kind="ExternalOutput").ap()
    program(nc, t)
    r = _run(nc, [sent], core_ids=[0]).results[0]
    o = {name: np.asarray(r[f"out_{name}"]) for name in _OUTS}

    y = o["y_rows"]
    k = o["k_T"].reshape(NG, GW, NT).transpose(0, 2, 1)
    v = np.empty((NG, NT, GW), np.float32)
    for g, (a, b, s) in enumerate(BLOCKS):
        for n in range(NBLK):
            start = a * (n // 4) + b * (n % 4)
            v[g, start:start + s * P:s][:P] = o["v_out"][g, n]
        v[g, SEQ:] = o["v_new"][g]
    kv = np.stack([k, v], axis=2).reshape(NG, NT, 2, HPG, DH)
    win_p = [kv[g, SEQ - min(w, SEQ):SEQ][None, None] for g, (w, _) in enumerate(GROUPS)]
    win_s = [kv[g, SEQ:].reshape(1, NSEQ, TS, 2, HPG, DH) for g in range(NG)]
    tail = o["conv_tail"]
    conv_p = tail[:, :, 0:U_PRE].transpose(2, 0, 1).reshape(1, 1, U_PRE, CONV)
    conv_s = tail[:, :, U_PRE:].reshape(T_CONV, P, NSEQ, EXT)[..., TS:].transpose(2, 3, 0, 1).reshape(1, NSEQ, U_PRE, CONV)
    out = (y[:SEQ][None], y[SEQ:].reshape(NSEQ, TS, D), *win_p, o["gdn_p"][None, None], conv_p,
           *win_s, o["gdn_s"][None], conv_s)
    return tuple(np.ascontiguousarray(x) for x in out)
```

```python
from contextlib import ExitStack

import numpy as np
import concourse.bass as bass
from concourse import mybir

F32 = mybir.dt.float32
F32R = mybir.dt.float32r
ALU = mybir.AluOpType
ACT = mybir.ActivationFunctionType
AX = mybir.AxisListType

P = 128
D = 1024
KT = D // P
SEQ = 2048
NSEQ, TS = 8, 8
SAMP = NSEQ * TS
NT = SEQ + SAMP
NC = 1 + NSEQ
GROUPS = ((128, 1), (512, 4), (2048, 16))
NG = len(GROUPS)
HPG, DH = 4, 64
GW = HPG * DH
WA = NG * GW
NHB, DB = 6, 128
WB = NHB * DB
CONV = 3 * WB
TAPS = 4
PAST = tuple(min(w, 1024) for w, _ in GROUPS)
ALPHA = 2.0 ** 0.25
LN_EPS = 1e-5
RMS_EPS = 1e-6
NBLK = SEQ // P
NCH = -(-NT // 512)
CH = -(-NT // NCH) + 1
CHUNKS = [(c * CH, min(CH, NT - c * CH)) for c in range(NCH)]

T_CONV, T_Q, T_K, T_ZA, T_ZB, T_G = CONV // P, WA // P, WA // P, WA // P, WB // P, 2 * D // P
FT = T_CONV + T_Q + T_K + T_ZA + T_ZB + T_G
NAB = 2 * NHB
VW = GW + NAB
SIDE = TAPS + NSEQ * (TAPS - 1)
EXT = TAPS - 1 + TS
U_PRE = TAPS - 1
U_SAMP = U_PRE + SEQ
U_W = U_SAMP + NSEQ * EXT
BLOCKS = ((512, 128, 1), (1, 512, 4), (4, 1, 16))


def f32(ap):
    return ap.bitcast(F32)


def bc(ap, n):
    return ap.unsqueeze(len(ap.shape)).broadcast_to(list(ap.shape) + [n])


def mm3(pe, out, lhs, rhs, start, stop):
    (ah, al), (bh, bl) = lhs, rhs
    pe.matmul(out, ah, bl, start=start, stop=False)
    pe.matmul(out, al, bh, start=False, stop=False)
    return pe.matmul(out, ah, bh, start=False, stop=stop)


def modulate(nc, t, h_hi, h_lo):
    with ExitStack() as ctx:
        sb = lambda name, shape, dt=F32: ctx.enter_context(nc.sbuf_tensor(name, shape, dt))
        sem = t["sem"]
        c_sb = sb("ada_c", [P, KT, NC])
        sc = sb("ada_silu_c", [P, KT, NC])
        w = sb("ada_w", [P, 2, KT, 512])
        b_ss = sb("ada_b_ss", [P, 2 * KT])
        b_gate = sb("ada_b_gate", [NC, D])
        mods = sb("ada_mods", [P, 2 * KT, NC])
        gate = sb("ada_gate", [NC, D])
        x_in = sb("x_in", [P, 2, NT])
        ps_mod = ctx.enter_context(nc.psum_tensor("ps_mod", [P, 512], F32))
        ps_gate = ctx.enter_context(nc.psum_tensor("ps_gate", [P, 2, 512], F32))
        small_in, silu_done, mod_done, gate_done = sem("small_in"), sem("silu_done"), sem("mod_done"), sem("gate_done")
        w_in = [sem(f"ada_w_in{j}") for j in range(2)]
        w_used = sem("ada_w_used")
        mod_ready, gate_ready, gate_out = sem("mod_ready"), sem("gate_ready"), sem("gate_out")
        x_loaded = [sem(f"x_loaded{j}") for j in range(2)]
        h_step, hi_done, lo_done = sem("h_step"), sem("hi_done"), sem("lo_done")
        w_src = t["w_ada"].rearrange("(k p) n -> p k n", p=P)
        block = ctx.enter_context(nc.Block(name="modulate"))

        @block.sync
        def _(sp):
            sp.dma_start(c_sb[:, :, :], t["c_T"]).then_inc(small_in, 16)
            sp.dma_start(b_ss[:, :], t["b_ss"]).then_inc(small_in, 16)
            sp.dma_start(b_gate[:, :], t["b_gate"].partition_broadcast(NC)).then_inc(small_in, 16)
            for n in range(6):
                if n >= 2:
                    sp.wait_ge(w_used, n - 1)
                sp.dma_start(w[:, n % 2], w_src[:, :, n * 512:(n + 1) * 512]).then_inc(w_in[n % 2], 16)
            for k in range(2):
                sp.dma_start(x_in[:, k], t["x_T"][:, k]).then_inc(x_loaded[k], 16)
            sp.wait_ge(gate_ready, 1)
            sp.dma_start(t["gate_d"], gate[:, :]).then_inc(gate_out, 16)
            for k in range(2, KT):
                sp.wait_ge(lo_done, k - 1)
                sp.dma_start(x_in[:, k % 2], t["x_T"][:, k]).then_inc(x_loaded[k % 2], 16)
            sp.wait_ge(gate_out, 16)

        @block.tensor
        def _(pe):
            pe.wait_ge(silu_done, 1)
            for n in range(4):
                pe.wait_ge(w_in[n % 2], 16 * (n // 2 + 1))
                for j in range(4):
                    for k in range(KT):
                        last = pe.matmul(ps_mod[:, (4 * n + j) * NC:(4 * n + j + 1) * NC],
                                         w[:, n % 2, k, j * P:(j + 1) * P], sc[:, k, :],
                                         start=k == 0, stop=k == KT - 1)
                last.then_inc(w_used, 1)
            for n in range(4, 6):
                pe.wait_ge(w_in[n % 2], 16 * (n // 2 + 1))
                for k in range(KT):
                    last = pe.matmul(ps_gate[0:NC, n - 4, :], sc[:, k, :], w[:, n % 2, k, :],
                                     start=k == 0, stop=k == KT - 1)
                last.then_inc(w_used, 1)

        @block.scalar
        def _(act):
            act.wait_ge(small_in, 48)
            act.activation(sc[:, :, :], c_sb[:, :, :], ACT.Silu).then_inc(silu_done, 1)
            for k in range(KT):
                act.wait_ge(h_step, 3 * k + 3)
                act.activation(h_hi[:, k, :], x_in[:, k % 2, :], ACT.Copy).then_inc(hi_done, 1)

        @block.vector
        def _(dve):
            dve.wait_ge(small_in, 48)
            dve.wait_ge(w_used, 4)
            dve.tensor_tensor(mods[:, :, :], ps_mod[:, 0:2 * KT * NC].rearrange("p (f c) -> p f c", c=NC),
                              bc(b_ss[:, :], NC), ALU.add).then_inc(mod_ready, 1)
            dve.wait_ge(mod_ready, 1)
            dve.tensor_scalar(mods[:, KT:, :], mods[:, KT:, :], 1.0, None, ALU.add).then_inc(mod_ready, 1)
            dve.wait_ge(mod_ready, 2)
            dve.wait_ge(w_used, 6)
            dve.tensor_tensor(gate[:, :], ps_gate[0:NC, :, :].rearrange("p a n -> p (a n)"), b_gate[:, :],
                              ALU.add).then_inc(gate_ready, 1)
            for k in range(KT):
                x = x_in[:, k % 2, :]
                xs = x[:, SEQ:].rearrange("p (s t) -> p s t", s=NSEQ)
                dve.wait_ge(x_loaded[k % 2], 16 * (k // 2 + 1))
                dve.tensor_scalar(x[:, 0:SEQ], x[:, 0:SEQ], mods[:, KT + k, 0:1], mods[:, k, 0:1],
                                  ALU.mult, ALU.add).then_inc(h_step, 1)
                dve.tensor_tensor(xs, xs, bc(mods[:, KT + k, 1:], TS), ALU.mult).then_inc(h_step, 1)
                dve.wait_ge(h_step, 3 * k + 2)
                dve.tensor_tensor(xs, xs, bc(mods[:, k, 1:], TS), ALU.add).then_inc(h_step, 1)
                dve.wait_ge(hi_done, k + 1)
                dve.tensor_tensor(h_lo[:, k, :], x, f32(h_hi[:, k, :]), ALU.subtract).then_inc(lo_done, 1)


def project_features(nc, t, h_hi, h_lo):
    PAIRS = FT // 2
    seg, at = {}, 0
    for name, n in (("conv", T_CONV), ("q", T_Q), ("k", T_K), ("z", T_ZA + T_ZB), ("g", T_G)):
        seg[name] = (at // 2, (at + n) // 2)
        at += n
    with ExitStack() as ctx:
        sb = lambda name, shape, dt=F32: ctx.enter_context(nc.sbuf_tensor(name, shape, dt))
        sem = t["sem"]
        w_raw = sb("w_raw", [P, 2, KT * P])
        w_hi = sb("w_hi", [P, 2, KT * P], F32R)
        w_lo = sb("w_lo", [P, 2, KT * P], F32R)
        side = sb("side", [P, 2, SIDE])
        stage = sb("stage", [P, 2, U_W + 1])
        conv = sb("conv", [P, 2, NT])
        ps = ctx.enter_context(nc.psum_tensor("ps_proj", [P, len(CHUNKS), 512], F32))
        raw_loaded = [sem(f"raw_loaded{j}") for j in range(2)]
        side_loaded = [sem(f"side_loaded{j}") for j in range(2)]
        hi_done = [sem(f"w_hi_done{j}") for j in range(2)]
        lo_done = [sem(f"w_lo_done{j}") for j in range(2)]
        bank_full = [sem(f"bank_full{c}") for c in range(len(CHUNKS))]
        bank_read = [sem(f"bank_read{c}") for c in range(len(CHUNKS))]
        stored = [sem(f"stored{j}") for j in range(2)]
        conv_stored = [sem(f"conv_stored{j}") for j in range(2)]
        pad_zero, state_put, conv_step, conv_silu = sem("pad_zero"), sem("state_put"), sem("conv_step"), sem("conv_silu")
        STEPS = 2 * TAPS
        block = ctx.enter_context(nc.Block(name="project_features"))
        first = lambda i: isinstance(i, int) and i == 0

        @block.sync
        def _(sp):
            def load(i, j, is_conv):
                if not first(i):
                    sp.wait_ge(lo_done[j], i)
                sp.dma_start(w_raw[:, j, :], t["w_feat"][bass.ds(2 * i + j, 1)].rearrange("a p n -> p (a n)")
                             ).then_inc(raw_loaded[j], 16)
                if is_conv:
                    if not first(i):
                        sp.wait_ge(conv_step, STEPS * (2 * i + j - 1))
                        sp.wait_ge(state_put, 2 * i + j - 1)
                    sp.dma_start(side[:, j, :], t["conv_side"][bass.ds(2 * i + j, 1)].rearrange("a p n -> p (a n)")
                                 ).then_inc(side_loaded[j], 16)
            for j in range(2):
                load(0, j, True)
            with sp.Fori(1, seg["conv"][1]) as i:
                for j in range(2):
                    load(i, j, True)
            with sp.Fori(seg["conv"][1], PAIRS) as i:
                for j in range(2):
                    load(i, j, False)

        @block.tensor
        def _(pe):
            def pair(i):
                for j in range(2):
                    pe.wait_ge(lo_done[j], i + 1)
                    for c, (at, n) in enumerate(CHUNKS):
                        if not (first(i) and j == 0):
                            pe.wait_ge(bank_read[c], 2 * i + j)
                        for k in range(KT):
                            cols = slice(k * P, (k + 1) * P)
                            last = mm3(pe, ps[:, c, 0:n], (w_hi[:, j, cols], w_lo[:, j, cols]),
                                       (h_hi[:, k, at:at + n], h_lo[:, k, at:at + n]), k == 0, k == KT - 1)
                        last.then_inc(bank_full[c], 1)
            pair(0)
            with pe.Fori(1, PAIRS) as i:
                pair(i)

        @block.scalar
        def _(act):
            def split(i, j):
                act.wait_ge(raw_loaded[j], 16 * (i + 1))
                if not first(i):
                    act.wait_ge(bank_full[-1], 2 * i + j - 1)
                act.activation(w_hi[:, j, :], w_raw[:, j, :], ACT.Copy).then_inc(hi_done[j], 1)

            def empty(i, j, func, is_conv):
                if is_conv:
                    act.wait_ge(side_loaded[j], 16 * (i + 1))
                    if not first(i):
                        act.wait_ge(conv_step, STEPS * (2 * i + j - 1))
                        act.wait_ge(stored[j], 16 * i)
                    ext = stage[:, j, U_SAMP:U_W].rearrange("p (s e) -> p s e", e=EXT)
                    act.activation(ext[:, :, 0:U_PRE], side[:, j, TAPS:].rearrange("p (s e) -> p s e", e=U_PRE),
                                   ACT.Copy).then_inc(state_put, 1)
                else:
                    act.wait_ge(stored[j], 16 * i)
                for c, (at, n) in enumerate(CHUNKS):
                    act.wait_ge(bank_full[c], 2 * i + j + 1)
                    if not is_conv:
                        last = act.activation(stage[:, j, at:at + n], ps[:, c, 0:n], func)
                    else:
                        m = min(n, SEQ - at)
                        last = act.activation(stage[:, j, U_PRE + at:U_PRE + at + m], ps[:, c, 0:m], func)
                        if m < n:
                            last = act.activation(ext[:, :, U_PRE:], ps[:, c, m:n].rearrange("p (s e) -> p s e", e=TS), func)
                    last.then_inc(bank_read[c], 1)

            def silu(i, j):
                act.wait_ge(conv_step, STEPS * (2 * i + j + 1))
                act.activation(conv[:, j, :], conv[:, j, :], ACT.Silu).then_inc(conv_silu, 1)

            act.wait_ge(pad_zero, 1)
            lo, hi = seg["conv"]
            split(0, 0), split(0, 1)
            for j in range(2):
                empty(0, j, ACT.Copy, True), split(1, j), silu(0, j)
            with act.Fori(1, hi) as i:
                for j in range(2):
                    empty(i, j, ACT.Copy, True), split(i + 1, j), silu(i, j)
            for name, func in (("q", ACT.Copy), ("k", ACT.Copy), ("z", ACT.Silu)):
                with act.Fori(*seg[name]) as i:
                    for j in range(2):
                        empty(i, j, func, False), split(i + 1, j)
            with act.Fori(seg["g"][0], PAIRS - 1) as i:
                for j in range(2):
                    empty(i, j, ACT.Sigmoid, False), split(i + 1, j)
            for j in range(2):
                empty(PAIRS - 1, j, ACT.Sigmoid, False)

        @block.vector
        def _(dve):
            def split(i, j):
                dve.wait_ge(hi_done[j], i + 1)
                dve.tensor_tensor(w_lo[:, j, :], w_raw[:, j, :], f32(w_hi[:, j, :]), ALU.subtract).then_inc(lo_done[j], 1)

            def convolve(i, j):
                for c in range(len(CHUNKS)):
                    dve.wait_ge(bank_read[c], 2 * i + j + 1)
                dve.wait_ge(state_put, 2 * i + j + 1)
                if not first(i):
                    dve.wait_ge(conv_stored[j], 16 * i)
                ext = stage[:, j, U_SAMP:U_W].rearrange("p (s e) -> p s e", e=EXT)
                out_s = conv[:, j, SEQ:].rearrange("p (s e) -> p s e", e=TS)
                for n in range(TAPS):
                    w = side[:, j, n:n + 1]
                    if n == 0:
                        dve.tensor_scalar(conv[:, j, 0:SEQ], stage[:, j, 0:SEQ], w, None, ALU.mult).then_inc(conv_step, 1)
                        dve.tensor_scalar(out_s, ext[:, :, 0:TS], w, None, ALU.mult).then_inc(conv_step, 1)
                        continue
                    dve.wait_ge(conv_step, STEPS * (2 * i + j) + 2 * n - 1)
                    dve.scalar_tensor_tensor(out=conv[:, j, 0:SEQ], in0=stage[:, j, n:n + SEQ], scalar=w,
                                             in1=conv[:, j, 0:SEQ], op0=ALU.mult, op1=ALU.add).then_inc(conv_step, 1)
                    dve.wait_ge(conv_step, STEPS * (2 * i + j) + 2 * n)
                    dve.scalar_tensor_tensor(out=out_s, in0=ext[:, :, n:n + TS], scalar=w, in1=out_s,
                                             op0=ALU.mult, op1=ALU.add).then_inc(conv_step, 1)
            for j in range(2):
                split(0, j)
            for j in range(2):
                split(1, j), convolve(0, j)
            with dve.Fori(1, seg["conv"][1]) as i:
                for j in range(2):
                    split(i + 1, j), convolve(i, j)
            with dve.Fori(seg["conv"][1] + 1, PAIRS) as i:
                for j in range(2):
                    split(i, j)

        @block.gpsimd
        def _(pool):
            pool.memset(stage[:, :, 0:U_PRE], 0.0).then_inc(pad_zero, 1)

            def store(dst, i, j, base):
                for c in range(len(CHUNKS)):
                    pool.wait_ge(bank_read[c], 2 * i + j + 1)
                pool.dma_start(dst[bass.ds(2 * i + j - 2 * base, 1)].rearrange("a p n -> p (a n)"),
                               stage[:, j, 0:NT]).then_inc(stored[j], 16)

            def store_conv(i, j):
                for c in range(len(CHUNKS)):
                    pool.wait_ge(bank_read[c], 2 * i + j + 1)
                pool.dma_start(t["conv_tail"][bass.ds(2 * i + j, 1)].rearrange("a p n -> p (a n)"),
                               stage[:, j, U_SAMP - U_PRE:U_W]).then_inc(stored[j], 16)
                pool.wait_ge(conv_silu, 2 * i + j + 1)
                pool.dma_start(t["conv_d"][bass.ds(2 * i + j, 1)].rearrange("a p n -> p (a n)"),
                               conv[:, j, :]).then_inc(conv_stored[j], 16)
            with pool.Fori(*seg["conv"]) as i:
                for j in range(2):
                    store_conv(i, j)
            for name, dst in (("q", "q_d"), ("k", "k_T"), ("z", "z_d"), ("g", "g_d")):
                with pool.Fori(*seg[name]) as i:
                    for j in range(2):
                        store(t[dst], i, j, seg[name][0])
            for j in range(2):
                pool.wait_ge(stored[j], 16 * PAIRS)
                pool.wait_ge(conv_stored[j], 16 * seg["conv"][1])


def project_values(nc, t, h_hi, h_lo, ab):
    NB = NBLK + 1
    with ExitStack() as ctx:
        sb = lambda name, shape, dt=F32: ctx.enter_context(nc.sbuf_tensor(name, shape, dt))
        sem = t["sem"]
        wv_raw = sb("wv_raw", [P, KT, VW])
        wv_hi = sb("wv_hi", [P, KT, VW], F32R)
        wv_lo = sb("wv_lo", [P, KT, VW], F32R)
        x_hi = sb("tok_hi", [P, 2, KT, P], F32R)
        x_lo = sb("tok_lo", [P, 2, KT, P], F32R)
        v_out = sb("v_out", [P, 2, GW])
        ps = ctx.enter_context(nc.psum_tensor("ps_val", [P, 2, 512], F32))
        w_loaded, w_hi_done, w_lo_done = sem("wv_loaded"), sem("wv_hi_done"), sem("wv_lo_done")
        hi_put = [sem(f"tok_hi_put{j}") for j in range(2)]
        lo_put = [sem(f"tok_lo_put{j}") for j in range(2)]
        full = [sem(f"val_full{j}") for j in range(2)]
        read = [sem(f"val_read{j}") for j in range(2)]
        ab_read = [sem(f"ab_read{j}") for j in range(2)]
        stored = [sem(f"val_stored{j}") for j in range(2)]
        block = ctx.enter_context(nc.Block(name="project_values"))
        PASS = NBLK // 4
        base = lambda g, j: g * (NBLK // 2) + (g if j == 0 else 0)
        use = lambda g, i, j: base(g, j % 2) + 2 * i + j // 2

        def view(x, g, i, j):
            a, b, s = BLOCKS[g]
            if s == 1:
                return x[:, :, bass.ds(a * i + b * j, P)]
            if s == 4:
                return x[:, :, 512 * j:512 * (j + 1)].rearrange("p k (m s) -> p k m s", s=4)[:, :, :, bass.ds(i, 1)]
            return x[:, :, 0:SEQ].rearrange("p k (m s) -> p k m s", s=16)[:, :, :, bass.ds(4 * i + j, 1)]

        def rounds(eng, g, body):
            if g == 0:
                body(0)
            with eng.Fori(1 if g == 0 else 0, PASS) as i:
                body(i)
        zero = lambda u: isinstance(u, int) and u == 0

        @block.sync
        def _(sp):
            for g in range(NG):
                if g:
                    sp.wait_ge(w_lo_done, g)
                sp.dma_start(wv_raw[:, :, :], t["w_val"][g]).then_inc(w_loaded, 16)

        @block.tensor
        def _(pe):
            def tile(g, u, s, n):
                pe.wait_ge(hi_put[s], u + 1)
                pe.wait_ge(lo_put[s], u + 1)
                if not (isinstance(u, int) and u == 0):
                    pe.wait_ge(read[s], u)
                for k in range(KT):
                    last = mm3(pe, ps[:, s, 0:n], (x_hi[:, s, k, :], x_lo[:, s, k, :]),
                               (wv_hi[:, k, 0:n], wv_lo[:, k, 0:n]), k == 0, k == KT - 1)
                last.then_inc(full[s], 1)
            for g in range(NG):
                pe.wait_ge(w_lo_done, g + 1)
                n = VW if g == 0 else GW

                def four(i):
                    for j in range(4):
                        tile(g, use(g, i, j), j % 2, n)
                rounds(pe, g, four)
                tile(g, use(g, PASS, 0), 0, n)

        def put(eng, copy, dst, src, done):
            for g in range(NG):
                def four(i):
                    for j in range(4):
                        s, u = j % 2, use(g, i, j)
                        if not zero(u):
                            eng.wait_ge(full[s], u)
                        v = view(src, g, i, j)
                        o = dst[:, s] if len(v.shape) == 3 else dst[:, s].unsqueeze(3)
                        copy(o, f32(v)).then_inc(done[s], 1)
                rounds(eng, g, four)
                eng.wait_ge(full[0], use(g, PASS, 0))
                copy(dst[:, 0, :, 0:SAMP], f32(src[:, :, SEQ:])).then_inc(done[0], 1)
                yield g

        @block.scalar
        def _(act):
            def split(g):
                act.wait_ge(w_loaded, 16 * (g + 1))
                if g:
                    act.wait_ge(full[0], base(g, 0))
                    act.wait_ge(full[1], base(g, 1))
                act.activation(wv_hi[:, :, :], wv_raw[:, :, :], ACT.Copy).then_inc(w_hi_done, 1)
            split(0)
            for g in put(act, lambda o, i: act.activation(o, i, ACT.Copy), x_hi, h_hi, hi_put):
                if g + 1 < NG:
                    split(g + 1)

        @block.vector
        def _(dve):
            def split(g):
                dve.wait_ge(w_hi_done, g + 1)
                dve.tensor_tensor(wv_lo[:, :, :], wv_raw[:, :, :], f32(wv_hi[:, :, :]), ALU.subtract).then_inc(w_lo_done, 1)

            def empty(g, u, s, b, samples=False):
                dve.wait_ge(full[s], u + 1)
                rows = SAMP if samples else P
                if not (isinstance(u, int) and u == 0):
                    dve.wait_ge(stored[s], 16 * u)
                if g == 0:
                    dve.tensor_copy(ab[0:rows, bass.ds(b, 1), :], ps[0:rows, s, GW:VW].unsqueeze(1)).then_inc(ab_read[s], 1)
                dve.tensor_copy(v_out[0:rows, s, :], ps[0:rows, s, 0:GW]).then_inc(read[s], 1)

            def put_one(g, i, j):
                s, u = j % 2, use(g, i, j)
                if not zero(u):
                    dve.wait_ge(full[s], u)
                v = view(h_lo, g, i, j)
                o = x_lo[:, s] if len(v.shape) == 3 else x_lo[:, s].unsqueeze(3)
                dve.tensor_copy(o, f32(v)).then_inc(lo_put[s], 1)

            for g in range(NG):
                split(g)

                def four(i):
                    for j in range(4):
                        put_one(g, i, j)
                        if j:
                            empty(g, use(g, i, j - 1), (j - 1) % 2, 4 * i + j - 1)
                    empty(g, use(g, i, 3), 1, 4 * i + 3)
                rounds(dve, g, four)
                dve.wait_ge(full[0], use(g, PASS, 0))
                dve.tensor_copy(x_lo[:, 0, :, 0:SAMP], f32(h_lo[:, :, SEQ:])).then_inc(lo_put[0], 1)
                empty(g, use(g, PASS, 0), 0, NBLK, samples=True)

        @block.gpsimd
        def _(pool):
            for g in range(NG):
                with pool.Fori(0, PASS) as i:
                    for j in range(4):
                        pool.wait_ge(read[j % 2], use(g, i, j) + 1)
                        pool.dma_start(t["v_out"][g, bass.ds(4 * i + j, 1)].rearrange("a p n -> p (a n)"),
                                       v_out[:, j % 2, :]).then_inc(stored[j % 2], 16)
                pool.wait_ge(read[0], use(g, PASS, 0) + 1)
                pool.dma_start(t["v_new"][g], v_out[0:SAMP, 0, :]).then_inc(stored[0], 16)
            for j in range(2):
                pool.wait_ge(stored[j], 16 * base(NG, j))


NSTAT = 2 * HPG
PAIR = 2 * DH
NP_ = HPG // 2
NPT = NG * NP_
MASKED = -1.0e30


def attend_prompt(nc, t):
    with ExitStack() as ctx:
        sb = lambda name, shape, dt=F32: ctx.enter_context(nc.sbuf_tensor(name, shape, dt))
        pb = lambda name, shape: ctx.enter_context(nc.psum_tensor(name, shape, F32))
        sem = t["sem"]
        q_sb = sb("q_sb", [P, NG, NP_, SEQ])
        k_sb = sb("k_sb", [P, NG, NP_, SEQ])
        v_sb = sb("v_sb", [P, NG, NBLK, GW])
        bias = sb("bias_p", [P, NG, HPG, 2 * P])
        ident = sb("ident_a", [P, P])
        q_bd = sb("q_bd", [P, NP_, 2, P])
        scores = sb("scores", [P, NP_, 2, 2 * P])
        probs = sb("probs", [P, NP_, 2, 2 * P])
        probs_T = sb("probs_T", [P, NP_, 4, P])
        top = sb("top", [P, HPG])
        neg = sb("neg", [P, HPG])
        turnstile = sb("turnstile", [P, NP_])
        rows = sb("rows", [P, NBLK, GW])
        stats = sb("stats", [P, NG, NBLK, NSTAT])
        ps_s = [pb(f"ps_s{p}", [P, 2, 2 * P]) for p in range(NP_)]
        ps_t = [pb(f"ps_t{p}", [P, 4, P]) for p in range(NP_)]
        ps_o = pb("ps_o", [P, HPG, DH])
        const_in, zeroed = sem("const_in"), sem("q_zeroed")
        qk_in = [sem(f"qk_in{g}") for g in range(NG)]
        v_in = [sem(f"v_in{g}") for g in range(NG)]
        stat_put = sem("stat_put")
        q_put, neg_put, o_full, o_read = sem("q_put"), sem("neg_put"), sem("o_full"), sem("o_read")
        s_full = [sem(f"s_full{p}") for p in range(NP_)]
        s_read = [sem(f"s_read{p}") for p in range(NP_)]
        exp_done = [sem(f"exp_done{p}") for p in range(NP_)]
        t_full = [sem(f"t_full{p}") for p in range(NP_)]
        t_read = [sem(f"t_read{p}") for p in range(NP_)]
        row_stored = [sem(f"row_stored{g}") for g in range(NG)]
        stats_stored = sem("stats_stored")
        block = ctx.enter_context(nc.Block(name="attend_prompt"))

        class Unit:

            def __init__(self, g, i, j=0):
                self.g, self.i, self.j = g, i, j
                self.b = 4 * i + j if g == 1 else i
                self.u = g * NBLK + self.b
                self.first = g == 0 and isinstance(i, int) and i == 0
                self.kb = 1 if g == 2 or (g == 1 and j == 0) or self.first else 2

            def tokens(self, x, back):
                if self.g == 0:
                    return x[..., bass.ds(P * (self.i - back), P * (1 + back))]
                if self.g == 1:
                    part = x[..., 512 * (self.j - back):512 * (self.j + 1)]
                    return part.rearrange(self.pat(x, 4), s=4)[..., bass.ds(self.i, 1)]
                return x.rearrange(self.pat(x, 16), s=16)[..., bass.ds(self.i, 1)]

            def pat(self, x, s):
                lead = " ".join("abcd"[:len(x.shape) - 1])
                return f"{lead} (m s) -> {lead} m s"

        def schedule(eng, ahead, behind, enter=lambda g: None):
            step = lambda nxt, now: (ahead(nxt), behind(now))
            ahead(Unit(0, 0))
            enter(0)
            step(Unit(0, 1), Unit(0, 0))
            with eng.Fori(1, NBLK - 1) as i:
                step(Unit(0, i + 1), Unit(0, i))
            step(Unit(1, 0, 0), Unit(0, NBLK - 1))
            enter(1)
            with eng.Fori(0, 3) as i:
                for j in range(4):
                    step(Unit(1, i, j + 1) if j < 3 else Unit(1, i + 1, 0), Unit(1, i, j))
            for j in range(4):
                step(Unit(1, 3, j + 1) if j < 3 else Unit(2, 0), Unit(1, 3, j))
            enter(2)
            with eng.Fori(0, NBLK - 1) as i:
                step(Unit(2, i + 1), Unit(2, i))
            behind(Unit(2, NBLK - 1))

        nothing = lambda x: None

        @block.sync
        def _(sp):
            for g in range(NG):
                sp.dma_start(q_sb[:, g], t["q_d"][2 * g:2 * g + 2, :, 0:SEQ].rearrange("a p n -> p a n")).then_inc(qk_in[g], 16)
                sp.dma_start(v_sb[:, g], t["v_out"][g, 0:NBLK].rearrange("b p n -> p b n")).then_inc(v_in[g], 16)
                sp.dma_start(k_sb[:, g], t["k_T"][2 * g:2 * g + 2, :, 0:SEQ].rearrange("a p n -> p a n")).then_inc(qk_in[g], 16)
                if g == 0:
                    sp.dma_start(bias[:, :, :, :], t["bias_prompt"]).then_inc(const_in, 16)
                    sp.dma_start(ident[:, :], t["ident"]).then_inc(const_in, 16)

            def store(x):
                sp.wait_ge(o_read, x.u + 1)
                att = t["att_d"][:, x.g, :]
                if x.g == 0:
                    dst = att[bass.ds(P * x.i, P)]
                elif x.g == 1:
                    dst = att[512 * x.j:512 * (x.j + 1)].rearrange("(m s) n -> m s n", s=4)[:, bass.ds(x.i, 1)]
                else:
                    dst = att.rearrange("(m s) n -> m s n", s=16)[:, bass.ds(x.i, 1)]
                src = rows[:, bass.ds(x.b, 1), :]
                sp.dma_start(dst, src if x.g else src.rearrange("p a n -> p (a n)")).then_inc(row_stored[x.g], 16)
            schedule(sp, nothing, store)
            sp.wait_ge(stat_put, NG * NBLK)
            for p in range(NP_):
                sp.wait_ge(exp_done[p], 2 * NG * NBLK)
            for g, (_, s) in enumerate(GROUPS):
                st = t["stats_d"][:, g, :]
                if g == 0:
                    pairs = [(st.rearrange("(b p) n -> p b n", p=P), stats[:, g])]
                elif g == 1:
                    pairs = [(st[512 * j:512 * (j + 1)].rearrange("(m s) n -> m s n", s=s), stats[:, g, j::4]) for j in range(4)]
                else:
                    pairs = [(st.rearrange("(m s) n -> m s n", s=s), stats[:, g])]
                for dst, src in pairs:
                    sp.dma_start(dst, src).then_inc(stats_stored, 16)
            sp.wait_ge(stats_stored, 16 * 6)
            for g in range(NG):
                sp.wait_ge(row_stored[g], 16 * NBLK)

        @block.gpsimd
        def _(pool):
            pool.memset(q_bd[:, :, :, :], 0.0).then_inc(zeroed, 1)
            pool.wait_ge(zeroed, 1)

            def put(x):
                if x.g == 0 and isinstance(x.i, int) or (x.g and isinstance(x.i, int) and x.i == 0 and x.j == 0):
                    pool.wait_ge(qk_in[x.g], 32)
                if not x.first:
                    for p in range(NP_):
                        pool.wait_ge(s_full[p], x.u)
                for h in range(2):
                    half = slice(DH * h, DH * (h + 1))
                    src = x.tokens(q_sb[half, x.g], 0)
                    dst = q_bd[half, :, h, :]
                    pool.tensor_copy(dst if x.g == 0 else dst.unsqueeze(3), src).then_inc(q_put, 1)
            schedule(pool, put, nothing)

        @block.tensor
        def _(pe):
            pe.wait_ge(const_in, 32)

            def score(x):
                pe.wait_ge(q_put, 2 * (x.u + 1))
                for p in range(NP_):
                    if not x.first:
                        pe.wait_ge(s_read[p], 2 * x.u)
                    k = x.tokens(k_sb[:, x.g, p], x.kb - 1)
                    for h in range(2):
                        out = ps_s[p][:, h, 0:P * x.kb]
                        last = pe.matmul(out if x.g == 0 else out.unsqueeze(2), q_bd[:, p, h, :], k, start=True, stop=True)
                    last.then_inc(s_full[p], 1)

            def combine(x):
                for p in range(NP_):
                    pe.wait_ge(exp_done[p], 2 * (x.u + 1))
                    if not x.first:
                        pe.wait_ge(t_read[p], x.u)
                    for h in range(2):
                        for b in range(x.kb):
                            last = pe.transpose(ps_t[p][:, 2 * h + b, :], probs[:, p, h, b * P:(b + 1) * P], ident[:, :])
                    last.then_inc(t_full[p], 1)
                if not x.first:
                    pe.wait_ge(o_read, x.u)
                for p in range(NP_):
                    pe.wait_ge(t_read[p], x.u + 1)
                    for h in range(2):
                        head = 2 * p + h
                        for b in range(x.kb):
                            v = v_sb[:, x.g, bass.ds(x.b - (x.kb - 1) + b, 1), DH * head:DH * (head + 1)]
                            last = pe.matmul(ps_o[:, head, :].unsqueeze(1), probs_T[:, p, 2 * h + b, :], v,
                                             start=b == 0, stop=b == x.kb - 1)
                last.then_inc(o_full, 1)
            schedule(pe, score, combine, lambda g: pe.wait_ge(v_in[g], 16))

        def turn(eng, copy, p, x):
            eng.wait_ge(t_full[p], x.u + 1)
            if not x.first:
                eng.wait_ge(o_full, x.u)
            src, dst = ps_t[p][:, :, :], probs_T[:, p, :, :]
            if x.kb == 1:
                src, dst = ps_t[p][:, 0:4:2, :], probs_T[:, p, 0:4:2, :]
            copy(dst, src).then_inc(t_read[p], 1)

        @block.vector
        def _(dve):
            dve.wait_ge(const_in, 32)

            def maxima(x):
                for p in range(NP_):
                    dve.wait_ge(s_full[p], x.u + 1)
                    if not x.first:
                        dve.wait_ge(exp_done[p], 2 * x.u)
                        dve.wait_ge(stat_put, x.u)
                    dve.memset(turnstile[:, p:p + 1], 0.0)
                    for h in range(2):
                        head = 2 * p + h
                        off = 2 * P - P * x.kb
                        dve.tensor_tensor_reduce(out=scores[:, p, h, 0:P * x.kb], in0=ps_s[p][:, h, 0:P * x.kb],
                                                 in1=bias[:, x.g, head, off:], scale=DH ** -0.5, scalar=-3.0e38, op0=ALU.add,
                                                 op1=ALU.max, accum_out=top[:, head:head + 1]).then_inc(s_read[p], 1)
                for p in range(NP_):
                    dve.wait_ge(s_read[p], 2 * (x.u + 1))
                dve.tensor_scalar(neg[:, :], top[:, :], -1.0, None, ALU.mult).then_inc(neg_put, 1)
                dve.tensor_scalar(stats[:, x.g, bass.ds(x.b, 1), 0:HPG], top[:, :].unsqueeze(1), -1.0, None,
                                  ALU.mult).then_inc(stat_put, 1)

            def results(x):
                turn(dve, lambda o, i: dve.tensor_copy(o, i), 0, x)
                dve.wait_ge(o_full, x.u + 1)
                dve.tensor_copy(rows[:, bass.ds(x.b, 1), 0:GW], ps_o[:, :, :].rearrange("p h d -> p (h d)").unsqueeze(1)
                                ).then_inc(o_read, 1)

            def enter(g):
                if g:
                    dve.wait_ge(row_stored[g - 1], 16 * NBLK)
            schedule(dve, maxima, results, enter)

        @block.scalar
        def _(act):
            def exps(x):
                act.wait_ge(neg_put, x.u + 1)
                for p in range(NP_):
                    if not x.first:
                        act.wait_ge(t_full[p], x.u)
                    for h in range(2):
                        head = 2 * p + h
                        act.activation(probs[:, p, h, 0:P * x.kb], scores[:, p, h, 0:P * x.kb], ACT.Exp,
                                       bias=neg[:, head:head + 1],
                                       accum_out=stats[:, x.g, bass.ds(x.b, 1), HPG + head]).then_inc(exp_done[p], 1)
            schedule(act, exps, lambda x: turn(act, lambda o, i: act.activation(o, i, ACT.Copy), 1, x))


CACHED = sum(PAST)
KT_C = CACHED // P
HALF = NSEQ // 2
QR = HPG * TS
NEWC = NG * SAMP
BANKS = [P + NEWC, PAST[1]] + [512] * (PAST[2] // 512)
KEYS = sum(BANKS)


def attend_samples(nc, t):
    with ExitStack() as ctx:
        sb = lambda name, shape, dt=F32: ctx.enter_context(nc.sbuf_tensor(name, shape, dt))
        pb = lambda name, shape: ctx.enter_context(nc.psum_tensor(name, shape, F32))
        sem = t["sem"]
        RING = 3
        kc = sb("kc", [P, RING, NP_, CACHED])
        vc = sb("vc", [P, RING, KT_C, GW])
        q_in = sb("q_s", [P, NPT, SAMP])
        k_new = sb("k_new", [P, NPT, SAMP])
        v_new = sb("v_new", [SAMP, NG, GW])
        bias = sb("bias_s", [P, 2, KEYS])
        ident = sb("ident_s", [P, P])
        q_bd = sb("q_bd_s", [P, NPT, NSEQ, HPG, TS])
        probs = sb("probs_s", [P, KEYS])
        probs_T = sb("probs_T_s", [P, KT_C, P])
        new_T = sb("new_T_s", [SAMP, NG, P])
        top = sb("top_s", [P, len(BANKS)])
        neg = sb("neg_s", [P, 1])
        den = sb("den_s", [P, 1])
        rden = sb("rden_s", [P, 1])
        att = sb("att_s", [P, NPT, SAMP])
        ps_s = [pb(f"ps_ss{b}", [P, 512]) for b in range(len(BANKS))]
        ps_t = [pb(f"ps_st{b}", [P, 4, P]) for b in range(2)]
        ps_o = [pb(f"ps_so{b}", [P, NPT, HALF, 2 * TS]) for b in range(2)]
        small_in, zeroed, q_put = sem("small_in_s"), sem("zeroed_s"), sem("q_put_s")
        k_in = [sem(f"kc_in{r}") for r in range(RING)]
        v_in = [sem(f"vc_in{r}") for r in range(RING)]
        scored, attended, maxed, softened = sem("scored"), sem("attended"), sem("maxed"), sem("softened")
        chain, neg_done = sem("chain_s"), sem("neg_done_s")
        exped, t_full, t_read, att_put, att_out = sem("exped"), sem("t_full_s"), sem("t_read_s"), sem("att_put"), sem("att_out")
        block = ctx.enter_context(nc.Block(name="attend_samples"))
        ROUNDS = [list(range(r, min(r + 4, KT_C))) for r in range(0, KT_C, 4)] + ["new"]
        col = [0] + [P + NEWC + P * n for n in range(KT_C - 1)]
        tile0 = [0, PAST[0] // P, (PAST[0] + PAST[1]) // P, KT_C]

        @block.sync
        def _(sp):
            sp.dma_start(q_in[:, :, :], t["q_d"][:, :, SEQ:].rearrange("a p n -> p a n")).then_inc(small_in, 16)
            sp.dma_start(k_new[:, :, :], t["k_T"][:, :, SEQ:].rearrange("a p n -> p a n")).then_inc(small_in, 16)
            sp.dma_start(v_new[:, :, :], t["v_new"].rearrange("g p n -> p g n")).then_inc(small_in, 16)
            sp.dma_start(bias[:, :, :], t["bias_samples"]).then_inc(small_in, 16)
            sp.dma_start(ident[:, :], t["ident"]).then_inc(small_in, 16)
            for s in range(NSEQ):
                if s >= RING:
                    sp.wait_ge(scored, s - RING + 1)
                sp.dma_start(kc[:, s % RING], t["k_cache"][s]).then_inc(k_in[s % RING], 16)
                if s >= RING:
                    sp.wait_ge(attended, s - RING + 1)
                sp.dma_start(vc[:, s % RING], t["v_cache"][s]).then_inc(v_in[s % RING], 16)
            sp.wait_ge(att_put, 4)
            sp.dma_start(t["att_s"], att[:, :, :]).then_inc(att_out, 16)
            sp.wait_ge(att_out, 16)

        @block.gpsimd
        def _(pool):
            pool.memset(q_bd[:, :, :, :, :], 0.0).then_inc(zeroed, 1)
            pool.wait_ge(zeroed, 1)
            pool.wait_ge(small_in, 80)
            for p in range(NP_):
                for h in range(2):
                    half = slice(DH * h, DH * (h + 1))
                    for g in range(NG):
                        pool.tensor_scalar(q_bd[half, NP_ * g + p, :, 2 * p + h, :],
                                           q_in[half, NP_ * g + p, :].rearrange("p (s e) -> p s e", e=TS),
                                           DH ** -0.5, None, ALU.mult).then_inc(q_put, 1)

        @block.tensor
        def _(pe):
            pe.wait_ge(q_put, 4 * NG)

            def score(s):
                pe.wait_ge(k_in[s % RING], 16 * (s // RING + 1))
                out = slice(QR * (s % HALF), QR * (s % HALF + 1))

                def add(dst, g, keys):
                    for p in range(NP_):
                        last = pe.matmul(dst, q_bd[:, NP_ * g + p, s].rearrange("p h e -> p (h e)"), keys(p),
                                         start=p == 0, stop=p == NP_ - 1, tile_position=(0, QR * (s % HALF)))
                    return last
                add(ps_s[0][out, 0:P], 0, lambda p: kc[:, s % RING, p, 0:P])
                for g in range(NG):
                    add(ps_s[0][out, P + SAMP * g:P + SAMP * (g + 1)], g, lambda p: k_new[:, NP_ * g + p, :])
                at = P
                for n in range(1, len(BANKS)):
                    last = add(ps_s[n][out, :], min(n, 2), lambda p: kc[:, s % RING, p, at:at + 512])
                    at += 512
                last.then_inc(scored, 1)

            def turn(a):
                pe.wait_ge(softened, a + 1)
                for r, tiles in enumerate(ROUNDS):
                    u = len(ROUNDS) * a + r
                    if u >= 2:
                        pe.wait_ge(t_read, u - 1)
                    if tiles == "new":
                        for g in range(NG):
                            last = pe.transpose(ps_t[u % 2][0:SAMP, g, :], probs[:, P + SAMP * g:P + SAMP * (g + 1)], ident[:, :])
                    else:
                        for n, k in enumerate(tiles):
                            last = pe.transpose(ps_t[u % 2][:, n, :], probs[:, col[k]:col[k] + P], ident[:, :])
                    last.then_inc(t_full, 1)

            def weigh(s):
                pe.wait_ge(v_in[s % RING], 16 * (s // RING + 1))
                pe.wait_ge(t_read, len(ROUNDS) * (s // HALF + 1))
                for g in range(NG):
                    for p in range(NP_):
                        dst = ps_o[s // HALF][:, NP_ * g + p, s % HALF, :]
                        rows = slice(QR * (s % HALF) + 2 * TS * p, QR * (s % HALF) + 2 * TS * (p + 1))
                        feats = slice(PAIR * p, PAIR * (p + 1))
                        for k in range(tile0[g], tile0[g + 1]):
                            pe.matmul(dst, vc[:, s % RING, k, feats], probs_T[:, k, rows], start=k == tile0[g], stop=False)
                        last = pe.matmul(dst, v_new[:, g, feats], new_T[:, g, rows], start=False, stop=True)
                last.then_inc(attended, 1)
            for a in range(2):
                if a:
                    pe.wait_ge(maxed, 1)
                for s in range(HALF):
                    score(HALF * a + s)
                turn(a)
                for s in range(HALF):
                    weigh(HALF * a + s)

        @block.vector
        def _(dve):
            n = [0]

            def link(ins):
                n[0] += 1
                ins.then_inc(chain, 1)
                dve.wait_ge(chain, n[0])
            for a in range(2):
                dve.wait_ge(small_in, 80)
                dve.wait_ge(scored, HALF * (a + 1))
                if a:
                    dve.wait_ge(t_full, len(ROUNDS))
                at = 0
                for b, w in enumerate(BANKS):
                    ins = dve.tensor_tensor_reduce(out=probs[:, at:at + w], in0=ps_s[b][:, 0:w], in1=bias[:, a, at:at + w],
                                                   scale=1.0, scalar=-3.0e38, op0=ALU.add, op1=ALU.max,
                                                   accum_out=top[:, b:b + 1])
                    at += w
                    if b < len(BANKS) - 1:
                        link(ins)
                ins.then_inc(maxed, 1)
                dve.wait_ge(maxed, a + 1)
                dve.tensor_reduce(neg[:, :], top[:, :], AX.X, ALU.max, negate=True).then_inc(neg_done, 1)
                dve.wait_ge(exped, a + 1)
                link(dve.reciprocal(rden[:, :], den[:, :]))
                dve.tensor_scalar(probs[:, :], probs[:, :], rden[:, :], None, ALU.mult).then_inc(softened, 1)
                for r, tiles in enumerate(ROUNDS):
                    dve.wait_ge(t_full, len(ROUNDS) * a + r + 1)
                    if a and r == 0:
                        dve.wait_ge(attended, HALF)
                    src = ps_t[(len(ROUNDS) * a + r) % 2]
                    if tiles == "new":
                        ins = dve.tensor_copy(new_T[:, :, :], src[0:SAMP, 0:NG, :])
                    else:
                        ins = dve.tensor_copy(probs_T[:, tiles[0]:tiles[-1] + 1, :], src[:, 0:len(tiles), :])
                    ins.then_inc(t_read, 1)
                dve.wait_ge(attended, HALF * (a + 1))
                for h in range(2):
                    half = slice(DH * h, DH * (h + 1))
                    dve.tensor_copy(att[half, :, SAMP // 2 * a:SAMP // 2 * (a + 1)].rearrange("p a (s e) -> p a s e", e=TS),
                                    ps_o[a][half, :, :, TS * h:TS * (h + 1)]).then_inc(att_put, 1)

        @block.scalar
        def _(act):
            for a in range(2):
                act.wait_ge(neg_done, a + 1)
                if a:
                    act.wait_ge(softened, 1)
                act.activation(probs[:, :], probs[:, :], ACT.Exp, bias=neg[:, :], accum_out=den[:, :]).then_inc(exped, 1)


COEF = ("beta", "neg_beta_eG", "eG", "decay_k", "decay_S", "G", "g")
NCO = len(COEF)
LEVELS = [2 ** n for n in range(1, 7)]
BIG = 1.0e30


class Steps:

    def __init__(self, sem, names):
        self.sem, self.names, self.n = sem, names, 0

    def done(self, ins, name):
        assert self.names[self.n % len(self.names)] == name, (name, self.names[self.n % len(self.names)])
        self.n += 1
        ins.then_inc(self.sem, 1)

    def wait(self, eng, name, i=0):
        eng.wait_ge(self.sem, len(self.names) * i + self.names.index(name) + 1)

    def wait_back(self, eng, name, i):
        if not (isinstance(i, int) and i < 2):
            eng.wait_ge(self.sem, len(self.names) * i + self.names.index(name) + 1 - 2 * len(self.names))

    def wait_last(self, eng, name, i):
        if not (isinstance(i, int) and i == 0):
            eng.wait_ge(self.sem, len(self.names) * i + self.names.index(name) + 1 - len(self.names))


def lower(x, b):
    return halves(x, b)[..., 0, :]


def upper(x, b):
    return halves(x, b)[..., 1, :]


def halves(x, b):
    lead = "p" if len(x.shape) == 2 else "p h"
    return x.rearrange(f"{lead} (n two b) -> {lead} n two b", two=2, b=b)


def heads(x):
    return x.unsqueeze(1).broadcast_to([x.shape[0], NHB] + list(x.shape[1:]))


def decay_coefficients(nc, t, ab, coef):
    NB = NBLK + 1
    with ExitStack() as ctx:
        sb = lambda name, shape, dt=F32: ctx.enter_context(nc.sbuf_tensor(name, shape, dt))
        sem = t["sem"]
        dt_b = sb("dt_b", [P, NHB])
        a_log = sb("a_log", [P, NHB])
        tri = sb("tri_incl", [P, 2, P])
        same = sb("same", [P, 2, P])
        x = sb("gx", [P, NB, NHB])
        y = sb("gy", [P, NB, NHB])
        ps = ctx.enter_context(nc.psum_tensor("ps_G", [P, 2, 512], F32))
        loaded, v, a, summed = sem("g_loaded"), sem("g_dve"), sem("g_act"), sem("g_summed")
        block = ctx.enter_context(nc.Block(name="decay_coefficients"))
        c = {n: coef[:, :, k, :] for k, n in enumerate(COEF)}
        over = lambda s: s.unsqueeze(1).broadcast_to([P, NB, NHB])

        @block.sync
        def _(sp):
            sp.dma_start(dt_b[:, :], t["dt_bias"].partition_broadcast(P)).then_inc(loaded, 16)
            sp.dma_start(a_log[:, :], t["a_log"].partition_broadcast(P)).then_inc(loaded, 16)
            sp.dma_start(tri[:, :, :], t["tri_incl"]).then_inc(loaded, 16)
            sp.dma_start(same[:, :, :], t["same"]).then_inc(loaded, 16)

        @block.vector
        def _(dve):
            n = [0]

            def link(ins):
                n[0] += 1
                ins.then_inc(v, 1)
                dve.wait_ge(v, n[0])
            dve.wait_ge(loaded, 64)
            link(dve.tensor_tensor(x[:, :, :], ab[:, :, 0:NHB], over(dt_b[:, :]), ALU.add))
            link(dve.scalar_tensor_tensor(out=y[:, :, :], in0=x[:, :, :], scalar=-1.0, in1=x[:, :, :],
                                          op0=ALU.mult, op1=ALU.min))
            link(dve.tensor_scalar(x[:, :, :], x[:, :, :], 0.0, None, ALU.max))
            dve.wait_ge(a, 4)
            link(dve.tensor_tensor(x[:, :, :], x[:, :, :], y[:, :, :], ALU.add))
            link(dve.scalar_tensor_tensor(out=c["g"], in0=x[:, :, :], scalar=-1.0, in1=over(a_log[:, :]),
                                          op0=ALU.mult, op1=ALU.mult))
            dve.wait_ge(summed, 1)
            pairs = [(slice(0, P), slice(0, NBLK), 0), (slice(0, SAMP), slice(NBLK, NB), NBLK * NHB)]
            for rows, bl, at in pairs:
                w = (bl.stop - bl.start) * NHB
                G = ps[rows, 0, at:at + w].rearrange("p (b h) -> p b h", h=NHB)
                last = ps[rows, 1, at:at + w].rearrange("p (b h) -> p b h", h=NHB)
                link(dve.tensor_copy(c["G"][rows, bl], G))
                link(dve.tensor_copy(c["decay_S"][rows, bl], last))
                link(dve.tensor_tensor(c["decay_k"][rows, bl], c["decay_S"][rows, bl], c["G"][rows, bl],
                                       ALU.subtract))
            dve.wait_ge(a, 8)
            dve.scalar_tensor_tensor(out=c["neg_beta_eG"], in0=c["eG"], scalar=-1.0, in1=c["beta"],
                                     op0=ALU.mult, op1=ALU.mult).then_inc(v, 1)

        @block.scalar
        def _(act):
            n = [0]

            def link(ins):
                n[0] += 1
                ins.then_inc(a, 1)
                act.wait_ge(a, n[0])
            link(act.activation(c["beta"], ab[:, :, NHB:], ACT.Sigmoid))
            act.wait_ge(v, 2)
            link(act.activation(y[:, :, :], y[:, :, :], ACT.Exp))
            link(act.activation(y[:, :, :], y[:, :, :], ACT.Ln, bias=1.0))
            act.wait_ge(loaded, 64)
            link(act.activation(a_log[:, :], a_log[:, :], ACT.Exp))
            act.wait_ge(v, 11)
            link(act.activation(c["eG"][:, 0:NBLK], c["G"][:, 0:NBLK], ACT.Exp))
            link(act.activation(c["eG"][0:SAMP, NBLK:], c["G"][0:SAMP, NBLK:], ACT.Exp))
            two = coef[:, 0:NBLK, 3:5, :].rearrange("p b c h -> p b (c h)")
            link(act.activation(two, two, ACT.Exp))
            two = coef[0:SAMP, NBLK:, 3:5, :].rearrange("p b c h -> p b (c h)")
            link(act.activation(two, two, ACT.Exp))

        @block.tensor
        def _(pe):
            pe.wait_ge(v, 5)
            pe.wait_ge(loaded, 64)
            for n, m in enumerate((tri, same)):
                pe.matmul(ps[:, n, 0:NBLK * NHB].rearrange("p (b h) -> p b h", h=NHB), m[:, 0, :], c["g"][:, 0:NBLK],
                          start=True, stop=True)
                last = pe.matmul(ps[0:SAMP, n, NBLK * NHB:NB * NHB].unsqueeze(1), m[0:SAMP, 1, 0:SAMP],
                                 c["g"][0:SAMP, NBLK:], start=True, stop=True)
            last.then_inc(summed, 1)


def delta_prompt(nc, t, coef):
    NP2 = NBLK // 2
    with ExitStack() as ctx:
        sb = lambda name, shape, dt=F32: ctx.enter_context(nc.sbuf_tensor(name, shape, dt))
        pb = lambda name, shape: ctx.enter_context(nc.psum_tensor(name, shape, F32))
        sem = t["sem"]
        two = lambda name, shape: [sb(f"{name}{j}", shape) for j in range(2)]
        HW = [P, NHB, P]
        ident, ones, tri = sb("ident_d", [P, P]), sb("ones_d", [P, P]), sb("tri_d", [P, P])
        upper_big = sb("upper_big", [P, P])
        level0, level0_T = sb("level0", [P, P]), sb("level0_T", [P, P])
        levels = sb("levels", [P, len(LEVELS), P // 2])
        slots = lambda name, shape: [two(f"{name}_{s}_", shape) for s in range(2)]
        xq, xkv = slots("xq", HW), two("xkv", [P, 2 * NHB, P])
        sq = two("sq", [P, 2 * NHB, P])
        cf = slots("cf", [P, NCO, NHB])
        rn, t1, t2 = two("rn", [P, 2 * NHB]), two("rn_t1", [P, 2 * NHB]), two("rn_t2", [P, 2 * NHB])
        q_eG = slots("q_eG", [P, NHB])
        gU, E, EB, EQ = two("gU", HW), two("E", HW), two("EB", HW), two("EQ", HW)
        k_tok, k_T, k_dec, bv = two("k_tok", HW), slots("k_hT", HW), slots("k_dec", HW), slots("bv", HW)
        L, LT, AT = two("L", HW), two("LT", HW), slots("AT", HW)
        A = gU
        T, TT = EB, slots("TT", HW)
        Y = [two(f"Y{b}_", HW) for b in LEVELS[:-1]]
        Y.append(E)
        S = sb("S", HW)
        rv, vn, qs, o = sb("rv", HW), sb("vn", HW), sb("qs", HW), two("o_d", HW)
        ps = [[pb(f"ps_p{j}{b}", [P, 4, P]) for b in range(2)] for j in range(2)]
        pss = [[pb(f"ps_c{z}{b}", [P, 4, P]) for b in range(2)] for z in range(2)]
        loaded, zeroed = sem("d_const"), sem("d_zeroed")
        xq_in = [sem(f"xq_in{j}") for j in range(2)]
        xkv_in = [sem(f"xkv_in{j}") for j in range(2)]
        o_out = [sem(f"o_out{j}") for j in range(2)]
        s_out = sem("s_out")
        lv = range(len(LEVELS))
        PE1 = ["norms", "G_rows", "k_turned", "v_turned", "kh_turned", "gram_k", "gram_q", "L_turned", "A_turned"]
        for n in lv:
            PE1 += [f"LT{n}", f"TY{n}", f"YT{n}"] if n < lv[-1] else [f"LT{n}", f"YT{n}"]
        DV1 = ["coef", "gU", "rsum", "newton1", "newton2", "r", "r_q", "q_eG", "rel", "k_tok", "bv", "L", "A",
               "T_pairs", "T_init", "TT_pairs", "TT_init"]
        for n in lv:
            DV1 += [f"Y{n}", f"T{n}", f"TT{n}"] if n < lv[-1] else [f"Y{n}", f"TT{n}"]
        AC1 = ["ln", "rough", "E", "kh_T", "LT", "AT"]
        PL1 = ["sq", "EB", "EQ", "k_dec"]
        pe1 = [Steps(sem(f"pe_prep{j}"), PE1) for j in range(2)]
        dv1 = [Steps(sem(f"dve_prep{j}"), DV1) for j in range(2)]
        ac1 = [Steps(sem(f"act_prep{j}"), AC1) for j in range(2)]
        pl1 = [Steps(sem(f"pool_prep{j}"), PL1) for j in range(2)]
        each = lambda names: [f"{n}{j}" for j in range(2) for n in names]
        pe2 = [Steps(sem(f"pe_scan{z}"), each(["kS", "qS", "Tr", "Av", "kv"])) for z in range(2)]
        dv2 = [Steps(sem(f"dve_scan{z}"), each(["rv", "S", "o"])) for z in range(2)]
        ac2 = [Steps(sem(f"act_scan{z}"), each(["qs", "vn"])) for z in range(2)]
        block = ctx.enter_context(nc.Block(name="delta_prompt"))
        H3 = [slice(0, 3), slice(3, 6)]

        def passes(eng, prep, scan):
            prep(0, 0, lambda piece: None)
            prep(1, 1, lambda piece: scan(0, 0, piece))
            with eng.Fori(0, NP2 // 2 - 1) as i:
                prep(2 * i + 2, 0, lambda piece: scan(2 * i + 1, 1, piece))
                prep(2 * i + 3, 1, lambda piece: scan(2 * i + 2, 0, piece))
            for piece in range(6):
                scan(NP2 - 1, 1, piece)

        @block.sync
        def _(sp):
            for dst, name in ((ident, "ident"), (ones, "ones"), (tri, "tri"), (upper_big, "upper_big"),
                              (level0, "level0"), (level0_T, "level0_T")):
                sp.dma_start(dst[:, :], t[name]).then_inc(loaded, 16)
            sp.dma_start(levels[:, :, :], t["levels"]).then_inc(loaded, 16)

            chunk = t["conv_d"][:, :, 0:SEQ].rearrange("a p (n c m) -> c p a n m", c=4, m=P)

            def load(p, s, i):
                for j in range(2):
                    src = chunk[2 * s + j, :, :, bass.ds(i, 1)].rearrange("p a n m -> p a (n m)")
                    for z in range(2):
                        pe2[z].wait_back(sp, f"qS{j}", p)
                    pe1[j].wait_last(sp, "v_turned", p)
                    sp.dma_start(xkv[j][:, :, :], src[:, NHB:]).then_inc(xkv_in[j], 16)
                    sp.dma_start(xq[s][j][:, :, :], src[:, 0:NHB]).then_inc(xq_in[j], 16)
            load(0, 0, 0)
            load(1, 1, 0)
            with sp.Fori(1, NP2 // 2) as i:
                load(2 * i, 0, i)
                load(2 * i + 1, 1, i)
            for z in range(2):
                dv2[z].wait(sp, "S1", NP2 - 1)
            sp.dma_start(t["gdn_p"].rearrange("h k v -> k h v"), S[:, :, :]).then_inc(s_out, 16)
            sp.wait_ge(s_out, 16)

        @block.gpsimd
        def _(pool):
            for y in Y[:-1]:
                for j in range(2):
                    pool.memset(y[j][:, :, :], 0.0).then_inc(zeroed, 1)
            pool.memset(S[:, :, :], 0.0).then_inc(zeroed, 1)

            def store(p):
                for j in range(2):
                    for z in range(2):
                        dv2[z].wait(pool, f"o{j}", p)
                    pool.dma_start(t["o_d"][bass.ds(2 * P * p + P * j, P), :], o[j][:, :, :].rearrange("p h v -> p (h v)")
                                   ).then_inc(o_out[j], 16)

            def prep(p, s, scan):
                for j in range(2):
                    pool.wait_ge(xq_in[j], 16 * (p + 1))
                    pe1[j].wait_last(pool, "norms", p)
                    pool.wait_ge(xkv_in[j], 16 * (p + 1))
                    pool.tensor_tensor(sq[j][:, 0:NHB, :], xq[s][j][:, :, :], xq[s][j][:, :, :], ALU.mult)
                    pl1[j].done(pool.tensor_tensor(sq[j][:, NHB:, :], xkv[j][:, 0:NHB, :], xkv[j][:, 0:NHB, :], ALU.mult), "sq")
                if not (isinstance(p, int) and p < 2):
                    store(p - 2)
                for j in range(2):
                    ac1[j].wait(pool, "E", p)
                    pl1[j].done(pool.tensor_tensor(EB[j][:, :, :], E[j][:, :, :], bc(cf[s][j][:, 0, :], P), ALU.mult), "EB")
                    dv1[j].wait(pool, "r_q", p)
                    pl1[j].done(pool.tensor_tensor(EQ[j][:, :, :], E[j][:, :, :], bc(rn[j][:, 0:NHB], P), ALU.mult), "EQ")
                    dv1[j].wait(pool, "k_tok", p)
                    for z in range(2):
                        pe2[z].wait_back(pool, f"kv{j}", p)
                    pl1[j].done(pool.tensor_tensor(k_dec[s][j][:, :, :], k_tok[j][:, :, :], bc(cf[s][j][:, 3, :], P), ALU.mult), "k_dec")
            passes(pool, prep, lambda p, s, piece: None)
            store(NP2 - 2)
            store(NP2 - 1)
            for j in range(2):
                pool.wait_ge(o_out[j], 16 * NP2)

        @block.tensor
        def _(pe):
            pe.wait_ge(loaded, 16 * 7)
            pe.wait_ge(zeroed, 2 * len(Y) - 1)

            def six(j, f):
                for h in range(NHB):
                    last = f(ps[j][h // 3][:, h % 3, :], h)
                return last

            def prep(p, s, scan):
                for j in range(2):
                    pl1[j].wait(pe, "sq", p)
                    dv1[j].wait_last(pe, f"TT{lv[-1]}", p)
                    for n in range(2 * NHB):
                        last = pe.matmul(ps[j][0][:, 0, n:n + 1], sq[j][:, n, :], ones[:, 0:1], start=True, stop=True)
                    pe1[j].done(last, "norms")
                for j in range(2):
                    dv1[j].wait(pe, "rsum", p)
                    for z in range(2):
                        last = pe.matmul(ps[j][z][:, 0:3, :].rearrange("p h n -> p (h n)"), ones[:, :],
                                         gU[j][:, H3[z], :].rearrange("p h n -> p (h n)"), start=True, stop=True)
                    pe1[j].done(last, "G_rows")
                for j in range(2):
                    dv1[j].wait(pe, "rel", p)
                    pe1[j].done(six(j, lambda out, h: pe.transpose(out, xkv[j][:, h, :], ident[:, :])), "k_turned")
                scan(0)
                for j in range(2):
                    dv1[j].wait(pe, "k_tok", p)
                    pe1[j].done(six(j, lambda out, h: pe.transpose(out, xkv[j][:, NHB + h, :], ident[:, :])), "v_turned")
                for j in range(2):
                    dv1[j].wait(pe, "bv", p)
                    pe1[j].done(six(j, lambda out, h: pe.transpose(out, k_tok[j][:, h, :], ident[:, :])), "kh_turned")
                for j in range(2):
                    ac1[j].wait(pe, "kh_T", p)
                    pe1[j].done(six(j, lambda out, h: pe.matmul(out, k_T[s][j][:, h, :], k_T[s][j][:, h, :], start=True, stop=True)), "gram_k")
                scan(1)
                for j in range(2):
                    dv1[j].wait(pe, "L", p)
                    pe1[j].done(six(j, lambda out, h: pe.matmul(out, xq[s][j][:, h, :], k_T[s][j][:, h, :], start=True, stop=True)), "gram_q")
                for j in range(2):
                    dv1[j].wait(pe, "A", p)
                    pe1[j].done(six(j, lambda out, h: pe.transpose(out, L[j][:, h, :], ident[:, :])), "L_turned")
                for j in range(2):
                    ac1[j].wait(pe, "LT", p)
                    pe1[j].done(six(j, lambda out, h: pe.transpose(out, A[j][:, h, :], ident[:, :])), "A_turned")
                scan(2)
                for n, b in enumerate(LEVELS):
                    def level(j, bank, lhs, rhs, name, rows=P):
                        for h in range(NHB):
                            out = bank[0:rows].rearrange("p a n -> p (a n)")[:, 64 * h:64 * (h + 1)].rearrange("p (n b) -> p n b", b=b)
                            last = pe.matmul(out, lhs[:, h, 0:rows], rhs(h), start=True, stop=True)
                        pe1[j].done(last, name)
                    for j in range(2):
                        if n == 0:
                            ac1[j].wait(pe, "AT", p)
                        dv1[j].wait(pe, f"TT{n - 1}" if n else "TT_init", p)
                        level(j, ps[j][0], LT[j], lambda h: lower(T[j][:, h, :], b), f"LT{n}")
                    for j in range(2):
                        dv1[j].wait(pe, f"Y{n}", p)
                        if n < lv[-1]:
                            level(j, ps[j][1], TT[s][j], lambda h: lower(Y[n][j][:, h, :], b), f"TY{n}")
                        level(j, ps[j][0], Y[n][j], lambda h: upper(TT[s][j][:, h, :], b), f"YT{n}",
                              P if n < lv[-1] else b)
                    if n % 2:
                        scan(3 + n // 2)

            def scan(p, s, piece):
                j, part = piece // 3, piece % 3

                def three(z, b, f):
                    for h in range(3 * z, 3 * z + 3):
                        last = f(pss[z][b][:, h % 3, :], h)
                    return last
                for z in range(2):
                    if part == 0:
                        if j == 0:
                            dv2[z].wait_last(pe, "o1", p)
                        else:
                            dv2[z].wait(pe, "o0", p)
                        pe2[z].done(three(z, 0, lambda out, h: pe.matmul(out, k_T[s][j][:, h, :], S[:, h, :], start=True, stop=True)), f"kS{j}")
                        pe2[z].done(three(z, 1, lambda out, h: pe.matmul(out, xq[s][j][:, h, :], S[:, h, :], start=True, stop=True)), f"qS{j}")
                    elif part == 1:
                        dv1[j].wait(pe, f"TT{lv[-1]}", p)
                        dv2[z].wait(pe, f"rv{j}", p)
                        pe2[z].done(three(z, 0, lambda out, h: pe.matmul(out, TT[s][j][:, h, :], rv[:, h, :], start=True, stop=True)), f"Tr{j}")
                    else:
                        ac2[z].wait(pe, f"vn{j}", p)
                        pe2[z].done(three(z, 1, lambda out, h: pe.matmul(out, AT[s][j][:, h, :], vn[:, h, :], start=True, stop=True)), f"Av{j}")
                        pl1[j].wait(pe, "k_dec", p)
                        pe2[z].done(three(z, 0, lambda out, h: pe.matmul(out, k_dec[s][j][:, h, :], vn[:, h, :], start=True, stop=True)), f"kv{j}")

            passes(pe, prep, scan)

        @block.vector
        def _(dve):
            dve.wait_ge(loaded, 16 * 7)
            dve.wait_ge(zeroed, 2 * len(Y) - 1)

            def both(j, f):
                for z in range(2):
                    last = f(ps[j][z][:, 0:3, :], H3[z])
                return last

            def prep(p, s, scan):
                for j in range(2):
                    C, R = cf[s][j], rn[j]
                    for z in range(2):
                        dv2[z].wait_back(dve, f"S{j}", p)
                    dv1[j].wait_last(dve, f"TT{lv[-1]}", p)
                    pl1[j].wait_last(dve, "k_dec", p)
                    dv1[j].done(dve.tensor_copy(C[:, :, :].rearrange("p c h -> p (c h)").unsqueeze(1),
                                                coef[:, bass.ds(2 * p + j, 1), :, :].rearrange("p a c h -> p a (c h)")), "coef")
                    dv1[j].wait(dve, "coef", p)
                    pe1[j].wait_last(dve, "A_turned", p)
                    dv1[j].done(dve.tensor_tensor(gU[j][:, :, :], heads2(tri), bc(C[:, 6, :], P), ALU.mult), "gU")
                    pe1[j].wait(dve, "norms", p)
                    ac1[j].wait_last(dve, "rough", p)
                    dv1[j].done(dve.tensor_scalar(t1[j][:, :], ps[j][0][:, 0, 0:2 * NHB], RMS_EPS, None, ALU.add), "rsum")
                for j in range(2):
                    R = rn[j]
                    ac1[j].wait(dve, "rough", p)
                    dv1[j].done(dve.tensor_tensor(t2[j][:, :], R[:, :], R[:, :], ALU.mult), "newton1")
                    dv1[j].wait(dve, "newton1", p)
                    dv1[j].done(dve.scalar_tensor_tensor(out=t2[j][:, :], in0=t1[j][:, :], scalar=-0.5, in1=t2[j][:, :],
                                                         op0=ALU.mult, op1=ALU.mult), "newton2")
                    dv1[j].wait(dve, "newton2", p)
                    dv1[j].done(dve.scalar_tensor_tensor(out=R[:, :], in0=t2[j][:, :], scalar=1.5, in1=R[:, :],
                                                         op0=ALU.add, op1=ALU.mult), "r")
                    dv1[j].wait(dve, "r", p)
                    dv1[j].done(dve.tensor_scalar(R[:, 0:NHB], R[:, 0:NHB], DB ** -0.5, None, ALU.mult), "r_q")
                    dv1[j].wait(dve, "r_q", p)
                    dv1[j].done(dve.tensor_tensor(q_eG[s][j][:, :], R[:, 0:NHB], cf[s][j][:, 2, :], ALU.mult), "q_eG")
                for j in range(2):
                    pe1[j].wait(dve, "G_rows", p)
                    for h in range(NHB):
                        last = dve.scalar_tensor_tensor(out=E[j][:, h, :], in0=ps[j][h // 3][:, h % 3, :],
                                                        scalar=cf[s][j][:, 5, h:h + 1], in1=upper_big[:, :],
                                                        op0=ALU.subtract, op1=ALU.max)
                    dv1[j].done(last, "rel")
                for j in range(2):
                    pe1[j].wait(dve, "k_turned", p)
                    dv1[j].done(both(j, lambda p, h: dve.tensor_tensor(k_tok[j][:, h, :], p, bc(rn[j][:, NHB:][:, h], P), ALU.mult)), "k_tok")
                scan(0)
                for j in range(2):
                    pe1[j].wait(dve, "v_turned", p)
                    dv1[j].done(both(j, lambda p, h: dve.tensor_tensor(bv[s][j][:, h, :], p, bc(cf[s][j][:, 0, h], P), ALU.mult)), "bv")
                for j in range(2):
                    pe1[j].wait(dve, "gram_k", p)
                    pl1[j].wait(dve, "EB", p)
                    dv1[j].done(both(j, lambda p, h: dve.tensor_tensor(L[j][:, h, :], p, EB[j][:, h, :], ALU.mult)), "L")
                for j in range(2):
                    pe1[j].wait(dve, "gram_q", p)
                    pl1[j].wait(dve, "EQ", p)
                    dv1[j].done(both(j, lambda p, h: dve.tensor_tensor(A[j][:, h, :], p, EQ[j][:, h, :], ALU.mult)), "A")
                for j in range(2):
                    dv1[j].wait(dve, "L", p)
                    dv1[j].done(dve.tensor_tensor(T[j][:, :, :], L[j][:, :, :], heads2(level0), ALU.mult), "T_pairs")
                    dv1[j].wait(dve, "T_pairs", p)
                    dv1[j].done(dve.tensor_tensor(T[j][:, :, :], T[j][:, :, :], heads2(ident), ALU.add), "T_init")
                    ac1[j].wait(dve, "LT", p)
                    dv1[j].done(dve.tensor_tensor(TT[s][j][:, :, :], LT[j][:, :, :], heads2(level0_T), ALU.mult), "TT_pairs")
                    dv1[j].wait(dve, "TT_pairs", p)
                    dv1[j].done(dve.tensor_tensor(TT[s][j][:, :, :], TT[s][j][:, :, :], heads2(ident), ALU.add), "TT_init")
                scan(2)
                for n, b in enumerate(LEVELS):
                    got = lambda bank: bank[:, 0:3, :].rearrange("p a n -> p (a n)").rearrange("p (h n b) -> p h n b", h=NHB, b=b)
                    mask = heads(levels[:, n, :].rearrange("p (n b) -> p n b", b=b))
                    for j in range(2):
                        pe1[j].wait(dve, f"LT{n}", p)
                        y = Y[n][j]
                        dv1[j].done(dve.tensor_tensor(lower(y[:, :, :], b), got(ps[j][0]), mask, ALU.mult), f"Y{n}")
                    for j in range(2):
                        if n < lv[-1]:
                            pe1[j].wait(dve, f"TY{n}", p)
                            v = lower(T[j][:, :, :], b)
                            dv1[j].done(dve.tensor_tensor(v, v, got(ps[j][1]), ALU.subtract), f"T{n}")
                        pe1[j].wait(dve, f"YT{n}", p)
                        r = P if n < lv[-1] else b
                        v = upper(TT[s][j][0:r, :, :], b)
                        dv1[j].done(dve.tensor_tensor(v, v, got(ps[j][0][0:r]), ALU.subtract), f"TT{n}")
                    if n % 2:
                        scan(3 + n // 2)

            def scan(p, s, piece):
                j, part = piece // 3, piece % 3
                for z in range(2):
                    if part == 0:
                        pe2[z].wait(dve, f"kS{j}", p)
                        for h in range(3 * z, 3 * z + 3):
                            last = dve.scalar_tensor_tensor(out=rv[:, h, :], in0=pss[z][0][:, h % 3, :],
                                                            scalar=cf[s][j][:, 1, h:h + 1], in1=bv[s][j][:, h, :],
                                                            op0=ALU.mult, op1=ALU.add)
                        dv2[z].done(last, f"rv{j}")
                    elif part == 2:
                        pe2[z].wait(dve, f"kv{j}", p)
                        for h in range(3 * z, 3 * z + 3):
                            last = dve.scalar_tensor_tensor(out=S[:, h, :], in0=S[:, h, :], scalar=cf[s][j][:, 4, h:h + 1],
                                                            in1=pss[z][0][:, h % 3, :], op0=ALU.mult, op1=ALU.add)
                        dv2[z].done(last, f"S{j}")
                        pe2[z].wait(dve, f"Av{j}", p)
                        if not (isinstance(p, int) and p == 0):
                            dve.wait_ge(o_out[j], 16 * p)
                        dv2[z].done(dve.tensor_tensor(o[j][:, H3[z], :], pss[z][1][:, 0:3, :], qs[:, H3[z], :], ALU.add), f"o{j}")

            passes(dve, prep, scan)

        @block.scalar
        def _(act):
            def turn(j, dst, name, src, p):
                pe1[j].wait(act, src, p)
                for z in range(2):
                    last = act.activation(dst[:, H3[z], :], ps[j][z][:, 0:3, :], ACT.Copy)
                ac1[j].done(last, name)

            def prep(p, s, scan):
                for j in range(2):
                    dv1[j].wait(act, "rsum", p)
                    pl1[j].wait_last(act, "EQ", p)
                    ac1[j].done(act.activation(rn[j][:, :], t1[j][:, :], ACT.Ln), "ln")
                    ac1[j].wait(act, "ln", p)
                    ac1[j].done(act.activation(rn[j][:, :], rn[j][:, :], ACT.Exp, scale=-0.5), "rough")
                for j in range(2):
                    dv1[j].wait(act, "rel", p)
                    ac1[j].done(act.activation(E[j][:, :, :], E[j][:, :, :], ACT.Exp, scale=-1.0), "E")
                scan(0)
                for j in range(2):
                    for z in range(2):
                        pe2[z].wait_back(act, f"kS{j}", p)
                    turn(j, k_T[s][j], "kh_T", "kh_turned", p)
                scan(1)
                for j in range(2):
                    turn(j, LT[j], "LT", "L_turned", p)
                for j in range(2):
                    for z in range(2):
                        pe2[z].wait_back(act, f"Av{j}", p)
                    turn(j, AT[s][j], "AT", "A_turned", p)
                scan(3)
                scan(4)

            def scan(p, s, piece):
                j, part = piece // 3, piece % 3
                for z in range(2):
                    if part == 0:
                        pe2[z].wait(act, f"qS{j}", p)
                        for h in range(3 * z, 3 * z + 3):
                            last = act.activation(qs[:, h, :], pss[z][1][:, h % 3, :], ACT.Copy, scale=q_eG[s][j][:, h:h + 1])
                        ac2[z].done(last, f"qs{j}")
                    elif part == 1:
                        pe2[z].wait(act, f"Tr{j}", p)
                        ac2[z].done(act.activation(vn[:, H3[z], :], pss[z][0][:, 0:3, :], ACT.Copy), f"vn{j}")

            passes(act, prep, scan)


def heads2(x):
    return x[:, :].unsqueeze(1).broadcast_to([P, NHB, P])


def delta_samples(nc, t, coef):
    with ExitStack() as ctx:
        sb = lambda name, shape, dt=F32: ctx.enter_context(nc.sbuf_tensor(name, shape, dt))
        pb = lambda name, shape: ctx.enter_context(nc.psum_tensor(name, shape, F32))
        sem = t["sem"]
        R = SAMP
        ident, ones = sb("ident_e", [P, P]), sb("ones_e", [P, P])
        tri, limit = sb("tri_e", [P, 2, P]), sb("limit_e", [P, P])
        level0, level0_T, levels = sb("level0_e", [P, P]), sb("level0_T_e", [P, P]), sb("levels_e", [P, len(LEVELS), P // 2])
        of_seq, in_seq = sb("of_seq", [P, NSEQ, R]), sb("in_seq", [P, NSEQ])
        x = sb("x_e", [P, T_CONV, R])
        sq = sb("sq_e", [P, 2 * NHB, R])
        st = sb("state_e", [P, NHB, NSEQ, P])
        rn, t1, t2, q_eG = sb("rn_e", [R, 2 * NHB]), sb("t1_e", [R, 2 * NHB]), sb("t2_e", [R, 2 * NHB]), sb("q_eG_e", [R, NHB])
        gs, decay = sb("gs", [R, NHB, NSEQ]), sb("decay_e", [P, NHB, NSEQ])
        gU, E, L, A = sb("gU_e", [R, NHB, R]), sb("E_e", [R, NHB, R]), sb("L_e", [R, NHB, R]), sb("A_e", [R, NHB, R])
        EB, EQ = sb("EB_e", [R, NHB, R]), sb("EQ_e", [R, NHB, R])
        LT, AT, T, TT = sb("LT_e", [R, NHB, R]), sb("AT_e", [R, NHB, R]), sb("T_e", [R, NHB, R]), sb("TT_e", [R, NHB, R])
        LV = [2, 4]
        Y = [sb(f"Y{b}_e", [R, NHB, R]) for b in LV]
        k_tok, bv, k_dec, k_T = sb("k_tok_e", [R, NHB, P]), sb("bv_e", [R, NHB, P]), sb("k_dec_e", [R, NHB, P]), sb("k_T_e", [P, NHB, R])
        k_seq, q_seq = sb("k_seq", [P, NHB, NSEQ, R]), sb("q_seq", [P, NHB, NSEQ, R])
        rv, vn, qs, o = sb("rv_e", [R, NHB, P]), sb("vn_e", [R, NHB, P]), sb("qs_e", [R, NHB, P]), sb("o_e", [R, NHB, P])
        v_seq = sb("v_seq", [R, 2, NSEQ, P])
        bank = [pb(f"ps_e{b}", [P, 512]) for b in range(8)]
        loaded, out = sem("e_loaded"), sem("e_out")
        D_, A_, T_ = ["zero0", "zero1", "sq", "gs", "gU", "rsum", "n1", "n2", "r", "rq", "q_eG", "decay", "rel", "k_tok", "bv", "EB", "EQ",
                      "k_dec", "L", "A", "T_pairs", "T_init", "TT_pairs", "TT_init", "Y0", "T0", "TT0", "Y1", "T1", "TT1", "k_seq",
                      "q_seq", "rv", "o"] + [f"{n}{h}" for h in range(NHB) for n in ("vs", "st")], \
            ["ln", "rough", "decay", "E", "k_T", "LT", "AT", "qs", "vn"], \
            ["norms", "decay", "G_rows", "k", "v", "k_T", "gk", "gq", "LT", "AT", "LT0", "TY0", "YT0", "LT1", "TY1", "YT1",
             "kS", "qS", "Tr", "Av"] + [f"kv{h}" for h in range(NHB)]
        dv, ac, pe_ = Steps(sem("e_dve"), D_), Steps(sem("e_act"), A_), Steps(sem("e_pe"), T_)
        block = ctx.enter_context(nc.Block(name="delta_samples"))
        c = {n: coef[0:R, NBLK, k, :] for k, n in enumerate(COEF)}
        six = lambda x: x.unsqueeze(1).broadcast_to([x.shape[0], NHB] + list(x.shape[1:]))
        sixty = lambda b, n=R: bank[b][0:n, 0:NHB * R].rearrange("p (h n) -> p h n", n=R)
        wide = lambda z: bank[z][0:R, 0:3 * P].rearrange("p (h n) -> p h n", n=P)
        H3 = [slice(0, 3), slice(3, 6)]

        @block.sync
        def _(sp):
            for dst, src in ((ident, "ident"), (ones, "ones"), (limit, "limit"), (level0, "level0"), (level0_T, "level0_T")):
                sp.dma_start(dst[:, :], t[src]).then_inc(loaded, 16)
            for dst, src in ((tri, "tri_incl"), (levels, "levels"), (of_seq, "of_seq")):
                sp.dma_start(dst[:, :, :], t[src]).then_inc(loaded, 16)
            sp.dma_start(in_seq[:, :], t["in_seq"]).then_inc(loaded, 16)
            sp.dma_start(x[:, :, :], t["conv_d"][:, :, SEQ:].rearrange("a p n -> p a n")).then_inc(loaded, 16)
            for s in range(NSEQ):
                sp.dma_start(st[:, :, s, :], t["state_gdn"][s].rearrange("h k v -> k h v")).then_inc(loaded, 16)
            dv.wait(sp, "o")
            sp.dma_start(t["o_d"][SEQ:], o[:, :, :].rearrange("p h v -> p (h v)")).then_inc(out, 16)
            dv.wait(sp, f"st{NHB - 1}")
            for s in range(NSEQ):
                sp.dma_start(t["gdn_s"][s].rearrange("h k v -> k h v"), st[:, :, s, :]).then_inc(out, 16)
            sp.wait_ge(out, 16 * (NSEQ + 1))

        @block.tensor
        def _(pe):
            pe.wait_ge(loaded, 16 * (10 + NSEQ))

            def per_head(b, rows, f, n=R):
                for h in range(NHB):
                    last = f(bank[b][0:rows, n * h:n * (h + 1)], h)
                return last

            def halves3(z0, f):
                for h in range(NHB):
                    last = f(bank[z0 + h // 3][0:R, P * (h % 3):P * (h % 3 + 1)], h)
                return last
            mm = lambda out, a, b: pe.matmul(out, a, b, start=True, stop=True)
            dv.wait(pe, "sq")
            for n in range(2 * NHB):
                last = mm(bank[0][0:R, n:n + 1], sq[:, n, :], ones[:, 0:1])
            pe_.done(last, "norms")
            dv.wait(pe, "gs")
            pe_.done(mm(bank[1][:, 0:NHB * NSEQ], ones[0:R, :], gs[:, :, :].rearrange("p h s -> p (h s)")), "decay")
            dv.wait(pe, "gU")
            pe_.done(mm(bank[2][0:R, 0:NHB * R], ones[0:R, 0:R], gU[:, :, :].rearrange("p h n -> p (h n)")), "G_rows")
            pe_.done(halves3(4, lambda out, h: pe.transpose(out, x[:, NHB + h, :], ident[:, :])), "k")
            pe_.done(halves3(6, lambda out, h: pe.transpose(out, x[:, 2 * NHB + h, :], ident[:, :])), "v")
            dv.wait(pe, "k_tok")
            pe_.done(per_head(0, P, lambda out, h: pe.transpose(out, k_tok[:, h, :], ident[0:R, 0:R])), "k_T")
            ac.wait(pe, "k_T")
            dv.wait(pe, "rel")
            pe_.done(per_head(1, R, lambda out, h: mm(out, k_T[:, h, :], k_T[:, h, :])), "gk")
            pe_.done(per_head(2, R, lambda out, h: mm(out, x[:, h, :], k_T[:, h, :])), "gq")
            dv.wait(pe, "L")
            pe_.done(per_head(3, R, lambda out, h: pe.transpose(out, L[:, h, :], ident[0:R, 0:R])), "LT")
            dv.wait(pe, "A")
            pe_.done(per_head(0, R, lambda out, h: pe.transpose(out, A[:, h, :], ident[0:R, 0:R])), "AT")
            for n, b in enumerate(LV):
                cols = lambda bk: (lambda h: bank[bk][0:R, 32 * h:32 * (h + 1)].rearrange("p (n b) -> p n b", b=b))

                def level(bk, lhs, rhs, name):
                    for h in range(NHB):
                        last = mm(cols(bk)(h), lhs[:, h, :], rhs(h))
                    pe_.done(last, name)
                dv.wait(pe, f"TT{n - 1}" if n else "TT_init")
                level(1, LT, lambda h: lower(T[:, h, :], b), f"LT{n}")
                dv.wait(pe, f"Y{n}")
                level(2, TT, lambda h: lower(Y[n][:, h, :], b), f"TY{n}")
                level(1, Y[n], lambda h: upper(TT[:, h, :], b), f"YT{n}")
            dv.wait(pe, "q_seq")
            for name, w, z0 in (("kS", k_seq, 4), ("qS", q_seq, 6)):
                for h in range(NHB):
                    for s in range(NSEQ):
                        last = pe.matmul(bank[z0 + h // 3][0:R, P * (h % 3):P * (h % 3 + 1)], w[:, h, s, :], st[:, h, s, :],
                                         start=s == 0, stop=s == NSEQ - 1)
                pe_.done(last, name)
            dv.wait(pe, "rv")
            pe_.done(halves3(4, lambda out, h: mm(out, TT[:, h, :], rv[:, h, :])), "Tr")
            ac.wait(pe, "vn")
            pe_.done(halves3(6, lambda out, h: mm(out, AT[:, h, :], vn[:, h, :])), "Av")
            for h in range(NHB):
                dv.wait(pe, f"vs{h}")
                for z in range(2):
                    last = mm(bank[2 * (h % 2) + z][:, :], k_dec[:, h, :],
                              v_seq[:, h % 2, 4 * z:4 * (z + 1), :].rearrange("p s v -> p (s v)"))
                pe_.done(last, f"kv{h}")

        @block.scalar
        def _(act):
            dv.wait(act, "rsum")
            ac.done(act.activation(rn[:, :], t1[:, :], ACT.Ln), "ln")
            ac.wait(act, "ln")
            ac.done(act.activation(rn[:, :], rn[:, :], ACT.Exp, scale=-0.5), "rough")
            dv.wait(act, "decay")
            ac.done(act.activation(decay[:, :, :], decay[:, :, :], ACT.Exp), "decay")
            dv.wait(act, "rel")
            ac.done(act.activation(E[:, :, :], E[:, :, :], ACT.Exp, scale=-1.0), "E")
            pe_.wait(act, "k_T")
            ac.done(act.activation(k_T[:, :, :], sixty(0, P), ACT.Copy), "k_T")
            pe_.wait(act, "LT")
            ac.done(act.activation(LT[:, :, :], sixty(3), ACT.Copy), "LT")
            pe_.wait(act, "AT")
            ac.done(act.activation(AT[:, :, :], sixty(0), ACT.Copy), "AT")
            pe_.wait(act, "qS")
            for h in range(NHB):
                last = act.activation(qs[:, h, :], wide(6 + h // 3)[:, h % 3, :], ACT.Copy, scale=q_eG[:, h:h + 1])
            ac.done(last, "qs")
            pe_.wait(act, "Tr")
            for z in range(2):
                last = act.activation(vn[:, H3[z], :], wide(4 + z), ACT.Copy)
            ac.done(last, "vn")

        @block.vector
        def _(dve):
            def do(ins, name):
                dv.done(ins, name)
                dv.wait(dve, name)
            tt, sts = dve.tensor_tensor, dve.scalar_tensor_tensor
            do(dve.memset(Y[0][:, :, :], 0.0), "zero0")
            do(dve.memset(Y[1][:, :, :], 0.0), "zero1")
            dve.wait_ge(loaded, 16 * (10 + NSEQ))
            do(tt(sq[:, :, :], x[:, 0:2 * NHB, :], x[:, 0:2 * NHB, :], ALU.mult), "sq")
            do(tt(gs[:, :, :], bc(c["g"], NSEQ), six(in_seq[0:R, :]), ALU.mult), "gs")
            do(tt(gU[:, :, :], six(tri[0:R, 1, 0:R]), bc(c["g"], R), ALU.mult), "gU")
            pe_.wait(dve, "norms")
            do(dve.tensor_scalar(t1[:, :], bank[0][0:R, 0:2 * NHB], RMS_EPS, None, ALU.add), "rsum")
            ac.wait(dve, "rough")
            do(tt(t2[:, :], rn[:, :], rn[:, :], ALU.mult), "n1")
            do(sts(out=t2[:, :], in0=t1[:, :], scalar=-0.5, in1=t2[:, :], op0=ALU.mult, op1=ALU.mult), "n2")
            do(sts(out=rn[:, :], in0=t2[:, :], scalar=1.5, in1=rn[:, :], op0=ALU.add, op1=ALU.mult), "r")
            do(dve.tensor_scalar(rn[:, 0:NHB], rn[:, 0:NHB], DB ** -0.5, None, ALU.mult), "rq")
            do(tt(q_eG[:, :], rn[:, 0:NHB], c["eG"], ALU.mult), "q_eG")
            pe_.wait(dve, "decay")
            do(dve.tensor_copy(decay[:, :, :], bank[1][:, 0:NHB * NSEQ].rearrange("p (h s) -> p h s", s=NSEQ)), "decay")
            pe_.wait(dve, "G_rows")
            for h in range(NHB):
                last = sts(out=E[:, h, :], in0=sixty(2)[:, h, :], scalar=c["G"][:, h:h + 1], in1=limit[0:R, 0:R],
                           op0=ALU.subtract, op1=ALU.max)
            do(last, "rel")
            pe_.wait(dve, "k")
            for z in range(2):
                last = tt(k_tok[:, H3[z], :], wide(4 + z), bc(rn[:, NHB:][:, H3[z]], P), ALU.mult)
            do(last, "k_tok")
            pe_.wait(dve, "v")
            for z in range(2):
                last = tt(bv[:, H3[z], :], wide(6 + z), bc(c["beta"][:, H3[z]], P), ALU.mult)
            do(last, "bv")
            ac.wait(dve, "E")
            do(tt(EB[:, :, :], E[:, :, :], bc(c["beta"], R), ALU.mult), "EB")
            do(tt(EQ[:, :, :], E[:, :, :], bc(rn[:, 0:NHB], R), ALU.mult), "EQ")
            do(tt(k_dec[:, :, :], k_tok[:, :, :], bc(c["decay_k"], P), ALU.mult), "k_dec")
            pe_.wait(dve, "gk")
            do(tt(L[:, :, :], sixty(1), EB[:, :, :], ALU.mult), "L")
            pe_.wait(dve, "gq")
            do(tt(A[:, :, :], sixty(2), EQ[:, :, :], ALU.mult), "A")
            do(tt(T[:, :, :], L[:, :, :], six(level0[0:R, 0:R]), ALU.mult), "T_pairs")
            do(tt(T[:, :, :], T[:, :, :], six(ident[0:R, 0:R]), ALU.add), "T_init")
            ac.wait(dve, "LT")
            do(tt(TT[:, :, :], LT[:, :, :], six(level0_T[0:R, 0:R]), ALU.mult), "TT_pairs")
            do(tt(TT[:, :, :], TT[:, :, :], six(ident[0:R, 0:R]), ALU.add), "TT_init")
            for n, b in enumerate(LV):
                got = lambda bk: bank[bk][0:R, 0:NHB * 32].rearrange("p (h n b) -> p h n b", h=NHB, b=b)
                pe_.wait(dve, f"LT{n}")
                do(tt(lower(Y[n][:, :, :], b), got(1), six(levels[0:R, n, 0:32].rearrange("p (n b) -> p n b", b=b)), ALU.mult), f"Y{n}")
                pe_.wait(dve, f"TY{n}")
                do(tt(lower(T[:, :, :], b), lower(T[:, :, :], b), got(2), ALU.subtract), f"T{n}")
                pe_.wait(dve, f"YT{n}")
                do(tt(upper(TT[:, :, :], b), upper(TT[:, :, :], b), got(1), ALU.subtract), f"TT{n}")
            ac.wait(dve, "k_T")
            over_s = lambda a: a.unsqueeze(1).broadcast_to([P, NSEQ, R])
            for h in range(NHB):
                last = tt(k_seq[:, h], over_s(k_T[:, h, :]), of_seq[:, :, :], ALU.mult)
            do(last, "k_seq")
            for h in range(NHB):
                last = tt(q_seq[:, h], over_s(x[:, h, :]), of_seq[:, :, :], ALU.mult)
            do(last, "q_seq")
            pe_.wait(dve, "kS")
            for h in range(NHB):
                last = sts(out=rv[:, h, :], in0=wide(4 + h // 3)[:, h % 3, :], scalar=c["neg_beta_eG"][:, h:h + 1],
                           in1=bv[:, h, :], op0=ALU.mult, op1=ALU.add)
            do(last, "rv")
            pe_.wait(dve, "Av")
            for z in range(2):
                last = tt(o[:, H3[z], :], wide(6 + z), qs[:, H3[z], :], ALU.add)
            do(last, "o")
            for h in range(NHB):
                if h >= 2:
                    pe_.wait(dve, f"kv{h - 2}")
                do(tt(v_seq[:, h % 2], vn[:, h, :].unsqueeze(1).broadcast_to([R, NSEQ, P]), bc(in_seq[0:R, :], P), ALU.mult), f"vs{h}")
                pe_.wait(dve, f"kv{h}")
                for s in range(NSEQ):
                    last = sts(out=st[:, h, s, :], in0=st[:, h, s, :], scalar=decay[:, h, s:s + 1],
                               in1=bank[2 * (h % 2) + s // 4][:, P * (s % 4):P * (s % 4 + 1)], op0=ALU.mult, op1=ALU.add)
                do(last, f"st{h}")


SUP = 256
NSUP = SEQ // SUP
KA = WA // P
FEW = T_ZA + T_ZB


RAW = 4
RING_M = 4


def split_weights(act, src, tiles, w_raw, w_hi, wr_in, w_hi_done, w_lo_done):
    def load(k):
        act.dma_start(w_raw[:, k % RAW, :], src[P * k:P * (k + 1), :]).then_inc(wr_in[k % RAW], 16)
    for k in range(RAW - 1):
        load(k)
    for k in range(tiles):
        if k + RAW - 1 < tiles:
            if k:
                act.wait_ge(w_lo_done, k)
            load(k + RAW - 1)
        act.wait_ge(wr_in[k % RAW], 16 * (k // RAW + 1))
        act.activation(w_hi[:, k, :], w_raw[:, k % RAW, :], ACT.Copy).then_inc(w_hi_done, 1)


def merge_branches(nc, t):
    with ExitStack() as ctx:
        sb = lambda name, shape, dt=F32: ctx.enter_context(nc.sbuf_tensor(name, shape, dt))
        pb = lambda name, shape: ctx.enter_context(nc.psum_tensor(name, shape, F32))
        sem = t["sem"]
        w_hi, w_lo = sb("wab_hi", [P, 2 * KA, D], F32R), sb("wab_lo", [P, 2 * KA, D], F32R)
        u_hi, u_lo = sb("u_hi", [P, 2, FEW, SUP], F32R), sb("u_lo", [P, 2, FEW, SUP], F32R)
        w_raw = sb("wab_raw", [P, RAW, D])
        ident, norm = sb("ident_f", [P, P]), sb("norm_f", [P, 1])
        rows2 = sb("rows_f", [P, 2, 2 * KA, P])
        stat2 = sb("stat_f", [P, 2, NG, NSTAT])
        z = sb("z_f", [P, FEW, P])
        gated = sb("gated", [P, FEW, P])
        least, share, total = sb("least", [P, HPG]), sb("share", [P, NG, HPG]), sb("total", [P, HPG])
        wd = sb("wd", [P, NG, HPG])
        ss, root, rs = sb("ss", [P, NHB]), sb("root", [P, NHB]), sb("rs", [P, NHB])
        sqs = gated[:, T_ZA:, :]
        gates = sb("gates", [P, RING_M, 2, SUP])
        prod = sb("prod", [P, 2, 2, SUP])
        merged = sb("merged", [P, 2, SUP])
        ps_t = [pb(f"ps_ft{b}", [P, 4, P]) for b in range(3)]
        ps_m = [pb(f"ps_fm{b}", [P, 2, SUP]) for b in range(RING_M)]
        const_in = sem("f_const")
        wr_in = [sem(f"f_wr_in{j}") for j in range(RAW)]
        w_hi_done, w_lo_done = sem("f_w_hi"), sem("f_w_lo")
        row_in = [sem(f"f_rows{j}") for j in range(2)]
        z_in, gate_in = sem("f_z"), [sem(f"f_gate{j}") for j in range(RING_M)]
        d_steps = Steps(sem("f_dve"), ["least", "diff", "wd", "total", "rtotal", "share", "att", "ss", "eps", "rs", "o"]
                        + [f"g{b}" for b in range(3)] + ["split"])
        a_steps = Steps(sem("f_act"), ["share", "squares", "root", "hi"])
        p_steps = Steps(sem("f_pe"), [f"turn{b}" for b in range(3)])
        mm_done, prod_done, sum_done = sem("f_mm"), sem("f_prod"), sem("f_sum")
        out = [sem(f"f_out{j}") for j in range(2)]
        block = ctx.enter_context(nc.Block(name="merge_branches"))
        NF = D // P

        def blocks(n):
            return [2 * n] if isinstance(n, int) and n == NSUP else [2 * n, 2 * n + 1]

        def flow(eng, part, mult):
            def step(nxt, now):
                for f in range(NF):
                    if f // 4 < len(blocks(nxt[0])):
                        part(*nxt, f // 4, f % 4)
                    mult(*now, f)
            for f in range(NF):
                part(0, 0, f // 4, f % 4)
            step((1, 1), (0, 0))
            with eng.Fori(0, NSUP // 2 - 1) as i:
                step((2 * i + 2, 0), (2 * i + 1, 1))
                step((2 * i + 3, 1), (2 * i + 2, 0))
            step((NSUP, 0), (NSUP - 1, 1))
            for f in range(NF):
                mult(NSUP, 0, f)
        zero = lambda n: isinstance(n, int) and n == 0
        size = lambda n: SAMP if isinstance(n, int) and n == NSUP else SUP
        rows_of = lambda n: SAMP if isinstance(n, int) and n == NSUP else P

        @block.sync
        def _(sp):
            sp.dma_start(ident[:, :], t["ident"]).then_inc(const_in, 16)
            sp.dma_start(norm[:, :], t["gdn_norm"].rearrange("(p a) -> p a", a=1)).then_inc(const_in, 16)

            def part(n, j, k, q):
                b, m = blocks(n)[k], rows_of(n)
                tok = bass.ds(P * b, P) if m == P else slice(SEQ, NT)
                if q == 0:
                    if not zero(n):
                        p_steps.wait(sp, "turn2", b - 2)
                    if m == P:
                        sp.dma_start(rows2[:, k, 0:KA, :].rearrange("p a n -> p (a n)"),
                                     t["att_d"][tok].rearrange("p g n -> p (g n)")).then_inc(row_in[k], 16)
                        sp.dma_start(stat2[:, k], t["stats_d"][tok]).then_inc(row_in[k], 16)
                    else:
                        d_steps.wait(sp, "split", b - 1)
                        sp.dma_start(gated[:, 0:T_ZA, 0:SAMP], t["att_s"]).then_inc(row_in[k], 16)
                        sp.dma_start(stat2[0:SAMP, k], t["stats_d"][0:SAMP]).then_inc(row_in[k], 16)
                    sp.dma_start(rows2[0:m, k, KA:, :].rearrange("p a n -> p (a n)"), t["o_d"][tok]).then_inc(row_in[k], 16)

            def mult(n, j, f):
                w = size(n)
                tok = bass.ds(SUP * n, SUP) if w == SUP else slice(SEQ, NT)
                if not (zero(n) and f < RING_M):
                    sp.wait_ge(prod_done, NF * n + f + 1 - RING_M)
                sp.dma_start(gates[:, f % RING_M, :, 0:w], t["g_d"][f::NF, :, tok].rearrange("a p n -> p a n")
                             ).then_inc(gate_in[f % RING_M], 16)
            flow(sp, part, mult)

        @block.tensor
        def _(pe):
            pe.wait_ge(const_in, 32)

            def part(n, j, k, q):
                if q != 2:
                    return
                b, m = blocks(n)[k], rows_of(n)
                for r in range(3):
                    if not (zero(n) and k == 0):
                        d_steps.wait(pe, f"g{r}", b - 1)
                    if r == 0:
                        d_steps.wait(pe, "o", b)
                    for a in range(4):
                        last = pe.transpose(ps_t[r][:, a, 0:m], rows2[0:m, k, 4 * r + a, :], ident[0:m, 0:m])
                    p_steps.done(last, f"turn{r}")

            def mult(n, j, f):
                w = size(n)
                if f == 0:
                    d_steps.wait(pe, "split", blocks(n)[-1])
                if not (zero(n) and f < RING_M):
                    pe.wait_ge(prod_done, NF * n + f + 1 - RING_M)
                for side in range(2):
                    for k in range(KA):
                        kk = KA * side + k
                        if zero(n) and f == 0:
                            pe.wait_ge(w_lo_done, kk + 1)
                        cols = slice(P * f, P * (f + 1))
                        last = mm3(pe, ps_m[f % RING_M][:, side, 0:w], (w_hi[:, kk, cols], w_lo[:, kk, cols]),
                                   (u_hi[:, j, kk, 0:w], u_lo[:, j, kk, 0:w]), k == 0, k == KA - 1)
                last.then_inc(mm_done, 1)
            flow(pe, part, mult)

        @block.vector
        def _(dve):
            dve.wait_ge(const_in, 32)
            tt, sts = dve.tensor_tensor, dve.scalar_tensor_tensor
            over_g = lambda x, m: x[0:m, :].unsqueeze(1).broadcast_to([m, NG, HPG])

            def part(n, j, k, q):
                b, m = blocks(n)[k], rows_of(n)
                rows, stat = rows2[:, k], stat2[:, k]

                def do(ins, name):
                    d_steps.done(ins, name)
                    d_steps.wait(dve, name, b)
                if q == 0:
                    dve.wait_ge(row_in[k], 48 * (n + 1))
                    do(dve.tensor_reduce(least[0:m, :], stat[0:m, :, 0:HPG].rearrange("p g h -> p h g"), AX.X, ALU.min), "least")
                    do(tt(share[0:m], over_g(least, m), stat[0:m, :, 0:HPG], ALU.subtract), "diff")
                    a_steps.wait(dve, "share", b)
                    do(tt(wd[0:m], share[0:m], stat[0:m, :, HPG:], ALU.mult), "wd")
                    do(dve.tensor_reduce(total[0:m, :], wd[0:m].rearrange("p g h -> p h g"), AX.X, ALU.add), "total")
                    do(dve.reciprocal(total[0:m, :], total[0:m, :]), "rtotal")
                    do(tt(share[0:m], share[0:m], over_g(total, m), ALU.mult), "share")
                    att = rows[0:m, 0:KA, :].rearrange("p a n -> p (a n)").rearrange("p (g d) -> p g d", d=DH)
                    if m == P:
                        do(tt(att, att, bc(share[0:m].rearrange("p g h -> p (g h)"), DH), ALU.mult), "att")
                    else:
                        do(dve.memset(rows[0:m, 0:KA, :], 0.0), "att")
                elif q == 1:
                    a_steps.wait(dve, "squares", b)
                    do(dve.tensor_reduce(ss[0:m, :], sqs[0:m], AX.X, ALU.add), "ss")
                    do(dve.tensor_scalar(ss[0:m, :], ss[0:m, :], 1.0 / DB, RMS_EPS, ALU.mult, ALU.add), "eps")
                    a_steps.wait(dve, "root", b)
                    do(dve.reciprocal(rs[0:m, :], root[0:m, :]), "rs")
                    do(tt(rows[0:m, KA:, :], rows[0:m, KA:, :], bc(rs[0:m, :], P), ALU.mult), "o")
                elif q == 2:
                    dve.wait_ge(z_in, 16 * (b + 1))
                    for r in range(3):
                        p_steps.wait(dve, f"turn{r}", b)
                        cut = [(4 * r, 4 * r + 4)] if r != 1 else [(4, 6), (6, 8)]
                        for lo, hi in cut:
                            src = ps_t[r][:, lo - 4 * r:hi - 4 * r, 0:m]
                            if hi <= KA and m < P:
                                ins = tt(gated[:, lo:hi, 0:m], gated[:, lo:hi, 0:m], z[:, lo:hi, 0:m], ALU.mult)
                            elif hi <= KA:
                                ins = tt(gated[:, lo:hi, 0:m], src, z[:, lo:hi, 0:m], ALU.mult)
                            else:
                                ins = sts(out=gated[:, lo:hi, 0:m], in0=src, scalar=norm[:, 0:1], in1=z[:, lo:hi, 0:m],
                                          op0=ALU.mult, op1=ALU.mult)
                        do(ins, f"g{r}")
                else:
                    a_steps.wait(dve, "hi", b)
                    at = slice(P * k, P * k + m)
                    do(tt(u_lo[:, j, :, at], gated[:, :, 0:m], f32(u_hi[:, j, :, at]), ALU.subtract), "split")

            def mult(n, j, f):
                w, u = size(n), NF * n + f
                dve.wait_ge(mm_done, u + 1)
                dve.wait_ge(gate_in[f % RING_M], 16 * (NF // RING_M * n + f // RING_M + 1))
                dve.tensor_tensor(prod[:, f % 2, :, 0:w], ps_m[f % RING_M][:, :, 0:w], gates[:, f % RING_M, :, 0:w],
                                  ALU.mult).then_inc(prod_done, 1)
                dve.wait_ge(prod_done, u + 1)
                if not (zero(n) and f < 2):
                    dve.wait_ge(out[f % 2], 16 * (NF // 2 * n + f // 2))
                dve.tensor_tensor(merged[:, f % 2, 0:w], prod[:, f % 2, 0, 0:w], prod[:, f % 2, 1, 0:w],
                                  ALU.add).then_inc(sum_done, 1)
            for k in range(2 * KA):
                dve.wait_ge(w_hi_done, k + 1)
                dve.tensor_tensor(w_lo[:, k, :], w_raw[:, k % RAW, :], f32(w_hi[:, k, :]), ALU.subtract).then_inc(w_lo_done, 1)
            flow(dve, part, mult)

        @block.scalar
        def _(act):
            def part(n, j, k, q):
                b, m = blocks(n)[k], rows_of(n)
                if q == 0:
                    tok = bass.ds(P * b, P) if m == P else slice(SEQ, NT)
                    act.dma_start(z[:, :, 0:m], t["z_d"][:, :, tok].rearrange("a p n -> p a n")).then_inc(z_in, 16)
                    act.wait_ge(row_in[k], 48 * (n + 1))
                    d_steps.wait(act, "diff", b)
                    a_steps.done(act.activation(share[0:m], share[0:m], ACT.Exp), "share")
                    a_steps.done(act.activation(sqs[0:m], rows2[0:m, k, KA:, :], ACT.Square), "squares")
                elif q == 1:
                    d_steps.wait(act, "eps", b)
                    a_steps.done(act.activation(root[0:m, :], ss[0:m, :], ACT.Sqrt), "root")
                elif q == 2:
                    d_steps.wait(act, "g2", b)
                    if not (isinstance(n, int) and n < 2):
                        act.wait_ge(mm_done, NF * (n - 1))
                    a_steps.done(act.activation(u_hi[:, j, :, P * k:P * k + m], gated[:, :, 0:m], ACT.Copy), "hi")
            split_weights(act, t["w_out"], 2 * KA, w_raw, w_hi, wr_in, w_hi_done, w_lo_done)
            flow(act, part, lambda n, j, f: None)

        @block.gpsimd
        def _(pool):
            def mult(n, j, f):
                tok = bass.ds(SUP * n, SUP) if size(n) == SUP else slice(SEQ, NT)
                pool.wait_ge(sum_done, NF * n + f + 1)
                pool.dma_start(t["merged_d"][f, :, tok], merged[:, f % 2, 0:size(n)]).then_inc(out[f % 2], 16)
            flow(pool, lambda n, j, k, q: None, mult)
            for j in range(2):
                pool.wait_ge(out[j], 16 * (NF // 2) * (NSUP + 1))


def finish(nc, t):
    with ExitStack() as ctx:
        sb = lambda name, shape, dt=F32: ctx.enter_context(nc.sbuf_tensor(name, shape, dt))
        pb = lambda name, shape: ctx.enter_context(nc.psum_tensor(name, shape, F32))
        sem = t["sem"]
        w_hi, w_lo, w_raw = sb("wo_hi", [P, KT, D], F32R), sb("wo_lo", [P, KT, D], F32R), sb("wo_raw", [P, RAW, D])
        m_raw = sb("m_raw", [P, 2, KT, P])
        m_hi, m_lo = sb("m_hi", [P, 2, KT, P], F32R), sb("m_lo", [P, 2, KT, P], F32R)
        x = sb("x_res", [P, 2, D])
        gate_p, gate_s = sb("gate_p", [P, D]), sb("gate_s", [SAMP, D])
        ln_g, ln_b = sb("ln_g", [P, D]), sb("ln_b", [P, D])
        y = sb("y_res", [P, 2, D])
        junk = sb("ln_junk", [P, D])
        total, mean, ssq = sb("ln_total", [P, 1]), sb("ln_mean", [P, 1]), sb("ln_ssq", [P, 1])
        var, root, rstd, shift = sb("ln_var", [P, 1]), sb("ln_root", [P, 1]), sb("ln_rstd", [P, 1]), sb("ln_shift", [P, 1])
        ps = [pb(f"ps_out{j}", [P, 2, 512]) for j in range(2)]
        const_in, w_hi_done, w_lo_done = sem("o_const"), sem("o_w_hi"), sem("o_w_lo")
        wr_in = [sem(f"o_wr_in{j}") for j in range(RAW)]
        m_in = [sem(f"o_m_in{j}") for j in range(2)]
        x_in = [sem(f"o_x_in{j}") for j in range(2)]
        out = [sem(f"o_out_{j}") for j in range(2)]
        mm_done = [sem(f"o_mm{j}") for j in range(2)]
        d_steps = Steps(sem("o_dve"), ["gated", "sum", "mean", "var", "rstd", "shift", "scaled", "y"])
        split_done = [sem(f"o_split{j}") for j in range(2)]
        hi_done = [sem(f"o_hi{j}") for j in range(2)]
        a_steps = Steps(sem("o_act"), ["total", "squares", "root", "norm"])
        block = ctx.enter_context(nc.Block(name="finish"))
        NB = NBLK + 1

        @block.sync
        def _(sp):
            sp.dma_start(gate_p[:, :], t["gate_d"][0].partition_broadcast(P)).then_inc(const_in, 16)
            for s in range(NSEQ):
                sp.dma_start(gate_s[TS * s:TS * (s + 1), :], t["gate_d"][1 + s].partition_broadcast(TS)).then_inc(const_in, 16)
            sp.dma_start(ln_g[:, :], t["ln_g"].partition_broadcast(P)).then_inc(const_in, 16)
            sp.dma_start(ln_b[:, :], t["ln_b"].partition_broadcast(P)).then_inc(const_in, 16)

            def body(i, j):
                if not (isinstance(i, int) and i == 0):
                    sp.wait_ge(split_done[j], i)
                m = SAMP if isinstance(i, int) and i == NBLK // 2 else P
                tok = slice(SEQ, NT) if m < P else bass.ds(2 * P * i + P * j, P)
                sp.dma_start(m_raw[:, j, :, 0:m], t["merged_d"][:, :, tok].rearrange("a p n -> p a n")).then_inc(m_in[j], 16)
                if not (isinstance(i, int) and i == 0):
                    d_steps.wait(sp, "sum", 2 * i + j - 2)
                sp.dma_start(x[0:m, j, :], t["x_rows"][tok]).then_inc(x_in[j], 16)
            body(0, 0)
            body(0, 1)
            with sp.Fori(1, NBLK // 2) as i:
                body(i, 0)
                body(i, 1)
            body(NBLK // 2, 0)

        @block.scalar
        def _(act):
            split_weights(act, t["w_o"], KT, w_raw, w_hi, wr_in, w_hi_done, w_lo_done)

            def split(i, j, m=P):
                act.wait_ge(m_in[j], 16 * (i + 1))
                if not (isinstance(i, int) and i == 0):
                    act.wait_ge(mm_done[j], i)
                act.activation(m_hi[:, j, :, 0:m], m_raw[:, j, :, 0:m], ACT.Copy).then_inc(hi_done[j], 1)

            def rest(i, j, m=P):
                b = 2 * i + j
                d_steps.wait(act, "sum", b)
                a_steps.done(act.activation(junk[0:m], y[0:m, j, :], ACT.Copy, accum_out=total[0:m]), "total")
                d_steps.wait(act, "mean", b)
                a_steps.done(act.activation(junk[0:m], y[0:m, j, :], ACT.Square, bias=mean[0:m], accum_out=ssq[0:m]), "squares")
                d_steps.wait(act, "var", b)
                a_steps.done(act.activation(root[0:m], var[0:m], ACT.Sqrt), "root")
                d_steps.wait(act, "shift", b)
                a_steps.done(act.activation(y[0:m, j, :], y[0:m, j, :], ACT.Identity, bias=shift[0:m], scale=rstd[0:m]), "norm")
            split(0, 0)
            split(0, 1), rest(0, 0)
            split(1, 0), rest(0, 1)
            with act.Fori(1, NBLK // 2 - 1) as i:
                split(i, 1), rest(i, 0)
                split(i + 1, 0), rest(i, 1)
            i = NBLK // 2 - 1
            split(i, 1), rest(i, 0)
            split(i + 1, 0, SAMP), rest(i, 1)
            rest(i + 1, 0, SAMP)

        @block.vector
        def _(dve):
            for k in range(KT):
                dve.wait_ge(w_hi_done, k + 1)
                dve.tensor_tensor(w_lo[:, k, :], w_raw[:, k % RAW, :], f32(w_hi[:, k, :]), ALU.subtract).then_inc(w_lo_done, 1)
            dve.wait_ge(const_in, 16 * (3 + NSEQ))

            def split(i, j, m=P):
                dve.wait_ge(hi_done[j], i + 1)
                dve.tensor_tensor(m_lo[:, j, :, 0:m], m_raw[:, j, :, 0:m], f32(m_hi[:, j, :, 0:m]), ALU.subtract).then_inc(split_done[j], 1)

            def rest(i, j, m=P):
                b = 2 * i + j

                def do(ins, name):
                    d_steps.done(ins, name)
                    d_steps.wait(dve, name, b)
                yj = y[0:m, j, :]
                dve.wait_ge(mm_done[j], i + 1)
                if not (isinstance(i, int) and i == 0):
                    dve.wait_ge(out[j], 16 * i)
                do(dve.tensor_tensor(yj, ps[j][0:m].rearrange("p a n -> p (a n)"), (gate_p if m == P else gate_s)[0:m, :], ALU.mult), "gated")
                dve.wait_ge(x_in[j], 16 * (i + 1))
                do(dve.scalar_tensor_tensor(out=yj, in0=x[0:m, j, :], scalar=ALPHA, in1=yj, op0=ALU.mult, op1=ALU.add), "sum")
                a_steps.wait(dve, "total", b)
                do(dve.tensor_scalar(mean[0:m], total[0:m], -1.0 / D, None, ALU.mult), "mean")
                a_steps.wait(dve, "squares", b)
                do(dve.tensor_scalar(var[0:m], ssq[0:m], 1.0 / D, LN_EPS, ALU.mult, ALU.add), "var")
                a_steps.wait(dve, "root", b)
                do(dve.reciprocal(rstd[0:m], root[0:m]), "rstd")
                do(dve.tensor_tensor(shift[0:m], mean[0:m], rstd[0:m], ALU.mult), "shift")
                a_steps.wait(dve, "norm", b)
                do(dve.tensor_tensor(yj, yj, ln_g[0:m, :], ALU.mult), "scaled")
                d_steps.done(dve.tensor_tensor(yj, yj, ln_b[0:m, :], ALU.add), "y")
            split(0, 0)
            split(0, 1), rest(0, 0)
            split(1, 0), rest(0, 1)
            with dve.Fori(1, NBLK // 2 - 1) as i:
                split(i, 1), rest(i, 0)
                split(i + 1, 0), rest(i, 1)
            i = NBLK // 2 - 1
            split(i, 1), rest(i, 0)
            split(i + 1, 0, SAMP), rest(i, 1)
            rest(i + 1, 0, SAMP)

        @block.tensor
        def _(pe):
            def body(i, j, m=P):
                pe.wait_ge(split_done[j], i + 1)
                if not (isinstance(i, int) and i == 0):
                    d_steps.wait(pe, "gated", 2 * i + j - 2)
                for h in range(2):
                    for k in range(KT):
                        cols = slice(512 * h, 512 * (h + 1))
                        if isinstance(i, int) and i == 0 and j == 0 and h == 0:
                            pe.wait_ge(w_lo_done, k + 1)
                        last = mm3(pe, ps[j][:, h, :], (m_hi[:, j, k, :], m_lo[:, j, k, :]),
                                   (w_hi[:, k, cols], w_lo[:, k, cols]), k == 0, k == KT - 1)
                last.then_inc(mm_done[j], 1)
            body(0, 0), body(0, 1)
            with pe.Fori(1, NBLK // 2) as i:
                body(i, 0), body(i, 1)
            body(NBLK // 2, 0)

        @block.gpsimd
        def _(pool):
            def body(i, j, m=P):
                d_steps.wait(pool, "y", 2 * i + j)
                tok = slice(SEQ, NT) if m < P else bass.ds(2 * P * i + P * j, P)
                pool.dma_start(t["y_rows"][tok], y[0:m, j, :]).then_inc(out[j], 16)
            with pool.Fori(0, NBLK // 2) as i:
                body(i, 0), body(i, 1)
            body(NBLK // 2, 0, SAMP)
            pool.wait_ge(out[0], 16 * (NBLK // 2 + 1))
            pool.wait_ge(out[1], 16 * (NBLK // 2))


def layouts(x_prompt, x_sample, c_prompt, c_sample, state_conv, w_ada, b_ada, w_in, conv_w, **_):
    A = np.ascontiguousarray
    x = np.concatenate([x_prompt[0], x_sample.reshape(SAMP, D)])
    w = w_in[0]
    q, k, v, z, c, zb, a, b, g = np.split(w, np.cumsum([WA, WA, WA, WA, CONV, WB, NHB, NHB]), axis=1)
    tiles = lambda m: m.reshape(KT, P, -1, P).transpose(2, 1, 0, 3).reshape(-1, P, KT * P)
    val = np.zeros((NG, P, KT, VW), np.float32)
    for n in range(NG):
        val[n, :, :, :GW] = v[:, n * GW:(n + 1) * GW].reshape(KT, P, GW).transpose(1, 0, 2)
    val[0, :, :, GW:] = np.concatenate([a, b], 1).reshape(KT, P, NAB).transpose(1, 0, 2)
    side = np.concatenate([conv_w[0].reshape(TAPS, T_CONV, P).transpose(1, 2, 0),
                           state_conv[0].reshape(NSEQ, TAPS - 1, T_CONV, P).transpose(2, 3, 0, 1)
                           .reshape(T_CONV, P, -1)], 2)
    return dict(
        x_T=A(x.reshape(NT, KT, P).transpose(2, 1, 0)), x_rows=x,
        c_T=A(np.concatenate([c_prompt, c_sample]).reshape(NC, KT, P).transpose(2, 1, 0)),
        b_ss=A(b_ada[0, :2 * D].reshape(2 * KT, P).T), b_gate=A(b_ada[0, 2 * D:]),
        w_ada=w_ada[0], w_feat=A(np.concatenate([tiles(m) for m in (c, q, k, z, zb, g)])),
        w_val=val, conv_side=A(side))


def tables():
    f = np.float32
    heads = NG * HPG
    slopes = np.exp2(f(-8.0) * np.arange(1, heads + 1, dtype=f) / f(heads)).astype(f).reshape(NG, HPG)
    steps = P + np.arange(P)[:, None] - np.arange(2 * P)[None, :]
    bias = np.full((P, NG, HPG, 2 * P), MASKED, f)
    for g, (_, dil) in enumerate(GROUPS):
        for h in range(HPG):
            bias[:, g, h] = np.where((steps >= 0) & (steps <= P), -slopes[g, h] * (steps * dil).astype(f), f(MASKED))
    bs = np.full((2, HALF, HPG, TS, KEYS), MASKED, f)
    tok = np.arange(TS)
    at = [0, P + NEWC, P + NEWC + PAST[1]]
    for g, (_, dil) in enumerate(GROUPS):
        dist = PAST[g] + tok[:, None] - np.arange(PAST[g])[None, :]
        seen = (dist % dil == 0) & (dist <= P * dil)
        new = tok[:, None] - tok[None, :]
        new_seen = (new >= 0) & (new % dil == 0)
        for h in range(HPG):
            bs[:, :, h, :, at[g]:at[g] + PAST[g]] = np.where(seen, -slopes[g, h] * dist.astype(f), f(MASKED))
            for a in range(2):
                for s in range(HALF):
                    c = P + SAMP * g + TS * (HALF * a + s)
                    bs[a, s, h, :, c:c + TS] = np.where(new_seen, -slopes[g, h] * new.astype(f), f(MASKED))
    i, j = np.arange(P)[:, None], np.arange(P)[None, :]
    seq = (i // TS == j // TS)
    one = np.ones((P, P), f)
    pair = lambda b: ((i // (2 * b) == j // (2 * b)) & (i // b % 2 == 1) & (j // b % 2 == 0)).astype(f)
    low = lambda m, b: m.reshape(P, -1, 2, b)[:, :, 0, :].reshape(P, P // 2)
    tri = (i <= j).astype(f)
    more = dict(ones=one, tri=tri, tri_incl=np.stack([tri, tri * seq], 1), same=np.stack([one, one * seq], 1),
                upper_big=np.where(j > i, f(BIG), f(0)), level0=-pair(1), level0_T=np.ascontiguousarray(-pair(1).T),
                limit=np.where((j > i) | ~seq, f(BIG), f(0)),
                of_seq=np.tile((np.arange(NSEQ)[:, None] == np.arange(SAMP) // TS).astype(f), (P, 1, 1)),
                in_seq=(np.arange(P)[:, None] // TS == np.arange(NSEQ)).astype(f),
                levels=np.stack([low(pair(b), b) for b in LEVELS], 1))
    return dict(**more, bias_prompt=bias / f(DH ** -0.5), bias_samples=bs.reshape(2, P, KEYS).transpose(1, 0, 2).copy(), ident=np.eye(P, dtype=f))


def caches(cache_win1, cache_win2, cache_win3, **_):
    c = np.concatenate([cache_win1[0], cache_win2[0], cache_win3[0]], axis=1)
    k = c[:, :, 0].reshape(NSEQ, CACHED, NP_, PAIR).transpose(0, 3, 2, 1)
    v = c[:, :, 1].reshape(NSEQ, KT_C, P, GW).transpose(0, 2, 1, 3)
    return dict(k_cache=np.ascontiguousarray(k), v_cache=np.ascontiguousarray(v))


def program(nc, t):
    with ExitStack() as ctx:
        sb = lambda name, shape, dt=F32: ctx.enter_context(nc.sbuf_tensor(name, shape, dt))
        taken = []

        def sem(name):
            taken.append(nc.alloc_semaphore(name=name))
            return taken[-1]
        t = dict(t, sem=sem)
        coef = sb("coef", [P, NBLK + 1, len(COEF), NHB])
        ab = sb("ab", [P, NBLK + 1, NAB])
        with nc.Block(name="clear") as block:
            @block.vector
            def _(dve):
                dve.memset(coef[:, :, :, :], 0.0)
                dve.memset(ab[:, :, :], 0.0)
        with ExitStack() as inner:
            h_hi = inner.enter_context(nc.sbuf_tensor("h_hi", [P, KT, NT], F32R))
            h_lo = inner.enter_context(nc.sbuf_tensor("h_lo", [P, KT, NT], F32R))
            modulate(nc, t, h_hi, h_lo)
            project_features(nc, t, h_hi, h_lo)
            project_values(nc, t, h_hi, h_lo, ab)
        nc.clear_and_free_semaphores(taken)
        nc.all_engine_barrier()
        attend_prompt(nc, t)
        attend_samples(nc, t)
        decay_coefficients(nc, t, ab, coef)
        delta_prompt(nc, t, coef)
        delta_samples(nc, t, coef)
        merge_branches(nc, t)
        finish(nc, t)


_SCRATCH = dict(gate_d=(NC, D), conv_d=(T_CONV, P, NT), q_d=(T_Q, P, NT), z_d=(T_ZA + T_ZB, P, NT), g_d=(T_G, P, NT),
                att_d=(SEQ, NG, GW), stats_d=(SEQ, NG, NSTAT), att_s=(P, NPT, SAMP), o_d=(NT, WB), merged_d=(KT, P, NT))
_OUTS = dict(y_rows=(NT, D), k_T=(T_K, P, NT), v_out=(NG, NBLK, P, GW), v_new=(NG, SAMP, GW),
             conv_tail=(T_CONV, P, U_W - U_SAMP + U_PRE), gdn_p=(NHB, P, P), gdn_s=(NSEQ, NHB, P, P))


def kernel(**inputs):
    import concourse.bacc as _bacc
    from concourse.bass_utils import run_bass_kernel_spmd as _run

    inputs = {k: np.asarray(v) for k, v in inputs.items()}
    arrays = {**layouts(**inputs), **caches(**inputs), **tables()}
    for name in ("dt_bias", "a_log", "gdn_norm", "w_o", "ln_g", "ln_b", "state_gdn"):
        arrays[name] = inputs[name][0]
    arrays["w_out"] = np.concatenate([inputs["w_out_a"][0], inputs["w_out_b"][0]])
    nc = _bacc.Bacc("TRN2", target_bir_lowering=False, num_devices=1)
    sent, t = {}, {}
    for name, a in arrays.items():
        a = np.ascontiguousarray(a)
        sent[f"in_{name}"] = a
        t[name] = nc.dram_tensor(f"in_{name}", a.shape, F32, kind="ExternalInput").ap()
    for name, shape in _SCRATCH.items():
        t[name] = nc.dram_tensor(f"scratch_{name}", shape, F32).ap()
    for name, shape in _OUTS.items():
        t[name] = nc.dram_tensor(f"out_{name}", shape, F32, kind="ExternalOutput").ap()
    program(nc, t)
    r = _run(nc, [sent], core_ids=[0]).results[0]
    o = {name: np.asarray(r[f"out_{name}"]) for name in _OUTS}

    y = o["y_rows"]
    k = o["k_T"].reshape(NG, GW, NT).transpose(0, 2, 1)
    v = np.empty((NG, NT, GW), np.float32)
    for g, (a, b, s) in enumerate(BLOCKS):
        for n in range(NBLK):
            start = a * (n // 4) + b * (n % 4)
            v[g, start:start + s * P:s][:P] = o["v_out"][g, n]
        v[g, SEQ:] = o["v_new"][g]
    kv = np.stack([k, v], axis=2).reshape(NG, NT, 2, HPG, DH)
    win_p = [kv[g, SEQ - min(w, SEQ):SEQ][None, None] for g, (w, _) in enumerate(GROUPS)]
    win_s = [kv[g, SEQ:].reshape(1, NSEQ, TS, 2, HPG, DH) for g in range(NG)]
    tail = o["conv_tail"]
    conv_p = tail[:, :, 0:U_PRE].transpose(2, 0, 1).reshape(1, 1, U_PRE, CONV)
    conv_s = tail[:, :, U_PRE:].reshape(T_CONV, P, NSEQ, EXT)[..., TS:].transpose(2, 3, 0, 1).reshape(1, NSEQ, U_PRE, CONV)
    out = (y[:SEQ][None], y[SEQ:].reshape(NSEQ, TS, D), *win_p, o["gdn_p"][None, None], conv_p,
           *win_s, o["gdn_s"][None], conv_s)
    return tuple(np.ascontiguousarray(x) for x in out)
```

```python
from contextlib import ExitStack

import numpy as np
import concourse.bass as bass
from concourse import mybir

F32 = mybir.dt.float32
F32R = mybir.dt.float32r
ALU = mybir.AluOpType
ACT = mybir.ActivationFunctionType
AX = mybir.AxisListType

P = 128
D = 1024
KT = D // P
SEQ = 2048
NSEQ, TS = 8, 8
SAMP = NSEQ * TS
NT = SEQ + SAMP
NC = 1 + NSEQ
GROUPS = ((128, 1), (512, 4), (2048, 16))
NG = len(GROUPS)
HPG, DH = 4, 64
GW = HPG * DH
WA = NG * GW
NHB, DB = 6, 128
WB = NHB * DB
CONV = 3 * WB
TAPS = 4
PAST = tuple(min(w, 1024) for w, _ in GROUPS)
SEEN = [[p for p in range(n) if any((n + e - p) % d == 0 for e in range(TS))] for n, (_, d) in zip(PAST, GROUPS)]
KEPT = tuple(len(p) for p in SEEN)
ALPHA = 2.0 ** 0.25
LN_EPS = 1e-5
RMS_EPS = 1e-6
NBLK = SEQ // P
NCH = -(-NT // 512)
CH = -(-NT // NCH) + 1
CHUNKS = [(c * CH, min(CH, NT - c * CH)) for c in range(NCH)]

T_CONV, T_Q, T_K, T_ZA, T_ZB, T_G = CONV // P, WA // P, WA // P, WA // P, WB // P, 2 * D // P
FT = T_CONV + T_Q + T_K + T_ZA + T_ZB + T_G
NAB = 2 * NHB
VW = GW + NAB
SIDE = TAPS + NSEQ * (TAPS - 1)
EXT = TAPS - 1 + TS
U_PRE = TAPS - 1
U_SAMP = U_PRE + SEQ
U_W = U_SAMP + NSEQ * EXT
BLOCKS = ((512, 128, 1), (1, 512, 4), (4, 1, 16))


def f32(ap):
    return ap.bitcast(F32)


def bc(ap, n):
    return ap.unsqueeze(len(ap.shape)).broadcast_to(list(ap.shape) + [n])


def mm3(pe, out, lhs, rhs, start, stop):
    (ah, al), (bh, bl) = lhs, rhs
    pe.matmul(out, ah, bl, start=start, stop=False)
    pe.matmul(out, al, bh, start=False, stop=False)
    return pe.matmul(out, ah, bh, start=False, stop=stop)


def modulate(nc, t, h_hi, h_lo):
    with ExitStack() as ctx:
        sb = lambda name, shape, dt=F32: ctx.enter_context(nc.sbuf_tensor(name, shape, dt))
        sem = t["sem"]
        c_sb = sb("ada_c", [P, KT, NC])
        sc = sb("ada_silu_c", [P, KT, NC])
        w = sb("ada_w", [P, 2, KT, 512])
        b_ss = sb("ada_b_ss", [P, 2 * KT])
        b_gate = sb("ada_b_gate", [NC, D])
        mods = sb("ada_mods", [P, 2 * KT, NC])
        gate = sb("ada_gate", [NC, D])
        XS = 3
        x_in = sb("x_in", [P, XS, NT])
        ident = sb("ada_ident", [P, P])
        mod_rows = sb("ada_mod_rows", [NC, 2, 512])
        ps_mod = ctx.enter_context(nc.psum_tensor("ps_mod", [P, 512], F32))
        ps_row = ctx.enter_context(nc.psum_tensor("ps_row", [P, 6, 512], F32))
        small_in, silu_done, mod_done, gate_done = sem("small_in"), sem("silu_done"), sem("mod_done"), sem("gate_done")
        w_in = [sem(f"ada_w_in{j}") for j in range(2)]
        w_used, row_put, turned = sem("ada_w_used"), sem("ada_row_put"), sem("ada_turned")
        mod_ready, gate_ready, gate_out = sem("mod_ready"), sem("gate_ready"), sem("gate_out")
        x_loaded = [sem(f"x_loaded{j}") for j in range(XS)]
        h_step, hi_done, lo_done = sem("h_step"), sem("hi_done"), sem("lo_done")
        w_src = t["w_ada"].rearrange("(k p) n -> p k n", p=P)
        block = ctx.enter_context(nc.Block(name="modulate"))

        @block.sync
        def _(sp):
            sp.dma_start(c_sb[:, :, :], t["c_T"]).then_inc(small_in, 16)
            sp.dma_start(b_ss[:, :], t["b_ss"]).then_inc(small_in, 16)
            sp.dma_start(b_gate[:, :], t["b_gate"].partition_broadcast(NC)).then_inc(small_in, 16)
            sp.dma_start(ident[:, :], t["ident"]).then_inc(small_in, 16)
            for n in range(6):
                if n >= 2:
                    sp.wait_ge(w_used, n - 1)
                sp.dma_start(w[:, n % 2], w_src[:, :, n * 512:(n + 1) * 512]).then_inc(w_in[n % 2], 16)
                if n == 3:
                    for k in range(XS):
                        sp.dma_start(x_in[:, k], t["x_T"][:, k]).then_inc(x_loaded[k], 16)
            for k in range(XS, KT):
                sp.wait_ge(lo_done, k - XS + 1)
                sp.dma_start(x_in[:, k % XS], t["x_T"][:, k]).then_inc(x_loaded[k % XS], 16)
            sp.wait_ge(gate_ready, 1)
            sp.dma_start(t["gate_d"], gate[:, :]).then_inc(gate_out, 16)
            sp.wait_ge(gate_out, 16)

        @block.tensor
        def _(pe):
            pe.wait_ge(silu_done, 1)
            pe.wait_ge(small_in, 64)

            def turn(n):
                pe.wait_ge(row_put, n + 1)
                for j in range(4):
                    last = pe.transpose(ps_mod[:, (4 * n + j) * NC:(4 * n + j + 1) * NC],
                                        mod_rows[:, n % 2, j * P:(j + 1) * P], ident[0:NC, 0:NC])
                last.then_inc(turned, 1)
            for n in range(6):
                pe.wait_ge(w_in[n % 2], 16 * (n // 2 + 1))
                for k in range(KT):
                    last = pe.matmul(ps_row[0:NC, n, :], sc[:, k, :], w[:, n % 2, k, :],
                                     start=k == 0, stop=k == KT - 1)
                last.then_inc(w_used, 1)
                if 1 <= n <= 3:
                    turn(n - 1)
                if n == 3:
                    turn(3)

        @block.scalar
        def _(act):
            act.wait_ge(small_in, 64)
            act.activation(sc[:, :, :], c_sb[:, :, :], ACT.Silu).then_inc(silu_done, 1)
            for n in range(4):
                act.wait_ge(w_used, n + 1)
                if n >= 2:
                    act.wait_ge(turned, n - 1)
                act.activation(mod_rows[:, n % 2, :], ps_row[0:NC, n, :], ACT.Copy).then_inc(row_put, 1)
            for k in range(KT):
                act.wait_ge(h_step, 3 * k + 3)
                act.activation(h_hi[:, k, :], x_in[:, k % XS, :], ACT.Copy).then_inc(hi_done, 1)

        @block.vector
        def _(dve):
            dve.wait_ge(small_in, 64)
            dve.wait_ge(turned, 4)
            dve.tensor_tensor(mods[:, :, :], ps_mod[:, 0:2 * KT * NC].rearrange("p (f c) -> p f c", c=NC),
                              bc(b_ss[:, :], NC), ALU.add).then_inc(mod_ready, 1)
            dve.wait_ge(mod_ready, 1)
            dve.tensor_scalar(mods[:, KT:, :], mods[:, KT:, :], 1.0, None, ALU.add).then_inc(mod_ready, 1)
            dve.wait_ge(mod_ready, 2)

            def modulated(k):
                x = x_in[:, k % XS, :]
                xs = x[:, SEQ:].rearrange("p (s t) -> p s t", s=NSEQ)
                dve.wait_ge(x_loaded[k % XS], 16 * (k // XS + 1))
                dve.tensor_scalar(x[:, 0:SEQ], x[:, 0:SEQ], mods[:, KT + k, 0:1], mods[:, k, 0:1],
                                  ALU.mult, ALU.add).then_inc(h_step, 1)
                dve.tensor_tensor(xs, xs, bc(mods[:, KT + k, 1:], TS), ALU.mult).then_inc(h_step, 1)
                dve.wait_ge(h_step, 3 * k + 2)
                dve.tensor_tensor(xs, xs, bc(mods[:, k, 1:], TS), ALU.add).then_inc(h_step, 1)
            modulated(0)
            for k in range(KT):
                if k + 1 < KT:
                    modulated(k + 1)
                dve.wait_ge(hi_done, k + 1)
                dve.tensor_tensor(h_lo[:, k, :], x_in[:, k % XS, :], f32(h_hi[:, k, :]), ALU.subtract).then_inc(lo_done, 1)
            dve.wait_ge(w_used, 6)
            dve.tensor_tensor(gate[:, :], ps_row[0:NC, 4:6, :].rearrange("p a n -> p (a n)"), b_gate[:, :],
                              ALU.add).then_inc(gate_ready, 1)


def project_features(nc, t, h_hi, h_lo):
    PAIRS = FT // 2
    seg, at = {}, 0
    for name, n in (("conv", T_CONV), ("q", T_Q), ("k", T_K), ("z", T_ZA + T_ZB), ("g", T_G)):
        seg[name] = (at // 2, (at + n) // 2)
        at += n
    with ExitStack() as ctx:
        sb = lambda name, shape, dt=F32: ctx.enter_context(nc.sbuf_tensor(name, shape, dt))
        sem = t["sem"]
        w_raw = sb("w_raw", [P, 2, KT * P])
        w_hi = sb("w_hi", [P, 2, KT * P], F32R)
        w_lo = sb("w_lo", [P, 2, KT * P], F32R)
        side = sb("side", [P, 2, SIDE])
        stage = sb("stage", [P, 2, U_W + 1])
        conv = sb("conv", [P, 2, NT])
        ps = ctx.enter_context(nc.psum_tensor("ps_proj", [P, len(CHUNKS), 512], F32))
        raw_loaded = [sem(f"raw_loaded{j}") for j in range(2)]
        side_loaded = [sem(f"side_loaded{j}") for j in range(2)]
        hi_done = [sem(f"w_hi_done{j}") for j in range(2)]
        lo_done = [sem(f"w_lo_done{j}") for j in range(2)]
        bank_full = [sem(f"bank_full{c}") for c in range(len(CHUNKS))]
        bank_read = [sem(f"bank_read{c}") for c in range(len(CHUNKS))]
        stored = [sem(f"stored{j}") for j in range(2)]
        conv_stored = [sem(f"conv_stored{j}") for j in range(2)]
        pad_zero, state_put, conv_step, conv_silu = sem("pad_zero"), sem("state_put"), sem("conv_step"), sem("conv_silu")
        STEPS = 2 * TAPS
        block = ctx.enter_context(nc.Block(name="project_features"))
        first = lambda i: isinstance(i, int) and i == 0

        @block.sync
        def _(sp):
            def load(i, j, is_conv):
                if not first(i):
                    sp.wait_ge(lo_done[j], i)
                sp.dma_start(w_raw[:, j, :], t["w_feat"][bass.ds(2 * i + j, 1)].rearrange("a p n -> p (a n)")
                             ).then_inc(raw_loaded[j], 16)
                if is_conv:
                    if not first(i):
                        sp.wait_ge(conv_step, STEPS * (2 * i + j - 1))
                        sp.wait_ge(state_put, 2 * i + j - 1)
                    sp.dma_start(side[:, j, :], t["conv_side"][bass.ds(2 * i + j, 1)].rearrange("a p n -> p (a n)")
                                 ).then_inc(side_loaded[j], 16)
            for j in range(2):
                load(0, j, True)
            with sp.Fori(1, seg["conv"][1]) as i:
                for j in range(2):
                    load(i, j, True)
            with sp.Fori(seg["conv"][1], PAIRS) as i:
                for j in range(2):
                    load(i, j, False)

        @block.tensor
        def _(pe):
            def pair(i):
                for j in range(2):
                    pe.wait_ge(lo_done[j], i + 1)
                    for c, (at, n) in enumerate(CHUNKS):
                        if not (first(i) and j == 0):
                            pe.wait_ge(bank_read[c], 2 * i + j)
                        for k in range(KT):
                            cols = slice(k * P, (k + 1) * P)
                            last = mm3(pe, ps[:, c, 0:n], (w_hi[:, j, cols], w_lo[:, j, cols]),
                                       (h_hi[:, k, at:at + n], h_lo[:, k, at:at + n]), k == 0, k == KT - 1)
                        last.then_inc(bank_full[c], 1)
            pair(0)
            with pe.Fori(1, PAIRS) as i:
                pair(i)

        @block.scalar
        def _(act):
            def split(i, j):
                act.wait_ge(raw_loaded[j], 16 * (i + 1))
                if not first(i):
                    act.wait_ge(bank_full[-1], 2 * i + j - 1)
                act.activation(w_hi[:, j, :], w_raw[:, j, :], ACT.Copy).then_inc(hi_done[j], 1)

            def empty(i, j, func, is_conv):
                if is_conv:
                    act.wait_ge(side_loaded[j], 16 * (i + 1))
                    if not first(i):
                        act.wait_ge(conv_step, STEPS * (2 * i + j - 1))
                        act.wait_ge(stored[j], 16 * i)
                    ext = stage[:, j, U_SAMP:U_W].rearrange("p (s e) -> p s e", e=EXT)
                    act.activation(ext[:, :, 0:U_PRE], side[:, j, TAPS:].rearrange("p (s e) -> p s e", e=U_PRE),
                                   ACT.Copy).then_inc(state_put, 1)
                else:
                    act.wait_ge(stored[j], 16 * i)
                for c, (at, n) in enumerate(CHUNKS):
                    act.wait_ge(bank_full[c], 2 * i + j + 1)
                    if not is_conv:
                        last = act.activation(stage[:, j, at:at + n], ps[:, c, 0:n], func)
                    else:
                        m = min(n, SEQ - at)
                        last = act.activation(stage[:, j, U_PRE + at:U_PRE + at + m], ps[:, c, 0:m], func)
                        if m < n:
                            last = act.activation(ext[:, :, U_PRE:], ps[:, c, m:n].rearrange("p (s e) -> p s e", e=TS), func)
                    last.then_inc(bank_read[c], 1)

            def silu(i, j):
                act.wait_ge(conv_step, STEPS * (2 * i + j + 1))
                act.activation(conv[:, j, :], conv[:, j, :], ACT.Silu).then_inc(conv_silu, 1)

            act.wait_ge(pad_zero, 1)
            lo, hi = seg["conv"]
            split(0, 0), split(0, 1)
            for j in range(2):
                empty(0, j, ACT.Copy, True), split(1, j), silu(0, j)
            with act.Fori(1, hi) as i:
                for j in range(2):
                    empty(i, j, ACT.Copy, True), split(i + 1, j), silu(i, j)
            for name, func in (("q", ACT.Copy), ("k", ACT.Copy), ("z", ACT.Silu)):
                with act.Fori(*seg[name]) as i:
                    for j in range(2):
                        empty(i, j, func, False), split(i + 1, j)
            with act.Fori(seg["g"][0], PAIRS - 1) as i:
                for j in range(2):
                    empty(i, j, ACT.Sigmoid, False), split(i + 1, j)
            for j in range(2):
                empty(PAIRS - 1, j, ACT.Sigmoid, False)

        @block.vector
        def _(dve):
            def split(i, j):
                dve.wait_ge(hi_done[j], i + 1)
                dve.tensor_tensor(w_lo[:, j, :], w_raw[:, j, :], f32(w_hi[:, j, :]), ALU.subtract).then_inc(lo_done[j], 1)

            def convolve(i, j):
                for c in range(len(CHUNKS)):
                    dve.wait_ge(bank_read[c], 2 * i + j + 1)
                dve.wait_ge(state_put, 2 * i + j + 1)
                if not first(i):
                    dve.wait_ge(conv_stored[j], 16 * i)
                ext = stage[:, j, U_SAMP:U_W].rearrange("p (s e) -> p s e", e=EXT)
                out_s = conv[:, j, SEQ:].rearrange("p (s e) -> p s e", e=TS)
                for n in range(TAPS):
                    w = side[:, j, n:n + 1]
                    if n == 0:
                        dve.tensor_scalar(conv[:, j, 0:SEQ], stage[:, j, 0:SEQ], w, None, ALU.mult).then_inc(conv_step, 1)
                        dve.tensor_scalar(out_s, ext[:, :, 0:TS], w, None, ALU.mult).then_inc(conv_step, 1)
                        continue
                    dve.wait_ge(conv_step, STEPS * (2 * i + j) + 2 * n - 1)
                    dve.scalar_tensor_tensor(out=conv[:, j, 0:SEQ], in0=stage[:, j, n:n + SEQ], scalar=w,
                                             in1=conv[:, j, 0:SEQ], op0=ALU.mult, op1=ALU.add).then_inc(conv_step, 1)
                    dve.wait_ge(conv_step, STEPS * (2 * i + j) + 2 * n)
                    dve.scalar_tensor_tensor(out=out_s, in0=ext[:, :, n:n + TS], scalar=w, in1=out_s,
                                             op0=ALU.mult, op1=ALU.add).then_inc(conv_step, 1)
            for j in range(2):
                split(0, j)
            for j in range(2):
                split(1, j), convolve(0, j)
            with dve.Fori(1, seg["conv"][1]) as i:
                for j in range(2):
                    split(i + 1, j), convolve(i, j)
            with dve.Fori(seg["conv"][1] + 1, PAIRS) as i:
                for j in range(2):
                    split(i, j)

        @block.gpsimd
        def _(pool):
            pool.memset(stage[:, :, 0:U_PRE], 0.0).then_inc(pad_zero, 1)

            def store(dst, i, j, base):
                for c in range(len(CHUNKS)):
                    pool.wait_ge(bank_read[c], 2 * i + j + 1)
                pool.dma_start(dst[bass.ds(2 * i + j - 2 * base, 1)].rearrange("a p n -> p (a n)"),
                               stage[:, j, 0:NT]).then_inc(stored[j], 16)

            def store_conv(i, j):
                for c in range(len(CHUNKS)):
                    pool.wait_ge(bank_read[c], 2 * i + j + 1)
                pool.dma_start(t["conv_tail"][bass.ds(2 * i + j, 1)].rearrange("a p n -> p (a n)"),
                               stage[:, j, U_SAMP - U_PRE:U_W]).then_inc(stored[j], 16)
                pool.wait_ge(conv_silu, 2 * i + j + 1)
                pool.dma_start(t["conv_d"][bass.ds(2 * i + j, 1)].rearrange("a p n -> p (a n)"),
                               conv[:, j, :]).then_inc(conv_stored[j], 16)
            with pool.Fori(*seg["conv"]) as i:
                for j in range(2):
                    store_conv(i, j)
            for name, dst in (("q", "q_d"), ("k", "k_T"), ("z", "z_d"), ("g", "g_d")):
                with pool.Fori(*seg[name]) as i:
                    for j in range(2):
                        store(t[dst], i, j, seg[name][0])
            for j in range(2):
                pool.wait_ge(stored[j], 16 * PAIRS)
                pool.wait_ge(conv_stored[j], 16 * seg["conv"][1])


def project_values(nc, t, h_hi, h_lo, ab):
    NB = NBLK + 1
    with ExitStack() as ctx:
        sb = lambda name, shape, dt=F32: ctx.enter_context(nc.sbuf_tensor(name, shape, dt))
        sem = t["sem"]
        wv_raw = sb("wv_raw", [P, KT, VW])
        wv_hi = sb("wv_hi", [P, KT, VW], F32R)
        wv_lo = sb("wv_lo", [P, KT, VW], F32R)
        x_hi = sb("tok_hi", [P, 2, KT, P], F32R)
        x_lo = sb("tok_lo", [P, 2, KT, P], F32R)
        v_out = sb("v_out", [P, 2, GW])
        ps = ctx.enter_context(nc.psum_tensor("ps_val", [P, 2, 512], F32))
        w_loaded, w_hi_done, w_lo_done = sem("wv_loaded"), sem("wv_hi_done"), sem("wv_lo_done")
        hi_put = [sem(f"tok_hi_put{j}") for j in range(2)]
        lo_put = [sem(f"tok_lo_put{j}") for j in range(2)]
        full = [sem(f"val_full{j}") for j in range(2)]
        read = [sem(f"val_read{j}") for j in range(2)]
        ab_read = [sem(f"ab_read{j}") for j in range(2)]
        stored = [sem(f"val_stored{j}") for j in range(2)]
        block = ctx.enter_context(nc.Block(name="project_values"))
        PASS = NBLK // 4
        base = lambda g, j: g * (NBLK // 2) + (g if j == 0 else 0)
        use = lambda g, i, j: base(g, j % 2) + 2 * i + j // 2

        def view(x, g, i, j):
            a, b, s = BLOCKS[g]
            if s == 1:
                return x[:, :, bass.ds(a * i + b * j, P)]
            if s == 4:
                return x[:, :, 512 * j:512 * (j + 1)].rearrange("p k (m s) -> p k m s", s=4)[:, :, :, bass.ds(i, 1)]
            return x[:, :, 0:SEQ].rearrange("p k (m s) -> p k m s", s=16)[:, :, :, bass.ds(4 * i + j, 1)]

        def rounds(eng, g, body):
            if g == 0:
                body(0)
            with eng.Fori(1 if g == 0 else 0, PASS) as i:
                body(i)
        zero = lambda u: isinstance(u, int) and u == 0

        @block.sync
        def _(sp):
            for g in range(NG):
                if g:
                    sp.wait_ge(w_lo_done, g)
                sp.dma_start(wv_raw[:, :, :], t["w_val"][g]).then_inc(w_loaded, 16)

        @block.tensor
        def _(pe):
            def tile(g, u, s, n):
                pe.wait_ge(hi_put[s], u + 1)
                pe.wait_ge(lo_put[s], u + 1)
                if not (isinstance(u, int) and u == 0):
                    pe.wait_ge(read[s], u)
                for k in range(KT):
                    last = mm3(pe, ps[:, s, 0:n], (x_hi[:, s, k, :], x_lo[:, s, k, :]),
                               (wv_hi[:, k, 0:n], wv_lo[:, k, 0:n]), k == 0, k == KT - 1)
                last.then_inc(full[s], 1)
            for g in range(NG):
                pe.wait_ge(w_lo_done, g + 1)
                n = VW if g == 0 else GW

                def four(i):
                    for j in range(4):
                        tile(g, use(g, i, j), j % 2, n)
                rounds(pe, g, four)
                tile(g, use(g, PASS, 0), 0, n)

        def put(eng, copy, dst, src, done):
            for g in range(NG):
                def four(i):
                    for j in range(4):
                        s, u = j % 2, use(g, i, j)
                        if not zero(u):
                            eng.wait_ge(full[s], u)
                        v = view(src, g, i, j)
                        o = dst[:, s] if len(v.shape) == 3 else dst[:, s].unsqueeze(3)
                        copy(o, f32(v)).then_inc(done[s], 1)
                rounds(eng, g, four)
                eng.wait_ge(full[0], use(g, PASS, 0))
                copy(dst[:, 0, :, 0:SAMP], f32(src[:, :, SEQ:])).then_inc(done[0], 1)
                yield g

        @block.scalar
        def _(act):
            def split(g):
                act.wait_ge(w_loaded, 16 * (g + 1))
                if g:
                    act.wait_ge(full[0], base(g, 0))
                    act.wait_ge(full[1], base(g, 1))
                act.activation(wv_hi[:, :, :], wv_raw[:, :, :], ACT.Copy).then_inc(w_hi_done, 1)
            split(0)
            for g in put(act, lambda o, i: act.activation(o, i, ACT.Copy), x_hi, h_hi, hi_put):
                if g + 1 < NG:
                    split(g + 1)

        @block.vector
        def _(dve):
            def split(g):
                dve.wait_ge(w_hi_done, g + 1)
                dve.tensor_tensor(wv_lo[:, :, :], wv_raw[:, :, :], f32(wv_hi[:, :, :]), ALU.subtract).then_inc(w_lo_done, 1)

            def empty(g, u, s, b, samples=False):
                dve.wait_ge(full[s], u + 1)
                rows = SAMP if samples else P
                if not (isinstance(u, int) and u == 0):
                    dve.wait_ge(stored[s], 16 * u)
                if g == 0:
                    dve.tensor_copy(ab[0:rows, bass.ds(b, 1), :], ps[0:rows, s, GW:VW].unsqueeze(1)).then_inc(ab_read[s], 1)
                dve.tensor_copy(v_out[0:rows, s, :], ps[0:rows, s, 0:GW]).then_inc(read[s], 1)

            def put_one(g, i, j):
                s, u = j % 2, use(g, i, j)
                if not zero(u):
                    dve.wait_ge(full[s], u)
                v = view(h_lo, g, i, j)
                o = x_lo[:, s] if len(v.shape) == 3 else x_lo[:, s].unsqueeze(3)
                dve.tensor_copy(o, f32(v)).then_inc(lo_put[s], 1)

            for g in range(NG):
                split(g)

                def four(i):
                    for j in range(4):
                        put_one(g, i, j)
                        if j:
                            empty(g, use(g, i, j - 1), (j - 1) % 2, 4 * i + j - 1)
                    empty(g, use(g, i, 3), 1, 4 * i + 3)
                rounds(dve, g, four)
                dve.wait_ge(full[0], use(g, PASS, 0))
                dve.tensor_copy(x_lo[:, 0, :, 0:SAMP], f32(h_lo[:, :, SEQ:])).then_inc(lo_put[0], 1)
                empty(g, use(g, PASS, 0), 0, NBLK, samples=True)

        @block.gpsimd
        def _(pool):
            for g in range(NG):
                with pool.Fori(0, PASS) as i:
                    for j in range(4):
                        pool.wait_ge(read[j % 2], use(g, i, j) + 1)
                        pool.dma_start(t["v_out"][g, bass.ds(4 * i + j, 1)].rearrange("a p n -> p (a n)"),
                                       v_out[:, j % 2, :]).then_inc(stored[j % 2], 16)
                pool.wait_ge(read[0], use(g, PASS, 0) + 1)
                pool.dma_start(t["v_new"][g], v_out[0:SAMP, 0, :]).then_inc(stored[0], 16)
            for j in range(2):
                pool.wait_ge(stored[j], 16 * base(NG, j))


NSTAT = 2 * HPG
PAIR = 2 * DH
NP_ = HPG // 2
NPT = NG * NP_
MASKED = -1.0e30


def attend_prompt(nc, t):
    with ExitStack() as ctx:
        sb = lambda name, shape, dt=F32: ctx.enter_context(nc.sbuf_tensor(name, shape, dt))
        pb = lambda name, shape: ctx.enter_context(nc.psum_tensor(name, shape, F32))
        sem = t["sem"]
        q_sb = sb("q_sb", [P, NG, NP_, SEQ])
        k_sb = sb("k_sb", [P, NG, NP_, SEQ])
        v_sb = sb("v_sb", [P, NG, NBLK, GW])
        bias = sb("bias_p", [P, NG, HPG, 2 * P])
        ident = sb("ident_a", [P, P])
        q_bd = sb("q_bd", [P, 2, NP_, 2, P])
        scores = sb("scores", [P, NP_, 2, 2 * P])
        probs = sb("probs", [P, 2, NP_, 2, 2 * P])
        probs_T = sb("probs_T", [P, NP_, 4, P])
        top = sb("top", [P, HPG])
        neg = sb("neg", [P, HPG])
        turnstile = sb("turnstile", [P, NP_])
        rows = sb("rows", [P, NBLK, GW])
        stats = sb("stats", [P, NG, NBLK, NSTAT])
        ps_s = [pb(f"ps_s{p}", [P, 2, 2 * P]) for p in range(NP_)]
        ps_t = [pb(f"ps_t{p}", [P, 4, P]) for p in range(NP_)]
        ps_o = pb("ps_o", [P, HPG, DH])
        const_in, zeroed = sem("const_in"), sem("q_zeroed")
        qk_in = [sem(f"qk_in{g}") for g in range(NG)]
        v_in = [sem(f"v_in{g}") for g in range(NG)]
        stat_put = sem("stat_put")
        q_put, neg_put, o_full, o_read = sem("q_put"), sem("neg_put"), sem("o_full"), sem("o_read")
        s_full = [sem(f"s_full{p}") for p in range(NP_)]
        s_read = [sem(f"s_read{p}") for p in range(NP_)]
        exp_done = [sem(f"exp_done{p}") for p in range(NP_)]
        t_full = [sem(f"t_full{p}") for p in range(NP_)]
        t_read = [sem(f"t_read{p}") for p in range(NP_)]
        row_stored = [sem(f"row_stored{g}") for g in range(NG)]
        stats_stored = sem("stats_stored")
        block = ctx.enter_context(nc.Block(name="attend_prompt"))

        class Unit:

            def __init__(self, g, i, j):
                self.g, self.i, self.j = g, i, j
                self.b = 4 * i + j
                self.u = g * NBLK + self.b
                self.slot = j % 2
                self.kb = 1 if g == 2 or (g == 1 and j == 0) or not self.after(1) else 2

            def after(self, n):
                return not (isinstance(self.u, int) and self.u < n)

            def tokens(self, x, back):
                if self.g == 0:
                    return x[..., bass.ds(P * (self.b - back), P * (1 + back))]
                if self.g == 1:
                    part = x[..., 512 * (self.j - back):512 * (self.j + 1)]
                    return part.rearrange(self.pat(x, 4), s=4)[..., bass.ds(self.i, 1)]
                return x.rearrange(self.pat(x, 16), s=16)[..., bass.ds(self.b, 1)]

            def pat(self, x, s):
                lead = " ".join("abcd"[:len(x.shape) - 1])
                return f"{lead} (m s) -> {lead} m s"

        def schedule(eng, step, enter=lambda g: None):
            def at(g, k):
                if k < 0:
                    return at(g - 1, k + NBLK) if g else None
                if k >= NBLK:
                    return at(g + 1, k - NBLK) if g + 1 < NG else None
                return Unit(g, k // 4, k % 4)
            step(at(0, 0), None, None)
            step(at(0, 1), at(0, 0), None)
            for g in range(NG):
                enter(g)
                straight = 4 if g == 0 else 0
                for k in range(1, straight + 1):
                    step(at(g, k + 1), at(g, k), at(g, k - 1))
                with eng.Fori(straight // 4, 3) as i:
                    line = [Unit(g, i, j) for j in range(4)] + [Unit(g, i + 1, j) for j in range(2)]
                    for k in range(1, 5):
                        step(line[k + 1], line[k], line[k - 1])
                for k in range(NBLK - 3, NBLK + 1):
                    step(at(g, k + 1), at(g, k), at(g, k - 1))

        def in_order(eng, do, enter=lambda g: None):
            for g in range(NG):
                enter(g)
                if g == 0:
                    for j in range(4):
                        do(Unit(0, 0, j))
                with eng.Fori(1 if g == 0 else 0, 4) as i:
                    for j in range(4):
                        do(Unit(g, i, j))

        @block.sync
        def _(sp):
            for g in range(NG):
                sp.dma_start(q_sb[:, g], t["q_d"][2 * g:2 * g + 2, :, 0:SEQ].rearrange("a p n -> p a n")).then_inc(qk_in[g], 16)
                sp.dma_start(k_sb[:, g], t["k_T"][2 * g:2 * g + 2, :, 0:SEQ].rearrange("a p n -> p a n")).then_inc(qk_in[g], 16)
                if g == 0:
                    sp.dma_start(bias[:, :, :, :], t["bias_prompt"]).then_inc(const_in, 16)
                    sp.dma_start(ident[:, :], t["ident"]).then_inc(const_in, 16)
                sp.dma_start(v_sb[:, g], t["v_out"][g, 0:NBLK].rearrange("b p n -> p b n")).then_inc(v_in[g], 16)

            def store(x):
                sp.wait_ge(o_read, x.u + 1)
                att = t["att_d"][:, x.g, :]
                if x.g == 0:
                    dst = att[bass.ds(P * x.b, P)]
                elif x.g == 1:
                    dst = att[512 * x.j:512 * (x.j + 1)].rearrange("(m s) n -> m s n", s=4)[:, bass.ds(x.i, 1)]
                else:
                    dst = att.rearrange("(m s) n -> m s n", s=16)[:, bass.ds(x.b, 1)]
                src = rows[:, bass.ds(x.b, 1), :]
                sp.dma_start(dst, src if x.g else src.rearrange("p a n -> p (a n)")).then_inc(row_stored[x.g], 16)
            in_order(sp, store)
            sp.wait_ge(stat_put, NG * NBLK)
            for p in range(NP_):
                sp.wait_ge(exp_done[p], 2 * NG * NBLK)
            for g, (_, s) in enumerate(GROUPS):
                st = t["stats_d"][:, g, :]
                if g == 0:
                    pairs = [(st.rearrange("(b p) n -> p b n", p=P), stats[:, g])]
                elif g == 1:
                    pairs = [(st[512 * j:512 * (j + 1)].rearrange("(m s) n -> m s n", s=s), stats[:, g, j::4]) for j in range(4)]
                else:
                    pairs = [(st.rearrange("(m s) n -> m s n", s=s), stats[:, g])]
                for dst, src in pairs:
                    sp.dma_start(dst, src).then_inc(stats_stored, 16)
            sp.wait_ge(stats_stored, 16 * 6)
            for g in range(NG):
                sp.wait_ge(row_stored[g], 16 * NBLK)

        @block.gpsimd
        def _(pool):
            pool.memset(q_bd[:, :, :, :, :], 0.0).then_inc(zeroed, 1)
            pool.wait_ge(zeroed, 1)

            def put(x):
                if x.after(2):
                    for p in range(NP_):
                        pool.wait_ge(s_full[p], x.u - 1)
                for h in range(2):
                    half = slice(DH * h, DH * (h + 1))
                    src = x.tokens(q_sb[half, x.g], 0)
                    dst = q_bd[half, x.slot, :, h, :]
                    pool.tensor_copy(dst if x.g == 0 else dst.unsqueeze(3), src).then_inc(q_put, 1)
            in_order(pool, put, lambda g: pool.wait_ge(qk_in[g], 32))

        @block.tensor
        def _(pe):
            pe.wait_ge(const_in, 32)

            def score(x):
                pe.wait_ge(q_put, 2 * (x.u + 1))
                for p in range(NP_):
                    if x.after(1):
                        pe.wait_ge(s_read[p], 2 * x.u)
                    k = x.tokens(k_sb[:, x.g, p], x.kb - 1)
                    for h in range(2):
                        out = ps_s[p][:, h, 0:P * x.kb]
                        last = pe.matmul(out if x.g == 0 else out.unsqueeze(2), q_bd[:, x.slot, p, h, :], k, start=True, stop=True)
                    last.then_inc(s_full[p], 1)

            def transpose(x):
                for p in range(NP_):
                    pe.wait_ge(exp_done[p], 2 * (x.u + 1))
                    if x.after(1):
                        pe.wait_ge(t_read[p], x.u)
                    for h in range(2):
                        for b in range(x.kb):
                            last = pe.transpose(ps_t[p][:, 2 * h + b, :], probs[:, x.slot, p, h, b * P:(b + 1) * P], ident[:, :])
                    last.then_inc(t_full[p], 1)

            def weigh(x):
                if x.after(1):
                    pe.wait_ge(o_read, x.u)
                for p in range(NP_):
                    pe.wait_ge(t_read[p], x.u + 1)
                    for h in range(2):
                        head = 2 * p + h
                        for b in range(x.kb):
                            v = v_sb[:, x.g, bass.ds(x.b - (x.kb - 1) + b, 1), DH * head:DH * (head + 1)]
                            last = pe.matmul(ps_o[:, head, :].unsqueeze(1), probs_T[:, p, 2 * h + b, :], v,
                                             start=b == 0, stop=b == x.kb - 1)
                last.then_inc(o_full, 1)

            def step(nxt, now, prev):
                if nxt:
                    score(nxt)
                if prev:
                    weigh(prev)
                if now:
                    transpose(now)
            schedule(pe, step, lambda g: pe.wait_ge(v_in[g], 16))

        def turn(eng, copy, p, x):
            eng.wait_ge(t_full[p], x.u + 1)
            if x.after(1):
                eng.wait_ge(o_full, x.u)
            src, dst = ps_t[p][:, :, :], probs_T[:, p, :, :]
            if x.kb == 1:
                src, dst = ps_t[p][:, 0:4:2, :], probs_T[:, p, 0:4:2, :]
            copy(dst, src).then_inc(t_read[p], 1)

        @block.vector
        def _(dve):
            dve.wait_ge(const_in, 32)

            def maxima(x):
                for p in range(NP_):
                    dve.wait_ge(s_full[p], x.u + 1)
                    if x.after(1):
                        dve.wait_ge(exp_done[p], 2 * x.u)
                        dve.wait_ge(stat_put, x.u)
                    dve.memset(turnstile[:, p:p + 1], 0.0)
                    for h in range(2):
                        head = 2 * p + h
                        off = 2 * P - P * x.kb
                        dve.tensor_tensor_reduce(out=scores[:, p, h, 0:P * x.kb], in0=ps_s[p][:, h, 0:P * x.kb],
                                                 in1=bias[:, x.g, head, off:], scale=DH ** -0.5, scalar=-3.0e38, op0=ALU.add,
                                                 op1=ALU.max, accum_out=top[:, head:head + 1]).then_inc(s_read[p], 1)
                for p in range(NP_):
                    dve.wait_ge(s_read[p], 2 * (x.u + 1))
                dve.tensor_scalar(neg[:, :], top[:, :], -1.0, None, ALU.mult).then_inc(neg_put, 1)
                dve.tensor_scalar(stats[:, x.g, bass.ds(x.b, 1), 0:HPG], top[:, :].unsqueeze(1), -1.0, None,
                                  ALU.mult).then_inc(stat_put, 1)

            def results(x):
                dve.wait_ge(o_full, x.u + 1)
                dve.tensor_copy(rows[:, bass.ds(x.b, 1), 0:GW], ps_o[:, :, :].rearrange("p h d -> p (h d)").unsqueeze(1)
                                ).then_inc(o_read, 1)

            def step(nxt, now, prev):
                if prev:
                    turn(dve, lambda o, i: dve.tensor_copy(o, i), 0, prev)
                if nxt:
                    maxima(nxt)
                if prev:
                    results(prev)

            def enter(g):
                if g:
                    dve.wait_ge(row_stored[g - 1], 16 * NBLK)
            schedule(dve, step, enter)

        @block.scalar
        def _(act):
            def exps(x):
                act.wait_ge(neg_put, x.u + 1)
                for p in range(NP_):
                    if x.after(2):
                        act.wait_ge(t_full[p], x.u - 1)
                    for h in range(2):
                        head = 2 * p + h
                        act.activation(probs[:, x.slot, p, h, 0:P * x.kb], scores[:, p, h, 0:P * x.kb], ACT.Exp,
                                       bias=neg[:, head:head + 1],
                                       accum_out=stats[:, x.g, bass.ds(x.b, 1), HPG + head]).then_inc(exp_done[p], 1)

            def step(nxt, now, prev):
                if prev:
                    turn(act, lambda o, i: act.activation(o, i, ACT.Copy), 1, prev)
                if nxt:
                    exps(nxt)
            schedule(act, step)


CACHED = sum(KEPT)
KT_C = CACHED // P
HALF = NSEQ // 2
QR = HPG * TS
NEWC = NG * SAMP
BANKS = [P + NEWC, KEPT[1]] + [512] * (KEPT[2] // 512)
KEYS = sum(BANKS)


def attend_samples(nc, t):
    with ExitStack() as ctx:
        sb = lambda name, shape, dt=F32: ctx.enter_context(nc.sbuf_tensor(name, shape, dt))
        pb = lambda name, shape: ctx.enter_context(nc.psum_tensor(name, shape, F32))
        sem = t["sem"]
        kc = sb("kc", [P, NSEQ, NP_, CACHED])
        vc = sb("vc", [P, NSEQ, KT_C, GW])
        q_in = sb("q_s", [P, NPT, SAMP])
        k_new = sb("k_new", [P, NPT, SAMP])
        v_new = sb("v_new", [SAMP, NG, GW])
        bias = sb("bias_s", [P, 2, KEYS])
        ident = sb("ident_s", [P, P])
        q_bd = sb("q_bd_s", [P, NPT, NSEQ, HPG, TS])
        probs = sb("probs_s", [P, KEYS])
        probs_T = sb("probs_T_s", [P, KT_C, P])
        new_T = sb("new_T_s", [SAMP, NG, P])
        top = sb("top_s", [P, len(BANKS)])
        neg = sb("neg_s", [P, 1])
        den = sb("den_s", [P, 1])
        rden = sb("rden_s", [P, 1])
        att = sb("att_s", [P, NPT, SAMP])
        ps_s = [pb(f"ps_ss{b}", [P, 512]) for b in range(len(BANKS))]
        ps_t = [pb(f"ps_st{b}", [P, 4, P]) for b in range(2)]
        ps_o = pb("ps_so", [P, 2 * 512])
        o_rows = sb("o_rows_s", [P, WA])
        small_in, zeroed, q_put = sem("small_in_s"), sem("zeroed_s"), sem("q_put_s")
        k_in = [sem(f"kc_in{r}") for r in range(NSEQ)]
        v_in = [sem(f"vc_in{r}") for r in range(NSEQ)]
        scored, attended, maxed, softened = sem("scored"), sem("attended"), sem("maxed"), sem("softened")
        chain, neg_done, o_put, o_turned = sem("chain_s"), sem("neg_done_s"), sem("o_put_s"), sem("o_turned_s")
        exped, t_full, t_read, att_put, att_out = sem("exped"), sem("t_full_s"), sem("t_read_s"), sem("att_put"), sem("att_out")
        block = ctx.enter_context(nc.Block(name="attend_samples"))
        ROUNDS = [list(range(r, min(r + 4, KT_C))) for r in range(0, KT_C, 4)] + ["new"]
        col = [0] + [P + NEWC + P * n for n in range(KT_C - 1)]
        tile0 = [0, KEPT[0] // P, (KEPT[0] + KEPT[1]) // P, KT_C]

        @block.sync
        def _(sp):
            sp.dma_start(q_in[:, :, :], t["q_d"][:, :, SEQ:].rearrange("a p n -> p a n")).then_inc(small_in, 16)
            sp.dma_start(k_new[:, :, :], t["k_T"][:, :, SEQ:].rearrange("a p n -> p a n")).then_inc(small_in, 16)
            sp.dma_start(v_new[:, :, :], t["v_new"].rearrange("g p n -> p g n")).then_inc(small_in, 16)
            sp.dma_start(bias[:, :, :], t["bias_samples"]).then_inc(small_in, 16)
            sp.dma_start(ident[:, :], t["ident"]).then_inc(small_in, 16)
            for s in range(NSEQ):
                sp.dma_start(kc[:, s], t["k_cache"][s]).then_inc(k_in[s], 16)
            for s in range(NSEQ):
                sp.dma_start(vc[:, s], t["v_cache"][s]).then_inc(v_in[s], 16)
            sp.wait_ge(att_put, 8)
            sp.dma_start(t["att_s"], att[:, :, :]).then_inc(att_out, 16)
            sp.wait_ge(att_out, 16)

        @block.gpsimd
        def _(pool):
            pool.memset(q_bd[:, :, :, :, :], 0.0).then_inc(zeroed, 1)
            pool.wait_ge(zeroed, 1)
            pool.wait_ge(small_in, 80)
            for p in range(NP_):
                for h in range(2):
                    half = slice(DH * h, DH * (h + 1))
                    for g in range(NG):
                        pool.tensor_scalar(q_bd[half, NP_ * g + p, :, 2 * p + h, :],
                                           q_in[half, NP_ * g + p, :].rearrange("p (s e) -> p s e", e=TS),
                                           DH ** -0.5, None, ALU.mult).then_inc(q_put, 1)

        @block.tensor
        def _(pe):
            pe.wait_ge(q_put, 4 * NG)

            def score(s):
                pe.wait_ge(k_in[s], 16)
                out = slice(QR * (s % HALF), QR * (s % HALF + 1))

                def add(dst, g, keys):
                    for p in range(NP_):
                        last = pe.matmul(dst, q_bd[:, NP_ * g + p, s].rearrange("p h e -> p (h e)"), keys(p),
                                         start=p == 0, stop=p == NP_ - 1, tile_position=(0, QR * (s % HALF)))
                    return last
                add(ps_s[0][out, 0:P], 0, lambda p: kc[:, s, p, 0:P])
                for g in range(NG):
                    add(ps_s[0][out, P + SAMP * g:P + SAMP * (g + 1)], g, lambda p: k_new[:, NP_ * g + p, :])
                at = P
                for n in range(1, len(BANKS)):
                    last = add(ps_s[n][out, :], min(n, 2), lambda p: kc[:, s, p, at:at + 512])
                    at += 512
                last.then_inc(scored, 1)

            def turn(a):
                pe.wait_ge(softened, a + 1)
                if a:
                    pe.wait_ge(att_put, 4)
                for r, tiles in enumerate(ROUNDS):
                    u = len(ROUNDS) * a + r
                    if u >= 2:
                        pe.wait_ge(t_read, u - 1)
                    if tiles == "new":
                        for g in range(NG):
                            last = pe.transpose(ps_t[u % 2][0:SAMP, g, :], probs[:, P + SAMP * g:P + SAMP * (g + 1)], ident[:, :])
                    else:
                        for n, k in enumerate(tiles):
                            last = pe.transpose(ps_t[u % 2][:, n, :], probs[:, col[k]:col[k] + P], ident[:, :])
                    last.then_inc(t_full, 1)

            def weigh(s):
                pe.wait_ge(v_in[s], 16)
                pe.wait_ge(t_read, len(ROUNDS) * (s // HALF + 1))
                rows = slice(QR * (s % HALF), QR * (s % HALF + 1))
                here = (0, QR * (s % HALF))
                for g in range(NG):
                    dst = ps_o[rows, GW * g:GW * (g + 1)]
                    for k in range(tile0[g], tile0[g + 1]):
                        pe.matmul(dst, probs_T[:, k, rows], vc[:, s, k, :], start=k == tile0[g], stop=False, tile_position=here)
                    last = pe.matmul(dst, new_T[:, g, rows], v_new[:, g, :], start=False, stop=True, tile_position=here)
                last.then_inc(attended, 1)

            def turn_back(a):
                pe.wait_ge(o_put, a + 1)
                for p in range(NP_):
                    for g in range(NG):
                        at = GW * g + PAIR * p
                        last = pe.transpose(ps_t[p][:, g, :], o_rows[:, at:at + PAIR], ident[:, :])
                last.then_inc(o_turned, 1)
            for s in range(HALF):
                score(s)
            pe.wait_ge(maxed, 1)
            for s in range(HALF, NSEQ):
                score(s)
            for a in range(2):
                turn(a)
                for s in range(HALF):
                    weigh(HALF * a + s)
                turn_back(a)

        @block.vector
        def _(dve):
            n = [0]

            def link(ins):
                n[0] += 1
                ins.then_inc(chain, 1)
                dve.wait_ge(chain, n[0])

            def soften(a):
                dve.wait_ge(small_in, 80)
                dve.wait_ge(scored, HALF * (a + 1))
                if a:
                    dve.wait_ge(t_full, len(ROUNDS))
                at = 0
                for b, w in enumerate(BANKS):
                    ins = dve.tensor_tensor_reduce(out=probs[:, at:at + w], in0=ps_s[b][:, 0:w], in1=bias[:, a, at:at + w],
                                                   scale=1.0, scalar=-3.0e38, op0=ALU.add, op1=ALU.max,
                                                   accum_out=top[:, b:b + 1])
                    at += w
                    if b < len(BANKS) - 1:
                        link(ins)
                ins.then_inc(maxed, 1)
                dve.wait_ge(maxed, a + 1)
                dve.tensor_reduce(neg[:, :], top[:, :], AX.X, ALU.max, negate=True).then_inc(neg_done, 1)
                dve.wait_ge(exped, a + 1)
                link(dve.reciprocal(rden[:, :], den[:, :]))
                dve.tensor_scalar(probs[:, :], probs[:, :], rden[:, :], None, ALU.mult).then_inc(softened, 1)

            def turned(a):
                for r, tiles in enumerate(ROUNDS):
                    dve.wait_ge(t_full, len(ROUNDS) * a + r + 1)
                    if a and r == 0:
                        dve.wait_ge(attended, HALF)
                    src = ps_t[(len(ROUNDS) * a + r) % 2]
                    if tiles == "new":
                        ins = dve.tensor_copy(new_T[:, :, :], src[0:SAMP, 0:NG, :])
                    else:
                        ins = dve.tensor_copy(probs_T[:, tiles[0]:tiles[-1] + 1, :], src[:, 0:len(tiles), :])
                    ins.then_inc(t_read, 1)

            def outputs(a):
                dve.wait_ge(attended, HALF * (a + 1))
                if a:
                    dve.wait_ge(o_turned, 1)
                dve.tensor_copy(o_rows[:, 0:2 * GW], ps_o[:, 0:2 * GW])
                dve.tensor_copy(o_rows[:, 2 * GW:], ps_o[:, 2 * GW:NG * GW]).then_inc(o_put, 1)
                dve.wait_ge(o_turned, a + 1)
                for p in range(NP_):
                    for h in range(2):
                        half = slice(DH * h, DH * (h + 1))
                        dst = att[half, :, SAMP // 2 * a:SAMP // 2 * (a + 1)].rearrange("p (g q) (s e) -> p g q s e", q=NP_, e=TS)
                        src = ps_t[p][half, 0:NG, :].rearrange("p g (s h e) -> p g s h e", s=HALF, e=TS)
                        dve.tensor_copy(dst[:, :, p], src[:, :, :, 2 * p + h, :]).then_inc(att_put, 1)
            soften(0), turned(0)
            soften(1), outputs(0)
            turned(1), outputs(1)

        @block.scalar
        def _(act):
            for a in range(2):
                act.wait_ge(neg_done, a + 1)
                if a:
                    act.wait_ge(softened, 1)
                act.activation(probs[:, :], probs[:, :], ACT.Exp, bias=neg[:, :], accum_out=den[:, :]).then_inc(exped, 1)


COEF = ("beta", "neg_beta_eG", "eG", "decay_k", "decay_S", "G", "g")
NCO = len(COEF)
LEVELS = [2 ** n for n in range(1, 7)]
BIG = 1.0e30


class Steps:

    def __init__(self, sem, names):
        self.sem, self.names, self.n = sem, names, 0

    def done(self, ins, name):
        assert self.names[self.n % len(self.names)] == name, (name, self.names[self.n % len(self.names)])
        self.n += 1
        ins.then_inc(self.sem, 1)

    def wait(self, eng, name, i=0):
        eng.wait_ge(self.sem, len(self.names) * i + self.names.index(name) + 1)

    def wait_back(self, eng, name, i):
        if not (isinstance(i, int) and i < 2):
            eng.wait_ge(self.sem, len(self.names) * i + self.names.index(name) + 1 - 2 * len(self.names))

    def wait_last(self, eng, name, i):
        if not (isinstance(i, int) and i == 0):
            eng.wait_ge(self.sem, len(self.names) * i + self.names.index(name) + 1 - len(self.names))


def lower(x, b):
    return halves(x, b)[..., 0, :]


def upper(x, b):
    return halves(x, b)[..., 1, :]


def halves(x, b):
    lead = "p" if len(x.shape) == 2 else "p h"
    return x.rearrange(f"{lead} (n two b) -> {lead} n two b", two=2, b=b)


def runs(x, b):
    return x.rearrange("p (n b) -> p n b", b=b)


def heads(x):
    return x.unsqueeze(1).broadcast_to([x.shape[0], NHB] + list(x.shape[1:]))


def decay_coefficients(nc, t, ab, coef):
    NB = NBLK + 1
    with ExitStack() as ctx:
        sb = lambda name, shape, dt=F32: ctx.enter_context(nc.sbuf_tensor(name, shape, dt))
        sem = t["sem"]
        dt_b = sb("dt_b", [P, NHB])
        a_log = sb("a_log", [P, NHB])
        tri = sb("tri_incl", [P, 2, P])
        same = sb("same", [P, 2, P])
        x = sb("gx", [P, NB, NHB])
        y = sb("gy", [P, NB, NHB])
        ps = ctx.enter_context(nc.psum_tensor("ps_G", [P, 2, 512], F32))
        loaded, v, a, summed = sem("g_loaded"), sem("g_dve"), sem("g_act"), sem("g_summed")
        block = ctx.enter_context(nc.Block(name="decay_coefficients"))
        c = {n: coef[:, :, k, :] for k, n in enumerate(COEF)}
        over = lambda s: s.unsqueeze(1).broadcast_to([P, NB, NHB])

        @block.sync
        def _(sp):
            sp.dma_start(dt_b[:, :], t["dt_bias"].partition_broadcast(P)).then_inc(loaded, 16)
            sp.dma_start(a_log[:, :], t["a_log"].partition_broadcast(P)).then_inc(loaded, 16)
            sp.dma_start(tri[:, :, :], t["tri_incl"]).then_inc(loaded, 16)
            sp.dma_start(same[:, :, :], t["same"]).then_inc(loaded, 16)

        @block.vector
        def _(dve):
            n = [0]

            def link(ins):
                n[0] += 1
                ins.then_inc(v, 1)
                dve.wait_ge(v, n[0])
            dve.wait_ge(loaded, 64)
            link(dve.tensor_tensor(x[:, :, :], ab[:, :, 0:NHB], over(dt_b[:, :]), ALU.add))
            link(dve.scalar_tensor_tensor(out=y[:, :, :], in0=x[:, :, :], scalar=-1.0, in1=x[:, :, :],
                                          op0=ALU.mult, op1=ALU.min))
            link(dve.tensor_scalar(x[:, :, :], x[:, :, :], 0.0, None, ALU.max))
            dve.wait_ge(a, 4)
            link(dve.tensor_tensor(x[:, :, :], x[:, :, :], y[:, :, :], ALU.add))
            link(dve.scalar_tensor_tensor(out=c["g"], in0=x[:, :, :], scalar=-1.0, in1=over(a_log[:, :]),
                                          op0=ALU.mult, op1=ALU.mult))
            dve.wait_ge(summed, 1)
            pairs = [(slice(0, P), slice(0, NBLK), 0), (slice(0, SAMP), slice(NBLK, NB), NBLK * NHB)]
            for rows, bl, at in pairs:
                w = (bl.stop - bl.start) * NHB
                G = ps[rows, 0, at:at + w].rearrange("p (b h) -> p b h", h=NHB)
                last = ps[rows, 1, at:at + w].rearrange("p (b h) -> p b h", h=NHB)
                link(dve.tensor_copy(c["G"][rows, bl], G))
                link(dve.tensor_copy(c["decay_S"][rows, bl], last))
                link(dve.tensor_tensor(c["decay_k"][rows, bl], c["decay_S"][rows, bl], c["G"][rows, bl],
                                       ALU.subtract))
            dve.wait_ge(a, 8)
            dve.scalar_tensor_tensor(out=c["neg_beta_eG"], in0=c["eG"], scalar=-1.0, in1=c["beta"],
                                     op0=ALU.mult, op1=ALU.mult).then_inc(v, 1)

        @block.scalar
        def _(act):
            n = [0]

            def link(ins):
                n[0] += 1
                ins.then_inc(a, 1)
                act.wait_ge(a, n[0])
            link(act.activation(c["beta"], ab[:, :, NHB:], ACT.Sigmoid))
            act.wait_ge(v, 2)
            link(act.activation(y[:, :, :], y[:, :, :], ACT.Exp))
            link(act.activation(y[:, :, :], y[:, :, :], ACT.Ln, bias=1.0))
            act.wait_ge(loaded, 64)
            link(act.activation(a_log[:, :], a_log[:, :], ACT.Exp))
            act.wait_ge(v, 11)
            link(act.activation(c["eG"][:, 0:NBLK], c["G"][:, 0:NBLK], ACT.Exp))
            link(act.activation(c["eG"][0:SAMP, NBLK:], c["G"][0:SAMP, NBLK:], ACT.Exp))
            two = coef[:, 0:NBLK, 3:5, :].rearrange("p b c h -> p b (c h)")
            link(act.activation(two, two, ACT.Exp))
            two = coef[0:SAMP, NBLK:, 3:5, :].rearrange("p b c h -> p b (c h)")
            link(act.activation(two, two, ACT.Exp))

        @block.tensor
        def _(pe):
            pe.wait_ge(v, 5)
            pe.wait_ge(loaded, 64)
            for n, m in enumerate((tri, same)):
                pe.matmul(ps[:, n, 0:NBLK * NHB].rearrange("p (b h) -> p b h", h=NHB), m[:, 0, :], c["g"][:, 0:NBLK],
                          start=True, stop=True)
                last = pe.matmul(ps[0:SAMP, n, NBLK * NHB:NB * NHB].unsqueeze(1), m[0:SAMP, 1, 0:SAMP],
                                 c["g"][0:SAMP, NBLK:], start=True, stop=True)
            last.then_inc(summed, 1)


def delta_prompt(nc, t, coef):
    NP2 = NBLK // 2
    with ExitStack() as ctx:
        sb = lambda name, shape, dt=F32: ctx.enter_context(nc.sbuf_tensor(name, shape, dt))
        pb = lambda name, shape: ctx.enter_context(nc.psum_tensor(name, shape, F32))
        sem = t["sem"]
        two = lambda name, shape: [sb(f"{name}{j}", shape) for j in range(2)]
        HW = [P, NHB, P]
        ident, ones, tri = sb("ident_d", [P, P]), sb("ones_d", [P, P]), sb("tri_d", [P, P])
        upper_big = sb("upper_big", [P, P])
        level0, level0_T = sb("level0", [P, P]), sb("level0_T", [P, P])
        levels = sb("levels", [P, len(LEVELS), P // 2])
        slots = lambda name, shape: [two(f"{name}_{s}_", shape) for s in range(2)]
        xq, xkv = slots("xq", HW), two("xkv", [P, 2 * NHB, P])
        sq = two("sq", [P, 2 * NHB, P])
        cf = slots("cf", [P, NCO, NHB])
        rn, t1, t2 = two("rn", [P, 2 * NHB]), two("rn_t1", [P, 2 * NHB]), two("rn_t2", [P, 2 * NHB])
        q_eG = slots("q_eG", [P, NHB])
        gU, E, EB, EQ = two("gU", HW), two("E", HW), two("EB", HW), two("EQ", HW)
        k_tok, k_T, k_dec, bv = two("k_tok", HW), slots("k_hT", HW), slots("k_dec", HW), slots("bv", HW)
        L, LT, AT = two("L", HW), two("LT", HW), slots("AT", HW)
        A = gU
        T, TT = EB, slots("TT", HW)
        Y = [two(f"Y{b}_", HW) for b in LEVELS[:-1]]
        Y.append(E)
        gathered = [[sq[j][:, 3 * n:3 * n + 3, :].rearrange("p a (b c) -> p (a b) c", b=2) for j in range(2)] for n in range(3)]
        T_low, TT_up, Y_low = gathered
        S = sb("S", HW)
        rv, vn, qs, o = sb("rv", HW), sb("vn", HW), sb("qs", HW), two("o_d", HW)
        ps = [[pb(f"ps_p{j}{b}", [P, 4, P]) for b in range(2)] for j in range(2)]
        pss = [[pb(f"ps_c{z}{b}", [P, 4, P]) for b in range(2)] for z in range(2)]
        loaded, zeroed = sem("d_const"), sem("d_zeroed")
        xq_in = [sem(f"xq_in{j}") for j in range(2)]
        xkv_in = [sem(f"xkv_in{j}") for j in range(2)]
        o_out = [sem(f"o_out{j}") for j in range(2)]
        s_out = sem("s_out")
        lv = range(len(LEVELS))
        PE1 = ["norms", "G_rows", "k_turned", "v_turned", "kh_turned", "gram_k", "gram_q", "L_turned", "A_turned"]
        for n in lv:
            PE1 += [f"LT{n}", f"TY{n}", f"YT{n}"] if n < lv[-1] else [f"LT{n}", f"YT{n}"]
        DV1 = ["coef", "gU", "rsum", "rel", "newton1", "newton2", "r", "r_q", "q_eG", "k_tok", "bv", "L", "A",
               "TT_pairs", "TT_init"]
        for n in lv:
            DV1 += [f"Y{n}", f"T{n}", f"TT{n}"] if n < lv[-1] else [f"Y{n}", f"TT{n}"]
        AC1 = ["ln", "rough", "E", "kh_T", "LT", "AT", "T_low", "TT_up", "Y_full"]
        PL1 = ["sq", "EB", "EQ", "T_pairs", "T_init", "k_dec"]
        pe1 = [Steps(sem(f"pe_prep{j}"), PE1) for j in range(2)]
        dv1 = [Steps(sem(f"dve_prep{j}"), DV1) for j in range(2)]
        ac1 = [Steps(sem(f"act_prep{j}"), AC1) for j in range(2)]
        pl1 = [Steps(sem(f"pool_prep{j}"), PL1) for j in range(2)]
        each = lambda names: [f"{n}{j}" for j in range(2) for n in names]
        pe2 = [Steps(sem(f"pe_scan{z}"), each(["kS", "qS", "Tr", "Av", "kv"])) for z in range(2)]
        dv2 = [Steps(sem(f"dve_scan{z}"), each(["rv", "S", "o"])) for z in range(2)]
        ac2 = [Steps(sem(f"act_scan{z}"), each(["qs", "vn"])) for z in range(2)]
        block = ctx.enter_context(nc.Block(name="delta_prompt"))
        H3 = [slice(0, 3), slice(3, 6)]

        def passes(eng, prep, scan):
            prep(0, 0, lambda piece: None)
            prep(1, 1, lambda piece: scan(0, 0, piece))
            with eng.Fori(0, NP2 // 2 - 1) as i:
                prep(2 * i + 2, 0, lambda piece: scan(2 * i + 1, 1, piece))
                prep(2 * i + 3, 1, lambda piece: scan(2 * i + 2, 0, piece))
            for piece in range(6):
                scan(NP2 - 1, 1, piece)

        @block.sync
        def _(sp):
            for dst, name in ((ident, "ident"), (ones, "ones"), (tri, "tri"), (upper_big, "upper_big"),
                              (level0, "level0"), (level0_T, "level0_T")):
                sp.dma_start(dst[:, :], t[name]).then_inc(loaded, 16)
            sp.dma_start(levels[:, :, :], t["levels"]).then_inc(loaded, 16)

            chunk = t["conv_d"][:, :, 0:SEQ].rearrange("a p (n c m) -> c p a n m", c=4, m=P)

            def load(p, s, i):
                for j in range(2):
                    src = chunk[2 * s + j, :, :, bass.ds(i, 1)].rearrange("p a n m -> p a (n m)")
                    for z in range(2):
                        pe2[z].wait_back(sp, f"qS{j}", p)
                    pe1[j].wait_last(sp, "v_turned", p)
                    sp.dma_start(xkv[j][:, :, :], src[:, NHB:]).then_inc(xkv_in[j], 16)
                    sp.dma_start(xq[s][j][:, :, :], src[:, 0:NHB]).then_inc(xq_in[j], 16)
            load(0, 0, 0)
            load(1, 1, 0)
            with sp.Fori(1, NP2 // 2) as i:
                load(2 * i, 0, i)
                load(2 * i + 1, 1, i)
            for z in range(2):
                dv2[z].wait(sp, "S1", NP2 - 1)
            sp.dma_start(t["gdn_p"].rearrange("h k v -> k h v"), S[:, :, :]).then_inc(s_out, 16)
            sp.wait_ge(s_out, 16)

        @block.gpsimd
        def _(pool):
            for y in Y[:-1]:
                for j in range(2):
                    pool.memset(y[j][:, :, :], 0.0).then_inc(zeroed, 1)
            pool.memset(S[:, :, :], 0.0).then_inc(zeroed, 1)

            def store(p):
                for j in range(2):
                    for z in range(2):
                        dv2[z].wait(pool, f"o{j}", p)
                    pool.dma_start(t["o_d"][bass.ds(2 * P * p + P * j, P), :], o[j][:, :, :].rearrange("p h v -> p (h v)")
                                   ).then_inc(o_out[j], 16)

            def prep(p, s, scan):
                for j in range(2):
                    pool.wait_ge(xq_in[j], 16 * (p + 1))
                    pe1[j].wait_last(pool, "YT0", p)
                    pool.wait_ge(xkv_in[j], 16 * (p + 1))
                    pool.tensor_tensor(sq[j][:, 0:NHB, :], xq[s][j][:, :, :], xq[s][j][:, :, :], ALU.mult)
                    pl1[j].done(pool.tensor_tensor(sq[j][:, NHB:, :], xkv[j][:, 0:NHB, :], xkv[j][:, 0:NHB, :], ALU.mult), "sq")
                if not (isinstance(p, int) and p < 2):
                    store(p - 2)
                for j in range(2):
                    ac1[j].wait(pool, "E", p)
                    pl1[j].done(pool.tensor_tensor(EB[j][:, :, :], E[j][:, :, :], bc(cf[s][j][:, 0, :], P), ALU.mult), "EB")
                    dv1[j].wait(pool, "r_q", p)
                    pl1[j].done(pool.tensor_tensor(EQ[j][:, :, :], E[j][:, :, :], bc(rn[j][:, 0:NHB], P), ALU.mult), "EQ")
                for j in range(2):
                    dv1[j].wait(pool, "L", p)
                    pl1[j].done(pool.tensor_tensor(T[j][:, :, :], L[j][:, :, :], heads2(level0), ALU.mult), "T_pairs")
                    pl1[j].wait(pool, "T_pairs", p)
                    pl1[j].done(pool.tensor_tensor(T[j][:, :, :], T[j][:, :, :], heads2(ident), ALU.add), "T_init")
                for j in range(2):
                    dv1[j].wait(pool, "k_tok", p)
                    for z in range(2):
                        pe2[z].wait_back(pool, f"kv{j}", p)
                    pl1[j].done(pool.tensor_tensor(k_dec[s][j][:, :, :], k_tok[j][:, :, :], bc(cf[s][j][:, 3, :], P), ALU.mult), "k_dec")
            passes(pool, prep, lambda p, s, piece: None)
            store(NP2 - 2)
            store(NP2 - 1)
            for j in range(2):
                pool.wait_ge(o_out[j], 16 * NP2)

        @block.tensor
        def _(pe):
            pe.wait_ge(loaded, 16 * 7)
            pe.wait_ge(zeroed, 2 * len(Y) - 1)

            def six(j, f):
                for h in range(NHB):
                    last = f(ps[j][h // 3][:, h % 3, :], h)
                return last

            def prep(p, s, scan):
                for j in range(2):
                    pl1[j].wait(pe, "sq", p)
                    dv1[j].wait_last(pe, f"TT{lv[-1]}", p)
                    for n in range(2 * NHB):
                        last = pe.matmul(ps[j][0][:, 0, n:n + 1], sq[j][:, n, :], ones[:, 0:1], start=True, stop=True)
                    pe1[j].done(last, "norms")
                    dv1[j].wait(pe, "gU", p)
                    dv2[j].wait_back(pe, "o1", p)
                    for z in range(2):
                        last = pe.matmul(pss[j][z][:, 0:3, :].rearrange("p h n -> p (h n)"), ones[:, :],
                                         gU[j][:, H3[z], :].rearrange("p h n -> p (h n)"), start=True, stop=True)
                    pe1[j].done(last, "G_rows")
                for j in range(2):
                    dv1[j].wait(pe, "rsum", p)
                    pe1[j].done(six(j, lambda out, h: pe.transpose(out, xkv[j][:, h, :], ident[:, :])), "k_turned")
                for j in range(2):
                    dv1[j].wait(pe, "rel", p)
                scan(0)
                for j in range(2):
                    dv1[j].wait(pe, "k_tok", p)
                    pe1[j].done(six(j, lambda out, h: pe.transpose(out, xkv[j][:, NHB + h, :], ident[:, :])), "v_turned")
                for j in range(2):
                    dv1[j].wait(pe, "bv", p)
                    pe1[j].done(six(j, lambda out, h: pe.transpose(out, k_tok[j][:, h, :], ident[:, :])), "kh_turned")
                for j in range(2):
                    ac1[j].wait(pe, "kh_T", p)
                    pe1[j].done(six(j, lambda out, h: pe.matmul(out, k_T[s][j][:, h, :], k_T[s][j][:, h, :], start=True, stop=True)), "gram_k")
                scan(1)
                for j in range(2):
                    dv1[j].wait(pe, "L", p)
                    pe1[j].done(six(j, lambda out, h: pe.matmul(out, xq[s][j][:, h, :], k_T[s][j][:, h, :], start=True, stop=True)), "gram_q")
                for j in range(2):
                    dv1[j].wait(pe, "A", p)
                    pe1[j].done(six(j, lambda out, h: pe.transpose(out, L[j][:, h, :], ident[:, :])), "L_turned")
                for j in range(2):
                    ac1[j].wait(pe, "LT", p)
                    pe1[j].done(six(j, lambda out, h: pe.transpose(out, A[j][:, h, :], ident[:, :])), "A_turned")
                scan(2)
                for n, b in enumerate(LEVELS):
                    def level(j, bank, lhs, rhs, name, rows=P):
                        for h in range(NHB):
                            out = bank[0:rows].rearrange("p a n -> p (a n)")[:, 64 * h:64 * (h + 1)]
                            if n:
                                out = runs(out, b)
                            last = pe.matmul(out, lhs[:, h, 0:rows], rhs(h), start=True, stop=True)
                        pe1[j].done(last, name)
                    for j in range(2):
                        if n == 0:
                            ac1[j].wait(pe, "T_low", p)
                            level(j, ps[j][0], LT[j], lambda h: T_low[j][:, h, :], f"LT{n}")
                        else:
                            dv1[j].wait(pe, f"TT{n - 1}", p)
                            level(j, ps[j][0], LT[j], lambda h: lower(T[j][:, h, :], b), f"LT{n}")
                    for j in range(2):
                        dv1[j].wait(pe, f"Y{n}", p)
                        if n < lv[-1]:
                            level(j, ps[j][1], TT[s][j], lambda h: Y_low[j][:, h, :] if n == 0 else
                                  lower(Y[n][j][:, h, :], b), f"TY{n}")
                        if n == 0:
                            ac1[j].wait(pe, "Y_full", p)
                        level(j, ps[j][0], Y[n][j], lambda h: TT_up[j][:, h, :] if n == 0 else
                              upper(TT[s][j][:, h, :], b), f"YT{n}",
                              P if n < lv[-1] else b)
                    if n % 2:
                        scan(3 + n // 2)

            def scan(p, s, piece):
                j, part = piece // 3, piece % 3

                def three(z, b, f):
                    for h in range(3 * z, 3 * z + 3):
                        last = f(pss[z][b][:, h % 3, :], h)
                    return last
                for z in range(2):
                    if part == 0:
                        if j == 0:
                            dv2[z].wait_last(pe, "o1", p)
                        else:
                            dv2[z].wait(pe, "o0", p)
                        pe2[z].done(three(z, 0, lambda out, h: pe.matmul(out, k_T[s][j][:, h, :], S[:, h, :], start=True, stop=True)), f"kS{j}")
                        pe2[z].done(three(z, 1, lambda out, h: pe.matmul(out, xq[s][j][:, h, :], S[:, h, :], start=True, stop=True)), f"qS{j}")
                    elif part == 1:
                        dv1[j].wait(pe, f"TT{lv[-1]}", p)
                        dv2[z].wait(pe, f"rv{j}", p)
                        pe2[z].done(three(z, 0, lambda out, h: pe.matmul(out, TT[s][j][:, h, :], rv[:, h, :], start=True, stop=True)), f"Tr{j}")
                    else:
                        ac2[z].wait(pe, f"vn{j}", p)
                        pe2[z].done(three(z, 1, lambda out, h: pe.matmul(out, AT[s][j][:, h, :], vn[:, h, :], start=True, stop=True)), f"Av{j}")
                        pl1[j].wait(pe, "k_dec", p)
                        pe2[z].done(three(z, 0, lambda out, h: pe.matmul(out, k_dec[s][j][:, h, :], vn[:, h, :], start=True, stop=True)), f"kv{j}")

            passes(pe, prep, scan)

        @block.vector
        def _(dve):
            dve.wait_ge(loaded, 16 * 7)
            dve.wait_ge(zeroed, 2 * len(Y) - 1)

            def both(j, f):
                for z in range(2):
                    last = f(ps[j][z][:, 0:3, :], H3[z])
                return last

            def prep(p, s, scan):
                for j in range(2):
                    C, R = cf[s][j], rn[j]
                    for z in range(2):
                        dv2[z].wait_back(dve, f"S{j}", p)
                    dv1[j].wait_last(dve, f"TT{lv[-1]}", p)
                    pl1[j].wait_last(dve, "k_dec", p)
                    dv1[j].done(dve.tensor_copy(C[:, :, :].rearrange("p c h -> p (c h)").unsqueeze(1),
                                                coef[:, bass.ds(2 * p + j, 1), :, :].rearrange("p a c h -> p a (c h)")), "coef")
                    dv1[j].wait(dve, "coef", p)
                    pe1[j].wait_last(dve, "A_turned", p)
                    dv1[j].done(dve.tensor_tensor(gU[j][:, :, :], heads2(tri), bc(C[:, 6, :], P), ALU.mult), "gU")
                    pe1[j].wait(dve, "norms", p)
                    ac1[j].wait_last(dve, "rough", p)
                    dv1[j].done(dve.tensor_scalar(t1[j][:, :], ps[j][0][:, 0, 0:2 * NHB], RMS_EPS, None, ALU.add), "rsum")
                for j in range(2):
                    pe1[j].wait(dve, "G_rows", p)
                    for h in range(NHB):
                        last = dve.scalar_tensor_tensor(out=E[j][:, h, :], in0=pss[j][h // 3][:, h % 3, :],
                                                        scalar=cf[s][j][:, 5, h:h + 1], in1=upper_big[:, :],
                                                        op0=ALU.subtract, op1=ALU.max)
                    dv1[j].done(last, "rel")
                for j in range(2):
                    R = rn[j]
                    ac1[j].wait(dve, "rough", p)
                    dv1[j].done(dve.tensor_tensor(t2[j][:, :], R[:, :], R[:, :], ALU.mult), "newton1")
                    dv1[j].wait(dve, "newton1", p)
                    dv1[j].done(dve.scalar_tensor_tensor(out=t2[j][:, :], in0=t1[j][:, :], scalar=-0.5, in1=t2[j][:, :],
                                                         op0=ALU.mult, op1=ALU.mult), "newton2")
                    dv1[j].wait(dve, "newton2", p)
                    dv1[j].done(dve.scalar_tensor_tensor(out=R[:, :], in0=t2[j][:, :], scalar=1.5, in1=R[:, :],
                                                         op0=ALU.add, op1=ALU.mult), "r")
                    dv1[j].wait(dve, "r", p)
                    dv1[j].done(dve.tensor_scalar(R[:, 0:NHB], R[:, 0:NHB], DB ** -0.5, None, ALU.mult), "r_q")
                    dv1[j].wait(dve, "r_q", p)
                    dv1[j].done(dve.tensor_tensor(q_eG[s][j][:, :], R[:, 0:NHB], cf[s][j][:, 2, :], ALU.mult), "q_eG")
                for j in range(2):
                    pe1[j].wait(dve, "k_turned", p)
                    dv1[j].done(both(j, lambda p, h: dve.tensor_tensor(k_tok[j][:, h, :], p, bc(rn[j][:, NHB:][:, h], P), ALU.mult)), "k_tok")
                scan(0)
                for j in range(2):
                    pe1[j].wait(dve, "v_turned", p)
                    dv1[j].done(both(j, lambda p, h: dve.tensor_tensor(bv[s][j][:, h, :], p, bc(cf[s][j][:, 0, h], P), ALU.mult)), "bv")
                for j in range(2):
                    pe1[j].wait(dve, "gram_k", p)
                    pl1[j].wait(dve, "EB", p)
                    dv1[j].done(both(j, lambda p, h: dve.tensor_tensor(L[j][:, h, :], p, EB[j][:, h, :], ALU.mult)), "L")
                for j in range(2):
                    pe1[j].wait(dve, "gram_q", p)
                    pl1[j].wait(dve, "EQ", p)
                    dv1[j].done(both(j, lambda p, h: dve.tensor_tensor(A[j][:, h, :], p, EQ[j][:, h, :], ALU.mult)), "A")
                for j in range(2):
                    ac1[j].wait(dve, "LT", p)
                    dv1[j].done(dve.tensor_tensor(TT[s][j][:, :, :], LT[j][:, :, :], heads2(level0_T), ALU.mult), "TT_pairs")
                    dv1[j].wait(dve, "TT_pairs", p)
                    dv1[j].done(dve.tensor_tensor(TT[s][j][:, :, :], TT[s][j][:, :, :], heads2(ident), ALU.add), "TT_init")
                scan(2)
                for n, b in enumerate(LEVELS):
                    got = lambda bank: bank[:, 0:3, :].rearrange("p a n -> p (a n)").rearrange("p (h n b) -> p h n b", h=NHB, b=b)
                    mask = heads(levels[:, n, :].rearrange("p (n b) -> p n b", b=b))
                    for j in range(2):
                        pe1[j].wait(dve, f"LT{n}", p)
                        y = Y_low[j].rearrange("p h (n b) -> p h n b", b=b) if n == 0 else lower(Y[n][j][:, :, :], b)
                        dv1[j].done(dve.tensor_tensor(y, got(ps[j][0]), mask, ALU.mult), f"Y{n}")
                    for j in range(2):
                        if n < lv[-1]:
                            pe1[j].wait(dve, f"TY{n}", p)
                            v = lower(T[j][:, :, :], b)
                            dv1[j].done(dve.tensor_tensor(v, v, got(ps[j][1]), ALU.subtract), f"T{n}")
                        pe1[j].wait(dve, f"YT{n}", p)
                        r = P if n < lv[-1] else b
                        v = upper(TT[s][j][0:r, :, :], b)
                        dv1[j].done(dve.tensor_tensor(v, v, got(ps[j][0][0:r]), ALU.subtract), f"TT{n}")
                    if n % 2:
                        scan(3 + n // 2)

            def scan(p, s, piece):
                j, part = piece // 3, piece % 3
                for z in range(2):
                    if part == 0:
                        pe2[z].wait(dve, f"kS{j}", p)
                        for h in range(3 * z, 3 * z + 3):
                            last = dve.scalar_tensor_tensor(out=rv[:, h, :], in0=pss[z][0][:, h % 3, :],
                                                            scalar=cf[s][j][:, 1, h:h + 1], in1=bv[s][j][:, h, :],
                                                            op0=ALU.mult, op1=ALU.add)
                        dv2[z].done(last, f"rv{j}")
                    elif part == 2:
                        pe2[z].wait(dve, f"kv{j}", p)
                        for h in range(3 * z, 3 * z + 3):
                            last = dve.scalar_tensor_tensor(out=S[:, h, :], in0=S[:, h, :], scalar=cf[s][j][:, 4, h:h + 1],
                                                            in1=pss[z][0][:, h % 3, :], op0=ALU.mult, op1=ALU.add)
                        dv2[z].done(last, f"S{j}")
                        pe2[z].wait(dve, f"Av{j}", p)
                        if not (isinstance(p, int) and p == 0):
                            dve.wait_ge(o_out[j], 16 * p)
                        dv2[z].done(dve.tensor_tensor(o[j][:, H3[z], :], pss[z][1][:, 0:3, :], qs[:, H3[z], :], ALU.add), f"o{j}")

            passes(dve, prep, scan)

        @block.scalar
        def _(act):
            def turn(j, dst, name, src, p):
                pe1[j].wait(act, src, p)
                for z in range(2):
                    last = act.activation(dst[:, H3[z], :], ps[j][z][:, 0:3, :], ACT.Copy)
                ac1[j].done(last, name)

            def prep(p, s, scan):
                for j in range(2):
                    dv1[j].wait(act, "rsum", p)
                    pl1[j].wait_last(act, "EQ", p)
                    ac1[j].done(act.activation(rn[j][:, :], t1[j][:, :], ACT.Ln), "ln")
                for j in range(2):
                    ac1[j].wait(act, "ln", p)
                    ac1[j].done(act.activation(rn[j][:, :], rn[j][:, :], ACT.Exp, scale=-0.5), "rough")
                for j in range(2):
                    dv1[j].wait(act, "rel", p)
                    ac1[j].done(act.activation(E[j][:, :, :], E[j][:, :, :], ACT.Exp, scale=-1.0), "E")
                scan(0)
                for j in range(2):
                    for z in range(2):
                        pe2[z].wait_back(act, f"kS{j}", p)
                    turn(j, k_T[s][j], "kh_T", "kh_turned", p)
                scan(1)
                for j in range(2):
                    turn(j, LT[j], "LT", "L_turned", p)
                for j in range(2):
                    for z in range(2):
                        pe2[z].wait_back(act, f"Av{j}", p)
                    turn(j, AT[s][j], "AT", "A_turned", p)
                b = LEVELS[0]
                split = lambda x: x.rearrange("p h (n b) -> p h n b", b=b)
                for j in range(2):
                    pl1[j].wait(act, "T_init", p)
                    ac1[j].done(act.activation(split(T_low[j]), lower(T[j][:, :, :], b), ACT.Copy), "T_low")
                    dv1[j].wait(act, "TT_init", p)
                    ac1[j].done(act.activation(split(TT_up[j]), upper(TT[s][j][:, :, :], b), ACT.Copy), "TT_up")
                for j in range(2):
                    dv1[j].wait(act, "Y0", p)
                    ac1[j].done(act.activation(lower(Y[0][j][:, :, :], b), split(Y_low[j]), ACT.Copy), "Y_full")
                scan(3)
                scan(4)

            def scan(p, s, piece):
                j, part = piece // 3, piece % 3
                for z in range(2):
                    if part == 0:
                        pe2[z].wait(act, f"qS{j}", p)
                        for h in range(3 * z, 3 * z + 3):
                            last = act.activation(qs[:, h, :], pss[z][1][:, h % 3, :], ACT.Copy, scale=q_eG[s][j][:, h:h + 1])
                        ac2[z].done(last, f"qs{j}")
                    elif part == 1:
                        pe2[z].wait(act, f"Tr{j}", p)
                        ac2[z].done(act.activation(vn[:, H3[z], :], pss[z][0][:, 0:3, :], ACT.Copy), f"vn{j}")

            passes(act, prep, scan)


def heads2(x):
    return x[:, :].unsqueeze(1).broadcast_to([P, NHB, P])


def delta_samples(nc, t, coef):
    with ExitStack() as ctx:
        sb = lambda name, shape, dt=F32: ctx.enter_context(nc.sbuf_tensor(name, shape, dt))
        pb = lambda name, shape: ctx.enter_context(nc.psum_tensor(name, shape, F32))
        sem = t["sem"]
        R = SAMP
        ident, ones = sb("ident_e", [P, P]), sb("ones_e", [P, P])
        tri, limit = sb("tri_e", [P, 2, P]), sb("limit_e", [P, P])
        level0, level0_T, levels = sb("level0_e", [P, P]), sb("level0_T_e", [P, P]), sb("levels_e", [P, len(LEVELS), P // 2])
        of_seq, in_seq = sb("of_seq", [P, NSEQ, R]), sb("in_seq", [P, NSEQ])
        x = sb("x_e", [P, T_CONV, R])
        sq = sb("sq_e", [P, 2 * NHB, R])
        st = sb("state_e", [P, NHB, NSEQ, P])
        rn, t1, t2, q_eG = sb("rn_e", [R, 2 * NHB]), sb("t1_e", [R, 2 * NHB]), sb("t2_e", [R, 2 * NHB]), sb("q_eG_e", [R, NHB])
        gs, decay = sb("gs", [R, NHB, NSEQ]), sb("decay_e", [P, NHB, NSEQ])
        gU, E, L, A = sb("gU_e", [R, NHB, R]), sb("E_e", [R, NHB, R]), sb("L_e", [R, NHB, R]), sb("A_e", [R, NHB, R])
        EB, EQ = sb("EB_e", [R, NHB, R]), sb("EQ_e", [R, NHB, R])
        LT, AT, T, TT = sb("LT_e", [R, NHB, R]), sb("AT_e", [R, NHB, R]), sb("T_e", [R, NHB, R]), sb("TT_e", [R, NHB, R])
        LV = [2, 4]
        Y = [sb(f"Y{b}_e", [R, NHB, R]) for b in LV]
        k_tok, bv, k_dec, k_T = sb("k_tok_e", [R, NHB, P]), sb("bv_e", [R, NHB, P]), sb("k_dec_e", [R, NHB, P]), sb("k_T_e", [P, NHB, R])
        k_seq, q_seq = sb("k_seq", [P, NHB, NSEQ, R]), sb("q_seq", [P, NHB, NSEQ, R])
        rv, vn, qs, o = sb("rv_e", [R, NHB, P]), sb("vn_e", [R, NHB, P]), sb("qs_e", [R, NHB, P]), sb("o_e", [R, NHB, P])
        v_seq = sb("v_seq", [R, 2, NSEQ, P])
        bank = [pb(f"ps_e{b}", [P, 512]) for b in range(8)]
        loaded, out = sem("e_loaded"), sem("e_out")
        D_, A_, T_ = ["zero0", "zero1", "sq", "gs", "gU", "rsum", "n1", "n2", "r", "rq", "q_eG", "decay", "rel", "k_tok", "bv", "EB", "EQ",
                      "k_dec", "L", "A", "T_pairs", "T_init", "TT_pairs", "TT_init", "Y0", "T0", "TT0", "Y1", "T1", "TT1", "k_seq",
                      "q_seq", "rv", "o", "vs0"] + [f"{n}{h + (n == 'vs')}" for h in range(NHB) for n in ("vs", "st") if h < NHB - 1 or n == "st"], \
            ["ln", "rough", "decay", "E", "k_T", "LT", "AT", "qs", "vn"], \
            ["norms", "decay", "G_rows", "k", "v", "k_T", "gk", "gq", "LT", "AT", "LT0", "TY0", "YT0", "LT1", "TY1", "YT1",
             "kS", "qS", "Tr", "Av"] + [f"kv{h}" for h in range(NHB)]
        dv, ac, pe_ = Steps(sem("e_dve"), D_), Steps(sem("e_act"), A_), Steps(sem("e_pe"), T_)
        block = ctx.enter_context(nc.Block(name="delta_samples"))
        c = {n: coef[0:R, NBLK, k, :] for k, n in enumerate(COEF)}
        six = lambda x: x.unsqueeze(1).broadcast_to([x.shape[0], NHB] + list(x.shape[1:]))
        sixty = lambda b, n=R: bank[b][0:n, 0:NHB * R].rearrange("p (h n) -> p h n", n=R)
        wide = lambda z: bank[z][0:R, 0:3 * P].rearrange("p (h n) -> p h n", n=P)
        H3 = [slice(0, 3), slice(3, 6)]

        @block.sync
        def _(sp):
            for dst, src in ((ident, "ident"), (ones, "ones"), (limit, "limit"), (level0, "level0"), (level0_T, "level0_T")):
                sp.dma_start(dst[:, :], t[src]).then_inc(loaded, 16)
            for dst, src in ((tri, "tri_incl"), (levels, "levels"), (of_seq, "of_seq")):
                sp.dma_start(dst[:, :, :], t[src]).then_inc(loaded, 16)
            sp.dma_start(in_seq[:, :], t["in_seq"]).then_inc(loaded, 16)
            sp.dma_start(x[:, :, :], t["conv_d"][:, :, SEQ:].rearrange("a p n -> p a n")).then_inc(loaded, 16)
            for s in range(NSEQ):
                sp.dma_start(st[:, :, s, :], t["state_gdn"][s].rearrange("h k v -> k h v")).then_inc(loaded, 16)
            dv.wait(sp, "o")
            sp.dma_start(t["o_d"][SEQ:], o[:, :, :].rearrange("p h v -> p (h v)")).then_inc(out, 16)
            dv.wait(sp, f"st{NHB - 1}")
            for s in range(NSEQ):
                sp.dma_start(t["gdn_s"][s].rearrange("h k v -> k h v"), st[:, :, s, :]).then_inc(out, 16)
            sp.wait_ge(out, 16 * (NSEQ + 1))

        @block.tensor
        def _(pe):
            pe.wait_ge(loaded, 16 * (10 + NSEQ))

            def per_head(b, rows, f, n=R):
                for h in range(NHB):
                    last = f(bank[b][0:rows, n * h:n * (h + 1)], h)
                return last

            def halves3(z0, f):
                for h in range(NHB):
                    last = f(bank[z0 + h // 3][0:R, P * (h % 3):P * (h % 3 + 1)], h)
                return last
            mm = lambda out, a, b: pe.matmul(out, a, b, start=True, stop=True)
            dv.wait(pe, "sq")
            for n in range(2 * NHB):
                last = mm(bank[0][0:R, n:n + 1], sq[:, n, :], ones[:, 0:1])
            pe_.done(last, "norms")
            dv.wait(pe, "gs")
            pe_.done(mm(bank[1][:, 0:NHB * NSEQ], ones[0:R, :], gs[:, :, :].rearrange("p h s -> p (h s)")), "decay")
            dv.wait(pe, "gU")
            pe_.done(mm(bank[2][0:R, 0:NHB * R], ones[0:R, 0:R], gU[:, :, :].rearrange("p h n -> p (h n)")), "G_rows")
            pe_.done(halves3(4, lambda out, h: pe.transpose(out, x[:, NHB + h, :], ident[:, :])), "k")
            pe_.done(halves3(6, lambda out, h: pe.transpose(out, x[:, 2 * NHB + h, :], ident[:, :])), "v")
            dv.wait(pe, "k_tok")
            pe_.done(per_head(0, P, lambda out, h: pe.transpose(out, k_tok[:, h, :], ident[0:R, 0:R])), "k_T")
            ac.wait(pe, "k_T")
            dv.wait(pe, "rel")
            pe_.done(per_head(1, R, lambda out, h: mm(out, k_T[:, h, :], k_T[:, h, :])), "gk")
            pe_.done(per_head(2, R, lambda out, h: mm(out, x[:, h, :], k_T[:, h, :])), "gq")
            dv.wait(pe, "L")
            pe_.done(per_head(3, R, lambda out, h: pe.transpose(out, L[:, h, :], ident[0:R, 0:R])), "LT")
            dv.wait(pe, "A")
            pe_.done(per_head(0, R, lambda out, h: pe.transpose(out, A[:, h, :], ident[0:R, 0:R])), "AT")
            for n, b in enumerate(LV):
                cols = lambda bk: (lambda h: bank[bk][0:R, 32 * h:32 * (h + 1)].rearrange("p (n b) -> p n b", b=b))

                def level(bk, lhs, rhs, name):
                    for h in range(NHB):
                        last = mm(cols(bk)(h), lhs[:, h, :], rhs(h))
                    pe_.done(last, name)
                dv.wait(pe, f"TT{n - 1}" if n else "TT_init")
                level(1, LT, lambda h: lower(T[:, h, :], b), f"LT{n}")
                dv.wait(pe, f"Y{n}")
                level(2, TT, lambda h: lower(Y[n][:, h, :], b), f"TY{n}")
                level(1, Y[n], lambda h: upper(TT[:, h, :], b), f"YT{n}")
            for name, w, z0 in (("kS", k_seq, 4), ("qS", q_seq, 6)):
                dv.wait(pe, "k_seq" if w is k_seq else "q_seq")
                for h in range(NHB):
                    for s in range(NSEQ):
                        last = pe.matmul(bank[z0 + h // 3][0:R, P * (h % 3):P * (h % 3 + 1)], w[:, h, s, :], st[:, h, s, :],
                                         start=s == 0, stop=s == NSEQ - 1)
                pe_.done(last, name)
            dv.wait(pe, "rv")
            pe_.done(halves3(4, lambda out, h: mm(out, TT[:, h, :], rv[:, h, :])), "Tr")
            ac.wait(pe, "vn")
            pe_.done(halves3(6, lambda out, h: mm(out, AT[:, h, :], vn[:, h, :])), "Av")
            for h in range(NHB):
                if h >= 2:
                    dv.wait(pe, f"st{h - 2}")
                dv.wait(pe, f"vs{h}")
                for z in range(2):
                    last = mm(bank[2 * (h % 2) + z][:, :], k_dec[:, h, :],
                              v_seq[:, h % 2, 4 * z:4 * (z + 1), :].rearrange("p s v -> p (s v)"))
                pe_.done(last, f"kv{h}")

        @block.scalar
        def _(act):
            dv.wait(act, "rsum")
            ac.done(act.activation(rn[:, :], t1[:, :], ACT.Ln), "ln")
            ac.wait(act, "ln")
            ac.done(act.activation(rn[:, :], rn[:, :], ACT.Exp, scale=-0.5), "rough")
            dv.wait(act, "decay")
            ac.done(act.activation(decay[:, :, :], decay[:, :, :], ACT.Exp), "decay")
            dv.wait(act, "rel")
            ac.done(act.activation(E[:, :, :], E[:, :, :], ACT.Exp, scale=-1.0), "E")
            pe_.wait(act, "k_T")
            ac.done(act.activation(k_T[:, :, :], sixty(0, P), ACT.Copy), "k_T")
            pe_.wait(act, "LT")
            ac.done(act.activation(LT[:, :, :], sixty(3), ACT.Copy), "LT")
            pe_.wait(act, "AT")
            ac.done(act.activation(AT[:, :, :], sixty(0), ACT.Copy), "AT")
            pe_.wait(act, "qS")
            for h in range(NHB):
                last = act.activation(qs[:, h, :], wide(6 + h // 3)[:, h % 3, :], ACT.Copy, scale=q_eG[:, h:h + 1])
            ac.done(last, "qs")
            pe_.wait(act, "Tr")
            for z in range(2):
                last = act.activation(vn[:, H3[z], :], wide(4 + z), ACT.Copy)
            ac.done(last, "vn")

        @block.vector
        def _(dve):
            def do(ins, name):
                dv.done(ins, name)
                dv.wait(dve, name)
            tt, sts = dve.tensor_tensor, dve.scalar_tensor_tensor
            do(dve.memset(Y[0][:, :, :], 0.0), "zero0")
            do(dve.memset(Y[1][:, :, :], 0.0), "zero1")
            dve.wait_ge(loaded, 16 * (10 + NSEQ))
            do(tt(sq[:, :, :], x[:, 0:2 * NHB, :], x[:, 0:2 * NHB, :], ALU.mult), "sq")
            do(tt(gs[:, :, :], bc(c["g"], NSEQ), six(in_seq[0:R, :]), ALU.mult), "gs")
            do(tt(gU[:, :, :], six(tri[0:R, 1, 0:R]), bc(c["g"], R), ALU.mult), "gU")
            pe_.wait(dve, "norms")
            do(dve.tensor_scalar(t1[:, :], bank[0][0:R, 0:2 * NHB], RMS_EPS, None, ALU.add), "rsum")
            ac.wait(dve, "rough")
            do(tt(t2[:, :], rn[:, :], rn[:, :], ALU.mult), "n1")
            do(sts(out=t2[:, :], in0=t1[:, :], scalar=-0.5, in1=t2[:, :], op0=ALU.mult, op1=ALU.mult), "n2")
            do(sts(out=rn[:, :], in0=t2[:, :], scalar=1.5, in1=rn[:, :], op0=ALU.add, op1=ALU.mult), "r")
            do(dve.tensor_scalar(rn[:, 0:NHB], rn[:, 0:NHB], DB ** -0.5, None, ALU.mult), "rq")
            do(tt(q_eG[:, :], rn[:, 0:NHB], c["eG"], ALU.mult), "q_eG")
            pe_.wait(dve, "decay")
            do(dve.tensor_copy(decay[:, :, :], bank[1][:, 0:NHB * NSEQ].rearrange("p (h s) -> p h s", s=NSEQ)), "decay")
            pe_.wait(dve, "G_rows")
            for h in range(NHB):
                last = sts(out=E[:, h, :], in0=sixty(2)[:, h, :], scalar=c["G"][:, h:h + 1], in1=limit[0:R, 0:R],
                           op0=ALU.subtract, op1=ALU.max)
            do(last, "rel")
            pe_.wait(dve, "k")
            for z in range(2):
                last = tt(k_tok[:, H3[z], :], wide(4 + z), bc(rn[:, NHB:][:, H3[z]], P), ALU.mult)
            do(last, "k_tok")
            pe_.wait(dve, "v")
            for z in range(2):
                last = tt(bv[:, H3[z], :], wide(6 + z), bc(c["beta"][:, H3[z]], P), ALU.mult)
            do(last, "bv")
            ac.wait(dve, "E")
            do(tt(EB[:, :, :], E[:, :, :], bc(c["beta"], R), ALU.mult), "EB")
            do(tt(EQ[:, :, :], E[:, :, :], bc(rn[:, 0:NHB], R), ALU.mult), "EQ")
            do(tt(k_dec[:, :, :], k_tok[:, :, :], bc(c["decay_k"], P), ALU.mult), "k_dec")
            pe_.wait(dve, "gk")
            do(tt(L[:, :, :], sixty(1), EB[:, :, :], ALU.mult), "L")
            pe_.wait(dve, "gq")
            do(tt(A[:, :, :], sixty(2), EQ[:, :, :], ALU.mult), "A")
            do(tt(T[:, :, :], L[:, :, :], six(level0[0:R, 0:R]), ALU.mult), "T_pairs")
            do(tt(T[:, :, :], T[:, :, :], six(ident[0:R, 0:R]), ALU.add), "T_init")
            ac.wait(dve, "LT")
            do(tt(TT[:, :, :], LT[:, :, :], six(level0_T[0:R, 0:R]), ALU.mult), "TT_pairs")
            do(tt(TT[:, :, :], TT[:, :, :], six(ident[0:R, 0:R]), ALU.add), "TT_init")
            for n, b in enumerate(LV):
                got = lambda bk: bank[bk][0:R, 0:NHB * 32].rearrange("p (h n b) -> p h n b", h=NHB, b=b)
                pe_.wait(dve, f"LT{n}")
                do(tt(lower(Y[n][:, :, :], b), got(1), six(levels[0:R, n, 0:32].rearrange("p (n b) -> p n b", b=b)), ALU.mult), f"Y{n}")
                pe_.wait(dve, f"TY{n}")
                do(tt(lower(T[:, :, :], b), lower(T[:, :, :], b), got(2), ALU.subtract), f"T{n}")
                pe_.wait(dve, f"YT{n}")
                do(tt(upper(TT[:, :, :], b), upper(TT[:, :, :], b), got(1), ALU.subtract), f"TT{n}")
            ac.wait(dve, "k_T")
            over_s = lambda a: a.unsqueeze(1).broadcast_to([P, NSEQ, R])
            for h in range(NHB):
                last = tt(k_seq[:, h], over_s(k_T[:, h, :]), of_seq[:, :, :], ALU.mult)
            do(last, "k_seq")
            for h in range(NHB):
                last = tt(q_seq[:, h], over_s(x[:, h, :]), of_seq[:, :, :], ALU.mult)
            do(last, "q_seq")
            pe_.wait(dve, "kS")
            for h in range(NHB):
                last = sts(out=rv[:, h, :], in0=wide(4 + h // 3)[:, h % 3, :], scalar=c["neg_beta_eG"][:, h:h + 1],
                           in1=bv[:, h, :], op0=ALU.mult, op1=ALU.add)
            do(last, "rv")
            pe_.wait(dve, "Av")
            for z in range(2):
                last = tt(o[:, H3[z], :], wide(6 + z), qs[:, H3[z], :], ALU.add)
            do(last, "o")

            def spread(h):
                if h >= 2:
                    pe_.wait(dve, f"kv{h - 2}")
                do(tt(v_seq[:, h % 2], vn[:, h, :].unsqueeze(1).broadcast_to([R, NSEQ, P]), bc(in_seq[0:R, :], P), ALU.mult), f"vs{h}")
            spread(0)
            for h in range(NHB):
                if h + 1 < NHB:
                    spread(h + 1)
                pe_.wait(dve, f"kv{h}")
                for s in range(NSEQ):
                    last = sts(out=st[:, h, s, :], in0=st[:, h, s, :], scalar=decay[:, h, s:s + 1],
                               in1=bank[2 * (h % 2) + s // 4][:, P * (s % 4):P * (s % 4 + 1)], op0=ALU.mult, op1=ALU.add)
                do(last, f"st{h}")


SUP = 256
NSUP = SEQ // SUP
KA = WA // P
FEW = T_ZA + T_ZB


RAW = 4
RING_M = 4


def split_weights(act, src, total, tiles, w_raw, w_hi, wr_in, w_hi_done, w_lo_done):
    def load(k):
        act.dma_start(w_raw[:, k % RAW, :], src[P * k:P * (k + 1), :]).then_inc(wr_in[k % RAW], 16)
    if 0 in tiles:
        for k in range(RAW - 1):
            load(k)
    for k in tiles:
        if k + RAW - 1 < total:
            if k:
                act.wait_ge(w_lo_done, k)
            load(k + RAW - 1)
        act.wait_ge(wr_in[k % RAW], 16 * (k // RAW + 1))
        act.activation(w_hi[:, k, :], w_raw[:, k % RAW, :], ACT.Copy).then_inc(w_hi_done, 1)


def merge_branches(nc, t):
    with ExitStack() as ctx:
        sb = lambda name, shape, dt=F32: ctx.enter_context(nc.sbuf_tensor(name, shape, dt))
        pb = lambda name, shape: ctx.enter_context(nc.psum_tensor(name, shape, F32))
        sem = t["sem"]
        w_hi, w_lo = sb("wab_hi", [P, 2 * KA, D], F32R), sb("wab_lo", [P, 2 * KA, D], F32R)
        u_hi, u_lo = sb("u_hi", [P, 2, FEW, SUP], F32R), sb("u_lo", [P, 2, FEW, SUP], F32R)
        w_raw = sb("wab_raw", [P, RAW, D])
        ident, norm = sb("ident_f", [P, P]), sb("norm_f", [P, 1])
        rows2 = sb("rows_f", [P, 2, 2 * KA, P])
        stat2 = sb("stat_f", [P, 2, NG, NSTAT])
        z = sb("z_f", [P, FEW, P])
        gated = sb("gated", [P, FEW, P])
        least, share, total = sb("least", [P, HPG]), sb("share", [P, NG, HPG]), sb("total", [P, HPG])
        wd = sb("wd", [P, NG, HPG])
        ss, root, rs = sb("ss", [P, NHB]), sb("root", [P, NHB]), sb("rs", [P, NHB])
        sqs = gated[:, T_ZA:, :]
        gates = sb("gates", [P, RING_M, 2, SUP])
        prod = sb("prod", [P, 2, 2, SUP])
        merged = sb("merged", [P, 2, SUP])
        ps_t = [pb(f"ps_ft{b}", [P, 4, P]) for b in range(3)]
        ps_m = [pb(f"ps_fm{b}", [P, 2, SUP]) for b in range(RING_M)]
        const_in = sem("f_const")
        wr_in = [sem(f"f_wr_in{j}") for j in range(RAW)]
        w_hi_done, w_lo_done = sem("f_w_hi"), sem("f_w_lo")
        row_in = [sem(f"f_rows{j}") for j in range(2)]
        z_in, gate_in = sem("f_z"), [sem(f"f_gate{j}") for j in range(RING_M)]
        d_steps = Steps(sem("f_dve"), ["least", "diff", "wd", "total", "rtotal", "share", "att", "ss", "eps", "rs", "o"]
                        + [f"g{b}" for b in range(3)] + ["split"])
        a_steps = Steps(sem("f_act"), ["share", "squares", "root", "hi"])
        p_steps = Steps(sem("f_pe"), [f"turn{b}" for b in range(3)])
        mm_done, prod_done, sum_done = sem("f_mm"), sem("f_prod"), sem("f_sum")
        out = [sem(f"f_out{j}") for j in range(2)]
        NF = D // P
        s_rows = rows2[0:SAMP].rearrange("p s a n -> p s (a n)")[:, :, 0:D]
        s_gates = gates[:, :, :, :].rearrange("p r s n -> p (r s n)")[:, 0:2 * D // P * SAMP].rearrange("p (s n) -> p s n", s=2)
        s_prod = prod[:, :, :, :].rearrange("p a s n -> p (a s n)").rearrange("p (s n) -> p s n", s=2)
        s_merged = merged[:, :, :].rearrange("p a n -> p (a n)")
        flat = lambda bank: bank[:, :, :].rearrange("p a n -> p (a n)")
        s_mm, s_put, s_turned, s_gate_in, s_prod_done, s_sum = (sem(f"f_s_{n}") for n in ("mm", "put", "turned", "gate", "prod", "sum"))
        block = ctx.enter_context(nc.Block(name="merge_branches"))

        def blocks(n):
            return [2 * n] if isinstance(n, int) and n == NSUP else [2 * n, 2 * n + 1]

        def flow(eng, part, mult, weights=lambda tiles: None):
            def step(nxt, now):
                for f in range(NF):
                    if f // 4 < len(blocks(nxt[0])):
                        part(*nxt, f // 4, f % 4)
                    mult(*now, f)
            for f in range(NF):
                weights(range(2 * KA * f // NF, 2 * KA * (f + 1) // NF))
                part(0, 0, f // 4, f % 4)
            step((1, 1), (0, 0))
            with eng.Fori(0, NSUP // 2 - 1) as i:
                step((2 * i + 2, 0), (2 * i + 1, 1))
                step((2 * i + 3, 1), (2 * i + 2, 0))
            step((NSUP, 0), (NSUP - 1, 1))
        zero = lambda n: isinstance(n, int) and n == 0
        rows_of = lambda n: SAMP if isinstance(n, int) and n == NSUP else P

        @block.sync
        def _(sp):
            sp.dma_start(ident[:, :], t["ident"]).then_inc(const_in, 16)
            sp.dma_start(norm[:, :], t["gdn_norm"].rearrange("(p a) -> p a", a=1)).then_inc(const_in, 16)

            def part(n, j, k, q):
                b, m = blocks(n)[k], rows_of(n)
                tok = bass.ds(P * b, P) if m == P else slice(SEQ, NT)
                if q == 0:
                    if not zero(n):
                        p_steps.wait(sp, "turn2", b - 2)
                    if m == P:
                        sp.dma_start(rows2[:, k, 0:KA, :].rearrange("p a n -> p (a n)"),
                                     t["att_d"][tok].rearrange("p g n -> p (g n)")).then_inc(row_in[k], 16)
                        sp.dma_start(stat2[:, k], t["stats_d"][tok]).then_inc(row_in[k], 16)
                    else:
                        d_steps.wait(sp, "split", b - 1)
                        sp.dma_start(gated[:, 0:T_ZA, 0:SAMP], t["att_s"]).then_inc(row_in[k], 16)
                        sp.dma_start(stat2[0:SAMP, k], t["stats_d"][0:SAMP]).then_inc(row_in[k], 16)
                    sp.dma_start(rows2[0:m, k, KA:, :].rearrange("p a n -> p (a n)"), t["o_d"][tok]).then_inc(row_in[k], 16)

            def mult(n, j, f):
                tok = bass.ds(SUP * n, SUP)
                if not (zero(n) and f < RING_M):
                    sp.wait_ge(prod_done, NF * n + f + 1 - RING_M)
                sp.dma_start(gates[:, f % RING_M, :, :], t["g_d"][f::NF, :, tok].rearrange("a p n -> p a n")
                             ).then_inc(gate_in[f % RING_M], 16)
            flow(sp, part, mult)
            sp.wait_ge(prod_done, NF * NSUP)
            sp.dma_start(s_gates.rearrange("p s (f n) -> p (s f) n", n=SAMP), t["g_d"][:, :, SEQ:].rearrange("a p n -> p a n")
                         ).then_inc(s_gate_in, 16)

        @block.tensor
        def _(pe):
            pe.wait_ge(const_in, 32)

            def part(n, j, k, q):
                if q != 2:
                    return
                b, m = blocks(n)[k], rows_of(n)
                for r in range(3):
                    if not (zero(n) and k == 0):
                        d_steps.wait(pe, f"g{r}", b - 1)
                    if r == 0:
                        d_steps.wait(pe, "o", b)
                    for a in range(4):
                        last = pe.transpose(ps_t[r][:, a, 0:m], rows2[0:m, k, 4 * r + a, :], ident[0:m, 0:m])
                    p_steps.done(last, f"turn{r}")

            def mult(n, j, f):
                if f == 0:
                    d_steps.wait(pe, "split", blocks(n)[-1])
                if not (zero(n) and f < RING_M):
                    pe.wait_ge(prod_done, NF * n + f + 1 - RING_M)
                for side in range(2):
                    for k in range(KA):
                        kk = KA * side + k
                        if zero(n) and f == 0:
                            pe.wait_ge(w_lo_done, kk + 1)
                        cols = slice(P * f, P * (f + 1))
                        last = mm3(pe, ps_m[f % RING_M][:, side, :], (w_hi[:, kk, cols], w_lo[:, kk, cols]),
                                   (u_hi[:, j, kk, :], u_lo[:, j, kk, :]), k == 0, k == KA - 1)
                last.then_inc(mm_done, 1)
            flow(pe, part, mult)
            d_steps.wait(pe, "split", 2 * NSUP)
            pe.wait_ge(prod_done, NF * NSUP)
            for side in range(2):
                for half in range(2):
                    for k in range(KA):
                        kk, cols = KA * side + k, slice(512 * half, 512 * (half + 1))
                        last = mm3(pe, flat(ps_m[2 * side + half])[0:SAMP], (u_hi[:, 0, kk, 0:SAMP], u_lo[:, 0, kk, 0:SAMP]),
                                   (w_hi[:, kk, cols], w_lo[:, kk, cols]), k == 0, k == KA - 1)
                last.then_inc(s_mm, 1)
            pe.wait_ge(s_put, 2)
            for side in range(2):
                for f in range(NF):
                    last = pe.transpose(flat(ps_t[side])[:, SAMP * f:SAMP * (f + 1)], s_rows[:, side, P * f:P * (f + 1)],
                                        ident[0:SAMP, 0:SAMP])
            last.then_inc(s_turned, 1)

        @block.vector
        def _(dve):
            dve.wait_ge(const_in, 32)
            tt, sts = dve.tensor_tensor, dve.scalar_tensor_tensor
            over_g = lambda x, m: x[0:m, :].unsqueeze(1).broadcast_to([m, NG, HPG])

            def part(n, j, k, q):
                b, m = blocks(n)[k], rows_of(n)
                rows, stat = rows2[:, k], stat2[:, k]

                def do(ins, name):
                    d_steps.done(ins, name)
                    d_steps.wait(dve, name, b)
                if q == 0:
                    dve.wait_ge(row_in[k], 48 * (n + 1))
                    do(dve.tensor_reduce(least[0:m, :], stat[0:m, :, 0:HPG].rearrange("p g h -> p h g"), AX.X, ALU.min), "least")
                    do(tt(share[0:m], over_g(least, m), stat[0:m, :, 0:HPG], ALU.subtract), "diff")
                    a_steps.wait(dve, "share", b)
                    do(tt(wd[0:m], share[0:m], stat[0:m, :, HPG:], ALU.mult), "wd")
                    do(dve.tensor_reduce(total[0:m, :], wd[0:m].rearrange("p g h -> p h g"), AX.X, ALU.add), "total")
                    do(dve.reciprocal(total[0:m, :], total[0:m, :]), "rtotal")
                    do(tt(share[0:m], share[0:m], over_g(total, m), ALU.mult), "share")
                    att = rows[0:m, 0:KA, :].rearrange("p a n -> p (a n)").rearrange("p (g d) -> p g d", d=DH)
                    if m == P:
                        do(tt(att, att, bc(share[0:m].rearrange("p g h -> p (g h)"), DH), ALU.mult), "att")
                    else:
                        do(dve.memset(rows[0:m, 0:KA, :], 0.0), "att")
                elif q == 1:
                    a_steps.wait(dve, "squares", b)
                    do(dve.tensor_reduce(ss[0:m, :], sqs[0:m], AX.X, ALU.add), "ss")
                    do(dve.tensor_scalar(ss[0:m, :], ss[0:m, :], 1.0 / DB, RMS_EPS, ALU.mult, ALU.add), "eps")
                    a_steps.wait(dve, "root", b)
                    do(dve.reciprocal(rs[0:m, :], root[0:m, :]), "rs")
                    do(tt(rows[0:m, KA:, :], rows[0:m, KA:, :], bc(rs[0:m, :], P), ALU.mult), "o")
                elif q == 2:
                    dve.wait_ge(z_in, 16 * (b + 1))
                    for r in range(3):
                        p_steps.wait(dve, f"turn{r}", b)
                        cut = [(4 * r, 4 * r + 4)] if r != 1 else [(4, 6), (6, 8)]
                        for lo, hi in cut:
                            src = ps_t[r][:, lo - 4 * r:hi - 4 * r, 0:m]
                            if hi <= KA and m < P:
                                ins = tt(gated[:, lo:hi, 0:m], gated[:, lo:hi, 0:m], z[:, lo:hi, 0:m], ALU.mult)
                            elif hi <= KA:
                                ins = tt(gated[:, lo:hi, 0:m], src, z[:, lo:hi, 0:m], ALU.mult)
                            else:
                                ins = sts(out=gated[:, lo:hi, 0:m], in0=src, scalar=norm[:, 0:1], in1=z[:, lo:hi, 0:m],
                                          op0=ALU.mult, op1=ALU.mult)
                        do(ins, f"g{r}")
                else:
                    a_steps.wait(dve, "hi", b)
                    at = slice(P * k, P * k + m)
                    do(tt(u_lo[:, j, :, at], gated[:, :, 0:m], f32(u_hi[:, j, :, at]), ALU.subtract), "split")

            def mult(n, j, f):
                u = NF * n + f
                dve.wait_ge(mm_done, u + 1)
                dve.wait_ge(gate_in[f % RING_M], 16 * (NF // RING_M * n + f // RING_M + 1))
                dve.tensor_tensor(prod[:, f % 2, :, :], ps_m[f % RING_M][:, :, :], gates[:, f % RING_M, :, :],
                                  ALU.mult).then_inc(prod_done, 1)
                dve.wait_ge(prod_done, u + 1)
                if not (zero(n) and f < 2):
                    dve.wait_ge(out[f % 2], 16 * (NF // 2 * n + f // 2))
                dve.tensor_tensor(merged[:, f % 2, :], prod[:, f % 2, 0, :], prod[:, f % 2, 1, :],
                                  ALU.add).then_inc(sum_done, 1)
            def weights(tiles):
                for k in tiles:
                    dve.wait_ge(w_hi_done, k + 1)
                    dve.tensor_tensor(w_lo[:, k, :], w_raw[:, k % RAW, :], f32(w_hi[:, k, :]), ALU.subtract).then_inc(w_lo_done, 1)
            flow(dve, part, mult, weights)
            dve.wait_ge(s_mm, 2)
            for half in range(2):
                last = dve.tensor_copy(s_rows[:, 1, 512 * half:512 * (half + 1)], flat(ps_m[2 + half])[0:SAMP])
            last.then_inc(s_put, 1)
            dve.wait_ge(s_turned, 1)
            dve.wait_ge(s_gate_in, 16)
            for side in range(2):
                last = tt(s_prod[:, side, :], flat(ps_t[side]), s_gates[:, side, :], ALU.mult)
            last.then_inc(s_prod_done, 1)
            dve.wait_ge(s_prod_done, 1)
            for j in range(2):
                dve.wait_ge(out[j], 16 * (NF // 2) * NSUP)
            tt(s_merged, s_prod[:, 0, :], s_prod[:, 1, :], ALU.add).then_inc(s_sum, 1)

        @block.scalar
        def _(act):
            def part(n, j, k, q):
                b, m = blocks(n)[k], rows_of(n)
                if q == 0:
                    tok = bass.ds(P * b, P) if m == P else slice(SEQ, NT)
                    act.dma_start(z[:, :, 0:m], t["z_d"][:, :, tok].rearrange("a p n -> p a n")).then_inc(z_in, 16)
                    act.wait_ge(row_in[k], 48 * (n + 1))
                    d_steps.wait(act, "diff", b)
                    a_steps.done(act.activation(share[0:m], share[0:m], ACT.Exp), "share")
                    a_steps.done(act.activation(sqs[0:m], rows2[0:m, k, KA:, :], ACT.Square), "squares")
                elif q == 1:
                    d_steps.wait(act, "eps", b)
                    a_steps.done(act.activation(root[0:m, :], ss[0:m, :], ACT.Sqrt), "root")
                elif q == 2:
                    d_steps.wait(act, "g2", b)
                    if not (isinstance(n, int) and n < 2):
                        act.wait_ge(mm_done, NF * (n - 1))
                    a_steps.done(act.activation(u_hi[:, j, :, P * k:P * k + m], gated[:, :, 0:m], ACT.Copy), "hi")
            flow(act, part, lambda n, j, f: None,
                 lambda tiles: split_weights(act, t["w_out"], 2 * KA, tiles, w_raw, w_hi, wr_in, w_hi_done, w_lo_done))
            act.wait_ge(s_mm, 1)
            for half in range(2):
                last = act.activation(s_rows[:, 0, 512 * half:512 * (half + 1)], flat(ps_m[half])[0:SAMP], ACT.Copy)
            last.then_inc(s_put, 1)

        @block.gpsimd
        def _(pool):
            def mult(n, j, f):
                tok = bass.ds(SUP * n, SUP)
                pool.wait_ge(sum_done, NF * n + f + 1)
                pool.dma_start(t["merged_d"][f, :, tok], merged[:, f % 2, :]).then_inc(out[f % 2], 16)
            flow(pool, lambda n, j, k, q: None, mult)
            pool.wait_ge(s_sum, 1)
            pool.dma_start(t["merged_d"][:, :, SEQ:].rearrange("f p n -> p f n"), s_merged.rearrange("p (f n) -> p f n", n=SAMP)
                           ).then_inc(out[0], 16)
            for j in range(2):
                pool.wait_ge(out[j], 16 * ((NF // 2) * NSUP + (j == 0)))


def finish(nc, t):
    with ExitStack() as ctx:
        sb = lambda name, shape, dt=F32: ctx.enter_context(nc.sbuf_tensor(name, shape, dt))
        pb = lambda name, shape: ctx.enter_context(nc.psum_tensor(name, shape, F32))
        sem = t["sem"]
        w_hi, w_lo, w_raw = sb("wo_hi", [P, KT, D], F32R), sb("wo_lo", [P, KT, D], F32R), sb("wo_raw", [P, RAW, D])
        m_raw = sb("m_raw", [P, 2, KT, P])
        m_hi, m_lo = sb("m_hi", [P, 2, KT, P], F32R), sb("m_lo", [P, 2, KT, P], F32R)
        x = sb("x_res", [P, 2, D])
        gate_p, gate_s = sb("gate_p", [P, D]), sb("gate_s", [SAMP, D])
        ln_g, ln_b = sb("ln_g", [P, D]), sb("ln_b", [P, D])
        y = sb("y_res", [P, 2, D])
        junk = sb("ln_junk", [P, D])
        total, mean, ssq = sb("ln_total", [P, 1]), sb("ln_mean", [P, 1]), sb("ln_ssq", [P, 1])
        var, root, rstd, shift = sb("ln_var", [P, 1]), sb("ln_root", [P, 1]), sb("ln_rstd", [P, 1]), sb("ln_shift", [P, 1])
        ps = [pb(f"ps_out{j}", [P, 2, 512]) for j in range(2)]
        const_in, w_hi_done, w_lo_done = sem("o_const"), sem("o_w_hi"), sem("o_w_lo")
        wr_in = [sem(f"o_wr_in{j}") for j in range(RAW)]
        m_in = [sem(f"o_m_in{j}") for j in range(2)]
        x_in = [sem(f"o_x_in{j}") for j in range(2)]
        out = [sem(f"o_out_{j}") for j in range(2)]
        mm_done = [sem(f"o_mm{j}") for j in range(2)]
        d_steps = Steps(sem("o_dve"), ["gated", "sum", "mean", "var", "rstd", "shift", "scaled", "y"])
        split_done = [sem(f"o_split{j}") for j in range(2)]
        hi_done = [sem(f"o_hi{j}") for j in range(2)]
        a_steps = Steps(sem("o_act"), ["total", "squares", "root", "norm"])
        block = ctx.enter_context(nc.Block(name="finish"))
        NB = NBLK + 1

        @block.sync
        def _(sp):
            sp.dma_start(gate_p[:, :], t["gate_d"][0].partition_broadcast(P)).then_inc(const_in, 16)
            for s in range(NSEQ):
                sp.dma_start(gate_s[TS * s:TS * (s + 1), :], t["gate_d"][1 + s].partition_broadcast(TS)).then_inc(const_in, 16)
            sp.dma_start(ln_g[:, :], t["ln_g"].partition_broadcast(P)).then_inc(const_in, 16)
            sp.dma_start(ln_b[:, :], t["ln_b"].partition_broadcast(P)).then_inc(const_in, 16)

            def body(i, j):
                if not (isinstance(i, int) and i == 0):
                    sp.wait_ge(split_done[j], i)
                m = SAMP if isinstance(i, int) and i == NBLK // 2 else P
                tok = slice(SEQ, NT) if m < P else bass.ds(2 * P * i + P * j, P)
                sp.dma_start(m_raw[:, j, :, 0:m], t["merged_d"][:, :, tok].rearrange("a p n -> p a n")).then_inc(m_in[j], 16)
                if not (isinstance(i, int) and i == 0):
                    d_steps.wait(sp, "sum", 2 * i + j - 2)
                sp.dma_start(x[0:m, j, :], t["x_rows"][tok]).then_inc(x_in[j], 16)
            body(0, 0)
            body(0, 1)
            with sp.Fori(1, NBLK // 2) as i:
                body(i, 0)
                body(i, 1)
            body(NBLK // 2, 0)

        @block.scalar
        def _(act):
            split_weights(act, t["w_o"], KT, range(KT), w_raw, w_hi, wr_in, w_hi_done, w_lo_done)

            def split(i, j, m=P):
                act.wait_ge(m_in[j], 16 * (i + 1))
                if not (isinstance(i, int) and i == 0):
                    act.wait_ge(mm_done[j], i)
                act.activation(m_hi[:, j, :, 0:m], m_raw[:, j, :, 0:m], ACT.Copy).then_inc(hi_done[j], 1)

            def rest(i, j, m=P):
                b = 2 * i + j
                d_steps.wait(act, "sum", b)
                a_steps.done(act.activation(junk[0:m], y[0:m, j, :], ACT.Copy, accum_out=total[0:m]), "total")
                d_steps.wait(act, "mean", b)
                a_steps.done(act.activation(junk[0:m], y[0:m, j, :], ACT.Square, bias=mean[0:m], accum_out=ssq[0:m]), "squares")
                d_steps.wait(act, "var", b)
                a_steps.done(act.activation(root[0:m], var[0:m], ACT.Sqrt), "root")
                d_steps.wait(act, "shift", b)
                a_steps.done(act.activation(y[0:m, j, :], y[0:m, j, :], ACT.Identity, bias=shift[0:m], scale=rstd[0:m]), "norm")
            split(0, 0)
            split(0, 1), rest(0, 0)
            split(1, 0), rest(0, 1)
            with act.Fori(1, NBLK // 2 - 1) as i:
                split(i, 1), rest(i, 0)
                split(i + 1, 0), rest(i, 1)
            i = NBLK // 2 - 1
            split(i, 1), rest(i, 0)
            split(i + 1, 0, SAMP), rest(i, 1)
            rest(i + 1, 0, SAMP)

        @block.vector
        def _(dve):
            for k in range(KT):
                dve.wait_ge(w_hi_done, k + 1)
                dve.tensor_tensor(w_lo[:, k, :], w_raw[:, k % RAW, :], f32(w_hi[:, k, :]), ALU.subtract).then_inc(w_lo_done, 1)
            dve.wait_ge(const_in, 16 * (3 + NSEQ))

            def split(i, j, m=P):
                dve.wait_ge(hi_done[j], i + 1)
                dve.tensor_tensor(m_lo[:, j, :, 0:m], m_raw[:, j, :, 0:m], f32(m_hi[:, j, :, 0:m]), ALU.subtract).then_inc(split_done[j], 1)

            def rest(i, j, m=P):
                b = 2 * i + j

                def do(ins, name):
                    d_steps.done(ins, name)
                    d_steps.wait(dve, name, b)
                yj = y[0:m, j, :]
                dve.wait_ge(mm_done[j], i + 1)
                if not (isinstance(i, int) and i == 0):
                    dve.wait_ge(out[j], 16 * i)
                do(dve.tensor_tensor(yj, ps[j][0:m].rearrange("p a n -> p (a n)"), (gate_p if m == P else gate_s)[0:m, :], ALU.mult), "gated")
                dve.wait_ge(x_in[j], 16 * (i + 1))
                do(dve.scalar_tensor_tensor(out=yj, in0=x[0:m, j, :], scalar=ALPHA, in1=yj, op0=ALU.mult, op1=ALU.add), "sum")
                a_steps.wait(dve, "total", b)
                do(dve.tensor_scalar(mean[0:m], total[0:m], -1.0 / D, None, ALU.mult), "mean")
                a_steps.wait(dve, "squares", b)
                do(dve.tensor_scalar(var[0:m], ssq[0:m], 1.0 / D, LN_EPS, ALU.mult, ALU.add), "var")
                a_steps.wait(dve, "root", b)
                do(dve.reciprocal(rstd[0:m], root[0:m]), "rstd")
                do(dve.tensor_tensor(shift[0:m], mean[0:m], rstd[0:m], ALU.mult), "shift")
                a_steps.wait(dve, "norm", b)
                do(dve.tensor_tensor(yj, yj, ln_g[0:m, :], ALU.mult), "scaled")
                d_steps.done(dve.tensor_tensor(yj, yj, ln_b[0:m, :], ALU.add), "y")
            split(0, 0)
            split(0, 1), rest(0, 0)
            split(1, 0), rest(0, 1)
            with dve.Fori(1, NBLK // 2 - 1) as i:
                split(i, 1), rest(i, 0)
                split(i + 1, 0), rest(i, 1)
            i = NBLK // 2 - 1
            split(i, 1), rest(i, 0)
            split(i + 1, 0, SAMP), rest(i, 1)
            rest(i + 1, 0, SAMP)

        @block.tensor
        def _(pe):
            def body(i, j, m=P):
                pe.wait_ge(split_done[j], i + 1)
                if not (isinstance(i, int) and i == 0):
                    d_steps.wait(pe, "gated", 2 * i + j - 2)
                for h in range(2):
                    for k in range(KT):
                        cols = slice(512 * h, 512 * (h + 1))
                        if isinstance(i, int) and i == 0 and j == 0 and h == 0:
                            pe.wait_ge(w_lo_done, k + 1)
                        last = mm3(pe, ps[j][:, h, :], (m_hi[:, j, k, :], m_lo[:, j, k, :]),
                                   (w_hi[:, k, cols], w_lo[:, k, cols]), k == 0, k == KT - 1)
                last.then_inc(mm_done[j], 1)
            body(0, 0), body(0, 1)
            with pe.Fori(1, NBLK // 2) as i:
                body(i, 0), body(i, 1)
            body(NBLK // 2, 0)

        @block.gpsimd
        def _(pool):
            def body(i, j, m=P):
                d_steps.wait(pool, "y", 2 * i + j)
                tok = slice(SEQ, NT) if m < P else bass.ds(2 * P * i + P * j, P)
                pool.dma_start(t["y_rows"][tok], y[0:m, j, :]).then_inc(out[j], 16)
            with pool.Fori(0, NBLK // 2) as i:
                body(i, 0), body(i, 1)
            body(NBLK // 2, 0, SAMP)
            pool.wait_ge(out[0], 16 * (NBLK // 2 + 1))
            pool.wait_ge(out[1], 16 * (NBLK // 2))
def layouts(x_prompt, x_sample, c_prompt, c_sample, state_conv, w_ada, b_ada, w_in, conv_w, **_):
    A = np.ascontiguousarray
    x = np.concatenate([x_prompt[0], x_sample.reshape(SAMP, D)])
    w = w_in[0]
    q, k, v, z, c, zb, a, b, g = np.split(w, np.cumsum([WA, WA, WA, WA, CONV, WB, NHB, NHB]), axis=1)
    tiles = lambda m: m.reshape(KT, P, -1, P).transpose(2, 1, 0, 3).reshape(-1, P, KT * P)
    val = np.zeros((NG, P, KT, VW), np.float32)
    for n in range(NG):
        val[n, :, :, :GW] = v[:, n * GW:(n + 1) * GW].reshape(KT, P, GW).transpose(1, 0, 2)
    val[0, :, :, GW:] = np.concatenate([a, b], 1).reshape(KT, P, NAB).transpose(1, 0, 2)
    side = np.concatenate([conv_w[0].reshape(TAPS, T_CONV, P).transpose(1, 2, 0),
                           state_conv[0].reshape(NSEQ, TAPS - 1, T_CONV, P).transpose(2, 3, 0, 1)
                           .reshape(T_CONV, P, -1)], 2)
    return dict(
        x_T=A(x.reshape(NT, KT, P).transpose(2, 1, 0)), x_rows=x,
        c_T=A(np.concatenate([c_prompt, c_sample]).reshape(NC, KT, P).transpose(2, 1, 0)),
        b_ss=A(b_ada[0, :2 * D].reshape(2 * KT, P).T), b_gate=A(b_ada[0, 2 * D:]),
        w_ada=w_ada[0], w_feat=A(np.concatenate([tiles(m) for m in (c, q, k, z, zb, g)])),
        w_val=val, conv_side=A(side))


def tables():
    f = np.float32
    heads = NG * HPG
    slopes = np.exp2(f(-8.0) * np.arange(1, heads + 1, dtype=f) / f(heads)).astype(f).reshape(NG, HPG)
    steps = P + np.arange(P)[:, None] - np.arange(2 * P)[None, :]
    bias = np.full((P, NG, HPG, 2 * P), MASKED, f)
    for g, (_, dil) in enumerate(GROUPS):
        for h in range(HPG):
            bias[:, g, h] = np.where((steps >= 0) & (steps <= P), -slopes[g, h] * (steps * dil).astype(f), f(MASKED))
    bs = np.full((2, HALF, HPG, TS, KEYS), MASKED, f)
    tok = np.arange(TS)
    at = [0, P + NEWC, P + NEWC + KEPT[1]]
    for g, (_, dil) in enumerate(GROUPS):
        dist = PAST[g] + tok[:, None] - np.array(SEEN[g])[None, :]
        seen = (dist % dil == 0) & (dist <= P * dil)
        new = tok[:, None] - tok[None, :]
        new_seen = (new >= 0) & (new % dil == 0)
        for h in range(HPG):
            bs[:, :, h, :, at[g]:at[g] + KEPT[g]] = np.where(seen, -slopes[g, h] * dist.astype(f), f(MASKED))
            for a in range(2):
                for s in range(HALF):
                    c = P + SAMP * g + TS * (HALF * a + s)
                    bs[a, s, h, :, c:c + TS] = np.where(new_seen, -slopes[g, h] * new.astype(f), f(MASKED))
    i, j = np.arange(P)[:, None], np.arange(P)[None, :]
    seq = (i // TS == j // TS)
    one = np.ones((P, P), f)
    pair = lambda b: ((i // (2 * b) == j // (2 * b)) & (i // b % 2 == 1) & (j // b % 2 == 0)).astype(f)
    low = lambda m, b: m.reshape(P, -1, 2, b)[:, :, 0, :].reshape(P, P // 2)
    tri = (i <= j).astype(f)
    more = dict(ones=one, tri=tri, tri_incl=np.stack([tri, tri * seq], 1), same=np.stack([one, one * seq], 1),
                upper_big=np.where(j > i, f(BIG), f(0)), level0=-pair(1), level0_T=np.ascontiguousarray(-pair(1).T),
                limit=np.where((j > i) | ~seq, f(BIG), f(0)),
                of_seq=np.tile((np.arange(NSEQ)[:, None] == np.arange(SAMP) // TS).astype(f), (P, 1, 1)),
                in_seq=(np.arange(P)[:, None] // TS == np.arange(NSEQ)).astype(f),
                levels=np.stack([low(pair(b), b) for b in LEVELS], 1))
    return dict(**more, bias_prompt=bias / f(DH ** -0.5), bias_samples=bs.reshape(2, P, KEYS).transpose(1, 0, 2).copy(), ident=np.eye(P, dtype=f))


def caches(cache_win1, cache_win2, cache_win3, **_):
    c = np.concatenate([x[0][:, p] for x, p in zip((cache_win1, cache_win2, cache_win3), SEEN)], axis=1)
    k = c[:, :, 0].reshape(NSEQ, CACHED, NP_, PAIR).transpose(0, 3, 2, 1)
    v = c[:, :, 1].reshape(NSEQ, KT_C, P, GW).transpose(0, 2, 1, 3)
    return dict(k_cache=np.ascontiguousarray(k), v_cache=np.ascontiguousarray(v))


def program(nc, t):
    with ExitStack() as ctx:
        sb = lambda name, shape, dt=F32: ctx.enter_context(nc.sbuf_tensor(name, shape, dt))
        taken = []

        def sem(name):
            taken.append(nc.alloc_semaphore(name=name))
            return taken[-1]
        t = dict(t, sem=sem)
        coef = sb("coef", [P, NBLK + 1, len(COEF), NHB])
        ab = sb("ab", [P, NBLK + 1, NAB])
        with nc.Block(name="clear") as block:
            @block.vector
            def _(dve):
                dve.memset(coef[:, :, :, :], 0.0)
                dve.memset(ab[:, :, :], 0.0)
        with ExitStack() as inner:
            h_hi = inner.enter_context(nc.sbuf_tensor("h_hi", [P, KT, NT], F32R))
            h_lo = inner.enter_context(nc.sbuf_tensor("h_lo", [P, KT, NT], F32R))
            modulate(nc, t, h_hi, h_lo)
            project_features(nc, t, h_hi, h_lo)
            project_values(nc, t, h_hi, h_lo, ab)
        nc.clear_and_free_semaphores(taken)
        nc.all_engine_barrier()
        attend_prompt(nc, t)
        attend_samples(nc, t)
        decay_coefficients(nc, t, ab, coef)
        delta_prompt(nc, t, coef)
        delta_samples(nc, t, coef)
        merge_branches(nc, t)
        finish(nc, t)


_SCRATCH = dict(gate_d=(NC, D), conv_d=(T_CONV, P, NT), q_d=(T_Q, P, NT), z_d=(T_ZA + T_ZB, P, NT), g_d=(T_G, P, NT),
                att_d=(SEQ, NG, GW), stats_d=(SEQ, NG, NSTAT), att_s=(P, NPT, SAMP), o_d=(NT, WB), merged_d=(KT, P, NT))
_OUTS = dict(y_rows=(NT, D), k_T=(T_K, P, NT), v_out=(NG, NBLK, P, GW), v_new=(NG, SAMP, GW),
             conv_tail=(T_CONV, P, U_W - U_SAMP + U_PRE), gdn_p=(NHB, P, P), gdn_s=(NSEQ, NHB, P, P))


def kernel(**inputs):
    import concourse.bacc as _bacc
    from concourse.bass_utils import run_bass_kernel_spmd as _run

    inputs = {k: np.asarray(v) for k, v in inputs.items()}
    arrays = {**layouts(**inputs), **caches(**inputs), **tables()}
    for name in ("dt_bias", "a_log", "gdn_norm", "w_o", "ln_g", "ln_b", "state_gdn"):
        arrays[name] = inputs[name][0]
    arrays["w_out"] = np.concatenate([inputs["w_out_a"][0], inputs["w_out_b"][0]])
    nc = _bacc.Bacc("TRN2", target_bir_lowering=False, num_devices=1)
    sent, t = {}, {}
    for name, a in arrays.items():
        a = np.ascontiguousarray(a)
        sent[f"in_{name}"] = a
        t[name] = nc.dram_tensor(f"in_{name}", a.shape, F32, kind="ExternalInput").ap()
    for name, shape in _SCRATCH.items():
        t[name] = nc.dram_tensor(f"scratch_{name}", shape, F32).ap()
    for name, shape in _OUTS.items():
        t[name] = nc.dram_tensor(f"out_{name}", shape, F32, kind="ExternalOutput").ap()
    program(nc, t)
    r = _run(nc, [sent], core_ids=[0]).results[0]
    o = {name: np.asarray(r[f"out_{name}"]) for name in _OUTS}

    y = o["y_rows"]
    k = o["k_T"].reshape(NG, GW, NT).transpose(0, 2, 1)
    v = np.empty((NG, NT, GW), np.float32)
    for g, (a, b, s) in enumerate(BLOCKS):
        for n in range(NBLK):
            start = a * (n // 4) + b * (n % 4)
            v[g, start:start + s * P:s][:P] = o["v_out"][g, n]
        v[g, SEQ:] = o["v_new"][g]
    kv = np.stack([k, v], axis=2).reshape(NG, NT, 2, HPG, DH)
    win_p = [kv[g, SEQ - min(w, SEQ):SEQ][None, None] for g, (w, _) in enumerate(GROUPS)]
    win_s = [kv[g, SEQ:].reshape(1, NSEQ, TS, 2, HPG, DH) for g in range(NG)]
    tail = o["conv_tail"]
    conv_p = tail[:, :, 0:U_PRE].transpose(2, 0, 1).reshape(1, 1, U_PRE, CONV)
    conv_s = tail[:, :, U_PRE:].reshape(T_CONV, P, NSEQ, EXT)[..., TS:].transpose(2, 3, 0, 1).reshape(1, NSEQ, U_PRE, CONV)
    out = (y[:SEQ][None], y[SEQ:].reshape(NSEQ, TS, D), *win_p, o["gdn_p"][None, None], conv_p,
           *win_s, o["gdn_s"][None], conv_s)
    return tuple(np.ascontiguousarray(x) for x in out)
```
